# Optimizing a Trainium2 kernel written in Bass

```python
import jax, jax.numpy as jnp
from jax import lax
import numpy as np

D_MODEL = 1024
BATCH = 1
SEQ = 1024
DEPTH = 1
DEC_BATCH = 8
DEC_SEQ = 4
PAST_LEN = 8192
PAGE_SIZE = 128

MLA_HEADS = 8
Q_LORA = 384
KV_LORA = 256
QK_NOPE = 64
QK_ROPE = 32
V_DIM = 64
MLA_DIM = KV_LORA + QK_ROPE
MLA_SCALE = (QK_NOPE + QK_ROPE) ** -0.5
DIL_GROUPS = ((128, 1), (512, 4), (2048, 16))
N_DIL_GROUPS = 3
DIL_HEADS = 4
DIL_DIM = 64
ROT_DIM = DIL_DIM // 4
DIL_SCALE = DIL_DIM ** -0.5
DIL_QKV = 3 * N_DIL_GROUPS * DIL_HEADS * DIL_DIM
MEM_LEN = 256
MEM_HEADS = 4
MEM_DIM = 128
MEM_SCALE = MEM_DIM ** -0.5
N_BRANCHES = 3
IN_COLS = Q_LORA + KV_LORA + QK_ROPE + DIL_QKV + MEM_HEADS * MEM_DIM + N_BRANCHES * D_MODEL
PEER_HEADS = 8
N_KEYS = 128
N_EXPERTS = N_KEYS * N_KEYS
PEER_QDIM = 256
PEER_TOPK = 16
PEER_BLOCK = 128
ROPE_THETA = 500000.0
EPS = 1e-6
Q_BLOCK = 128
NEG_INF = -1e30

kernel_name = 'hybrid_mla_dilated_peer_decode_step'

def rmsnorm(x, g):
    xf = x.astype(jnp.float32)
    y = xf * lax.rsqrt(jnp.mean(xf * xf, axis=-1, keepdims=True) + EPS)
    return (y * g.astype(jnp.float32)).astype(x.dtype)

def rope(x, pos):
    r = x.shape[-1]
    half = r // 2
    inv = ROPE_THETA ** (-jnp.arange(half, dtype=jnp.float32) * (2.0 / r))
    ang = pos.astype(jnp.float32)[:, None] * inv[None, :]
    shp = (ang.shape[0],) + (1,) * (x.ndim - 3) + (half,)
    cos = jnp.cos(ang).reshape(shp)
    sin = jnp.sin(ang).reshape(shp)
    xf = x.astype(jnp.float32)
    x1, x2 = xf[..., :half], xf[..., half:]
    return jnp.concatenate([x1 * cos - x2 * sin, x2 * cos + x1 * sin], axis=-1).astype(x.dtype)

def partial_rope(x, pos):
    return jnp.concatenate([rope(x[..., :ROT_DIM], pos), x[..., ROT_DIM:]], axis=-1)

def split_points():
    sizes = (Q_LORA, KV_LORA, QK_ROPE, DIL_QKV, MEM_HEADS * MEM_DIM)
    pts, acc = [], 0
    for s in sizes:
        acc += s
        pts.append(acc)
    return pts

def mixer_project(x, pos, w_in, g_attn, g_q_lora, w_q_up, g_kv_lora):
    B, S, _ = x.shape
    proj = rmsnorm(x, g_attn) @ w_in
    c_q, c_kv, k_pe, dil, mem_q, gates = jnp.split(proj, split_points(), axis=-1)
    q = (rmsnorm(c_q, g_q_lora) @ w_q_up).reshape(B, S, MLA_HEADS, QK_NOPE + QK_ROPE)
    q_mla = jnp.concatenate([q[..., :QK_NOPE], rope(q[..., QK_NOPE:], pos)], axis=-1)
    row_mla = jnp.concatenate([rmsnorm(c_kv, g_kv_lora), rope(k_pe[:, :, None, :], pos)[:, :, 0]], axis=-1)
    dil = dil.reshape(B, S, 3, N_DIL_GROUPS, DIL_HEADS, DIL_DIM)
    q_d = partial_rope(dil[:, :, 0], pos)
    k_d = partial_rope(dil[:, :, 1], pos)
    v_d = dil[:, :, 2]
    q_mem = mem_q.reshape(B, S, MEM_HEADS, MEM_DIM)
    gates = jax.nn.sigmoid(gates.reshape(B, S, N_BRANCHES, D_MODEL))
    return q_mla, row_mla, q_d, k_d, v_d, q_mem, gates

def mla_prompt(q, row, w_uk, w_uv):
    B, S, H, _ = q.shape
    ckv = row[..., :KV_LORA]
    k = jnp.concatenate([jnp.einsum('bsc,chn->bshn', ckv, w_uk),
                         jnp.broadcast_to(row[:, :, None, KV_LORA:], (B, S, H, QK_ROPE))], axis=-1)
    v = jnp.einsum('bsc,chv->bshv', ckv, w_uv)
    nb = S // Q_BLOCK
    qb = q.reshape(B, nb, Q_BLOCK, H, QK_NOPE + QK_ROPE).transpose(1, 0, 2, 3, 4)
    kpos = jnp.arange(S)

    def block(args):
        qi, bi = args
        s = jnp.einsum('bqhe,bkhe->bhqk', qi, k).astype(jnp.float32) * MLA_SCALE
        qpos = bi * Q_BLOCK + jnp.arange(Q_BLOCK)
        s = jnp.where(kpos[None, :] <= qpos[:, None], s, NEG_INF)
        p = jax.nn.softmax(s, axis=-1)
        return jnp.einsum('bhqk,bkhe->bqhe', p.astype(v.dtype), v)

    o = lax.map(block, (qb, jnp.arange(nb)))
    return o.transpose(1, 0, 2, 3, 4).reshape(B, S, H, V_DIM)

def mla_sample(q, row_new, cache, page_table, w_uk, w_uv):
    T = q.shape[1]
    q_cat = jnp.concatenate([jnp.einsum('bthn,chn->bthc', q[..., :QK_NOPE], w_uk), q[..., QK_NOPE:]], axis=-1)

    def one(args):
        qs, rn, pt = args
        past = cache[pt].reshape(-1, MLA_DIM)
        P = past.shape[0]
        keys = jnp.concatenate([past, rn], axis=0)
        s = jnp.einsum('thc,kc->htk', qs, keys).astype(jnp.float32) * MLA_SCALE
        allowed = jnp.arange(P + T)[None, :] <= P + jnp.arange(T)[:, None]
        s = jnp.where(allowed, s, NEG_INF)
        p = jax.nn.softmax(s, axis=-1)
        return jnp.einsum('htk,kc->thc', p.astype(keys.dtype), keys[:, :KV_LORA])

    lat = lax.map(one, (q_cat, row_new, page_table))
    return jnp.einsum('bthc,chv->bthv', lat, w_uv)

def dilated_prompt(q, k, v, window, dil):
    B, S, H, E = q.shape
    n = S // dil
    wr = window // dil
    nb = -(-n // wr)
    pad = nb * wr - n

    def by_residue(t):
        return t.reshape(B, n, dil, H, E).transpose(0, 2, 1, 3, 4)

    qr = jnp.pad(by_residue(q), ((0, 0), (0, 0), (0, pad), (0, 0), (0, 0)))
    kr = jnp.pad(by_residue(k), ((0, 0), (0, 0), (wr, pad), (0, 0), (0, 0)))
    vr = jnp.pad(by_residue(v), ((0, 0), (0, 0), (wr, pad), (0, 0), (0, 0)))
    qb = qr.reshape(B, dil, nb, wr, H, E)
    kb = kr.reshape(B, dil, nb + 1, wr, H, E)
    vb = vr.reshape(B, dil, nb + 1, wr, H, E)
    kband = jnp.concatenate([kb[:, :, :-1], kb[:, :, 1:]], axis=3)
    vband = jnp.concatenate([vb[:, :, :-1], vb[:, :, 1:]], axis=3)
    s = jnp.einsum('brnqhe,brnkhe->brnhqk', qb, kband).astype(jnp.float32) * DIL_SCALE
    qi = jnp.arange(wr)[:, None]
    kk = jnp.arange(2 * wr)[None, :]
    dist = qi + wr - kk
    kidx = jnp.arange(nb)[:, None, None] * wr - wr + kk[None]
    mask = (dist >= 0) & (dist <= wr) & (kidx >= 0)
    s = jnp.where(mask[:, None], s, NEG_INF)
    lse = jax.nn.logsumexp(s, axis=-1)
    p = jnp.exp(s - lse[..., None])
    o = jnp.einsum('brnhqk,brnkhe->brnqhe', p.astype(v.dtype), vband)
    o = o.reshape(B, dil, nb * wr, H, E)[:, :, :n].transpose(0, 2, 1, 3, 4).reshape(B, S, H, E)
    lse = lse.transpose(0, 1, 2, 4, 3).reshape(B, dil, nb * wr, H)[:, :, :n]
    lse = lse.transpose(0, 2, 1, 3).reshape(B, S, H)
    return o, lse

def dilated_sample(q, k_all, v_all, window, dil):
    T = q.shape[1]
    L = k_all.shape[1] - T
    wr = window // dil
    idx = L + jnp.arange(T)[:, None] - dil * jnp.arange(wr + 1)[None, :]
    valid = idx >= 0
    idx = jnp.maximum(idx, 0)
    kg = k_all[:, idx]
    vg = v_all[:, idx]
    s = jnp.einsum('bthe,btkhe->bhtk', q, kg).astype(jnp.float32) * DIL_SCALE
    s = jnp.where(valid[None, None], s, NEG_INF)
    lse = jax.nn.logsumexp(s, axis=-1)
    p = jnp.exp(s - lse[..., None])
    o = jnp.einsum('bhtk,btkhe->bthe', p.astype(v_all.dtype), vg)
    return o, lse.transpose(0, 2, 1)

def combine_dilations(outs, lses):
    w = jax.nn.softmax(jnp.stack(lses, axis=0), axis=0)
    o = jnp.sum(w[..., None] * jnp.stack(outs, axis=0).astype(jnp.float32), axis=0)
    return o.astype(outs[0].dtype)

def mem_attend(q, mem_kv):
    s = jnp.einsum('bshe,bmhe->bhsm', q, mem_kv[:, :, 0]).astype(jnp.float32) * MEM_SCALE
    p = jax.nn.softmax(s, axis=-1)
    return jnp.einsum('bhsm,bmhe->bshe', p.astype(q.dtype), mem_kv[:, :, 1])

def mixer_merge(x, gates, o_mla, o_dil, o_mem, w_o_mla, w_o_dil, w_o_mem, w_out):
    B, S = x.shape[:2]
    y_mla = o_mla.reshape(B, S, -1) @ w_o_mla
    y_dil = o_dil.reshape(B, S, -1) @ w_o_dil
    y_mem = o_mem.reshape(B, S, -1) @ w_o_mem
    merged = gates[:, :, 0] * y_mla + gates[:, :, 1] * y_dil + gates[:, :, 2] * y_mem
    return x + merged @ w_out

def peer(x, w_pq, sub_keys, u_tab, v_tab):
    lead = x.shape[:-1]
    xf = x.reshape(-1, D_MODEL)
    n = xf.shape[0]
    nblk = -(-n // PEER_BLOCK)
    xp = jnp.pad(xf, ((0, nblk * PEER_BLOCK - n), (0, 0))).reshape(nblk, PEER_BLOCK, D_MODEL)

    def block(xb):
        q = (xb @ w_pq).reshape(PEER_BLOCK, PEER_HEADS, 2, PEER_QDIM // 2)
        s = jnp.einsum('thpe,pke->thpk', q, sub_keys).astype(jnp.float32)
        s1, i1 = lax.top_k(s[:, :, 0], PEER_TOPK)
        s2, i2 = lax.top_k(s[:, :, 1], PEER_TOPK)
        cand = (s1[..., :, None] + s2[..., None, :]).reshape(PEER_BLOCK, PEER_HEADS, PEER_TOPK * PEER_TOPK)
        cidx = (i1[..., :, None] * N_KEYS + i2[..., None, :]).reshape(PEER_BLOCK, PEER_HEADS, PEER_TOPK * PEER_TOPK)
        best, j = lax.top_k(cand, PEER_TOPK)
        eidx = jnp.take_along_axis(cidx, j, axis=-1).reshape(PEER_BLOCK, PEER_HEADS * PEER_TOPK)
        gate = jax.nn.softmax(best, axis=-1).reshape(PEER_BLOCK, PEER_HEADS * PEER_TOPK)
        u = u_tab[eidx]
        a = jax.nn.gelu(jnp.einsum('td,tkd->tk', xb, u).astype(jnp.float32), approximate=False) * gate
        return jnp.einsum('tk,tkd->td', a.astype(xb.dtype), v_tab[eidx])

    out = lax.map(block, xp).reshape(-1, D_MODEL)[:n]
    return out.reshape(lead + (D_MODEL,))

def setup_inputs(seed: int = 0) -> dict:
    key = jax.random.key(seed)
    ks = iter(jax.random.split(key, 40))
    f32 = jnp.float32

    def nrm(shape, scale=1.0):
        return jax.random.normal(next(ks), shape, f32) * scale

    def gain(n):
        return 1.0 + 0.05 * nrm((DEPTH, n))

    n_pages = PAST_LEN // PAGE_SIZE
    n_used = DEC_BATCH * n_pages
    n_pool = n_used + (n_used + 3) // 4
    page_table = jax.random.permutation(next(ks), n_pool)[:n_used].reshape(DEC_BATCH, n_pages).astype(jnp.int32)
    dil_shapes = [(DEPTH, DEC_BATCH, min(w, PAST_LEN), 2, DIL_HEADS, DIL_DIM) for w, _ in DIL_GROUPS]
    return {
        'x_prompt': nrm((BATCH, SEQ, D_MODEL)),
        'x_sample': nrm((DEC_BATCH, DEC_SEQ, D_MODEL)),
        'mem_prompt': nrm((BATCH, MEM_LEN, D_MODEL)),
        'cache_mla': nrm((DEPTH, n_pool, PAGE_SIZE, MLA_DIM)),
        'page_table': page_table,
        'cache_dil0': nrm(dil_shapes[0]),
        'cache_dil1': nrm(dil_shapes[1]),
        'cache_dil2': nrm(dil_shapes[2]),
        'cache_mem': nrm((DEPTH, DEC_BATCH, MEM_LEN, 2, MEM_HEADS, MEM_DIM)),
        'w_in': nrm((DEPTH, D_MODEL, IN_COLS), D_MODEL ** -0.5),
        'g_attn': gain(D_MODEL),
        'g_q_lora': gain(Q_LORA),
        'w_q_up': nrm((DEPTH, Q_LORA, MLA_HEADS * (QK_NOPE + QK_ROPE)), Q_LORA ** -0.5),
        'g_kv_lora': gain(KV_LORA),
        'w_kv_up': nrm((DEPTH, KV_LORA, MLA_HEADS * (QK_NOPE + V_DIM)), KV_LORA ** -0.5),
        'w_o_mla': nrm((DEPTH, MLA_HEADS * V_DIM, D_MODEL), (MLA_HEADS * V_DIM) ** -0.5),
        'w_o_dil': nrm((DEPTH, DIL_HEADS * DIL_DIM, D_MODEL), (DIL_HEADS * DIL_DIM) ** -0.5),
        'w_mem_kv': nrm((DEPTH, D_MODEL, 2 * MEM_HEADS * MEM_DIM), D_MODEL ** -0.5),
        'g_mem': gain(D_MODEL),
        'w_o_mem': nrm((DEPTH, MEM_HEADS * MEM_DIM, D_MODEL), (MEM_HEADS * MEM_DIM) ** -0.5),
        'w_out': nrm((DEPTH, D_MODEL, D_MODEL), D_MODEL ** -0.5),
        'g_ffn': gain(D_MODEL),
        'w_peer_q': nrm((DEPTH, D_MODEL, PEER_HEADS * PEER_QDIM), D_MODEL ** -0.5),
        'peer_sub_keys': nrm((DEPTH, 2, N_KEYS, PEER_QDIM // 2), (PEER_QDIM // 2) ** -0.5),
        'peer_u': nrm((DEPTH, N_EXPERTS, D_MODEL), D_MODEL ** -0.5),
        'peer_v': nrm((DEPTH, N_EXPERTS, D_MODEL), PEER_HEADS ** -0.5),
        'g_final': 1.0 + 0.05 * nrm((D_MODEL,)),
    }

def reference(x_prompt, x_sample, mem_prompt, cache_mla, page_table, cache_dil0, cache_dil1, cache_dil2,
              cache_mem, w_in, g_attn, g_q_lora, w_q_up, g_kv_lora, w_kv_up, w_o_mla, w_o_dil, w_mem_kv,
              g_mem, w_o_mem, w_out, g_ffn, w_peer_q, peer_sub_keys, peer_u, peer_v, g_final):
    B, S = x_prompt.shape[:2]
    T = x_sample.shape[1]
    past_len = page_table.shape[1] * cache_mla.shape[2]
    pos_p = jnp.arange(S, dtype=jnp.int32)
    pos_s = past_len + jnp.arange(T, dtype=jnp.int32)
    dil_caches = (cache_dil0, cache_dil1, cache_dil2)
    hp, hs = x_prompt, x_sample
    new_mla_p, new_mem_p, new_mla_s = [], [], []
    new_dil_p = [[], [], []]
    new_dil_s = [[], [], []]
    for l in range(DEPTH):
        w_kv = w_kv_up[l].reshape(KV_LORA, MLA_HEADS, QK_NOPE + V_DIM)
        w_uk, w_uv = w_kv[..., :QK_NOPE], w_kv[..., QK_NOPE:]
        proj_w = (w_in[l], g_attn[l], g_q_lora[l], w_q_up[l], g_kv_lora[l])
        merge_w = (w_o_mla[l], w_o_dil[l], w_o_mem[l], w_out[l])
        peer_w = (w_peer_q[l], peer_sub_keys[l], peer_u[l], peer_v[l])

        q_mla, row_mla, q_d, k_d, v_d, q_mem, gates = mixer_project(hp, pos_p, *proj_w)
        o_mla = mla_prompt(q_mla, row_mla, w_uk, w_uv)
        outs, lses = [], []
        for gi, (win, dil) in enumerate(DIL_GROUPS):
            o, lse = dilated_prompt(q_d[:, :, gi], k_d[:, :, gi], v_d[:, :, gi], win, dil)
            outs.append(o)
            lses.append(lse)
            keep = min(win, S)
            new_dil_p[gi].append(jnp.stack([k_d[:, S - keep:, gi], v_d[:, S - keep:, gi]], axis=2))
        mem_kv = (rmsnorm(mem_prompt, g_mem[l]) @ w_mem_kv[l]).reshape(B, MEM_LEN, 2, MEM_HEADS, MEM_DIM)
        hp = mixer_merge(hp, gates, o_mla, combine_dilations(outs, lses), mem_attend(q_mem, mem_kv), *merge_w)
        hp = hp + peer(rmsnorm(hp, g_ffn[l]), *peer_w)
        new_mla_p.append(row_mla)
        new_mem_p.append(mem_kv)

        q_mla, row_mla, q_d, k_d, v_d, q_mem, gates = mixer_project(hs, pos_s, *proj_w)
        o_mla = mla_sample(q_mla, row_mla, cache_mla[l], page_table, w_uk, w_uv)
        outs, lses = [], []
        for gi, (win, dil) in enumerate(DIL_GROUPS):
            buf = dil_caches[gi][l]
            keep = buf.shape[1]
            kv_all = jnp.concatenate([buf, jnp.stack([k_d[:, :, gi], v_d[:, :, gi]], axis=2)], axis=1)
            o, lse = dilated_sample(q_d[:, :, gi], kv_all[:, :, 0], kv_all[:, :, 1], win, dil)
            outs.append(o)
            lses.append(lse)
            new_dil_s[gi].append(kv_all[:, -keep:])
        hs = mixer_merge(hs, gates, o_mla, combine_dilations(outs, lses), mem_attend(q_mem, cache_mem[l]), *merge_w)
        hs = hs + peer(rmsnorm(hs, g_ffn[l]), *peer_w)
        new_mla_s.append(row_mla)

    y_prompt = rmsnorm(hp, g_final)
    y_sample = rmsnorm(hs, g_final)
    return (y_prompt, y_sample,
            jnp.stack(new_mla_p), jnp.stack(new_dil_p[0]), jnp.stack(new_dil_p[1]), jnp.stack(new_dil_p[2]),
            jnp.stack(new_mem_p),
            jnp.stack(new_mla_s), jnp.stack(new_dil_s[0]), jnp.stack(new_dil_s[1]), jnp.stack(new_dil_s[2]))


_drawn_inputs = setup_inputs


def setup_inputs(seed=0):
    import zlib

    import numpy as np

    out = dict(_drawn_inputs(seed))
    spreads = {}
    factors = {'cache_mla': 2.752, 'g_q_lora': 5.216}
    for name, (base, spread) in spreads.items():
        noise = np.random.default_rng([zlib.crc32(name.encode()), seed]).standard_normal(out[name].shape)
        drawn = base * np.exp(spread * noise) if base else spread * noise
        out[name] = __import__('jax').numpy.asarray(drawn.astype(out[name].dtype))
    for name, factor in factors.items():
        out[name] = (out[name] * factor).astype(out[name].dtype)
    return out
```

```python
from collections import namedtuple
from contextlib import ExitStack

import numpy as np

import concourse.bass as bass
from concourse import mybir

F32 = mybir.dt.float32
I32 = mybir.dt.int32
U32 = mybir.dt.uint32
ALU = mybir.AluOpType
ACT = mybir.ActivationFunctionType
AX = mybir.AxisListType
ds = bass.ds

P = 128
D = 1024
SEQ = 1024
DB, DT = 8, 4
NS = DB * DT
PAST = 8192
PAGE = 128
N_PAGES = PAST // PAGE
POOL_PAGES = DB * N_PAGES + (DB * N_PAGES + 3) // 4
NTP = SEQ // P
NT = NTP + 1
T = NT * P
KD = D // P
H_MLA, Q_LORA, KV_LORA, NOPE, ROPE, V_DIM = 8, 384, 256, 64, 32, 64
QK = NOPE + ROPE
ROW = KV_LORA + ROPE
MLA_SCALE = float(QK) ** -0.5
GROUPS = ((128, 1), (512, 4), (2048, 16))
NG, HD, E = 3, 4, 64
GE = HD * E
ROT = E // 4
DIL_SCALE = float(E) ** -0.5
DIL_COLS = 3 * NG * GE
MEM, HM, EM = 256, 4, 128
MEM_SCALE = float(EM) ** -0.5
C_DIL = Q_LORA + ROW
C_MEM = C_DIL + DIL_COLS
C_GATE = C_MEM + HM * EM
PROJ = C_GATE
HP, NK, QH, TOPK = 8, 128, 128, 16
SLOTS = HP * TOPK
EPS = 1e-6
NEG = -1e30
THETA = 500000.0
CREDIT = 1


class Dram:
    pass


class Resident:
    pass


class Steps:

    def __init__(self, eng, sem, turn=0, per=0):
        self.eng, self.sem, self.base, self.per, self.n = eng, sem, turn * per if per else 0, per, 0

    def __call__(self, ins):
        self.n += 1
        ins.then_inc(self.sem, 1)
        self.eng.wait_ge(self.sem, self.base + self.n + CREDIT)

    def end(self):
        assert self.n == self.per, f"a turn has {self.n} steps, not {self.per}"


def stage(nc, tag):
    ctx, mine = ExitStack(), []

    @ctx.callback
    def _():
        nc.clear_and_free_semaphores(mine)
        nc.all_engine_barrier()

    sb = lambda n, shape, dt=F32: ctx.enter_context(nc.sbuf_tensor(f"{tag}_{n}", shape, dt))
    ps = lambda n, shape: ctx.enter_context(nc.psum_tensor(f"{tag}_{n}", shape, F32))

    def sem(name, credit):
        handle = nc.alloc_semaphore(f"{tag}_{name}")
        mine.append(handle)
        if credit:
            nc.gpsimd.sem_inc(handle, credit)
        return handle

    sems = lambda names, credit=CREDIT: namedtuple("Semaphores", names)(*[sem(n, credit) for n in names.split()])
    return ctx, sb, ps, sems


def norm_rows(nc, tag, src, gain, n_tiles, ident, dst_T, dst_rows=None):
    ctx, sb, ps, sems = stage(nc, tag)
    with ctx:
        x, sq, xn, g = sb("x", [P, D]), sb("sq", [P, D]), sb("xn", [P, D]), sb("g", [P, D])
        ss, ms, rt, rstd = sb("ss", [P, 1]), sb("ms", [P, 1]), sb("rt", [P, 1]), sb("rstd", [P, 1])
        lo, hi = ps("lo", [P, 4 * P]), ps("hi", [P, 4 * P])
        s = sems("gain_loaded x_loaded squares_summed mean_ready root_ready rstd_ready xn_ready "
                 "lo_ready hi_ready lo_copied hi_copied rows_stored")
        with nc.Block() as block:
            @block.sync
            def _(sp):
                sp.dma_start(g[:, :], gain.partition_broadcast(P)).then_inc(s.gain_loaded, 16)
                with sp.Fori(0, n_tiles) as i:
                    sp.wait_ge(s.xn_ready, i + CREDIT)
                    sp.dma_start(x[:, :], src[ds(i * P, P), :]).then_inc(s.x_loaded, 16)
                    if dst_rows is not None:
                        sp.wait_ge(s.xn_ready, i + 1 + CREDIT)
                        sp.dma_start(dst_rows[ds(i * P, P), :], xn[:, :]).then_inc(s.rows_stored, 16)
                if dst_rows is not None:
                    sp.wait_ge(s.rows_stored, 16 * n_tiles + CREDIT)

            @block.scalar
            def _(act):
                with act.Fori(0, n_tiles) as i:
                    act.wait_ge(s.x_loaded, i * 16 + 16 + CREDIT)
                    act.activation(sq[:, :], x[:, :], ACT.Square, accum_out=ss[:, :]).then_inc(s.squares_summed, 1)
                    act.wait_ge(s.mean_ready, i + 1 + CREDIT)
                    act.activation(rt[:, :], ms[:, :], ACT.Sqrt).then_inc(s.root_ready, 1)
                    act.wait_ge(s.hi_ready, i + 1 + CREDIT)
                    act.copy(dst_T[:, 4:8, ds(i * P, P)], hi[:, :].rearrange("p (k t) -> p k t", k=4)
                             ).then_inc(s.hi_copied, 1)

            @block.vector
            def _(dve):
                dve.wait_ge(s.gain_loaded, 16 + CREDIT)
                with dve.Fori(0, n_tiles) as i:
                    dve.wait_ge(s.squares_summed, i + 1 + CREDIT)
                    dve.tensor_scalar(ms[:, :], ss[:, :], 1.0 / D, EPS, ALU.mult, ALU.add).then_inc(s.mean_ready, 1)
                    dve.wait_ge(s.root_ready, i + 1 + CREDIT)
                    dve.reciprocal(rstd[:, :], rt[:, :]).then_inc(s.rstd_ready, 1)
                    dve.wait_ge(s.rstd_ready, i + 1 + CREDIT)
                    dve.wait_ge(s.hi_ready, i + CREDIT)
                    if dst_rows is not None:
                        dve.wait_ge(s.rows_stored, i * 16 + CREDIT)
                    dve.scalar_tensor_tensor(out=xn[:, :], in0=x[:, :], scalar=rstd[:, 0:1], in1=g[:, :],
                                             op0=ALU.mult, op1=ALU.mult).then_inc(s.xn_ready, 1)
                    dve.wait_ge(s.lo_ready, i + 1 + CREDIT)
                    dve.tensor_copy(dst_T[:, 0:4, ds(i * P, P)], lo[:, :].rearrange("p (k t) -> p k t", k=4)
                                    ).then_inc(s.lo_copied, 1)

            @block.tensor
            def _(pe):
                with pe.Fori(0, n_tiles) as i:
                    pe.wait_ge(s.xn_ready, i + 1 + CREDIT)
                    for half, bank, copied, ready in ((0, lo, s.lo_copied, s.lo_ready), (1, hi, s.hi_copied, s.hi_ready)):
                        pe.wait_ge(copied, i + CREDIT)
                        for k in range(4):
                            c = (4 * half + k) * P
                            mm = pe.transpose(bank[:, k * P:(k + 1) * P], xn[:, c:c + P], ident)
                        mm.then_inc(ready, 1)


def product_rows(nc, tag, xT, w, n_cols, chunk, n_tiles, dst, add=None):
    ctx, sb, ps, sems = stage(nc, tag)
    pairs = n_cols // chunk // 2
    assert pairs * 2 * chunk == n_cols
    with ctx:
        wt = [sb(f"w{u}", [P, KD, chunk]) for u in range(2)]
        o = [sb(f"o{u}", [P, n_tiles, chunk]) for u in range(2)]
        acc = [ps(f"acc{u}", [P, 512]) for u in range(2)]
        s = sems("w_loaded0 w_loaded1 add_loaded0 add_loaded1 product_ready w_used product_copied stored0 stored1")
        w_loaded, add_loaded, stored = (s.w_loaded0, s.w_loaded1), (s.add_loaded0, s.add_loaded1), (s.stored0, s.stored1)
        wv = w.rearrange("(k p) n -> p k n", p=P)
        dv = dst.rearrange("(t p) n -> p t n", p=P)
        av = add.rearrange("(t p) n -> p t n", p=P) if add is not None else None
        with nc.Block() as block:
            @block.sync
            def _(sp):
                with sp.Fori(0, pairs) as i:
                    for u in range(2):
                        col = i * (2 * chunk) + u * chunk
                        sp.wait_ge(s.product_ready, i * (2 * n_tiles) + CREDIT)
                        sp.dma_start(wt[u][:, :, :], wv[:, :, ds(col, chunk)]).then_inc(w_loaded[u], 16)

            @block.scalar
            def _(act):
                with act.Fori(0, pairs) as i:
                    if add is not None:
                        for u in range(2):
                            act.wait_ge(stored[u], i * 16 + CREDIT)
                            act.dma_start(o[u][:, :, :], av[:, :, ds(i * (2 * chunk) + u * chunk, chunk)]
                                          ).then_inc(add_loaded[u], 16)
                    for u in range(2):
                        act.wait_ge(s.product_copied, i * (2 * n_tiles) + (u + 1) * n_tiles + CREDIT)
                        act.dma_start(dv[:, :, ds(i * (2 * chunk) + u * chunk, chunk)], o[u][:, :, :]
                                      ).then_inc(stored[u], 16)
                for u in range(2):
                    act.wait_ge(stored[u], 16 * pairs + CREDIT)

            @block.tensor
            def _(pe):
                with pe.Fori(0, pairs) as i:
                    for u in range(2):
                        pe.wait_ge(w_loaded[u], i * 16 + 16 + CREDIT)
                        for t in range(n_tiles):
                            n = u * n_tiles + t
                            pe.wait_ge(s.product_copied, i * (2 * n_tiles) + max(n - 1, 0) + CREDIT)
                            for k in range(KD):
                                mm = pe.matmul(acc[n % 2][:, 0:chunk], xT[:, k, t * P:(t + 1) * P], wt[u][:, k, :],
                                               start=(k == 0), stop=(k == KD - 1))
                            mm.then_inc(s.product_ready, 1)

            @block.vector
            def _(dve):
                with dve.Fori(0, pairs) as i:
                    for u in range(2):
                        if add is not None:
                            dve.wait_ge(add_loaded[u], i * 16 + 16 + CREDIT)
                        else:
                            dve.wait_ge(stored[u], i * 16 + CREDIT)
                        for t in range(n_tiles):
                            n = u * n_tiles + t
                            dve.wait_ge(s.product_ready, i * (2 * n_tiles) + n + 1 + CREDIT)
                            if add is not None:
                                dve.tensor_tensor(o[u][:, t, :], acc[n % 2][:, 0:chunk], o[u][:, t, :], ALU.add
                                                  ).then_inc(s.product_copied, 1)
                            else:
                                dve.tensor_copy(o[u][:, t, :], acc[n % 2][:, 0:chunk]).then_inc(s.product_copied, 1)


def latents(nc, a, r):
    ctx, sb, ps, sems = stage(nc, "lat")
    with ctx:
        x, sq = sb("x", [P, C_DIL]), sb("sq", [P, Q_LORA])
        tab = sb("tab", [P, ROPE])
        gq, gkv = sb("gq", [P, Q_LORA]), sb("gkv", [P, KV_LORA])
        wq = sb("wq", [P, 3, H_MLA * QK])
        ss, ms, rt, rstd = sb("ss", [P, 2]), sb("ms", [P, 2]), sb("rt", [P, 2]), sb("rstd", [P, 2])
        cq, row, kpad = sb("cq", [P, Q_LORA]), sb("row", [P, ROW]), sb("kpad", [P, QK])
        tmp = sb("tmp", [P, 4, H_MLA, 16])
        cqT, q, qT = sb("cqT", [P, 3, P]), sb("q", [P, H_MLA, QK]), sb("qT", [QK, H_MLA, P])
        y, ytab = sb("y", [P, 2 * NG * HD, E]), sb("ytab", [P, ROT])
        yv = sb("yv", [P, NG * GE])
        ytmp = sb("ytmp", [P, 4, 2 * NG * HD, ROT // 2])
        pc, pk = ps("pc", [P, 512]), ps("pk", [P, 512])
        pq = [ps(f"pq{u}", [P, 512]) for u in range(2)]
        pt = [ps(f"pt{u}", [P, 512]) for u in range(2)]
        s = sems("const_loaded pad_zeroed x_loaded squares_summed means_ready roots_ready steps latents_ready "
                 "cq_turned kv_turned cqT_ready kvT_ready q_product q_copied q_roped q_turned qT_lo qT_hi "
                 "row_stored qT_stored y_loaded y_steps y_roped y_stored")
        N = 15
        with nc.Block() as block:
            @block.sync
            def _(sp):
                sp.dma_start(gq[:, :], a.g_q_lora.partition_broadcast(P)).then_inc(s.const_loaded, 16)
                sp.dma_start(gkv[:, :], a.g_kv_lora.partition_broadcast(P)).then_inc(s.const_loaded, 16)
                sp.dma_start(wq[:, :, :], a.w_q_up.rearrange("(k p) n -> p k n", p=P)).then_inc(s.const_loaded, 16)
                with sp.Fori(0, NT) as i:
                    sp.wait_ge(s.latents_ready, i + CREDIT)
                    sp.wait_ge(s.q_roped, i + CREDIT)
                    sp.dma_start(x[:, :], a.proj[ds(i * P, P), 0:C_DIL]).then_inc(s.x_loaded, 16)
                    sp.dma_start(tab[:, :], a.rope_mla[ds(i * P, P), :]).then_inc(s.x_loaded, 16)
                    sp.wait_ge(s.y_stored, i * 32 + CREDIT)
                    sp.dma_start(y[:, :, :].rearrange("p h e -> p (h e)"), a.proj[ds(i * P, P), C_DIL:C_DIL + 2 * NG * GE]
                                 ).then_inc(s.y_loaded, 16)
                    sp.dma_start(yv[:, :], a.proj[ds(i * P, P), C_DIL + 2 * NG * GE:C_MEM]).then_inc(s.y_loaded, 16)
                    sp.dma_start(ytab[:, :], a.rope_dil[ds(i * P, P), :]).then_inc(s.y_loaded, 16)
                    sp.wait_ge(s.y_roped, i + 1 + CREDIT)
                    sp.dma_start(a.dil[ds(i * P, P), 0:2 * NG * GE], y[:, :, :].rearrange("p h e -> p (h e)")
                                 ).then_inc(s.y_stored, 16)
                    sp.dma_start(a.dil[ds(i * P, P), 2 * NG * GE:DIL_COLS], yv[:, :]).then_inc(s.y_stored, 16)
                    sp.wait_ge(s.latents_ready, i + 1 + CREDIT)
                    sp.dma_start(a.rows[ds(i * P, P), :], row[:, :]).then_inc(s.row_stored, 16)
                sp.wait_ge(s.row_stored, 16 * NT + CREDIT)
                sp.wait_ge(s.y_stored, 32 * NT + CREDIT)

            @block.scalar
            def _(act):
                with act.Fori(0, NT) as i:
                    act.wait_ge(s.x_loaded, i * 32 + 32 + CREDIT)
                    act.activation(sq[:, :], x[:, 0:Q_LORA], ACT.Square, accum_out=ss[:, 0:1]).then_inc(s.squares_summed, 1)
                    act.wait_ge(s.squares_summed, i * 2 + 1 + CREDIT)
                    act.activation(sq[:, 0:KV_LORA], x[:, Q_LORA:Q_LORA + KV_LORA], ACT.Square,
                                   accum_out=ss[:, 1:2]).then_inc(s.squares_summed, 1)
                    act.wait_ge(s.means_ready, i + 1 + CREDIT)
                    act.activation(rt[:, :], ms[:, :], ACT.Sqrt).then_inc(s.roots_ready, 1)
                    act.wait_ge(s.cq_turned, i + 1 + CREDIT)
                    act.copy(cqT[:, :, :], pc[:, 0:Q_LORA].rearrange("p (k t) -> p k t", k=3)).then_inc(s.cqT_ready, 1)
                    act.wait_ge(s.q_turned, i * 2 + CREDIT)
                    for u in range(2):
                        act.wait_ge(s.q_product, i * 2 + u + 1 + CREDIT)
                        act.copy(q[:, 4 * u:4 * u + 4, :], pq[u][:, 0:4 * QK].rearrange("p (h e) -> p h e", h=4)
                                 ).then_inc(s.q_copied, 1)
                    act.wait_ge(s.q_turned, i * 2 + 1 + CREDIT)
                    act.wait_ge(s.qT_stored, i * 16 + CREDIT)
                    act.copy(qT[:, 0:4, :], pt[0][0:QK, :].rearrange("p (h t) -> p h t", h=4)).then_inc(s.qT_lo, 1)
                    act.wait_ge(s.qT_lo, i + 1 + CREDIT)
                    act.wait_ge(s.qT_hi, i + 1 + CREDIT)
                    act.dma_start(a.qT[:, :, ds(i * P, P)], qT[:, :, :]).then_inc(s.qT_stored, 16)
                act.wait_ge(s.qT_stored, 16 * NT + CREDIT)

            @block.vector
            def _(dve):
                dve.memset(kpad[:, :], 0.0).then_inc(s.pad_zeroed, 1)
                dve.wait_ge(s.pad_zeroed, 1 + CREDIT)
                dve.wait_ge(s.const_loaded, 48 + CREDIT)
                with dve.Fori(0, NT) as i:
                    step = Steps(dve, s.steps, i, N)
                    dve.wait_ge(s.squares_summed, i * 2 + 2 + CREDIT)
                    step(dve.tensor_scalar(ms[:, 0:1], ss[:, 0:1], 1.0 / Q_LORA, EPS, ALU.mult, ALU.add))
                    dve.tensor_scalar(ms[:, 1:2], ss[:, 1:2], 1.0 / KV_LORA, EPS, ALU.mult, ALU.add
                                      ).then_inc(s.means_ready, 1)
                    dve.wait_ge(s.roots_ready, i + 1 + CREDIT)
                    step(dve.reciprocal(rstd[:, :], rt[:, :]))
                    dve.wait_ge(s.row_stored, i * 16 + CREDIT)
                    dve.wait_ge(s.cq_turned, i + CREDIT)
                    dve.wait_ge(s.kv_turned, i + CREDIT)
                    step(dve.scalar_tensor_tensor(out=cq[:, :], in0=x[:, 0:Q_LORA], scalar=rstd[:, 0:1], in1=gq[:, :],
                                                  op0=ALU.mult, op1=ALU.mult))
                    step(dve.scalar_tensor_tensor(out=row[:, 0:KV_LORA], in0=x[:, Q_LORA:Q_LORA + KV_LORA],
                                                  scalar=rstd[:, 1:2], in1=gkv[:, :], op0=ALU.mult, op1=ALU.mult))
                    x1, x2 = x[:, C_DIL - 32:C_DIL - 16], x[:, C_DIL - 16:C_DIL]
                    cos, sin = tab[:, 0:16], tab[:, 16:32]
                    for n, (v, w) in enumerate(((x1, cos), (x2, sin), (x2, cos), (x1, sin))):
                        step(dve.tensor_tensor(tmp[:, n, 0, :], v, w, ALU.mult))
                    step(dve.tensor_tensor(row[:, KV_LORA:KV_LORA + 16], tmp[:, 0, 0, :], tmp[:, 1, 0, :], ALU.subtract))
                    step(dve.tensor_tensor(row[:, KV_LORA + 16:ROW], tmp[:, 2, 0, :], tmp[:, 3, 0, :], ALU.add))
                    dve.tensor_copy(kpad[:, NOPE:QK], row[:, KV_LORA:ROW]).then_inc(s.latents_ready, 1)
                    dve.wait_ge(s.kv_turned, i + 1 + CREDIT)
                    dve.tensor_copy(r.ckvT[:, :, ds(i * P, P)], pk[:, 0:2 * P].rearrange("p (k t) -> p k t", k=2)
                                    ).then_inc(s.kvT_ready, 1)
                    dve.tensor_copy(r.kpeT[NOPE:QK, ds(i * P, P)], pk[NOPE:QK, 2 * P:3 * P]).then_inc(s.kvT_ready, 1)
                    dve.wait_ge(s.q_copied, i * 2 + 2 + CREDIT)
                    q1, q2 = q[:, :, NOPE:NOPE + 16], q[:, :, NOPE + 16:QK]
                    cosb = cos.unsqueeze(1).broadcast_to([P, H_MLA, 16])
                    sinb = sin.unsqueeze(1).broadcast_to([P, H_MLA, 16])
                    for n, (v, w) in enumerate(((q1, cosb), (q2, sinb), (q2, cosb), (q1, sinb))):
                        step(dve.tensor_tensor(tmp[:, n, :, :], v, w, ALU.mult))
                    step(dve.tensor_tensor(q1, tmp[:, 0, :, :], tmp[:, 1, :, :], ALU.subtract))
                    dve.tensor_tensor(q2, tmp[:, 2, :, :], tmp[:, 3, :, :], ALU.add).then_inc(s.q_roped, 1)
                    dve.wait_ge(s.q_turned, i * 2 + 2 + CREDIT)
                    dve.wait_ge(s.qT_stored, i * 16 + CREDIT)
                    dve.tensor_copy(qT[:, 4:8, :], pt[1][0:QK, :].rearrange("p (h t) -> p h t", h=4)).then_inc(s.qT_hi, 1)
                    step.end()

            @block.tensor
            def _(pe):
                pe.wait_ge(s.const_loaded, 48 + CREDIT)
                with pe.Fori(0, NT) as i:
                    pe.wait_ge(s.latents_ready, i + 1 + CREDIT)
                    pe.wait_ge(s.cqT_ready, i + CREDIT)
                    pe.wait_ge(s.kvT_ready, i * 2 + CREDIT)
                    for k in range(3):
                        mm = pe.transpose(pc[:, k * P:(k + 1) * P], cq[:, k * P:(k + 1) * P], r.ident)
                    mm.then_inc(s.cq_turned, 1)
                    for k in range(2):
                        pe.transpose(pk[:, k * P:(k + 1) * P], row[:, k * P:(k + 1) * P], r.ident)
                    pe.transpose(pk[0:QK, 2 * P:3 * P], kpad[:, :], r.ident).then_inc(s.kv_turned, 1)
                    pe.wait_ge(s.cqT_ready, i + 1 + CREDIT)
                    pe.wait_ge(s.q_copied, i * 2 + CREDIT)
                    for u in range(2):
                        for k in range(3):
                            mm = pe.matmul(pq[u][:, 0:4 * QK], cqT[:, k, :], wq[:, k, 4 * QK * u:4 * QK * (u + 1)],
                                           start=(k == 0), stop=(k == 2))
                        mm.then_inc(s.q_product, 1)
                    pe.wait_ge(s.q_roped, i + 1 + CREDIT)
                    pe.wait_ge(s.qT_lo, i + CREDIT)
                    pe.wait_ge(s.qT_hi, i + CREDIT)
                    for u in range(2):
                        for h in range(4):
                            mm = pe.transpose(pt[u][0:QK, h * P:(h + 1) * P], q[:, 4 * u + h, :], r.ident)
                        mm.then_inc(s.q_turned, 1)

            @block.gpsimd
            def _(pool):
                NY = 5
                pair = "p (h e) -> p h e"
                with pool.Fori(0, NT) as i:
                    step = Steps(pool, s.y_steps, i, NY)
                    pool.wait_ge(s.y_loaded, i * 48 + 48 + CREDIT)
                    h2 = ROT // 2
                    y1, y2 = y[:, :, 0:h2], y[:, :, h2:ROT]
                    cosb = ytab[:, 0:h2].unsqueeze(1).broadcast_to([P, 2 * NG * HD, h2])
                    sinb = ytab[:, h2:ROT].unsqueeze(1).broadcast_to([P, 2 * NG * HD, h2])
                    for n, (v, w) in enumerate(((y1, cosb), (y2, sinb), (y2, cosb), (y1, sinb))):
                        step(pool.tensor_tensor(ytmp[:, n, :, :], v, w, ALU.mult))
                    step(pool.tensor_tensor(y1, ytmp[:, 0, :, :], ytmp[:, 1, :, :], ALU.subtract))
                    pool.tensor_tensor(y2, ytmp[:, 2, :, :], ytmp[:, 3, :, :], ALU.add).then_inc(s.y_roped, 1)
                    step.end()


def memory_attention(nc, a, r):
    ctx, sb, ps, sems = stage(nc, "mem")
    with ctx:
        kv, kT = sb("kv", [P, 2, 2 * HM * EM]), sb("kT", [P, HM, MEM])
        x, qT = sb("x", [P, HM * EM]), sb("qT", [P, HM, P])
        nm, nb, l, rl = sb("nm", [P, HM]), sb("nb", [P, HM]), sb("l", [P, HM]), sb("rl", [P, HM])
        p, pT, o = sb("p", [P, HM, MEM]), sb("pT", [P, HM, 2, P]), sb("o", [P, HM, EM])
        pq = ps("pq", [P, 512])
        sc = [ps(f"sc{u}", [P, 512]) for u in range(2)]
        pt = [ps(f"pt{u}", [P, 512]) for u in range(2)]
        po, pot = ps("po", [P, 512]), ps("pot", [P, 512])
        s = sems("kv_loaded k_turned kT_ready x_loaded q_turned qT_ready scores_ready max_found bias_ready probs_ready "
                 "probs_turned pT_ready attended sum_inverted o_ready o_turned oT_stored")
        with nc.Block() as block:
            @block.sync
            def _(sp):
                sp.dma_start(kv[:, :, :], a.mem_kv.rearrange("(m p) c -> p m c", p=P)).then_inc(s.kv_loaded, 16)
                with sp.Fori(0, NTP) as i:
                    sp.wait_ge(s.q_turned, i + CREDIT)
                    sp.dma_start(x[:, :], a.proj[ds(i * P, P), C_MEM:C_GATE]).then_inc(s.x_loaded, 16)

            @block.tensor
            def _(pe):
                pe.wait_ge(s.kv_loaded, 16 + CREDIT)
                for h in range(HM):
                    for m in range(2):
                        mm = pe.transpose(sc[h // 2][:, (h % 2 * 2 + m) * P:(h % 2 * 2 + m + 1) * P],
                                          kv[:, m, h * EM:(h + 1) * EM], r.ident)
                mm.then_inc(s.k_turned, 1)
                pe.wait_ge(s.kT_ready, 2 + CREDIT)
                with pe.Fori(0, NTP) as i:
                    pe.wait_ge(s.x_loaded, i * 16 + 16 + CREDIT)
                    pe.wait_ge(s.qT_ready, i + CREDIT)
                    for h in range(HM):
                        mm = pe.transpose(pq[:, h * P:(h + 1) * P], x[:, h * EM:(h + 1) * EM], r.ident)
                    mm.then_inc(s.q_turned, 1)
                    pe.wait_ge(s.qT_ready, i + 1 + CREDIT)
                    pe.wait_ge(s.probs_ready, i * HM + CREDIT)
                    for h in range(HM):
                        mm = pe.matmul(sc[h // 2][:, h % 2 * MEM:(h % 2 + 1) * MEM], qT[:, h, :], kT[:, h, :],
                                       start=True, stop=True)
                        if h % 2:
                            mm.then_inc(s.scores_ready, 1)
                    for u in range(2):
                        pe.wait_ge(s.probs_ready, i * HM + 2 * u + 2 + CREDIT)
                        pe.wait_ge(s.pT_ready, i * 2 + u + CREDIT)
                        for j in range(4):
                            mm = pe.transpose(pt[u][:, j * P:(j + 1) * P],
                                              p[:, 2 * u + j // 2, (j % 2) * P:(j % 2 + 1) * P], r.ident)
                        mm.then_inc(s.probs_turned, 1)
                    pe.wait_ge(s.pT_ready, i * 2 + 2 + CREDIT)
                    pe.wait_ge(s.o_ready, i + CREDIT)
                    for h in range(HM):
                        for m in range(2):
                            mm = pe.matmul(po[:, h * EM:(h + 1) * EM], pT[:, h, m, :],
                                           kv[:, m, (HM + h) * EM:(HM + h + 1) * EM], start=(m == 0), stop=(m == 1))
                    mm.then_inc(s.attended, 1)
                    pe.wait_ge(s.o_ready, i + 1 + CREDIT)
                    pe.wait_ge(s.oT_stored, i + CREDIT)
                    for h in range(HM):
                        mm = pe.transpose(pot[:, h * P:(h + 1) * P], o[:, h, :], r.ident)
                    mm.then_inc(s.o_turned, 1)

            @block.scalar
            def _(act):
                with act.Fori(0, NTP) as i:
                    act.wait_ge(s.q_turned, i + 1 + CREDIT)
                    act.wait_ge(s.scores_ready, i * 2 + CREDIT)
                    act.copy(qT[:, :, :], pq[:, :].rearrange("p (h t) -> p h t", h=HM)).then_inc(s.qT_ready, 1)
                    act.wait_ge(s.probs_turned, i * 2 + CREDIT)
                    act.wait_ge(s.sum_inverted, i + CREDIT)
                    for h in range(HM):
                        act.wait_ge(s.bias_ready, i * 2 + h // 2 + 1 + CREDIT)
                        act.activation(p[:, h, :], sc[h // 2][:, h % 2 * MEM:(h % 2 + 1) * MEM], ACT.Exp,
                                       bias=nb[:, h:h + 1], scale=MEM_SCALE, accum_out=l[:, h:h + 1]
                                       ).then_inc(s.probs_ready, 1)
                    act.wait_ge(s.o_turned, i + 1 + CREDIT)
                    act.copy(r.oT_mem[:, :, ds(i * P, P)], pot[:, :].rearrange("p (h t) -> p h t", h=HM)
                             ).then_inc(s.oT_stored, 1)

            @block.vector
            def _(dve):
                dve.wait_ge(s.k_turned, 1 + CREDIT)
                for u in range(2):
                    dve.tensor_copy(kT[:, 2 * u:2 * u + 2, :], sc[u][:, :].rearrange("p (h m) -> p h m", h=2)
                                    ).then_inc(s.kT_ready, 1)
                with dve.Fori(0, NTP) as i:
                    dve.wait_ge(s.probs_ready, i * HM + CREDIT)
                    for u in range(2):
                        dve.wait_ge(s.scores_ready, i * 2 + u + 1 + CREDIT)
                        dve.tensor_reduce(nm[:, 2 * u:2 * u + 2], sc[u][:, :].rearrange("p (h m) -> p h m", h=2),
                                          AX.X, ALU.max, negate=True).then_inc(s.max_found, 1)
                        dve.wait_ge(s.max_found, i * 2 + u + 1 + CREDIT)
                        dve.tensor_scalar(nb[:, 2 * u:2 * u + 2], nm[:, 2 * u:2 * u + 2], MEM_SCALE, None, ALU.mult
                                          ).then_inc(s.bias_ready, 1)
                    dve.wait_ge(s.attended, i + CREDIT)
                    for u in range(2):
                        dve.wait_ge(s.probs_turned, i * 2 + u + 1 + CREDIT)
                        dve.tensor_copy(pT[:, 2 * u:2 * u + 2, :, :].rearrange("p h m t -> p (h m t)"), pt[u][:, :]
                                        ).then_inc(s.pT_ready, 1)
                    dve.reciprocal(rl[:, :], l[:, :]).then_inc(s.sum_inverted, 1)
                    dve.wait_ge(s.sum_inverted, i + 1 + CREDIT)
                    dve.wait_ge(s.attended, i + 1 + CREDIT)
                    dve.wait_ge(s.o_turned, i + CREDIT)
                    dve.tensor_tensor(o[:, :, :], po[:, :].rearrange("p (h e) -> p h e", h=HM),
                                      rl[:, :].unsqueeze(2).broadcast_to([P, HM, EM]), ALU.mult).then_inc(s.o_ready, 1)


def dilated_attention(nc, a, r):
    ctx, sb, ps, sems = stage(nc, "dil")
    TURNS = NTP // 2
    with ctx:
        qk = [sb(f"qk{u}", [P, 2, GE]) for u in range(2)]
        v = [sb(f"v{u}", [P, GE]) for u in range(2)]
        mask = [sb(f"mask{u}", [P, 2 * P]) for u in range(2)]
        qT, kT = sb("qT", [P, HD // 2, P]), [sb(f"kT{u}", [P, HD // 2, P]) for u in range(2)]
        sm, p, pT = sb("sm", [P, HD, 2 * P]), sb("p", [P, HD, 2 * P]), sb("pT", [P, HD, 2, P])
        ou = sb("ou", [P, GE + 2 * HD])
        pq, pk = ps("pq", [P, 512]), ps("pk", [P, 512])
        sc = [ps(f"sc{u}", [P, 512]) for u in range(2)]
        pt = [ps(f"pt{u}", [P, 512]) for u in range(2)]
        po = ps("po", [P, 512])
        s = sems("zeroed qk_loaded v_loaded mask_loaded turned qT_ready kT_ready scores_ready masked max_found probs_ready "
                 "probs_turned pT_ready attended u_ready ou_free")
        own = sems("stored", 0)
        dil3 = a.dil.rearrange("t (j g c) -> t j g c", j=3, g=NG)

        def rows(g, i, u, half):
            dil = GROUPS[g][1]
            at = (i * 256 + u * P + half * 64, i + 4 * (P * u + 64 * half), i * 4 + 2 * u + half)[g]
            return ds(at, 64, step=dil)

        def turns(eng):
            for g in range(NG):
                with eng.Fori(0, TURNS) as i:
                    yield g, i

        with nc.Block() as block:
            @block.sync
            def _(sp):
                for g, i in turns(sp):
                    for u in range(2):
                        n = i * 2 + (2 * TURNS * g + u)
                        sp.wait_ge(s.turned, n + CREDIT)
                        for half in range(2):
                            sp.dma_start(qk[u][half * 64:half * 64 + 64, :, :], dil3[rows(g, i, u, half), 0:2, g, :]
                                         ).then_inc(s.qk_loaded, 16)
                        sp.wait_ge(s.masked, n * 2 + CREDIT)
                        sp.dma_start(mask[u][:, :], a.masks_dil[ds(i * 2 + (2 * TURNS * g + u), 1), :, :].squeeze(0)
                                     ).then_inc(s.mask_loaded, 16)
                        sp.wait_ge(s.attended, n + CREDIT)
                        if g == 0 and u == 1:
                            sp.wait_ge(s.zeroed, 1 + CREDIT)
                        for half in range(2):
                            sp.dma_start(v[u][half * 64:half * 64 + 64, :], dil3[rows(g, i, u, half), 2, g, :]
                                         ).then_inc(s.v_loaded, 16)

            @block.gpsimd
            def _(pool):
                pool.memset(kT[1][:, :, :], 0.0)
                pool.memset(v[1][:, :], 0.0).then_inc(s.zeroed, 1)
                for g, i in turns(pool):
                    for u in range(2):
                        n = i * 2 + (2 * TURNS * g + u)
                        pool.wait_ge(s.u_ready, n + 1 + CREDIT)
                        for half in range(2):
                            pool.dma_start(a.dilo[g, rows(g, i, u, half), :], ou[half * 64:half * 64 + 64, :]
                                           ).then_inc(own.stored, 16)
                        pool.wait_ge(own.stored, n * 32 + 32)
                        pool.sem_inc(s.ou_free, 1)

            @block.tensor
            def _(pe):
                pe.wait_ge(s.zeroed, 1 + CREDIT)
                for g, i in turns(pe):
                    for u in range(2):
                        n = i * 2 + (2 * TURNS * g + u)
                        pe.wait_ge(s.qk_loaded, n * 32 + 32 + CREDIT)
                        pe.wait_ge(s.qT_ready, n + CREDIT)
                        pe.wait_ge(s.kT_ready, n + CREDIT)
                        for k in range(2):
                            pe.transpose(pq[:, k * P:(k + 1) * P], qk[u][:, 0, k * P:(k + 1) * P], r.ident)
                        for k in range(2):
                            mm = pe.transpose(pk[:, k * P:(k + 1) * P], qk[u][:, 1, k * P:(k + 1) * P], r.ident)
                        mm.then_inc(s.turned, 1)
                        pe.wait_ge(s.qT_ready, n + 1 + CREDIT)
                        pe.wait_ge(s.kT_ready, n + 1 + CREDIT)
                        pe.wait_ge(s.masked, n * 2 + CREDIT)
                        for w in range(2):
                            at = slice(w * E, (w + 1) * E)
                            for k in range(2):
                                for j, keys in enumerate((kT[1 - u], kT[u])):
                                    c = (2 * k + j) * P
                                    mm = pe.matmul(sc[w][:, c:c + P], qT[at, k, :], keys[at, k, :], start=True, stop=True)
                            mm.then_inc(s.scores_ready, 1)
                        for w in range(2):
                            pe.wait_ge(s.probs_ready, n * HD + 2 * w + 2 + CREDIT)
                            pe.wait_ge(s.pT_ready, n * 2 + w + CREDIT)
                            for j in range(4):
                                mm = pe.transpose(pt[w][:, j * P:(j + 1) * P],
                                                  p[:, 2 * w + j // 2, (j % 2) * P:(j % 2 + 1) * P], r.ident)
                            mm.then_inc(s.probs_turned, 1)
                        pe.wait_ge(s.pT_ready, n * 2 + 2 + CREDIT)
                        pe.wait_ge(s.u_ready, n + CREDIT)
                        pe.wait_ge(s.v_loaded, n * 32 + 32 + CREDIT)
                        for n4, h in enumerate((0, 2, 1, 3)):
                            for j, vals in enumerate((v[1 - u], v[u])):
                                mm = pe.matmul(po[:, h * E:(h + 1) * E], pT[:, n4, j, :], vals[:, h * E:(h + 1) * E],
                                               start=(j == 0), stop=(j == 1))
                        mm.then_inc(s.attended, 1)

            @block.scalar
            def _(act):
                for g, i in turns(act):
                    for u in range(2):
                        n = i * 2 + (2 * TURNS * g + u)
                        act.wait_ge(s.turned, n + 1 + CREDIT)
                        act.wait_ge(s.scores_ready, n * 2 + CREDIT)
                        act.copy(qT[:, :, :], pq[:, 0:2 * P].rearrange("p (k t) -> p k t", k=2)).then_inc(s.qT_ready, 1)
                        act.wait_ge(s.probs_turned, n * 2 + CREDIT)
                        act.wait_ge(s.ou_free, n + CREDIT)
                        for n4, h in enumerate((0, 2, 1, 3)):
                            act.wait_ge(s.max_found, n * 2 + n4 // 2 + 1 + CREDIT)
                            act.activation(p[:, n4, :], sm[:, n4, :], ACT.Exp, bias=ou[:, GE + h:GE + h + 1],
                                           accum_out=ou[:, GE + HD + h:GE + HD + h + 1]).then_inc(s.probs_ready, 1)

            @block.vector
            def _(dve):
                for g, i in turns(dve):
                    for u in range(2):
                        n = i * 2 + (2 * TURNS * g + u)
                        dve.wait_ge(s.turned, n + 1 + CREDIT)
                        dve.wait_ge(s.scores_ready, n * 2 + CREDIT)
                        dve.tensor_copy(kT[u][:, :, :], pk[:, 0:2 * P].rearrange("p (k t) -> p k t", k=2)).then_inc(s.kT_ready, 1)
                        dve.wait_ge(s.mask_loaded, n * 16 + 16 + CREDIT)
                        dve.wait_ge(s.ou_free, n + CREDIT)
                        dve.wait_ge(s.probs_ready, n * HD + CREDIT)
                        for w in range(2):
                            dve.wait_ge(s.scores_ready, n * 2 + w + 1 + CREDIT)
                            dve.scalar_tensor_tensor(
                                out=sm[:, 2 * w:2 * w + 2, :], in0=sc[w][:, :].rearrange("p (h k) -> p h k", h=2),
                                scalar=DIL_SCALE, in1=mask[u][:, :].unsqueeze(1).broadcast_to([P, 2, 2 * P]),
                                op0=ALU.mult, op1=ALU.add).then_inc(s.masked, 1)
                            dve.wait_ge(s.masked, n * 2 + w + 1 + CREDIT)
                            dve.tensor_reduce(ou[:, GE + w:GE + HD:2], sm[:, 2 * w:2 * w + 2, :], AX.X, ALU.max,
                                              negate=True).then_inc(s.max_found, 1)
                        for w in range(2):
                            dve.wait_ge(s.probs_turned, n * 2 + w + 1 + CREDIT)
                            dve.tensor_copy(pT[:, 2 * w:2 * w + 2, :, :].rearrange("p h m t -> p (h m t)"), pt[w][:, :]
                                            ).then_inc(s.pT_ready, 1)
                        dve.wait_ge(s.attended, n + 1 + CREDIT)
                        dve.tensor_copy(ou[:, 0:GE], po[:, 0:GE]).then_inc(s.u_ready, 1)


def combine_groups(nc, a, r):
    ctx, sb, ps, sems = stage(nc, "comb")
    with ctx:
        x = sb("x", [P, NG, GE + 2 * HD])
        nmx, dm, w, wl, L = sb("nmx", [P, HD]), sb("dm", [P, NG, HD]), sb("w", [P, NG, HD]), sb("wl", [P, NG, HD]), sb("L", [P, HD])
        o = sb("o", [P, NG, GE])
        om = sb("om", [P, H_MLA * V_DIM])
        pd, pm = ps("pd", [P, 512]), ps("pm", [P, 512])
        s = sems("x_loaded om_loaded steps diff_ready weights_ready o_ready o_turned oT_ready om_turned omT_ready")
        N = 11
        with nc.Block() as block:
            @block.sync
            def _(sp):
                with sp.Fori(0, NTP) as i:
                    sp.wait_ge(s.o_ready, i + CREDIT)
                    for g in range(NG):
                        sp.dma_start(x[:, g, :], a.dilo[g, ds(i * P, P), :]).then_inc(s.x_loaded, 16)
                    sp.wait_ge(s.om_turned, i + CREDIT)
                    sp.dma_start(om[:, :], a.omla[ds(i * P, P), :]).then_inc(s.om_loaded, 16)

            @block.scalar
            def _(act):
                with act.Fori(0, NTP) as i:
                    act.wait_ge(s.diff_ready, i + 1 + CREDIT)
                    act.activation(w[:, :, :], dm[:, :, :], ACT.Exp).then_inc(s.weights_ready, 1)
                    act.wait_ge(s.om_turned, i + 1 + CREDIT)
                    act.copy(r.oT_mla[:, :, ds(i * P, P)], pm[:, :].rearrange("p (h t) -> p h t", h=4)).then_inc(s.omT_ready, 1)

            @block.vector
            def _(dve):
                with dve.Fori(0, NTP) as i:
                    step = Steps(dve, s.steps, i, N)
                    dve.wait_ge(s.x_loaded, i * 48 + 48 + CREDIT)
                    nm = x[:, :, GE:GE + HD]
                    step(dve.tensor_tensor(nmx[:, :], nm[:, 0, :], nm[:, 1, :], ALU.min))
                    step(dve.tensor_tensor(nmx[:, :], nmx[:, :], nm[:, 2, :], ALU.min))
                    dve.tensor_tensor(dm[:, :, :], nmx[:, :].unsqueeze(1).broadcast_to([P, NG, HD]), nm, ALU.subtract
                                      ).then_inc(s.diff_ready, 1)
                    dve.wait_ge(s.weights_ready, i + 1 + CREDIT)
                    step(dve.tensor_tensor(wl[:, :, :], w[:, :, :], x[:, :, GE + HD:GE + 2 * HD], ALU.mult))
                    step(dve.tensor_tensor(L[:, :], wl[:, 0, :], wl[:, 1, :], ALU.add))
                    step(dve.tensor_tensor(L[:, :], L[:, :], wl[:, 2, :], ALU.add))
                    step(dve.reciprocal(L[:, :], L[:, :]))
                    step(dve.tensor_tensor(wl[:, :, :], w[:, :, :], L[:, :].unsqueeze(1).broadcast_to([P, NG, HD]), ALU.mult))
                    dve.wait_ge(s.o_turned, i + CREDIT)
                    for g in range(NG):
                        step(dve.tensor_tensor(o[:, g, :].rearrange("p (h e) -> p h e", h=HD),
                                               x[:, g, 0:GE].rearrange("p (h e) -> p h e", h=HD),
                                               wl[:, g, :].unsqueeze(2).broadcast_to([P, HD, E]), ALU.mult))
                    step(dve.tensor_tensor(o[:, 1, :], o[:, 1, :], o[:, 2, :], ALU.add))
                    dve.tensor_tensor(o[:, 0, :], o[:, 0, :], o[:, 1, :], ALU.add).then_inc(s.o_ready, 1)
                    step.end()
                    dve.wait_ge(s.o_turned, i + 1 + CREDIT)
                    dve.tensor_copy(r.oT_dil[:, :, ds(i * P, P)], pd[:, 0:2 * P].rearrange("p (h t) -> p h t", h=2)
                                    ).then_inc(s.oT_ready, 1)

            @block.tensor
            def _(pe):
                with pe.Fori(0, NTP) as i:
                    pe.wait_ge(s.om_loaded, i * 16 + 16 + CREDIT)
                    pe.wait_ge(s.omT_ready, i + CREDIT)
                    for k in range(4):
                        mm = pe.transpose(pm[:, k * P:(k + 1) * P], om[:, k * P:(k + 1) * P], r.ident)
                    mm.then_inc(s.om_turned, 1)
                    pe.wait_ge(s.o_ready, i + 1 + CREDIT)
                    pe.wait_ge(s.oT_ready, i + CREDIT)
                    for k in range(2):
                        mm = pe.transpose(pd[:, k * P:(k + 1) * P], o[:, 0, k * P:(k + 1) * P], r.ident)
                    mm.then_inc(s.o_turned, 1)


def latent_attention(nc, a, r):
    ctx, sb, ps, sems = stage(nc, "mla")
    HALF = 512
    with ctx:
        qT, kT = sb("qT", [QK, SEQ]), sb("kT", [QK, SEQ])
        w, v = sb("w", [P, 2, NOPE + V_DIM]), sb("v", [P, NTP, V_DIM])
        mask = sb("mask", [P, P])
        nm, nb, l, rl = sb("nm", [P, 2]), sb("nb", [P, 2]), sb("l", [P, 2]), sb("rl", [P, 2])
        p = [sb(f"p{u}", [P, SEQ]) for u in range(2)]
        pT, o = sb("pT", [P, NTP, P]), sb("o", [P, NTP, V_DIM])
        sc = [ps(f"sc{u}", [P, SEQ]) for u in range(2)]
        pt = [ps(f"pt{u}", [P, 512]) for u in range(2)]
        pu, pkv = ps("pu", [P, 512]), ps("pkv", [P, 512])
        s = sems("mask_loaded pe_copied q_loaded w_loaded kv_product k_copied v_copied scores_ready max_found bias_ready "
                 "probs_ready turned_lo turned_hi copied_lo copied_hi attended sum_inverted o_ready stored")
        wkv = a.w_kv_up.rearrange("(k p) (h c) -> p k h c", p=P, h=H_MLA)
        with nc.Block() as block:
            @block.sync
            def _(sp):
                sp.dma_start(mask[:, :], a.mask_mla).then_inc(s.mask_loaded, 16)
                with sp.Fori(0, H_MLA) as i:
                    sp.wait_ge(s.scores_ready, i * NTP + CREDIT)
                    sp.dma_start(qT[:, :], a.qT[:, ds(i, 1), 0:SEQ].squeeze(1)).then_inc(s.q_loaded, 16)
                    sp.wait_ge(s.kv_product, i * 3 + CREDIT)
                    sp.dma_start(w[:, :, :], wkv[:, :, ds(i, 1), :].squeeze(2)).then_inc(s.w_loaded, 16)
                    sp.wait_ge(s.o_ready, i * NTP + NTP + CREDIT)
                    sp.dma_start(a.omla[0:SEQ, ds(i * V_DIM, V_DIM)].rearrange("(q p) e -> p q e", p=P), o[:, :, :]
                                 ).then_inc(s.stored, 16)
                sp.wait_ge(s.stored, 16 * H_MLA + CREDIT)

            @block.tensor
            def _(pe):
                pe.wait_ge(s.mask_loaded, 16 + CREDIT)
                pe.wait_ge(s.pe_copied, 1 + CREDIT)
                with pe.Fori(0, H_MLA) as i:
                    pe.wait_ge(s.w_loaded, i * 16 + 16 + CREDIT)
                    for c in range(2):
                        pe.wait_ge(s.k_copied, i * 2 + c + CREDIT)
                        if c == 0:
                            pe.wait_ge(s.v_copied, i + CREDIT)
                        for k in range(2):
                            mm = pe.matmul(pkv[0:NOPE, :], w[:, k, 0:NOPE], r.ckvT[:, k, c * HALF:(c + 1) * HALF],
                                           start=(k == 0), stop=(k == 1))
                        mm.then_inc(s.kv_product, 1)
                    pe.wait_ge(s.k_copied, i * 2 + 2 + CREDIT)
                    for t in range(NTP):
                        for k in range(2):
                            mm = pe.matmul(pkv[:, t * V_DIM:(t + 1) * V_DIM], r.ckvT[:, k, t * P:(t + 1) * P],
                                           w[:, k, NOPE:], start=(k == 0), stop=(k == 1))
                    mm.then_inc(s.kv_product, 1)
                    pe.wait_ge(s.q_loaded, i * 16 + 16 + CREDIT)

                    def scores(b):
                        n = (b + 1) * P
                        pe.wait_ge(s.probs_ready, i * NTP + max(b - 1, 0) + CREDIT)
                        for c in range(0, n, HALF):
                            e = min(n, c + HALF)
                            mm = pe.matmul(sc[b % 2][:, c:e], qT[:, b * P:(b + 1) * P], kT[:, c:e], start=True, stop=(e < n))
                        pe.matmul(sc[b % 2][:, b * P:n], r.ident, mask[:, :], start=False, stop=True
                                  ).then_inc(s.scores_ready, 1)

                    scores(0)
                    for b in range(NTP):
                        if b + 1 < NTP:
                            scores(b + 1)
                        pe.wait_ge(s.probs_ready, i * NTP + b + 1 + CREDIT)
                        pe.wait_ge(s.copied_lo, i * NTP + b + CREDIT)
                        for k in range(min(b + 1, 4)):
                            mm = pe.transpose(pt[0][:, k * P:(k + 1) * P], p[b % 2][:, k * P:(k + 1) * P], r.ident)
                        mm.then_inc(s.turned_lo, 1)
                        if b >= 4:
                            pe.wait_ge(s.copied_hi, i * 4 + b - 4 + CREDIT)
                            for k in range(4, b + 1):
                                mm = pe.transpose(pt[1][:, (k - 4) * P:(k - 3) * P], p[b % 2][:, k * P:(k + 1) * P], r.ident)
                            mm.then_inc(s.turned_hi, 1)
                            pe.wait_ge(s.copied_hi, i * 4 + b - 3 + CREDIT)
                        pe.wait_ge(s.copied_lo, i * NTP + b + 1 + CREDIT)
                        pe.wait_ge(s.o_ready, i * NTP + b + CREDIT)
                        if b == 0:
                            pe.wait_ge(s.v_copied, i + 1 + CREDIT)
                        for k in range(b + 1):
                            mm = pe.matmul(pu[:, 0:V_DIM], pT[:, k, :], v[:, k, :], start=(k == 0), stop=(k == b))
                        mm.then_inc(s.attended, 1)

            @block.scalar
            def _(act):
                act.copy(kT[NOPE:QK, :], r.kpeT[NOPE:QK, 0:SEQ]).then_inc(s.pe_copied, 1)
                with act.Fori(0, H_MLA) as i:
                    act.wait_ge(s.scores_ready, i * NTP + CREDIT)
                    for c in range(2):
                        act.wait_ge(s.kv_product, i * 3 + c + 1 + CREDIT)
                        act.copy(kT[0:NOPE, c * HALF:(c + 1) * HALF], pkv[0:NOPE, :]).then_inc(s.k_copied, 1)
                    for b in range(NTP):
                        n = (b + 1) * P
                        act.wait_ge(s.bias_ready, i * NTP + b + 1 + CREDIT)
                        act.wait_ge(s.turned_lo, i * NTP + max(b - 1, 0) + CREDIT)
                        act.wait_ge(s.turned_hi, i * 4 + max(b - 5, 0) + CREDIT)
                        act.wait_ge(s.sum_inverted, i * NTP + max(b - 1, 0) + CREDIT)
                        act.activation(p[b % 2][:, 0:n], sc[b % 2][:, 0:n], ACT.Exp, bias=nb[:, b % 2:b % 2 + 1],
                                       scale=MLA_SCALE, accum_out=l[:, b % 2:b % 2 + 1]).then_inc(s.probs_ready, 1)
                        if b >= 4:
                            act.wait_ge(s.turned_hi, i * 4 + b - 3 + CREDIT)
                            act.wait_ge(s.attended, i * NTP + b + CREDIT)
                            act.copy(pT[:, 4:b + 1, :], pt[1][:, 0:(b - 3) * P].rearrange("p (k t) -> p k t", t=P)
                                     ).then_inc(s.copied_hi, 1)

            @block.vector
            def _(dve):
                with dve.Fori(0, H_MLA) as i:
                    dve.wait_ge(s.attended, i * NTP + CREDIT)
                    dve.wait_ge(s.kv_product, i * 3 + 3 + CREDIT)
                    dve.tensor_copy(v[:, :, :], pkv[:, :].rearrange("p (t e) -> p t e", e=V_DIM)).then_inc(s.v_copied, 1)
                    dve.wait_ge(s.stored, i * 16 + CREDIT)

                    def maximum(b):
                        dve.wait_ge(s.scores_ready, i * NTP + b + 1 + CREDIT)
                        dve.tensor_reduce(nm[:, b % 2:b % 2 + 1], sc[b % 2][:, 0:(b + 1) * P], AX.X, ALU.max, negate=True
                                          ).then_inc(s.max_found, 1)
                        dve.wait_ge(s.max_found, i * NTP + b + 1 + CREDIT)
                        dve.wait_ge(s.probs_ready, i * NTP + max(b - 1, 0) + CREDIT)
                        dve.tensor_scalar(nb[:, b % 2:b % 2 + 1], nm[:, b % 2:b % 2 + 1], MLA_SCALE, None, ALU.mult
                                          ).then_inc(s.bias_ready, 1)

                    maximum(0)
                    for b in range(NTP):
                        if b + 1 < NTP:
                            maximum(b + 1)
                        dve.wait_ge(s.turned_lo, i * NTP + b + 1 + CREDIT)
                        dve.wait_ge(s.attended, i * NTP + b + CREDIT)
                        m = min(b + 1, 4)
                        dve.tensor_copy(pT[:, 0:m, :], pt[0][:, 0:m * P].rearrange("p (k t) -> p k t", t=P)
                                        ).then_inc(s.copied_lo, 1)
                        dve.reciprocal(rl[:, b % 2:b % 2 + 1], l[:, b % 2:b % 2 + 1]).then_inc(s.sum_inverted, 1)
                        dve.wait_ge(s.sum_inverted, i * NTP + b + 1 + CREDIT)
                        dve.wait_ge(s.attended, i * NTP + b + 1 + CREDIT)
                        dve.tensor_scalar(o[:, b, :], pu[:, 0:V_DIM], rl[:, b % 2:b % 2 + 1], None, ALU.mult
                                          ).then_inc(s.o_ready, 1)


def sample_latent_attention(nc, a, r):
    ctx, sb, ps, sems = stage(nc, "smla")
    PG, RB = 4, 4
    NC = N_PAGES // PG
    ROUNDS = DB // RB
    QR = H_MLA * DT
    with ctx:
        w = sb("w", [P, 2, H_MLA, NOPE + V_DIM])
        wukT = sb("wukT", [NOPE, H_MLA, KV_LORA])
        qn, qp = sb("qn", [NOPE, H_MLA, NS]), sb("qp", [ROPE, H_MLA, NS])
        qlat, qpe = sb("qlat", [P, 2, DB, H_MLA, DT]), sb("qpe", [ROPE, DB, H_MLA, DT])
        kpn, rn = sb("kpn", [ROPE, NS]), sb("rn", [DT, DB, KV_LORA])
        mnew = sb("mnew", [P, DT])
        table = sb("table", [1, DB * N_PAGES], I32)
        kv = [sb(f"kv{u}", [P, RB, PG, ROW]) for u in range(2)]
        kT = [sb(f"kT{u}", [P, 2, PG * P]) for u in range(2)]
        kp = [sb(f"kp{u}", [ROPE, PG * P]) for u in range(2)]
        nm, nb, l = sb("nm", [P, 1]), sb("nb", [P, NC + 1]), sb("l", [P, NC + 1])
        p, pT = sb("p", [P, PG * P]), sb("pT", [P, PG, P])
        U = sb("U", [P, NC + 1, KV_LORA])
        sn, pn, pnT = sb("sn", [P, DT]), sb("pn", [P, DT]), sb("pnT", [DT, P])
        nmx, dm, wt, wl, L = sb("nmx", [P, 1]), sb("dm", [P, NC + 1]), sb("wt", [P, NC + 1]), sb("wl", [P, NC + 1]), sb("L", [P, 1])
        lat, latT = sb("lat", [P, KV_LORA]), sb("latT", [P, 2, H_MLA, RB * DT])
        o = sb("o", [RB * DT, H_MLA * V_DIM])
        b0 = [ps(f"b0{u}", [P, 512]) for u in range(2)]
        b1 = [ps(f"b1{u}", [P, 512]) for u in range(2)]
        bp = ps("bp", [P, 512])
        psc, ppt, pu = ps("psc", [P, 512]), ps("ppt", [P, 512]), ps("pu", [P, 512])
        s = sems("loaded zeroed w_turned wukT_ready q_product q_ready pages_loaded0 pages_loaded1 turned k0_copied k1_copied "
                 "kp_copied scores_ready max_found bias_ready probs_ready probs_turned pT_ready attended U_ready "
                 "new_scores new_masked new_max new_probs new_turned new_T new_attended new_copied steps diff_ready weights_ready "
                 "lat_ready lat_turned latT_ready o_product o_copied o_turned oT_ready")
        own = sems("pages_loaded_pool0 pages_loaded_pool1", 0)
        pages_loaded, pages_loaded_pool = (s.pages_loaded0, s.pages_loaded1), (own.pages_loaded_pool0, own.pages_loaded_pool1)
        N_MERGE = 6 + NC
        HALF = 16 * RB * PG // 2

        def load_pages(eng, rd, i, u, seqs, loaded):
            eng.wait_ge(s.attended, i * 2 + (rd * NC + max(u - 1, 0)) + CREDIT)
            for bb in seqs:
                for g in range(PG):
                    at = i * (2 * PG) + ((rd * RB + bb) * N_PAGES + u * PG + g)
                    page = eng.value_load(table[0:1, ds(at, 1)], min_val=0, max_val=POOL_PAGES - 1)
                    eng.dma_start(kv[u][:, bb, g, :], a.cache_mla[ds(page, 1), :, :].squeeze(0)).then_inc(loaded[u], 16)

        with nc.Block() as block:
            @block.sync
            def _(sp):
                for dst, src in (
                    (w[:, :, :, :], a.w_kv_up.rearrange("(k p) (h c) -> p k h c", p=P, h=H_MLA)),
                    (qn[:, :, :], a.qT[0:NOPE, :, SEQ:SEQ + NS]),
                    (qp[:, :, :], a.qT[NOPE:QK, :, SEQ:SEQ + NS]),
                    (rn[:, :, :], a.rows[SEQ:SEQ + NS, 0:KV_LORA].rearrange("(b t) c -> t b c", t=DT)),
                    (mnew[:, :], a.mask_new),
                    (table[:, :], a.page_table),
                ):
                    sp.dma_start(dst, src).then_inc(s.loaded, 16)
                with nc.allow_non_contiguous_dma("the new tokens' rotary keys, turned: 32 x 32 numbers"):
                    sp.dma_start(kpn[:, :], a.rows[SEQ:SEQ + NS, KV_LORA:ROW].rearrange("t c -> c t")).then_inc(s.loaded, 16)
                sp.wait_ge(s.loaded, 112 + CREDIT)
                for rd in range(ROUNDS):
                    with sp.Fori(0, NC // 2) as i:
                        for u in range(2):
                            load_pages(sp, rd, i, u, range(0, RB // 2), pages_loaded)

            @block.gpsimd
            def _(pool):
                pool.memset(r.oT_mla[:, :, SEQ + NS:T], 0.0)
                pool.memset(r.oT_dil[:, :, SEQ + NS:T], 0.0)
                pool.memset(r.oT_mem[:, :, SEQ + NS:T], 0.0).then_inc(s.zeroed, 1)
                pool.wait_ge(s.zeroed, 1 + CREDIT)
                pool.wait_ge(s.loaded, 112 + CREDIT)
                for rd in range(ROUNDS):
                    with pool.Fori(0, NC // 2) as i:
                        for u in range(2):
                            load_pages(pool, rd, i, u, range(RB // 2, RB), pages_loaded_pool)

            @block.tensor
            def _(pe):
                pe.wait_ge(s.loaded, 112 + CREDIT)
                for h in range(H_MLA):
                    for k in range(2):
                        n = 2 * h + k
                        bank = (b0 + b1)[n // 4]
                        mm = pe.transpose(bank[:, n % 4 * P:(n % 4 + 1) * P], w[:, k, h, :], r.ident)
                mm.then_inc(s.w_turned, 1)
                pe.wait_ge(s.wukT_ready, 4 + CREDIT)
                for k in range(2):
                    for h in range(H_MLA):
                        n = k * H_MLA + h
                        mm = pe.matmul(psc[:, n * NS:(n + 1) * NS], wukT[:, h, k * P:(k + 1) * P], qn[:, h, :],
                                       start=True, stop=True)
                mm.then_inc(s.q_product, 1)
                pe.wait_ge(s.q_ready, 3 + CREDIT)
                for rd in range(ROUNDS):
                    with pe.Fori(0, NC // 2) as i:
                        for u in range(2):
                            n = i * 2 + (rd * NC + u)
                            full = i * HALF + (rd * (NC // 2) + 1) * HALF
                            pe.wait_ge(pages_loaded[u], full + CREDIT)
                            pe.wait_ge(pages_loaded_pool[u], full)

                            def turn(bb):
                                m = n * RB + bb
                                pe.wait_ge(s.k0_copied, n * RB + max(bb - 1, 0) + CREDIT)
                                pe.wait_ge(s.k1_copied, n * RB + max(bb - 1, 0) + CREDIT)
                                pe.wait_ge(s.kp_copied, m + CREDIT)
                                for g in range(PG):
                                    pe.transpose(b0[bb % 2][:, g * P:(g + 1) * P], kv[u][:, bb, g, 0:P], r.ident)
                                for g in range(PG):
                                    pe.transpose(b1[bb % 2][:, g * P:(g + 1) * P], kv[u][:, bb, g, P:2 * P], r.ident)
                                for g in range(PG):
                                    mm = pe.transpose(bp[0:ROPE, g * P:(g + 1) * P], kv[u][:, bb, g, 2 * P:ROW], r.ident)
                                mm.then_inc(s.turned, 1)

                            def scores(bb):
                                m = n * RB + bb
                                b = rd * RB + bb
                                pe.wait_ge(s.k0_copied, m + 1 + CREDIT)
                                pe.wait_ge(s.k1_copied, m + 1 + CREDIT)
                                pe.wait_ge(s.kp_copied, m + 1 + CREDIT)
                                out = psc[bb * QR:(bb + 1) * QR, :]
                                for k in range(2):
                                    pe.matmul(out, qlat[:, k, b, :, :].rearrange("p h t -> p (h t)"), kT[bb % 2][:, k, :],
                                              start=(k == 0), stop=False)
                                pe.matmul(out, qpe[:, b, :, :].rearrange("p h t -> p (h t)"), kp[bb % 2][:, :],
                                          start=False, stop=True).then_inc(s.scores_ready, 1)

                            turn(0)
                            pe.wait_ge(s.probs_ready, n + CREDIT)
                            for bb in range(RB):
                                if bb + 1 < RB:
                                    turn(bb + 1)
                                scores(bb)
                            pe.wait_ge(s.probs_ready, n + 1 + CREDIT)
                            pe.wait_ge(s.pT_ready, n + CREDIT)
                            for g in range(PG):
                                mm = pe.transpose(ppt[:, g * P:(g + 1) * P], p[:, g * P:(g + 1) * P], r.ident)
                            mm.then_inc(s.probs_turned, 1)
                            pe.wait_ge(s.pT_ready, n + 1 + CREDIT)
                            pe.wait_ge(s.U_ready, n + CREDIT)
                            for bb in range(RB):
                                for g in range(PG):
                                    mm = pe.matmul(pu[bb * QR:(bb + 1) * QR, 0:KV_LORA], pT[:, g, bb * QR:(bb + 1) * QR],
                                                   kv[u][:, bb, g, 0:KV_LORA], start=(g == 0), stop=(g == PG - 1))
                            mm.then_inc(s.attended, 1)
                    pe.wait_ge(s.probs_ready, (rd + 1) * NC + CREDIT)
                    for bb in range(RB):
                        b = rd * RB + bb
                        out = psc[bb * QR:(bb + 1) * QR, 0:DT]
                        for k in range(2):
                            pe.matmul(out, qlat[:, k, b, :, :].rearrange("p h t -> p (h t)"),
                                      r.ckvT[:, k, SEQ + b * DT:SEQ + (b + 1) * DT], start=(k == 0), stop=False)
                        mm = pe.matmul(out, qpe[:, b, :, :].rearrange("p h t -> p (h t)"), kpn[:, b * DT:(b + 1) * DT],
                                       start=False, stop=True)
                    mm.then_inc(s.new_scores, 1)
                    pe.wait_ge(s.new_probs, rd + 1 + CREDIT)
                    pe.wait_ge(s.pT_ready, (rd + 1) * NC + CREDIT)
                    pe.transpose(ppt[0:DT, 0:P], pn[:, :], r.ident).then_inc(s.new_turned, 1)
                    pe.wait_ge(s.new_T, rd + 1 + CREDIT)
                    pe.wait_ge(s.U_ready, (rd + 1) * NC + CREDIT)
                    for bb in range(RB):
                        mm = pe.matmul(pu[bb * QR:(bb + 1) * QR, 0:KV_LORA], pnT[:, bb * QR:(bb + 1) * QR],
                                       rn[:, rd * RB + bb, :], start=True, stop=True)
                    mm.then_inc(s.new_attended, 1)
                    pe.wait_ge(s.lat_ready, rd + 1 + CREDIT)
                    for k in range(2):
                        mm = pe.transpose(b0[0][:, k * P:(k + 1) * P], lat[:, k * P:(k + 1) * P], r.ident)
                    mm.then_inc(s.lat_turned, 1)
                    pe.wait_ge(s.latT_ready, 2 * rd + 2 + CREDIT)
                    for h in range(H_MLA):
                        for k in range(2):
                            mm = pe.matmul(b1[0][0:RB * DT, h * V_DIM:(h + 1) * V_DIM], latT[:, k, h, :],
                                           w[:, k, h, NOPE:], start=(k == 0), stop=(k == 1))
                    mm.then_inc(s.o_product, 1)
                    pe.wait_ge(s.o_copied, rd + 1 + CREDIT)
                    for k in range(4):
                        mm = pe.transpose(b0[1][:, k * RB * DT:(k + 1) * RB * DT], o[:, k * P:(k + 1) * P],
                                          r.ident[0:RB * DT, 0:RB * DT])
                    mm.then_inc(s.o_turned, 1)
                    pe.wait_ge(s.oT_ready, rd + 1 + CREDIT)

            @block.scalar
            def _(act):
                for rd in range(ROUNDS):
                    with act.Fori(0, NC // 2) as i:
                        for u in range(2):
                            n = i * 2 + (rd * NC + u)
                            for bb in range(RB):
                                m = n * RB + bb
                                act.wait_ge(s.turned, m + 1 + CREDIT)
                                act.wait_ge(s.scores_ready, n * RB + max(bb - 1, 0) + CREDIT)
                                act.copy(kT[bb % 2][:, 1, :], b1[bb % 2][:, :]).then_inc(s.k1_copied, 1)
                            act.wait_ge(s.probs_turned, n + CREDIT)
                            act.wait_ge(s.bias_ready, n + 1 + CREDIT)
                            act.activation(p[:, :], psc[:, :], ACT.Exp, bias=nb[:, ds(i * 2 + u, 1)], scale=MLA_SCALE,
                                           accum_out=l[:, ds(i * 2 + u, 1)]).then_inc(s.probs_ready, 1)
                    act.wait_ge(s.new_max, rd + 1 + CREDIT)
                    act.activation(pn[:, :], sn[:, :], ACT.Exp, bias=nb[:, NC:NC + 1], accum_out=l[:, NC:NC + 1]
                                   ).then_inc(s.new_probs, 1)
                    act.wait_ge(s.diff_ready, rd + 1 + CREDIT)
                    act.activation(wt[:, :], dm[:, :], ACT.Exp).then_inc(s.weights_ready, 1)

            @block.vector
            def _(dve):
                dve.wait_ge(s.w_turned, 1 + CREDIT)
                for j, bank in enumerate(b0 + b1):
                    dve.tensor_copy(wukT[:, 2 * j:2 * j + 2, :].rearrange("n h c -> n (h c)"), bank[0:NOPE, :]
                                    ).then_inc(s.wukT_ready, 1)
                dve.wait_ge(s.q_product, 1 + CREDIT)
                for k in range(2):
                    src = psc[:, k * H_MLA * NS:(k + 1) * H_MLA * NS].rearrange("p (h b t) -> p h b t", h=H_MLA, b=DB)
                    dve.tensor_copy(qlat[:, k, :, :, :].rearrange("p b h t -> p h b t"), src).then_inc(s.q_ready, 1)
                dve.wait_ge(s.loaded, 112 + CREDIT)
                dve.tensor_copy(qpe[:, :, :, :].rearrange("p b h t -> p h b t"),
                                qp[:, :, :].rearrange("p h (b t) -> p h b t", b=DB)).then_inc(s.q_ready, 1)
                for rd in range(ROUNDS):
                    with dve.Fori(0, NC // 2) as i:
                        for u in range(2):
                            n = i * 2 + (rd * NC + u)
                            for bb in range(RB):
                                m = n * RB + bb
                                dve.wait_ge(s.turned, m + 1 + CREDIT)
                                dve.wait_ge(s.scores_ready, n * RB + max(bb - 1, 0) + CREDIT)
                                dve.tensor_copy(kp[bb % 2][:, :], bp[0:ROPE, :]).then_inc(s.kp_copied, 1)
                                dve.tensor_copy(kT[bb % 2][:, 0, :], b0[bb % 2][:, :]).then_inc(s.k0_copied, 1)
                            dve.wait_ge(s.scores_ready, n * RB + RB + CREDIT)
                            dve.tensor_reduce(nm[:, :], psc[:, :], AX.X, ALU.max, negate=True).then_inc(s.max_found, 1)
                            dve.wait_ge(s.max_found, n + 1 + CREDIT)
                            dve.tensor_scalar(nb[:, ds(i * 2 + u, 1)], nm[:, :], MLA_SCALE, None, ALU.mult
                                              ).then_inc(s.bias_ready, 1)
                            dve.wait_ge(s.probs_turned, n + 1 + CREDIT)
                            dve.wait_ge(s.attended, n + CREDIT)
                            dve.tensor_copy(pT[:, :, :].rearrange("p g t -> p (g t)"), ppt[:, :]).then_inc(s.pT_ready, 1)
                            dve.wait_ge(s.attended, n + 1 + CREDIT)
                            dve.tensor_copy(U[:, ds(i * 2 + u, 1), :].squeeze(1), pu[:, 0:KV_LORA]).then_inc(s.U_ready, 1)
                    step = Steps(dve, s.steps)
                    step.n = rd * N_MERGE
                    dve.wait_ge(s.new_scores, rd + 1 + CREDIT)
                    step(dve.scalar_tensor_tensor(out=sn[:, :], in0=psc[:, 0:DT], scalar=MLA_SCALE, in1=mnew[:, :],
                                                  op0=ALU.mult, op1=ALU.add))
                    dve.tensor_reduce(nb[:, NC:NC + 1], sn[:, :], AX.X, ALU.max, negate=True).then_inc(s.new_max, 1)
                    dve.wait_ge(s.new_turned, rd + 1 + CREDIT)
                    dve.tensor_copy(pnT[:, :], ppt[0:DT, 0:P]).then_inc(s.new_T, 1)
                    dve.wait_ge(s.new_attended, rd + 1 + CREDIT)
                    dve.tensor_copy(U[:, NC, :], pu[:, 0:KV_LORA]).then_inc(s.new_copied, 1)
                    dve.wait_ge(s.new_max, rd + 1 + CREDIT)
                    step(dve.tensor_reduce(nmx[:, :], nb[:, :], AX.X, ALU.min))
                    dve.tensor_scalar(dm[:, :], nb[:, :], nmx[:, 0:1], -1.0, ALU.subtract, ALU.mult).then_inc(s.diff_ready, 1)
                    dve.wait_ge(s.weights_ready, rd + 1 + CREDIT)
                    step(dve.tensor_tensor(wl[:, :], wt[:, :], l[:, :], ALU.mult))
                    step(dve.tensor_reduce(L[:, :], wl[:, :], AX.X, ALU.add))
                    step(dve.reciprocal(L[:, :], L[:, :]))
                    step(dve.tensor_scalar(wt[:, :], wt[:, :], L[:, 0:1], None, ALU.mult))
                    dve.wait_ge(s.new_copied, rd + 1 + CREDIT)
                    step(dve.tensor_scalar(lat[:, :], U[:, 0, :], wt[:, 0:1], None, ALU.mult))
                    for c in range(1, NC + 1):
                        ins = dve.scalar_tensor_tensor(out=lat[:, :], in0=U[:, c, :], scalar=wt[:, c:c + 1], in1=lat[:, :],
                                                       op0=ALU.mult, op1=ALU.add)
                        if c < NC:
                            step(ins)
                        else:
                            ins.then_inc(s.lat_ready, 1)
                    assert step.n == (rd + 1) * N_MERGE, step.n
                    dve.wait_ge(s.lat_turned, rd + 1 + CREDIT)
                    for k in range(2):
                        dve.tensor_copy(latT[:, k, :, :].rearrange("p h (b t) -> p h b t", b=RB),
                                        b0[0][:, k * P:(k + 1) * P].rearrange("p (b h t) -> p h b t", b=RB, h=H_MLA)
                                        ).then_inc(s.latT_ready, 1)
                    dve.wait_ge(s.o_product, rd + 1 + CREDIT)
                    dve.tensor_copy(o[:, :], b1[0][0:RB * DT, :]).then_inc(s.o_copied, 1)
                    dve.wait_ge(s.o_turned, rd + 1 + CREDIT)
                    at = SEQ + rd * RB * DT
                    dve.tensor_copy(r.oT_mla[:, :, at:at + RB * DT],
                                    b0[1][:, 0:4 * RB * DT].rearrange("p (k t) -> p k t", k=4)).then_inc(s.oT_ready, 1)


def sample_dilated_attention(nc, a, r):
    ctx, sb, ps, sems = stage(nc, "sdil")
    W = P + 1
    with ctx:
        q = sb("q", [P, NG, E])
        k, v = sb("k", [P, W, E]), sb("v", [P, W, E])
        sc, p = sb("sc", [P, W]), sb("p", [P, W])
        nm, nb, l = sb("nm", [P, 1]), sb("nb", [P, NG]), sb("l", [P, NG])
        U = sb("U", [P, NG, E])
        nmx, dm, wt, wl, L = sb("nmx", [P, 1]), sb("dm", [P, NG]), sb("wt", [P, NG]), sb("wl", [P, NG]), sb("L", [P, 1])
        o = sb("o", [P, E])
        po = ps("po", [P, 512])
        s = sems("q_loaded k_loaded v_loaded steps scored bias_ready probs_ready weighed diff_ready weights_ready o_ready "
                 "o_turned oT_ready")

        def window(eng, dst, g, j, loaded):
            dil = GROUPS[g][1]
            new = a.dil[SEQ:SEQ + NS, (1 + j) * NG * GE + g * GE:(1 + j) * NG * GE + (g + 1) * GE
                        ].rearrange("(b t) c -> b t c", t=DT)
            for t in range(DT):
                n_old = P - t if g == 0 else P
                first = 0 if g == 0 else t
                for h in range(HD):
                    at = dst[(t * HD + h) * DB:(t * HD + h + 1) * DB, :, :]
                    part = slice(h * E, (h + 1) * E)
                    old = a.cache_dil[g][:, t:t + (n_old - 1) * dil + 1:dil, j, part]
                    eng.dma_start(at[:, 0:n_old, :], old).then_inc(loaded, 16)
                    eng.dma_start(at[:, n_old:W, :], new[:, first:t + 1, part]).then_inc(loaded, 16)

        FULL = 16 * 2 * DT * HD
        with nc.Block() as block:
            @block.sync
            def _(sp):
                qs = a.dil[SEQ:SEQ + NS, 0:NG * GE].rearrange("(b t) (g h e) -> t h b g e", t=DT, g=NG, h=HD)
                for t in range(DT):
                    for h in range(HD):
                        sp.dma_start(q[(t * HD + h) * DB:(t * HD + h + 1) * DB, :, :], qs[t, h]).then_inc(s.q_loaded, 16)
                for g in range(NG):
                    if g:
                        sp.wait_ge(s.scored, g + CREDIT)
                    window(sp, k, g, 0, s.k_loaded)

            @block.vector
            def _(dve):
                step = Steps(dve, s.steps)
                dve.wait_ge(s.q_loaded, 16 * DT * HD + CREDIT)
                for g in range(NG):
                    dve.wait_ge(s.k_loaded, FULL * (g + 1) + CREDIT)
                    step(dve.tensor_tensor(k[:, :, :], k[:, :, :], q[:, g, :].unsqueeze(1).broadcast_to([P, W, E]), ALU.mult))
                    dve.tensor_reduce(sc[:, :], k[:, :, :], AX.X, ALU.add).then_inc(s.scored, 1)
                    dve.wait_ge(s.scored, g + 1 + CREDIT)
                    step(dve.tensor_reduce(nm[:, :], sc[:, :], AX.X, ALU.max, negate=True))
                    dve.tensor_scalar(nb[:, g:g + 1], nm[:, :], DIL_SCALE, None, ALU.mult).then_inc(s.bias_ready, 1)
                    dve.wait_ge(s.probs_ready, g + 1 + CREDIT)
                    dve.wait_ge(s.v_loaded, FULL * (g + 1) + CREDIT)
                    step(dve.tensor_tensor(v[:, :, :], v[:, :, :], p[:, :].unsqueeze(2).broadcast_to([P, W, E]), ALU.mult))
                    dve.tensor_reduce(U[:, g, :], v[:, :, :].rearrange("p l e -> p e l"), AX.X, ALU.add).then_inc(s.weighed, 1)
                dve.wait_ge(s.bias_ready, NG + CREDIT)
                step(dve.tensor_reduce(nmx[:, :], nb[:, :], AX.X, ALU.min))
                dve.tensor_scalar(dm[:, :], nb[:, :], nmx[:, 0:1], -1.0, ALU.subtract, ALU.mult).then_inc(s.diff_ready, 1)
                dve.wait_ge(s.weights_ready, 1 + CREDIT)
                step(dve.tensor_tensor(wl[:, :], wt[:, :], l[:, :], ALU.mult))
                step(dve.tensor_reduce(L[:, :], wl[:, :], AX.X, ALU.add))
                step(dve.reciprocal(L[:, :], L[:, :]))
                step(dve.tensor_scalar(wt[:, :], wt[:, :], L[:, 0:1], None, ALU.mult))
                dve.wait_ge(s.weighed, NG + CREDIT)
                step(dve.tensor_scalar(o[:, :], U[:, 0, :], wt[:, 0:1], None, ALU.mult))
                step(dve.scalar_tensor_tensor(out=o[:, :], in0=U[:, 1, :], scalar=wt[:, 1:2], in1=o[:, :],
                                              op0=ALU.mult, op1=ALU.add))
                dve.scalar_tensor_tensor(out=o[:, :], in0=U[:, 2, :], scalar=wt[:, 2:3], in1=o[:, :],
                                         op0=ALU.mult, op1=ALU.add).then_inc(s.o_ready, 1)
                dve.wait_ge(s.o_turned, 1 + CREDIT)
                for h in range(HD):
                    at = slice(h % 2 * E, (h % 2 + 1) * E)
                    dve.tensor_copy(r.oT_dil[at, h // 2, SEQ:SEQ + NS].rearrange("e (b t) -> e t b", t=DT),
                                    po[0:E, 0:P].rearrange("e (t h b) -> e h t b", t=DT, h=HD)[:, h]).then_inc(s.oT_ready, 1)

            @block.scalar
            def _(act):
                for g in range(NG):
                    if g:
                        act.wait_ge(s.weighed, g + CREDIT)
                    window(act, v, g, 1, s.v_loaded)
                    act.wait_ge(s.bias_ready, g + 1 + CREDIT)
                    act.activation(p[:, :], sc[:, :], ACT.Exp, bias=nb[:, g:g + 1], scale=DIL_SCALE,
                                   accum_out=l[:, g:g + 1]).then_inc(s.probs_ready, 1)
                act.wait_ge(s.diff_ready, 1 + CREDIT)
                act.activation(wt[:, :], dm[:, :], ACT.Exp).then_inc(s.weights_ready, 1)

            @block.tensor
            def _(pe):
                pe.wait_ge(s.o_ready, 1 + CREDIT)
                pe.transpose(po[0:E, 0:P], o[:, :], r.ident).then_inc(s.o_turned, 1)


def sample_memory_attention(nc, a, r):
    ctx, sb, ps, sems = stage(nc, "smem")
    R = HM * DT
    with ctx:
        x, qT = sb("x", [NS, HM * EM]), sb("qT", [P, HM, NS])
        kv, kT = sb("kv", [P, 2, 2 * HM * EM]), sb("kT", [P, HM, 2, P])
        sT, p, pT = sb("sT", [P, 2, R]), sb("p", [P, MEM]), sb("pT", [P, 2, R])
        nm, nb, l = sb("nm", [R, 1]), sb("nb", [R, 1]), sb("l", [R, 1])
        pq = ps("pq", [P, 512])
        pk = [ps(f"pk{u}", [P, 512]) for u in range(2)]
        pst, psc, ppt, po = ps("pst", [P, 512]), ps("psc", [P, 512]), ps("ppt", [P, 512]), ps("po", [P, 512])
        s = sems("zeroed x_loaded q_turned qT_ready kv_loaded k_turned kT_ready product_ready sT_ready scores_ready max_found bias_ready "
                 "exp_ready inverted probs_ready probs_turned pT_ready attended oT_ready")
        with nc.Block() as block:
            @block.sync
            def _(sp):
                sp.dma_start(x[:, :], a.proj[SEQ:SEQ + NS, C_MEM:C_GATE]).then_inc(s.x_loaded, 16)
                with sp.Fori(0, DB) as i:
                    sp.wait_ge(s.attended, i + CREDIT)
                    sp.dma_start(kv[:, :, :], a.cache_mem[ds(i, 1), :, :].squeeze(0).rearrange("(m p) c -> p m c", p=P)
                                 ).then_inc(s.kv_loaded, 16)

            @block.gpsimd
            def _(pool):
                pool.memset(p[:, :], 0.0).then_inc(s.zeroed, 1)
                pool.wait_ge(s.zeroed, 1 + CREDIT)

            @block.tensor
            def _(pe):
                pe.wait_ge(s.x_loaded, 16 + CREDIT)
                for h in range(HM):
                    mm = pe.transpose(pq[:, h * NS:(h + 1) * NS], x[:, h * EM:(h + 1) * EM], r.ident[0:NS, 0:NS])
                mm.then_inc(s.q_turned, 1)
                pe.wait_ge(s.qT_ready, 1 + CREDIT)
                with pe.Fori(0, DB) as i:
                    pe.wait_ge(s.kv_loaded, i * 16 + 16 + CREDIT)
                    pe.wait_ge(s.kT_ready, i * 2 + CREDIT)
                    for h in range(HM):
                        for m in range(2):
                            mm = pe.transpose(pk[h // 2][:, (h % 2 * 2 + m) * P:(h % 2 * 2 + m + 1) * P],
                                              kv[:, m, h * EM:(h + 1) * EM], r.ident)
                    mm.then_inc(s.k_turned, 1)
                    pe.wait_ge(s.kT_ready, i * 2 + 2 + CREDIT)
                    pe.wait_ge(s.sT_ready, i + CREDIT)
                    for m in range(2):
                        for h in range(HM):
                            mm = pe.matmul(pst[:, m * R + h * DT:m * R + (h + 1) * DT], kT[:, h, m, :],
                                           qT[:, h, ds(i * DT, DT)], start=True, stop=True)
                    mm.then_inc(s.product_ready, 1)
                    pe.wait_ge(s.sT_ready, i + 1 + CREDIT)
                    pe.wait_ge(s.exp_ready, i + CREDIT)
                    for m in range(2):
                        mm = pe.transpose(psc[0:R, m * P:(m + 1) * P], sT[:, m, :], r.ident)
                    mm.then_inc(s.scores_ready, 1)
                    pe.wait_ge(s.probs_ready, i + 1 + CREDIT)
                    pe.wait_ge(s.pT_ready, i + CREDIT)
                    for m in range(2):
                        mm = pe.transpose(ppt[:, m * P:(m + 1) * P], p[:, m * P:(m + 1) * P], r.ident)
                    mm.then_inc(s.probs_turned, 1)
                    pe.wait_ge(s.pT_ready, i + 1 + CREDIT)
                    pe.wait_ge(s.oT_ready, i + CREDIT)
                    for h in range(HM):
                        for m in range(2):
                            mm = pe.matmul(po[:, h * DT:(h + 1) * DT], kv[:, m, (HM + h) * EM:(HM + h + 1) * EM],
                                           pT[:, m, h * DT:(h + 1) * DT], start=(m == 0), stop=(m == 1))
                    mm.then_inc(s.attended, 1)

            @block.scalar
            def _(act):
                act.wait_ge(s.zeroed, 1 + CREDIT)
                with act.Fori(0, DB) as i:
                    act.wait_ge(s.bias_ready, i + 1 + CREDIT)
                    act.wait_ge(s.probs_turned, i + CREDIT)
                    act.activation(p[0:R, :], psc[0:R, 0:MEM], ACT.Exp, bias=nb[:, :], scale=MEM_SCALE, accum_out=l[:, :]
                                   ).then_inc(s.exp_ready, 1)

            @block.vector
            def _(dve):
                dve.wait_ge(s.q_turned, 1 + CREDIT)
                dve.tensor_copy(qT[:, :, :].rearrange("p h t -> p (h t)"), pq[:, 0:HM * NS]).then_inc(s.qT_ready, 1)
                with dve.Fori(0, DB) as i:
                    dve.wait_ge(s.k_turned, i + 1 + CREDIT)
                    dve.wait_ge(s.product_ready, i + CREDIT)
                    for u in range(2):
                        dve.tensor_copy(kT[:, 2 * u:2 * u + 2, :, :].rearrange("p h m t -> p (h m t)"), pk[u][:, :]
                                        ).then_inc(s.kT_ready, 1)
                    dve.wait_ge(s.product_ready, i + 1 + CREDIT)
                    dve.wait_ge(s.scores_ready, i + CREDIT)
                    dve.tensor_copy(sT[:, :, :].rearrange("p m q -> p (m q)"), pst[:, 0:2 * R]).then_inc(s.sT_ready, 1)
                    dve.wait_ge(s.scores_ready, i + 1 + CREDIT)
                    dve.tensor_reduce(nm[:, :], psc[0:R, 0:MEM], AX.X, ALU.max, negate=True).then_inc(s.max_found, 1)
                    dve.wait_ge(s.max_found, i + 1 + CREDIT)
                    dve.tensor_scalar(nb[:, :], nm[:, :], MEM_SCALE, None, ALU.mult).then_inc(s.bias_ready, 1)
                    dve.wait_ge(s.exp_ready, i + 1 + CREDIT)
                    dve.reciprocal(nm[:, :], l[:, :]).then_inc(s.inverted, 1)
                    dve.wait_ge(s.inverted, i + 1 + CREDIT)
                    dve.tensor_scalar(p[0:R, :], p[0:R, :], nm[:, 0:1], None, ALU.mult).then_inc(s.probs_ready, 1)
                    dve.wait_ge(s.probs_turned, i + 1 + CREDIT)
                    dve.wait_ge(s.attended, i + CREDIT)
                    dve.tensor_copy(pT[:, :, :], ppt[:, 0:2 * P].rearrange("p (m q) -> p m q", m=2)[:, :, 0:R]).then_inc(s.pT_ready, 1)
                    dve.wait_ge(s.attended, i + 1 + CREDIT)
                    dve.tensor_copy(r.oT_mem[:, :, ds(i * DT + SEQ, DT)], po[:, 0:R].rearrange("p (h t) -> p h t", h=HM)
                                    ).then_inc(s.oT_ready, 1)


def mix_branches(nc, a, r, xT, mT):
    ctx, sb, ps, sems = stage(nc, "mix")
    TH = T // 3
    UN = 9
    with ctx:
        wg = [sb(f"wg{u}", [P, KD, 3, P]) for u in range(2)]
        wo = [sb(f"wo{u}", [P, 10, P]) for u in range(2)]
        sg = [sb(f"sg{u}", [P, TH]) for u in range(2)]
        pr = [sb(f"pr{u}", [P, TH]) for u in range(3)]
        pg, py = [ps(f"pg{u}", [P, 512]) for u in range(2)], [ps(f"py{u}", [P, 512]) for u in range(2)]
        s = sems("w_loaded0 w_loaded1 product_ready gate_ready weighed steps summed")
        w_loaded = (s.w_loaded0, s.w_loaded1)
        gates = a.w_in[:, C_GATE:].rearrange("(k p) (b n) -> p k b n", p=P, b=3)
        branches = ((a.w_o_mla, r.oT_mla, 0, 4), (a.w_o_dil, r.oT_dil, 4, 2), (a.w_o_mem, r.oT_mem, 6, 4))
        with nc.Block() as block:
            @block.sync
            def _(sp):
                with sp.Fori(0, KD // 2) as i:
                    for u in range(2):
                        sp.wait_ge(s.product_ready, i * (2 * UN) + CREDIT)
                        col = ds(i * (2 * P) + u * P, P)
                        for b in range(3):
                            sp.dma_start(wg[u][:, :, b, :], gates[:, :, b, col]).then_inc(w_loaded[u], 16)
                        for w, _, k0, kk in branches:
                            sp.dma_start(wo[u][:, k0:k0 + kk, :], w.rearrange("(k p) n -> p k n", p=P)[:, :, col]
                                         ).then_inc(w_loaded[u], 16)

            @block.tensor
            def _(pe):
                with pe.Fori(0, KD // 2) as i:
                    for u in range(2):
                        pe.wait_ge(w_loaded[u], i * 96 + 96 + CREDIT)
                        for n in range(UN):
                            m = u * UN + n
                            rows = slice(n // 3 * TH, (n // 3 + 1) * TH)
                            _, oT, k0, kk = branches[n % 3]
                            pe.wait_ge(s.weighed, i * (2 * UN) + max(m - 1, 0) + CREDIT)
                            for k in range(KD):
                                pe.matmul(pg[m % 2][:, 0:TH], wg[u][:, k, n % 3, :], xT[:, k, rows],
                                          start=(k == 0), stop=(k == KD - 1))
                            for k in range(kk):
                                mm = pe.matmul(py[m % 2][:, 0:TH], wo[u][:, k0 + k, :], oT[:, k, rows],
                                               start=(k == 0), stop=(k == kk - 1))
                            mm.then_inc(s.product_ready, 1)

            @block.scalar
            def _(act):
                with act.Fori(0, KD // 2) as i:
                    for m in range(2 * UN):
                        act.wait_ge(s.product_ready, i * (2 * UN) + m + 1 + CREDIT)
                        act.wait_ge(s.weighed, i * (2 * UN) + max(m - 1, 0) + CREDIT)
                        act.activation(sg[m % 2][:, :], pg[m % 2][:, 0:TH], ACT.Sigmoid).then_inc(s.gate_ready, 1)

            @block.vector
            def _(dve):
                with dve.Fori(0, KD // 2) as i:
                    step = Steps(dve, s.steps, i, 6)
                    for m in range(2 * UN):
                        dve.wait_ge(s.gate_ready, i * (2 * UN) + m + 1 + CREDIT)
                        dve.tensor_tensor(pr[m % 3][:, :], sg[m % 2][:, :], py[m % 2][:, 0:TH], ALU.mult).then_inc(s.weighed, 1)
                        if m % 3 == 2:
                            dve.wait_ge(s.weighed, i * (2 * UN) + m + 1 + CREDIT)
                            step(dve.tensor_tensor(pr[0][:, :], pr[0][:, :], pr[1][:, :], ALU.add))
                            third = m % UN // 3
                            dst = mT[:, ds(i * 2 + m // UN, 1), third * TH:(third + 1) * TH].squeeze(1)
                            dve.tensor_tensor(dst, pr[0][:, :], pr[2][:, :], ALU.add).then_inc(s.summed, 1)
                            dve.wait_ge(s.summed, i * 6 + m // 3 + 1 + CREDIT)
                    step.end()


def peer_scores(nc, a, r, xT):
    ctx, sb, ps, sems = stage(nc, "psc")
    TH = T // 3
    with ctx:
        keys, keysT = sb("keys", [P, 2, QH]), sb("keysT", [P, 2, NK])
        w = [sb(f"w{u}", [P, KD, QH]) for u in range(2)]
        qT = [sb(f"qT{u}", [P, T]) for u in range(2)]
        sc = [sb(f"sc{u}", [P, NT, NK]) for u in range(2)]
        pq = [ps(f"pq{u}", [P, 512]) for u in range(3)]
        psc = [ps(f"psc{u}", [P, 512]) for u in range(3)]
        s = sems("keys_loaded keys_turned keysT_ready w_loaded0 w_loaded1 q_product qT_ready scores_ready scores_copied "
                 "stored0 stored1")
        w_loaded, stored = (s.w_loaded0, s.w_loaded1), (s.stored0, s.stored1)
        wv = a.w_peer_q.rearrange("(k p) n -> p k n", p=P)
        dst = a.scores.rearrange("(t p) c n -> p t c n", p=P)
        with nc.Block() as block:
            @block.sync
            def _(sp):
                sp.dma_start(keys[:, :, :], a.peer_sub_keys.rearrange("c n e -> n c e")).then_inc(s.keys_loaded, 16)
                with sp.Fori(0, HP) as i:
                    for u in range(2):
                        sp.wait_ge(s.q_product, i * 6 + CREDIT)
                        sp.dma_start(w[u][:, :, :], wv[:, :, ds(i * (2 * QH) + u * QH, QH)]).then_inc(w_loaded[u], 16)

            @block.tensor
            def _(pe):
                pe.wait_ge(s.keys_loaded, 16 + CREDIT)
                for u in range(2):
                    mm = pe.transpose(pq[0][:, u * P:(u + 1) * P], keys[:, u, :], r.ident)
                mm.then_inc(s.keys_turned, 1)
                pe.wait_ge(s.keysT_ready, 1 + CREDIT)
                with pe.Fori(0, HP) as i:
                    for u in range(2):
                        pe.wait_ge(w_loaded[u], i * 16 + 16 + CREDIT)
                        for c in range(3):
                            pe.wait_ge(s.qT_ready, i * 6 + (c + 1 if u else 0) + CREDIT)
                            for k in range(KD):
                                mm = pe.matmul(pq[c][:, 0:TH], w[u][:, k, :], xT[:, k, c * TH:(c + 1) * TH],
                                               start=(k == 0), stop=(k == KD - 1))
                            mm.then_inc(s.q_product, 1)
                        for c in range(3):
                            pe.wait_ge(s.qT_ready, i * 6 + 3 * u + c + 1 + CREDIT)
                            pe.wait_ge(s.scores_copied, i * 6 + (c + 1 if u else 0) + CREDIT)
                            for t in range(3):
                                n = 3 * c + t
                                mm = pe.matmul(psc[c][:, t * NK:(t + 1) * NK], qT[u][:, n * P:(n + 1) * P], keysT[:, u, :],
                                               start=True, stop=True)
                            mm.then_inc(s.scores_ready, 1)

            @block.scalar
            def _(act):
                with act.Fori(0, HP) as i:
                    for u in range(2):
                        act.wait_ge(s.scores_ready, i * 6 + CREDIT)
                        for c in range(3):
                            act.wait_ge(s.q_product, i * 6 + 3 * u + c + 1 + CREDIT)
                            act.copy(qT[u][:, c * TH:(c + 1) * TH], pq[c][:, 0:TH]).then_inc(s.qT_ready, 1)
                        act.wait_ge(s.scores_copied, i * 6 + 3 * u + 3 + CREDIT)
                        act.dma_start(dst[:, :, ds(i * 2 + u, 1), :].squeeze(2), sc[u][:, :, :]).then_inc(stored[u], 16)
                for u in range(2):
                    act.wait_ge(stored[u], 16 * HP + CREDIT)

            @block.vector
            def _(dve):
                dve.wait_ge(s.keys_turned, 1 + CREDIT)
                dve.tensor_copy(keysT[:, :, :].rearrange("p c n -> p (c n)"), pq[0][:, 0:2 * P]).then_inc(s.keysT_ready, 1)
                with dve.Fori(0, HP) as i:
                    for u in range(2):
                        dve.wait_ge(stored[u], i * 16 + CREDIT)
                        for c in range(3):
                            dve.wait_ge(s.scores_ready, i * 6 + 3 * u + c + 1 + CREDIT)
                            dve.tensor_copy(sc[u][:, 3 * c:3 * c + 3, :].rearrange("p t n -> p (t n)"), psc[c][:, 0:3 * NK]
                                            ).then_inc(s.scores_copied, 1)


def peer_choose(nc, a, r):
    ctx, sb, ps, sems = stage(nc, "top")
    G2 = 2 * HP
    with ctx:
        S = sb("S", [P, G2, NK])
        m, ix, ixf = sb("m", [P, G2, TOPK]), sb("ix", [P, G2, TOPK], U32), sb("ixf", [P, G2, TOPK])
        cand = sb("cand", [P, HP, TOPK * TOPK])
        best, jx = sb("best", [P, HP, TOPK]), sb("jx", [P, HP, TOPK], U32)
        part, partf = sb("part", [P, 2, SLOTS], U32), sb("partf", [P, 2, SLOTS])
        hot = sb("hot", [P, SLOTS, TOPK])
        num, ef, eid = sb("num", [P, 2, SLOTS]), sb("ef", [P, SLOTS]), sb("eid", [P, SLOTS], U32)
        d, ex, sm, gate = sb("d", [P, HP, TOPK]), sb("ex", [P, HP, TOPK]), sb("sm", [P, HP]), sb("gate", [P, HP, TOPK])
        iota, held = sb("iota", [P, TOPK]), sb("held", [P, 1])
        s = sems("iota_loaded loaded steps chosen stored diff_ready exp_ready sum_ready sum_inverted")
        N = 22
        with nc.Block() as block:
            @block.sync
            def _(sp):
                sp.dma_start(iota[:, :], a.iota16).then_inc(s.iota_loaded, 16)
                with sp.Fori(0, NT) as i:
                    sp.wait_ge(s.chosen, i + CREDIT)
                    sp.dma_start(S[:, :, :], a.scores[ds(i * P, P), :, :]).then_inc(s.loaded, 16)
                    sp.wait_ge(s.chosen, i + 1 + CREDIT)
                    sp.dma_start(a.experts[ds(i * P, P), :], eid[:, :]).then_inc(s.stored, 16)
                    sp.dma_start(a.gates[ds(i * P, P), :], gate[:, :, :].rearrange("p h k -> p (h k)")).then_inc(s.stored, 16)
                sp.wait_ge(s.stored, 32 * NT + CREDIT)

            @block.scalar
            def _(act):
                with act.Fori(0, NT) as i:
                    act.wait_ge(s.diff_ready, i + 1 + CREDIT)
                    act.activation(ex[:, :, :], d[:, :, :], ACT.Exp).then_inc(s.exp_ready, 1)

            @block.vector
            def _(dve):
                dve.wait_ge(s.iota_loaded, 16 + CREDIT)
                with dve.Fori(0, NT) as i:
                    step = Steps(dve, s.steps, i, N)

                    def hold():
                        dve.memset(held[:, :], 0.0)

                    def top16(values, n, out, index):
                        for half in range(2):
                            at = slice(8 * half, 8 * half + 8)
                            hold()
                            for j in range(n):
                                ins = dve.max(out[:, j, at], values[:, j, :])
                            step(ins)
                            hold()
                            for j in range(n):
                                ins = dve.max_index(index[:, j, at], out[:, j, at], values[:, j, :])
                            step(ins)
                            if half == 0:
                                hold()
                                for j in range(n):
                                    ins = dve.match_replace(values[:, j, :], out[:, j, at], values[:, j, :], NEG)
                                step(ins)

                    dve.wait_ge(s.loaded, i * 16 + 16 + CREDIT)
                    top16(S, G2, m, ix)
                    step(dve.tensor_copy(ixf[:, :, :], ix[:, :, :]))
                    mv = m[:, :, :].rearrange("p (h c) k -> p h c k", c=2)
                    iv = ixf[:, :, :].rearrange("p (h c) k -> p h c k", c=2)
                    square = [P, HP, TOPK, TOPK]
                    step(dve.tensor_tensor(cand[:, :, :].rearrange("p h (x y) -> p h x y", x=TOPK),
                                           mv[:, :, 0, :].unsqueeze(3).broadcast_to(square),
                                           mv[:, :, 1, :].unsqueeze(2).broadcast_to(square), ALU.add))
                    top16(cand, HP, best, jx)
                    dve.tensor_tensor(d[:, :, :], best[:, :, :], best[:, :, 0:1].broadcast_to([P, HP, TOPK]), ALU.subtract
                                      ).then_inc(s.diff_ready, 1)
                    jf = jx[:, :, :].rearrange("p h k -> p (h k)")
                    step(dve.tensor_scalar(part[:, 0, :], jf, 4, None, ALU.logical_shift_right))
                    step(dve.tensor_scalar(part[:, 1, :], jf, TOPK - 1, None, ALU.bitwise_and))
                    step(dve.tensor_copy(partf[:, :, :], part[:, :, :]))
                    hv = hot[:, :, :].rearrange("p (h k) x -> p h k x", h=HP)
                    for c in range(2):
                        step(dve.tensor_tensor(hot[:, :, :], partf[:, c, :].unsqueeze(2).broadcast_to([P, SLOTS, TOPK]),
                                               iota[:, :].unsqueeze(1).broadcast_to([P, SLOTS, TOPK]), ALU.is_equal))
                        step(dve.tensor_tensor(hv, hv, iv[:, :, c, :].unsqueeze(2).broadcast_to(square), ALU.mult))
                        step(dve.tensor_reduce(num[:, c, :], hot[:, :, :], AX.X, ALU.add))
                    step(dve.scalar_tensor_tensor(out=ef[:, :], in0=num[:, 0, :], scalar=float(NK), in1=num[:, 1, :],
                                                  op0=ALU.mult, op1=ALU.add))
                    dve.wait_ge(s.stored, i * 32 + CREDIT)
                    step.end()
                    dve.tensor_copy(eid[:, :], ef[:, :])
                    dve.wait_ge(s.exp_ready, i + 1 + CREDIT)
                    dve.tensor_reduce(sm[:, :], ex[:, :, :], AX.X, ALU.add).then_inc(s.sum_ready, 1)
                    dve.wait_ge(s.sum_ready, i + 1 + CREDIT)
                    dve.reciprocal(sm[:, :], sm[:, :]).then_inc(s.sum_inverted, 1)
                    dve.wait_ge(s.sum_inverted, i + 1 + CREDIT)
                    dve.tensor_tensor(gate[:, :, :], ex[:, :, :], sm[:, :].unsqueeze(2).broadcast_to([P, HP, TOPK]), ALU.mult
                                      ).then_inc(s.chosen, 1)


def peer_experts(nc, a, r):
    ctx, sb, ps, sems = stage(nc, "peer")
    GROUP = 8
    NGR = SLOTS // GROUP
    RING = 2 * GROUP
    with ctx:
        x, h = sb("x", [P, D]), sb("h", [P, D])
        eid, gate = sb("eid", [P, SLOTS], U32), sb("gate", [P, SLOTS])
        ub = [sb(f"ub{u}", [P, D]) for u in range(RING)]
        vb = [sb(f"vb{u}", [P, D]) for u in range(RING)]
        zero, held_u, held_v = sb("zero", [P, 1]), sb("held_u", [P, 1]), sb("held_v", [P, 1])
        act_in, gl, coef = sb("act_in", [P, SLOTS]), sb("gl", [P, SLOTS]), sb("coef", [P, SLOTS])
        dg = [sb(f"dg{u}", [P, P]) for u in range(RING)]
        g, y = sb("g", [P, D]), sb("y", [P, D])
        ss, ms, rt, rstd = sb("ss", [P, 1]), sb("ms", [P, 1]), sb("rt", [P, 1]), sb("rstd", [P, 1])
        acc = [ps(f"acc{u}", [P, 512]) for u in range(2)]
        own = sems("u_loaded0 u_loaded1 v_loaded0 v_loaded1", 0)
        s = sems("zeroed u_wait_taken v_wait_taken g_loaded eid_loaded gate_loaded x_loaded h_loaded dotted gelu_ready "
                 "coef_ready diag_ready v_used squares_summed mean_ready root_ready rstd_ready y_ready h_added stored")
        u_loaded, v_loaded = (own.u_loaded0, own.u_loaded1), (own.v_loaded0, own.v_loaded1)
        FULL = 16 * GROUP

        def tiles(eng):
            with eng.Fori(0, NTP) as i:
                yield i, P, i * P
            yield NTP, NS, SEQ

        with nc.Block() as block:
            @block.sync
            def _(sp):
                sp.dma_start(g[:, :], a.g_final.partition_broadcast(P)).then_inc(s.g_loaded, 16)
                for i, n, at in tiles(sp):
                    rows = ds(at, n)
                    sp.wait_ge(s.v_used, i * NGR + CREDIT)
                    sp.dma_start(eid[0:n, :], a.experts[rows, :]).then_inc(s.eid_loaded, 16)
                    sp.wait_ge(s.dotted, i * NGR + CREDIT)
                    sp.dma_start(x[0:n, :], a.xn2[rows, :]).then_inc(s.x_loaded, 16)
                    sp.wait_ge(s.coef_ready, i + CREDIT)
                    sp.dma_start(gate[0:n, :], a.gates[rows, :]).then_inc(s.gate_loaded, 16)
                    sp.wait_ge(s.y_ready, i + CREDIT)
                    sp.dma_start(h[0:n, :], a.h[rows, :]).then_inc(s.h_loaded, 16)

            @block.gpsimd
            def _(pool):
                pool.memset(zero[:, :], 0.0).then_inc(s.zeroed, 1)
                pool.wait_ge(s.zeroed, 1 + CREDIT)
                for i, n, at in tiles(pool):
                    pool.wait_ge(s.eid_loaded, i * 16 + 16 + CREDIT)
                    for bufs, loaded, used, table, held, taken in ((ub, u_loaded, s.dotted, a.peer_u, held_u, s.u_wait_taken),
                                                                   (vb, v_loaded, s.v_used, a.peer_v, held_v, s.v_wait_taken)):
                        for j in range(NGR):
                            pool.wait_ge(taken, i * NGR + j + CREDIT)
                            pool.wait_ge(used, i * NGR + max(j - 1, 0) + CREDIT)
                            pool.tensor_tensor(held[:, :], zero[:, :], zero[:, :], ALU.add).then_inc(taken, 1)
                            for k in range(j * GROUP, (j + 1) * GROUP):
                                pool.indirect_dma_start(bufs[k % RING][0:n, :], None, table,
                                                        bass.IndirectOffsetOnAxis(ap=eid[0:n, k:k + 1], axis=0)
                                                        ).then_inc(loaded[j % 2], 16)

            @block.vector
            def _(dve):
                dve.wait_ge(s.g_loaded, 16 + CREDIT)
                for i, n, at in tiles(dve):
                    dve.wait_ge(s.x_loaded, i * 16 + 16 + CREDIT)
                    dve.wait_ge(s.gelu_ready, i + CREDIT)
                    for k in range(SLOTS):
                        j = k // GROUP
                        if k % GROUP == 0:
                            dve.wait_ge(u_loaded[j % 2], i * (FULL * NGR // 2) + FULL * (j // 2 + 1))
                        ins = dve.tensor_tensor_reduce(out=ub[k % RING][0:n, :], in0=ub[k % RING][0:n, :], in1=x[0:n, :], scale=1.0, scalar=0.0,
                                                 op0=ALU.mult, op1=ALU.add, accum_out=act_in[0:n, k:k + 1])
                        if k % GROUP == GROUP - 1:
                            ins.then_inc(s.dotted, 1)
                    dve.wait_ge(s.gelu_ready, i + 1 + CREDIT)
                    dve.wait_ge(s.gate_loaded, i * 16 + 16 + CREDIT)
                    dve.wait_ge(s.diag_ready, i * NGR + CREDIT)
                    dve.tensor_tensor(coef[0:n, :], gl[0:n, :], gate[0:n, :], ALU.mult).then_inc(s.coef_ready, 1)
                    dve.wait_ge(s.v_used, i * NGR + NGR + CREDIT)
                    dve.wait_ge(s.h_loaded, i * 16 + 16 + CREDIT)
                    for c in range(2):
                        half = slice(c * 512, (c + 1) * 512)
                        dve.tensor_tensor(h[0:n, half], acc[c][0:n, :], h[0:n, half], ALU.add).then_inc(s.h_added, 1)
                    dve.wait_ge(s.squares_summed, i + 1 + CREDIT)
                    dve.tensor_scalar(ms[0:n, :], ss[0:n, :], 1.0 / D, EPS, ALU.mult, ALU.add).then_inc(s.mean_ready, 1)
                    dve.wait_ge(s.root_ready, i + 1 + CREDIT)
                    dve.reciprocal(rstd[0:n, :], rt[0:n, :]).then_inc(s.rstd_ready, 1)
                    dve.wait_ge(s.rstd_ready, i + 1 + CREDIT)
                    dve.wait_ge(s.stored, i * 16 + CREDIT)
                    dve.scalar_tensor_tensor(out=y[0:n, :], in0=h[0:n, :], scalar=rstd[0:n, 0:1], in1=g[0:n, :],
                                             op0=ALU.mult, op1=ALU.mult).then_inc(s.y_ready, 1)

            @block.scalar
            def _(act):
                for i, n, at in tiles(act):
                    act.wait_ge(s.dotted, i * NGR + NGR + CREDIT)
                    act.wait_ge(s.coef_ready, i + CREDIT)
                    act.activation(gl[0:n, :], act_in[0:n, :], ACT.Gelu).then_inc(s.gelu_ready, 1)
                    act.wait_ge(s.coef_ready, i + 1 + CREDIT)
                    for k in range(SLOTS):
                        if k % GROUP == 0:
                            act.wait_ge(s.v_used, i * NGR + max(k // GROUP - 1, 0) + CREDIT)
                        ins = act.activation(dg[k % RING][0:n, 0:n], r.ident[0:n, 0:n], ACT.Copy, scale=coef[0:n, k:k + 1])
                        if k % GROUP == GROUP - 1:
                            ins.then_inc(s.diag_ready, 1)
                    act.wait_ge(s.h_added, i * 2 + 2 + CREDIT)
                    act.wait_ge(s.stored, i * 16 + CREDIT)
                    act.activation(y[0:n, :], h[0:n, :], ACT.Square, accum_out=ss[0:n, :]).then_inc(s.squares_summed, 1)
                    act.wait_ge(s.mean_ready, i + 1 + CREDIT)
                    act.activation(rt[0:n, :], ms[0:n, :], ACT.Sqrt).then_inc(s.root_ready, 1)
                    act.wait_ge(s.y_ready, i + 1 + CREDIT)
                    dst = a.y_sample if n == NS else a.y_prompt[ds(at, n), :]
                    act.dma_start(dst, y[0:n, :]).then_inc(s.stored, 16)
                act.wait_ge(s.stored, 16 * NT + CREDIT)

            @block.tensor
            def _(pe):
                for i, n, at in tiles(pe):
                    pe.wait_ge(s.h_added, i * 2 + CREDIT)
                    for k in range(SLOTS):
                        j = k // GROUP
                        if k % GROUP == 0:
                            pe.wait_ge(v_loaded[j % 2], i * (FULL * NGR // 2) + FULL * (j // 2 + 1))
                            pe.wait_ge(s.diag_ready, i * NGR + j + 1 + CREDIT)
                        for c in range(2):
                            mm = pe.matmul(acc[c][0:n, :], dg[k % RING][0:n, 0:n], vb[k % RING][0:n, c * 512:(c + 1) * 512],
                                           start=(k == 0), stop=(k == SLOTS - 1))
                        if k % GROUP == GROUP - 1:
                            mm.then_inc(s.v_used, 1)


OUTS = [(1, SEQ, D), (DB, DT, D), (1, 1, SEQ, ROW), (1, 1, 128, 2, HD, E), (1, 1, 512, 2, HD, E), (1, 1, SEQ, 2, HD, E),
        (1, 1, MEM, 2, HM, EM), (1, DB, DT, ROW), (1, DB, 128, 2, HD, E), (1, DB, 512, 2, HD, E), (1, DB, 2048, 2, HD, E)]


def keep_old_rows(nc, a, stored):
    for g in range(NG):
        L = GROUPS[g][0]
        for b in range(DB):
            nc.scalar.dma_start(a.new_dil_sample[g][b, 0:L - DT].rearrange("l j c -> l (j c)"),
                                a.cache_dil[g][b, DT:L].rearrange("l j c -> l (j c)")).then_inc(stored, 16)
    return 16 * NG * DB


def keep_new_rows(nc, a, stored):
    dil3 = a.dil.rearrange("t (j g c) -> t j g c", j=3, g=NG)
    nc.sync.dma_start(a.new_mla_prompt, a.rows[0:SEQ, :]).then_inc(stored, 16)
    nc.sync.dma_start(a.new_mla_sample, a.rows[SEQ:SEQ + NS, :]).then_inc(stored, 16)
    for g in range(NG):
        keep = min(GROUPS[g][0], SEQ)
        nc.sync.dma_start(a.new_dil_prompt[g], dil3[SEQ - keep:SEQ, 1:3, g, :]).then_inc(stored, 16)
        L = GROUPS[g][0]
        for b in range(DB):
            nc.sync.dma_start(a.new_dil_sample[g][b, L - DT:L], dil3[SEQ + b * DT:SEQ + (b + 1) * DT, 1:3, g, :]
                              ).then_inc(stored, 16)
    return 16 * (2 + NG * (1 + DB))


def build(nc, i, outs):
    def dram(name, shape, dt=F32):
        return nc.dram_tensor(name, shape, dt).ap()

    a = Dram()
    a.x = i["x"]
    a.mem = i["mem"]
    a.cache_mla = i["cache_mla"]
    a.page_table = i["page_table"]
    a.cache_mem = i["cache_mem"]
    a.w_in = i["w_in"]
    a.g_attn = i["g_attn"]
    a.g_q_lora = i["g_q_lora"]
    a.w_q_up = i["w_q_up"]
    a.g_kv_lora = i["g_kv_lora"]
    a.w_kv_up = i["w_kv_up"]
    a.w_o_mla = i["w_o_mla"]
    a.w_o_dil = i["w_o_dil"]
    a.w_mem_kv = i["w_mem_kv"]
    a.g_mem = i["g_mem"]
    a.w_o_mem = i["w_o_mem"]
    a.w_out = i["w_out"]
    a.g_ffn = i["g_ffn"]
    a.w_peer_q = i["w_peer_q"]
    a.peer_sub_keys = i["peer_sub_keys"]
    a.peer_u = i["peer_u"]
    a.peer_v = i["peer_v"]
    a.g_final = i["g_final"]
    a.identity = i["identity"]
    a.rope_mla = i["rope_mla"]
    a.rope_dil = i["rope_dil"]
    a.masks_dil = i["masks_dil"]
    a.mask_mla = i["mask_mla"]
    a.mask_new = i["mask_new"]
    a.iota16 = i["iota16"]
    a.cache_dil = [v.rearrange("a b l j h e -> (a b) l j (h e)") for v in (i["cache_dil0"], i["cache_dil1"], i["cache_dil2"])]
    a.new_mla_prompt = outs[2].rearrange("a b s c -> (a b s) c")
    a.new_dil_prompt = [v.rearrange("a b s j h e -> (a b s) j (h e)") for v in outs[3:6]]
    a.mem_kv = outs[6].rearrange("a b m j h e -> (a b m) (j h e)")
    a.new_mla_sample = outs[7].rearrange("a b s c -> (a b s) c")
    a.new_dil_sample = [v.rearrange("a b l j h e -> (a b) l j (h e)") for v in outs[8:11]]
    a.proj = dram("proj_scratch", (T, PROJ))
    a.rows = dram("rows_scratch", (T, ROW))
    a.qT = dram("qT_scratch", (QK, H_MLA, T))
    a.dil = dram("dil_scratch", (T, DIL_COLS))
    a.dilo = dram("dilo_scratch", (NG, SEQ, GE + 2 * HD))
    a.omla = dram("omla_scratch", (T, H_MLA * V_DIM))
    a.h = dram("h_scratch", (T, D))
    a.xn2 = dram("xn2_scratch", (T, D))
    a.scores = dram("scores_scratch", (T, 2 * HP, NK))
    a.experts = dram("experts_scratch", (T, SLOTS), U32)
    a.gates = dram("gates_scratch", (T, SLOTS))
    a.y_prompt = outs[0].rearrange("a s d -> (a s) d")
    a.y_sample = outs[1].rearrange("b t d -> (b t) d")

    with ExitStack() as ctx, nc.semaphore("old_rows_stored") as old_rows_stored, nc.semaphore("new_rows_stored") as new_rows_stored:
        keep = lambda n, shape, dt=F32: ctx.enter_context(nc.sbuf_tensor(n, shape, dt))
        ident = keep("ident", [P, P])
        r = Resident()
        r.ident = ident[:, :]
        ident_loaded = ctx.enter_context(nc.semaphore("ident_loaded"))
        with nc.Block() as block:
            @block.sync
            def _(sp):
                sp.dma_start(ident[:, :], a.identity).then_inc(ident_loaded, 16)
                sp.wait_ge(ident_loaded, 16)
        with nc.sbuf_tensor("memT", [P, KD, MEM], F32) as memT:
            norm_rows(nc, "nmem", a.mem, a.g_mem, MEM // P, r.ident, memT)
            product_rows(nc, "pmem", memT, a.w_mem_kv, 2 * HM * EM, 512, MEM // P, a.mem_kv)
        xT = ctx.enter_context(nc.sbuf_tensor("xT", [P, KD, T], F32))
        norm_rows(nc, "nx", a.x, a.g_attn, NT, r.ident, xT)
        n_old = keep_old_rows(nc, a, old_rows_stored)
        product_rows(nc, "proj", xT, a.w_in[:, 0:PROJ], PROJ, PROJ // 8, NT, a.proj)
        with ExitStack() as turned:
            r.oT_mla = keep("oT_mla", [P, 4, T])
            r.oT_dil = keep("oT_dil", [P, 2, T])
            r.oT_mem = keep("oT_mem", [P, HM, T])
            r.ckvT = turned.enter_context(nc.sbuf_tensor("ckvT", [P, 2, T], F32))
            r.kpeT = turned.enter_context(nc.sbuf_tensor("kpeT", [P, T], F32))
            latents(nc, a, r)
            n_new = keep_new_rows(nc, a, new_rows_stored)
            memory_attention(nc, a, r)
            dilated_attention(nc, a, r)
            latent_attention(nc, a, r)
            combine_groups(nc, a, r)
            sample_latent_attention(nc, a, r)
        sample_dilated_attention(nc, a, r)
        sample_memory_attention(nc, a, r)
        mT = keep("mT", [P, KD, T])
        mix_branches(nc, a, r, xT, mT)
        product_rows(nc, "out", mT, a.w_out, D, 512, NT, a.h, add=a.x)
        nc.sync.wait_ge(old_rows_stored, n_old)
        nc.sync.wait_ge(new_rows_stored, n_new)
    with nc.sbuf_tensor("ident2", [P, P], F32) as ident:
        r = Resident()
        r.ident = ident[:, :]
        with nc.semaphore("ident2_loaded") as ident_loaded, nc.Block() as block:
            @block.sync
            def _(sp):
                sp.dma_start(ident[:, :], a.identity).then_inc(ident_loaded, 16)
                sp.wait_ge(ident_loaded, 16)
        with nc.sbuf_tensor("xT2", [P, KD, T], F32) as xT:
            norm_rows(nc, "nh", a.h, a.g_ffn, NT, r.ident, xT, a.xn2)
            peer_scores(nc, a, r, xT)
        peer_choose(nc, a, r)
        peer_experts(nc, a, r)


def rope_table(dim):
    half = dim // 2
    inv = np.float32(THETA) ** (-np.arange(half, dtype=np.float32) * np.float32(2.0 / dim))
    pos = np.zeros(T, np.float32)
    pos[0:SEQ] = np.arange(SEQ)
    pos[SEQ:SEQ + NS] = PAST + np.arange(NS) % DT
    ang = pos[:, None] * inv[None, :]
    return np.concatenate([np.cos(ang), np.sin(ang)], axis=1).astype(np.float32)


def dilated_masks():
    q, k = np.arange(P)[:, None], np.arange(P)[None, :]
    m = np.full((NG * NTP, P, 2 * P), NEG, np.float32)
    own, before = k <= q, k >= q
    for t in range(NTP):
        m[t, :, P:] = np.where(own, 0, NEG)
        m[NTP + t, :, P:] = np.where(own, 0, NEG)
        m[2 * NTP + t, :, P:] = np.where(own & (q // 64 == k // 64), 0, NEG)
        if t > 0:
            m[t, :, :P] = np.where(before, 0, NEG)
        if t % 2:
            m[NTP + t, :, :P] = np.where(before, 0, NEG)
    return m


def constants():
    q, k = np.arange(P)[:, None], np.arange(P)[None, :]
    row = np.arange(P)[:, None]
    return {
        "identity": np.eye(P, dtype=np.float32),
        "rope_mla": rope_table(ROPE),
        "rope_dil": rope_table(ROT),
        "masks_dil": dilated_masks(),
        "mask_mla": np.where(k <= q, 0, NEG).astype(np.float32),
        "mask_new": np.where(np.arange(DT)[None, :] <= row % DT, 0, NEG).astype(np.float32),
        "iota16": np.broadcast_to(np.arange(TOPK, dtype=np.float32), (P, TOPK)).copy(),
    }


def kernel(**inputs):
    import concourse.bacc as bacc
    from concourse.bass_utils import run_bass_kernel_spmd

    given = {k: np.asarray(v) for k, v in inputs.items()}
    layer = {k: v[0] for k, v in given.items() if k.startswith(("w_", "g_", "peer_")) and k != "g_final"}
    layer["g_final"] = given["g_final"]
    arrays = {
        "x": np.concatenate([given["x_prompt"][0], given["x_sample"].reshape(NS, D),
                             np.zeros((T - SEQ - NS, D), np.float32)]),
        "mem": given["mem_prompt"][0],
        "cache_mla": given["cache_mla"][0],
        "page_table": given["page_table"].reshape(1, DB * N_PAGES),
        "cache_mem": given["cache_mem"][0].reshape(DB, MEM, 2 * HM * EM),
        **{f"cache_dil{g}": given[f"cache_dil{g}"] for g in range(NG)},
        **layer,
        **constants(),
    }
    nc = bacc.Bacc("TRN2", target_bir_lowering=False, num_devices=1)
    feed, ins = {}, {}
    for name, v in arrays.items():
        feed[f"in_{name}"] = np.ascontiguousarray(v)
        ins[name] = nc.dram_tensor(f"in_{name}", v.shape, mybir.dt.from_np(v.dtype), kind="ExternalInput").ap()
    outs = [nc.dram_tensor(f"out_{n}", shape, F32, kind="ExternalOutput").ap() for n, shape in enumerate(OUTS)]
    build(nc, ins, outs)
    got = run_bass_kernel_spmd(nc, [feed], core_ids=[0])
    return tuple(got.results[0][f"out_{n}"] for n in range(len(OUTS)))
```

```python
from collections import namedtuple
from contextlib import ExitStack

import numpy as np

import concourse.bass as bass
from concourse import mybir

F32 = mybir.dt.float32
I32 = mybir.dt.int32
U32 = mybir.dt.uint32
ALU = mybir.AluOpType
ACT = mybir.ActivationFunctionType
AX = mybir.AxisListType
ds = bass.ds

P = 128
D = 1024
SEQ = 1024
DB, DT = 8, 4
NS = DB * DT
PAST = 8192
PAGE = 128
N_PAGES = PAST // PAGE
POOL_PAGES = DB * N_PAGES + (DB * N_PAGES + 3) // 4
NTP = SEQ // P
NT = NTP + 1
T = NT * P
KD = D // P
H_MLA, Q_LORA, KV_LORA, NOPE, ROPE, V_DIM = 8, 384, 256, 64, 32, 64
QK = NOPE + ROPE
ROW = KV_LORA + ROPE
MLA_SCALE = float(QK) ** -0.5
GROUPS = ((128, 1), (512, 4), (2048, 16))
NG, HD, E = 3, 4, 64
GE = HD * E
ROT = E // 4
DIL_SCALE = float(E) ** -0.5
DIL_COLS = 3 * NG * GE
MEM, HM, EM = 256, 4, 128
MEM_SCALE = float(EM) ** -0.5
C_DIL = Q_LORA + ROW
C_MEM = C_DIL + DIL_COLS
C_GATE = C_MEM + HM * EM
PROJ = C_GATE
HP, NK, QH, TOPK = 8, 128, 128, 16
SLOTS = HP * TOPK
EPS = 1e-6
NEG = -1e30
THETA = 500000.0
CREDIT = 1


class Dram:
    pass


class Resident:
    pass


class Steps:

    def __init__(self, eng, sem, turn=0, per=0):
        self.eng, self.sem, self.base, self.per, self.n = eng, sem, turn * per if per else 0, per, 0

    def __call__(self, ins):
        self.n += 1
        ins.then_inc(self.sem, 1)
        self.eng.wait_ge(self.sem, self.base + self.n + CREDIT)

    def end(self):
        assert self.n == self.per, f"a turn has {self.n} steps, not {self.per}"


def stage(nc, tag):
    ctx, mine = ExitStack(), []

    @ctx.callback
    def _():
        nc.clear_and_free_semaphores(mine)
        nc.all_engine_barrier()

    sb = lambda n, shape, dt=F32: ctx.enter_context(nc.sbuf_tensor(f"{tag}_{n}", shape, dt))
    ps = lambda n, shape: ctx.enter_context(nc.psum_tensor(f"{tag}_{n}", shape, F32))

    def sem(name, credit):
        handle = nc.alloc_semaphore(f"{tag}_{name}")
        mine.append(handle)
        if credit:
            nc.gpsimd.sem_inc(handle, credit)
        return handle

    sems = lambda names, credit=CREDIT: namedtuple("Semaphores", names)(*[sem(n, credit) for n in names.split()])
    return ctx, sb, ps, sems


def norm_rows(nc, tag, src, gain, n_tiles, ident, dst_T, dst_rows=None):
    ctx, sb, ps, sems = stage(nc, tag)
    with ctx:
        x, sq, xn, g = sb("x", [P, D]), sb("sq", [P, D]), sb("xn", [P, D]), sb("g", [P, D])
        ss, ms, rt, rstd = sb("ss", [P, 1]), sb("ms", [P, 1]), sb("rt", [P, 1]), sb("rstd", [P, 1])
        lo, hi = ps("lo", [P, 4 * P]), ps("hi", [P, 4 * P])
        s = sems("gain_loaded x_loaded squares_summed mean_ready root_ready rstd_ready xn_ready "
                 "lo_ready hi_ready lo_copied hi_copied rows_stored")
        with nc.Block() as block:
            @block.sync
            def _(sp):
                sp.dma_start(g[:, :], gain.partition_broadcast(P)).then_inc(s.gain_loaded, 16)
                with sp.Fori(0, n_tiles) as i:
                    sp.wait_ge(s.xn_ready, i + CREDIT)
                    sp.dma_start(x[:, :], src[ds(i * P, P), :]).then_inc(s.x_loaded, 16)
                    if dst_rows is not None:
                        sp.wait_ge(s.xn_ready, i + 1 + CREDIT)
                        sp.dma_start(dst_rows[ds(i * P, P), :], xn[:, :]).then_inc(s.rows_stored, 16)
                if dst_rows is not None:
                    sp.wait_ge(s.rows_stored, 16 * n_tiles + CREDIT)

            @block.scalar
            def _(act):
                with act.Fori(0, n_tiles) as i:
                    act.wait_ge(s.x_loaded, i * 16 + 16 + CREDIT)
                    act.activation(sq[:, :], x[:, :], ACT.Square, accum_out=ss[:, :]).then_inc(s.squares_summed, 1)
                    act.wait_ge(s.mean_ready, i + 1 + CREDIT)
                    act.activation(rt[:, :], ms[:, :], ACT.Sqrt).then_inc(s.root_ready, 1)
                    act.wait_ge(s.hi_ready, i + 1 + CREDIT)
                    act.copy(dst_T[:, 4:8, ds(i * P, P)], hi[:, :].rearrange("p (k t) -> p k t", k=4)
                             ).then_inc(s.hi_copied, 1)

            @block.vector
            def _(dve):
                dve.wait_ge(s.gain_loaded, 16 + CREDIT)
                with dve.Fori(0, n_tiles) as i:
                    dve.wait_ge(s.squares_summed, i + 1 + CREDIT)
                    dve.tensor_scalar(ms[:, :], ss[:, :], 1.0 / D, EPS, ALU.mult, ALU.add).then_inc(s.mean_ready, 1)
                    dve.wait_ge(s.root_ready, i + 1 + CREDIT)
                    dve.reciprocal(rstd[:, :], rt[:, :]).then_inc(s.rstd_ready, 1)
                    dve.wait_ge(s.rstd_ready, i + 1 + CREDIT)
                    dve.wait_ge(s.hi_ready, i + CREDIT)
                    if dst_rows is not None:
                        dve.wait_ge(s.rows_stored, i * 16 + CREDIT)
                    dve.scalar_tensor_tensor(out=xn[:, :], in0=x[:, :], scalar=rstd[:, 0:1], in1=g[:, :],
                                             op0=ALU.mult, op1=ALU.mult).then_inc(s.xn_ready, 1)
                    dve.wait_ge(s.lo_ready, i + 1 + CREDIT)
                    dve.tensor_copy(dst_T[:, 0:4, ds(i * P, P)], lo[:, :].rearrange("p (k t) -> p k t", k=4)
                                    ).then_inc(s.lo_copied, 1)

            @block.tensor
            def _(pe):
                with pe.Fori(0, n_tiles) as i:
                    pe.wait_ge(s.xn_ready, i + 1 + CREDIT)
                    for half, bank, copied, ready in ((0, lo, s.lo_copied, s.lo_ready), (1, hi, s.hi_copied, s.hi_ready)):
                        pe.wait_ge(copied, i + CREDIT)
                        for k in range(4):
                            c = (4 * half + k) * P
                            mm = pe.transpose(bank[:, k * P:(k + 1) * P], xn[:, c:c + P], ident)
                        mm.then_inc(ready, 1)


def load_pairs(sp, pairs, used, per, load):
    load(0, 0)
    if pairs > 1:
        with sp.Fori(0, pairs - 1) as i:
            sp.wait_ge(used, i * (2 * per) + CREDIT)
            load(1, i * 2 + 1)
            sp.wait_ge(used, i * (2 * per) + per + CREDIT)
            load(0, i * 2 + 2)
    sp.wait_ge(used, (pairs - 1) * 2 * per + CREDIT)
    load(1, 2 * pairs - 1)


def product_rows(nc, tag, xT, w, n_cols, chunk, n_tiles, dst, add=None):
    ctx, sb, ps, sems = stage(nc, tag)
    pairs = n_cols // chunk // 2
    assert pairs * 2 * chunk == n_cols
    with ctx:
        wt = [sb(f"w{u}", [P, KD, chunk]) for u in range(2)]
        o = [sb(f"o{u}", [P, n_tiles, chunk]) for u in range(2)]
        acc = [ps(f"acc{u}", [P, 512]) for u in range(2)]
        s = sems("w_loaded0 w_loaded1 add_loaded0 add_loaded1 product_ready w_used product_copied stored0 stored1")
        w_loaded, add_loaded, stored = (s.w_loaded0, s.w_loaded1), (s.add_loaded0, s.add_loaded1), (s.stored0, s.stored1)
        wv = w.rearrange("(k p) n -> p k n", p=P)
        dv = dst.rearrange("(t p) n -> p t n", p=P)
        av = add.rearrange("(t p) n -> p t n", p=P) if add is not None else None
        with nc.Block() as block:
            @block.sync
            def _(sp):
                load_pairs(sp, pairs, s.product_ready, n_tiles, lambda u, c: sp.dma_start(
                    wt[u][:, :, :], wv[:, :, ds(c * chunk, chunk)]).then_inc(w_loaded[u], 16))

            @block.scalar
            def _(act):
                with act.Fori(0, pairs) as i:
                    if add is not None:
                        for u in range(2):
                            act.wait_ge(stored[u], i * 16 + CREDIT)
                            act.dma_start(o[u][:, :, :], av[:, :, ds(i * (2 * chunk) + u * chunk, chunk)]
                                          ).then_inc(add_loaded[u], 16)
                    for u in range(2):
                        act.wait_ge(s.product_copied, i * (2 * n_tiles) + (u + 1) * n_tiles + CREDIT)
                        act.dma_start(dv[:, :, ds(i * (2 * chunk) + u * chunk, chunk)], o[u][:, :, :]
                                      ).then_inc(stored[u], 16)
                for u in range(2):
                    act.wait_ge(stored[u], 16 * pairs + CREDIT)

            @block.tensor
            def _(pe):
                with pe.Fori(0, pairs) as i:
                    for u in range(2):
                        pe.wait_ge(w_loaded[u], i * 16 + 16 + CREDIT)
                        for t in range(n_tiles):
                            n = u * n_tiles + t
                            pe.wait_ge(s.product_copied, i * (2 * n_tiles) + max(n - 1, 0) + CREDIT)
                            for k in range(KD):
                                mm = pe.matmul(acc[n % 2][:, 0:chunk], xT[:, k, t * P:(t + 1) * P], wt[u][:, k, :],
                                               start=(k == 0), stop=(k == KD - 1))
                            mm.then_inc(s.product_ready, 1)

            @block.vector
            def _(dve):
                with dve.Fori(0, pairs) as i:
                    for u in range(2):
                        if add is not None:
                            dve.wait_ge(add_loaded[u], i * 16 + 16 + CREDIT)
                        else:
                            dve.wait_ge(stored[u], i * 16 + CREDIT)
                        for t in range(n_tiles):
                            n = u * n_tiles + t
                            dve.wait_ge(s.product_ready, i * (2 * n_tiles) + n + 1 + CREDIT)
                            if add is not None:
                                dve.tensor_tensor(o[u][:, t, :], acc[n % 2][:, 0:chunk], o[u][:, t, :], ALU.add
                                                  ).then_inc(s.product_copied, 1)
                            else:
                                dve.tensor_copy(o[u][:, t, :], acc[n % 2][:, 0:chunk]).then_inc(s.product_copied, 1)


def latents(nc, a, r):
    ctx, sb, ps, sems = stage(nc, "lat")
    with ctx:
        x, sq = sb("x", [P, C_DIL]), sb("sq", [P, Q_LORA])
        tab = sb("tab", [P, ROPE])
        gq, gkv = sb("gq", [P, Q_LORA]), sb("gkv", [P, KV_LORA])
        wq = sb("wq", [P, 3, H_MLA * QK])
        ss, ms, rt, rstd = sb("ss", [P, 2]), sb("ms", [P, 2]), sb("rt", [P, 2]), sb("rstd", [P, 2])
        cq, row, kpad = sb("cq", [P, Q_LORA]), sb("row", [P, ROW]), sb("kpad", [P, QK])
        tmp = sb("tmp", [P, 4, H_MLA, 16])
        cqT, q, qT = sb("cqT", [P, 3, P]), sb("q", [P, H_MLA, QK]), sb("qT", [QK, H_MLA, P])
        y, ytab = sb("y", [P, 2 * NG * HD, E]), sb("ytab", [P, ROT])
        yv = sb("yv", [P, NG * GE])
        ytmp = sb("ytmp", [P, 4, 2 * NG * HD, ROT // 2])
        pc, pk = ps("pc", [P, 512]), ps("pk", [P, 512])
        pq = [ps(f"pq{u}", [P, 512]) for u in range(2)]
        pt = [ps(f"pt{u}", [P, 512]) for u in range(2)]
        s = sems("const_loaded pad_zeroed x_loaded squares_summed means_ready roots_ready steps latents_ready "
                 "cq_turned kv_turned cqT_ready kvT_ready q_product q_copied q_roped q_turned qT_lo qT_hi "
                 "row_stored qT_stored y_loaded y_steps y_roped y_stored")
        N = 15
        with nc.Block() as block:
            @block.sync
            def _(sp):
                sp.dma_start(gq[:, :], a.g_q_lora.partition_broadcast(P)).then_inc(s.const_loaded, 16)
                sp.dma_start(gkv[:, :], a.g_kv_lora.partition_broadcast(P)).then_inc(s.const_loaded, 16)
                sp.dma_start(wq[:, :, :], a.w_q_up.rearrange("(k p) n -> p k n", p=P)).then_inc(s.const_loaded, 16)
                with sp.Fori(0, NT) as i:
                    sp.wait_ge(s.latents_ready, i + CREDIT)
                    sp.wait_ge(s.q_roped, i + CREDIT)
                    sp.dma_start(x[:, :], a.proj[ds(i * P, P), 0:C_DIL]).then_inc(s.x_loaded, 16)
                    sp.dma_start(tab[:, :], a.rope_mla[ds(i * P, P), :]).then_inc(s.x_loaded, 16)
                    sp.wait_ge(s.y_stored, i * 32 + CREDIT)
                    sp.dma_start(y[:, :, :].rearrange("p h e -> p (h e)"), a.proj[ds(i * P, P), C_DIL:C_DIL + 2 * NG * GE]
                                 ).then_inc(s.y_loaded, 16)
                    sp.dma_start(yv[:, :], a.proj[ds(i * P, P), C_DIL + 2 * NG * GE:C_MEM]).then_inc(s.y_loaded, 16)
                    sp.dma_start(ytab[:, :], a.rope_dil[ds(i * P, P), :]).then_inc(s.y_loaded, 16)
                    sp.wait_ge(s.y_roped, i + 1 + CREDIT)
                    sp.dma_start(a.dil[ds(i * P, P), 0:2 * NG * GE], y[:, :, :].rearrange("p h e -> p (h e)")
                                 ).then_inc(s.y_stored, 16)
                    sp.dma_start(a.dil[ds(i * P, P), 2 * NG * GE:DIL_COLS], yv[:, :]).then_inc(s.y_stored, 16)
                    sp.wait_ge(s.latents_ready, i + 1 + CREDIT)
                    sp.dma_start(a.rows[ds(i * P, P), :], row[:, :]).then_inc(s.row_stored, 16)
                sp.wait_ge(s.row_stored, 16 * NT + CREDIT)
                sp.wait_ge(s.y_stored, 32 * NT + CREDIT)

            @block.scalar
            def _(act):
                with act.Fori(0, NT) as i:
                    act.wait_ge(s.x_loaded, i * 32 + 32 + CREDIT)
                    act.activation(sq[:, :], x[:, 0:Q_LORA], ACT.Square, accum_out=ss[:, 0:1]).then_inc(s.squares_summed, 1)
                    act.wait_ge(s.squares_summed, i * 2 + 1 + CREDIT)
                    act.activation(sq[:, 0:KV_LORA], x[:, Q_LORA:Q_LORA + KV_LORA], ACT.Square,
                                   accum_out=ss[:, 1:2]).then_inc(s.squares_summed, 1)
                    act.wait_ge(s.means_ready, i + 1 + CREDIT)
                    act.activation(rt[:, :], ms[:, :], ACT.Sqrt).then_inc(s.roots_ready, 1)
                    act.wait_ge(s.cq_turned, i + 1 + CREDIT)
                    act.copy(cqT[:, :, :], pc[:, 0:Q_LORA].rearrange("p (k t) -> p k t", k=3)).then_inc(s.cqT_ready, 1)
                    act.wait_ge(s.q_turned, i * 2 + CREDIT)
                    for u in range(2):
                        act.wait_ge(s.q_product, i * 2 + u + 1 + CREDIT)
                        act.copy(q[:, 4 * u:4 * u + 4, :], pq[u][:, 0:4 * QK].rearrange("p (h e) -> p h e", h=4)
                                 ).then_inc(s.q_copied, 1)
                    act.wait_ge(s.q_turned, i * 2 + 1 + CREDIT)
                    act.wait_ge(s.qT_stored, i * 16 + CREDIT)
                    act.copy(qT[:, 0:4, :], pt[0][0:QK, :].rearrange("p (h t) -> p h t", h=4)).then_inc(s.qT_lo, 1)
                    act.wait_ge(s.qT_lo, i + 1 + CREDIT)
                    act.wait_ge(s.qT_hi, i + 1 + CREDIT)
                    act.dma_start(a.qT[:, :, ds(i * P, P)], qT[:, :, :]).then_inc(s.qT_stored, 16)
                act.wait_ge(s.qT_stored, 16 * NT + CREDIT)

            @block.vector
            def _(dve):
                dve.memset(kpad[:, :], 0.0).then_inc(s.pad_zeroed, 1)
                dve.wait_ge(s.pad_zeroed, 1 + CREDIT)
                dve.wait_ge(s.const_loaded, 48 + CREDIT)
                with dve.Fori(0, NT) as i:
                    step = Steps(dve, s.steps, i, N)
                    dve.wait_ge(s.squares_summed, i * 2 + 2 + CREDIT)
                    step(dve.tensor_scalar(ms[:, 0:1], ss[:, 0:1], 1.0 / Q_LORA, EPS, ALU.mult, ALU.add))
                    dve.tensor_scalar(ms[:, 1:2], ss[:, 1:2], 1.0 / KV_LORA, EPS, ALU.mult, ALU.add
                                      ).then_inc(s.means_ready, 1)
                    dve.wait_ge(s.roots_ready, i + 1 + CREDIT)
                    step(dve.reciprocal(rstd[:, :], rt[:, :]))
                    dve.wait_ge(s.row_stored, i * 16 + CREDIT)
                    dve.wait_ge(s.cq_turned, i + CREDIT)
                    dve.wait_ge(s.kv_turned, i + CREDIT)
                    step(dve.scalar_tensor_tensor(out=cq[:, :], in0=x[:, 0:Q_LORA], scalar=rstd[:, 0:1], in1=gq[:, :],
                                                  op0=ALU.mult, op1=ALU.mult))
                    step(dve.scalar_tensor_tensor(out=row[:, 0:KV_LORA], in0=x[:, Q_LORA:Q_LORA + KV_LORA],
                                                  scalar=rstd[:, 1:2], in1=gkv[:, :], op0=ALU.mult, op1=ALU.mult))
                    x1, x2 = x[:, C_DIL - 32:C_DIL - 16], x[:, C_DIL - 16:C_DIL]
                    cos, sin = tab[:, 0:16], tab[:, 16:32]
                    for n, (v, w) in enumerate(((x1, cos), (x2, sin), (x2, cos), (x1, sin))):
                        step(dve.tensor_tensor(tmp[:, n, 0, :], v, w, ALU.mult))
                    step(dve.tensor_tensor(row[:, KV_LORA:KV_LORA + 16], tmp[:, 0, 0, :], tmp[:, 1, 0, :], ALU.subtract))
                    step(dve.tensor_tensor(row[:, KV_LORA + 16:ROW], tmp[:, 2, 0, :], tmp[:, 3, 0, :], ALU.add))
                    dve.tensor_copy(kpad[:, NOPE:QK], row[:, KV_LORA:ROW]).then_inc(s.latents_ready, 1)
                    dve.wait_ge(s.kv_turned, i + 1 + CREDIT)
                    dve.tensor_copy(r.ckvT[:, :, ds(i * P, P)], pk[:, 0:2 * P].rearrange("p (k t) -> p k t", k=2)
                                    ).then_inc(s.kvT_ready, 1)
                    dve.tensor_copy(r.kpeT[NOPE:QK, ds(i * P, P)], pk[NOPE:QK, 2 * P:3 * P]).then_inc(s.kvT_ready, 1)
                    dve.wait_ge(s.q_copied, i * 2 + 2 + CREDIT)
                    q1, q2 = q[:, :, NOPE:NOPE + 16], q[:, :, NOPE + 16:QK]
                    cosb = cos.unsqueeze(1).broadcast_to([P, H_MLA, 16])
                    sinb = sin.unsqueeze(1).broadcast_to([P, H_MLA, 16])
                    for n, (v, w) in enumerate(((q1, cosb), (q2, sinb), (q2, cosb), (q1, sinb))):
                        step(dve.tensor_tensor(tmp[:, n, :, :], v, w, ALU.mult))
                    step(dve.tensor_tensor(q1, tmp[:, 0, :, :], tmp[:, 1, :, :], ALU.subtract))
                    dve.tensor_tensor(q2, tmp[:, 2, :, :], tmp[:, 3, :, :], ALU.add).then_inc(s.q_roped, 1)
                    dve.wait_ge(s.q_turned, i * 2 + 2 + CREDIT)
                    dve.wait_ge(s.qT_stored, i * 16 + CREDIT)
                    dve.tensor_copy(qT[:, 4:8, :], pt[1][0:QK, :].rearrange("p (h t) -> p h t", h=4)).then_inc(s.qT_hi, 1)
                    step.end()

            @block.tensor
            def _(pe):
                pe.wait_ge(s.const_loaded, 48 + CREDIT)
                with pe.Fori(0, NT) as i:
                    pe.wait_ge(s.latents_ready, i + 1 + CREDIT)
                    pe.wait_ge(s.cqT_ready, i + CREDIT)
                    pe.wait_ge(s.kvT_ready, i * 2 + CREDIT)
                    for k in range(3):
                        mm = pe.transpose(pc[:, k * P:(k + 1) * P], cq[:, k * P:(k + 1) * P], r.ident)
                    mm.then_inc(s.cq_turned, 1)
                    for k in range(2):
                        pe.transpose(pk[:, k * P:(k + 1) * P], row[:, k * P:(k + 1) * P], r.ident)
                    pe.transpose(pk[0:QK, 2 * P:3 * P], kpad[:, :], r.ident).then_inc(s.kv_turned, 1)
                    pe.wait_ge(s.cqT_ready, i + 1 + CREDIT)
                    pe.wait_ge(s.q_copied, i * 2 + CREDIT)
                    for u in range(2):
                        for k in range(3):
                            mm = pe.matmul(pq[u][:, 0:4 * QK], cqT[:, k, :], wq[:, k, 4 * QK * u:4 * QK * (u + 1)],
                                           start=(k == 0), stop=(k == 2))
                        mm.then_inc(s.q_product, 1)
                    pe.wait_ge(s.q_roped, i + 1 + CREDIT)
                    pe.wait_ge(s.qT_lo, i + CREDIT)
                    pe.wait_ge(s.qT_hi, i + CREDIT)
                    for u in range(2):
                        for h in range(4):
                            mm = pe.transpose(pt[u][0:QK, h * P:(h + 1) * P], q[:, 4 * u + h, :], r.ident)
                        mm.then_inc(s.q_turned, 1)

            @block.gpsimd
            def _(pool):
                NY = 5
                pair = "p (h e) -> p h e"
                with pool.Fori(0, NT) as i:
                    step = Steps(pool, s.y_steps, i, NY)
                    pool.wait_ge(s.y_loaded, i * 48 + 48 + CREDIT)
                    h2 = ROT // 2
                    y1, y2 = y[:, :, 0:h2], y[:, :, h2:ROT]
                    cosb = ytab[:, 0:h2].unsqueeze(1).broadcast_to([P, 2 * NG * HD, h2])
                    sinb = ytab[:, h2:ROT].unsqueeze(1).broadcast_to([P, 2 * NG * HD, h2])
                    for n, (v, w) in enumerate(((y1, cosb), (y2, sinb), (y2, cosb), (y1, sinb))):
                        step(pool.tensor_tensor(ytmp[:, n, :, :], v, w, ALU.mult))
                    step(pool.tensor_tensor(y1, ytmp[:, 0, :, :], ytmp[:, 1, :, :], ALU.subtract))
                    pool.tensor_tensor(y2, ytmp[:, 2, :, :], ytmp[:, 3, :, :], ALU.add).then_inc(s.y_roped, 1)
                    step.end()


def memory_attention(nc, a, r):
    ctx, sb, ps, sems = stage(nc, "mem")
    with ctx:
        kv, kT = sb("kv", [P, 2, 2 * HM * EM]), sb("kT", [P, HM, MEM])
        x, qT = sb("x", [P, HM * EM]), sb("qT", [P, HM, P])
        nm, nb, l, rl = sb("nm", [P, HM]), sb("nb", [P, HM]), sb("l", [P, HM]), sb("rl", [P, HM])
        p, pT, o = sb("p", [P, HM, MEM]), sb("pT", [P, HM, 2, P]), sb("o", [P, HM, EM])
        pq = ps("pq", [P, 512])
        sc = [ps(f"sc{u}", [P, 512]) for u in range(2)]
        pt = [ps(f"pt{u}", [P, 512]) for u in range(2)]
        po, pot = ps("po", [P, 512]), ps("pot", [P, 512])
        s = sems("kv_loaded k_turned kT_ready x_loaded q_turned qT_ready scores_ready max_found bias_ready probs_ready "
                 "probs_turned pT_ready attended sum_inverted o_ready o_turned oT_stored")
        with nc.Block() as block:
            @block.sync
            def _(sp):
                sp.dma_start(kv[:, :, :], a.mem_kv.rearrange("(m p) c -> p m c", p=P)).then_inc(s.kv_loaded, 16)
                with sp.Fori(0, NTP) as i:
                    sp.wait_ge(s.q_turned, i + CREDIT)
                    sp.dma_start(x[:, :], a.proj[ds(i * P, P), C_MEM:C_GATE]).then_inc(s.x_loaded, 16)

            @block.tensor
            def _(pe):
                pe.wait_ge(s.kv_loaded, 16 + CREDIT)
                for h in range(HM):
                    for m in range(2):
                        mm = pe.transpose(sc[h // 2][:, (h % 2 * 2 + m) * P:(h % 2 * 2 + m + 1) * P],
                                          kv[:, m, h * EM:(h + 1) * EM], r.ident)
                mm.then_inc(s.k_turned, 1)
                pe.wait_ge(s.kT_ready, 2 + CREDIT)
                with pe.Fori(0, NTP) as i:
                    pe.wait_ge(s.x_loaded, i * 16 + 16 + CREDIT)
                    pe.wait_ge(s.qT_ready, i + CREDIT)
                    for h in range(HM):
                        mm = pe.transpose(pq[:, h * P:(h + 1) * P], x[:, h * EM:(h + 1) * EM], r.ident)
                    mm.then_inc(s.q_turned, 1)
                    pe.wait_ge(s.qT_ready, i + 1 + CREDIT)
                    pe.wait_ge(s.probs_ready, i * HM + CREDIT)
                    for h in range(HM):
                        mm = pe.matmul(sc[h // 2][:, h % 2 * MEM:(h % 2 + 1) * MEM], qT[:, h, :], kT[:, h, :],
                                       start=True, stop=True)
                        if h % 2:
                            mm.then_inc(s.scores_ready, 1)
                    for u in range(2):
                        pe.wait_ge(s.probs_ready, i * HM + 2 * u + 2 + CREDIT)
                        pe.wait_ge(s.pT_ready, i * 2 + u + CREDIT)
                        for j in range(4):
                            mm = pe.transpose(pt[u][:, j * P:(j + 1) * P],
                                              p[:, 2 * u + j // 2, (j % 2) * P:(j % 2 + 1) * P], r.ident)
                        mm.then_inc(s.probs_turned, 1)
                    pe.wait_ge(s.pT_ready, i * 2 + 2 + CREDIT)
                    pe.wait_ge(s.o_ready, i + CREDIT)
                    for h in range(HM):
                        for m in range(2):
                            mm = pe.matmul(po[:, h * EM:(h + 1) * EM], pT[:, h, m, :],
                                           kv[:, m, (HM + h) * EM:(HM + h + 1) * EM], start=(m == 0), stop=(m == 1))
                    mm.then_inc(s.attended, 1)
                    pe.wait_ge(s.o_ready, i + 1 + CREDIT)
                    pe.wait_ge(s.oT_stored, i + CREDIT)
                    for h in range(HM):
                        mm = pe.transpose(pot[:, h * P:(h + 1) * P], o[:, h, :], r.ident)
                    mm.then_inc(s.o_turned, 1)

            @block.scalar
            def _(act):
                with act.Fori(0, NTP) as i:
                    act.wait_ge(s.q_turned, i + 1 + CREDIT)
                    act.wait_ge(s.scores_ready, i * 2 + CREDIT)
                    act.copy(qT[:, :, :], pq[:, :].rearrange("p (h t) -> p h t", h=HM)).then_inc(s.qT_ready, 1)
                    act.wait_ge(s.probs_turned, i * 2 + CREDIT)
                    act.wait_ge(s.sum_inverted, i + CREDIT)
                    for h in range(HM):
                        act.wait_ge(s.bias_ready, i * 2 + h // 2 + 1 + CREDIT)
                        act.activation(p[:, h, :], sc[h // 2][:, h % 2 * MEM:(h % 2 + 1) * MEM], ACT.Exp,
                                       bias=nb[:, h:h + 1], scale=MEM_SCALE, accum_out=l[:, h:h + 1]
                                       ).then_inc(s.probs_ready, 1)
                    act.wait_ge(s.o_turned, i + 1 + CREDIT)
                    act.copy(r.oT_mem[:, :, ds(i * P, P)], pot[:, :].rearrange("p (h t) -> p h t", h=HM)
                             ).then_inc(s.oT_stored, 1)

            @block.vector
            def _(dve):
                dve.wait_ge(s.k_turned, 1 + CREDIT)
                for u in range(2):
                    dve.tensor_copy(kT[:, 2 * u:2 * u + 2, :], sc[u][:, :].rearrange("p (h m) -> p h m", h=2)
                                    ).then_inc(s.kT_ready, 1)
                with dve.Fori(0, NTP) as i:
                    dve.wait_ge(s.probs_ready, i * HM + CREDIT)
                    for u in range(2):
                        dve.wait_ge(s.scores_ready, i * 2 + u + 1 + CREDIT)
                        dve.tensor_reduce(nm[:, 2 * u:2 * u + 2], sc[u][:, :].rearrange("p (h m) -> p h m", h=2),
                                          AX.X, ALU.max, negate=True).then_inc(s.max_found, 1)
                        dve.wait_ge(s.max_found, i * 2 + u + 1 + CREDIT)
                        dve.tensor_scalar(nb[:, 2 * u:2 * u + 2], nm[:, 2 * u:2 * u + 2], MEM_SCALE, None, ALU.mult
                                          ).then_inc(s.bias_ready, 1)
                    dve.wait_ge(s.attended, i + CREDIT)
                    for u in range(2):
                        dve.wait_ge(s.probs_turned, i * 2 + u + 1 + CREDIT)
                        dve.tensor_copy(pT[:, 2 * u:2 * u + 2, :, :].rearrange("p h m t -> p (h m t)"), pt[u][:, :]
                                        ).then_inc(s.pT_ready, 1)
                    dve.reciprocal(rl[:, :], l[:, :]).then_inc(s.sum_inverted, 1)
                    dve.wait_ge(s.sum_inverted, i + 1 + CREDIT)
                    dve.wait_ge(s.attended, i + 1 + CREDIT)
                    dve.wait_ge(s.o_turned, i + CREDIT)
                    dve.tensor_tensor(o[:, :, :], po[:, :].rearrange("p (h e) -> p h e", h=HM),
                                      rl[:, :].unsqueeze(2).broadcast_to([P, HM, EM]), ALU.mult).then_inc(s.o_ready, 1)


def dilated_attention(nc, a, r):
    ctx, sb, ps, sems = stage(nc, "dil")
    UN = 4
    TILES = NG * NTP
    AHEAD = 8
    ORDER = (0, 2, 1, 3)
    with ctx:
        qk = [sb(f"qk{u}", [P, 2, GE]) for u in range(UN)]
        v = [sb(f"v{u}", [P, GE]) for u in range(UN)]
        mask = [sb(f"mask{u}", [P, 2 * P]) for u in range(UN)]
        qT, kT = sb("qT", [P, HD // 2, P]), [sb(f"kT{u}", [P, HD // 2, P]) for u in range(2)]
        sm, p, pT = sb("sm", [P, HD, 2 * P]), sb("p", [P, HD, 2 * P]), sb("pT", [P, HD, 2, P])
        ou = [sb(f"ou{u}", [P, GE + 2 * HD]) for u in range(2)]
        pq, pk = ps("pq", [P, 512]), ps("pk", [P, 512])
        sc = [ps(f"sc{u}", [P, 512]) for u in range(2)]
        pt = [ps(f"pt{u}", [P, 512]) for u in range(2)]
        po = ps("po", [P, 512])
        s = sems("zeroed qT_ready kT_ready scores_ready max_found probs_ready "
                 "probs_turned pT_ready u_ready ou_free")
        qk_loaded = sems(" ".join(f"qk_loaded{u}" for u in range(UN)))
        v_loaded = sems(" ".join(f"v_loaded{u}" for u in range(UN)))
        mask_loaded = sems(" ".join(f"mask_loaded{u}" for u in range(UN)))
        early = sems("turned masked attended", AHEAD)
        own = sems("stored", 0)
        dil3 = a.dil.rearrange("t (j g c) -> t j g c", j=3, g=NG)

        def group_tiles(eng):
            for g in range(NG):
                with eng.Fori(0, NTP // UN) as i:
                    for u in range(UN):
                        halves = []
                        for half in range(2):
                            at = (i * (UN * P) + u * P + half * 64, i * 2 + (u // 2 + 4 * (P * (u % 2) + 64 * half)),
                                  i * (2 * UN) + 2 * u + half)[g]
                            halves.append(ds(at, 64, step=GROUPS[g][1]))
                        yield g, i * UN + (g * NTP + u), u, halves

        def tiles(eng):
            last = TILES // UN - 1
            with eng.Fori(0, last) as i:
                for u in range(UN):
                    yield i, i * UN + u, u, True
            for u in range(UN):
                yield last, last * UN + u, u, u < UN - 1

        with nc.Block() as block:
            @block.sync
            def _(sp):
                sp.wait_ge(s.zeroed, 1 + CREDIT)
                for g, n, u, halves in group_tiles(sp):
                    sp.wait_ge(early.turned, n - (UN - 1) + AHEAD)
                    for half, rows in enumerate(halves):
                        sp.dma_start(qk[u][half * 64:half * 64 + 64, :, :], dil3[rows, 0:2, g, :]).then_inc(qk_loaded[u], 16)
                    sp.wait_ge(early.masked, n * 2 - 2 * (UN - 1) + AHEAD)
                    sp.dma_start(mask[u][:, :], a.masks_dil[ds(n, 1), :, :].squeeze(0)).then_inc(mask_loaded[u], 16)
                    sp.wait_ge(early.attended, n - (UN - 2) + AHEAD)
                    for half, rows in enumerate(halves):
                        sp.dma_start(v[u][half * 64:half * 64 + 64, :], dil3[rows, 2, g, :]).then_inc(v_loaded[u], 16)

            @block.gpsimd
            def _(pool):
                pool.memset(kT[1][:, :, :], 0.0)
                pool.memset(v[UN - 1][:, :], 0.0).then_inc(s.zeroed, 1)
                for g, n, u, halves in group_tiles(pool):
                    pool.wait_ge(s.u_ready, n + 1 + CREDIT)
                    for half, rows in enumerate(halves):
                        pool.dma_start(a.dilo[g, rows, :], ou[u % 2][half * 64:half * 64 + 64, :]).then_inc(own.stored, 16)
                    pool.wait_ge(own.stored, n * 32 + 32)
                    pool.sem_inc(s.ou_free, 1)

            @block.tensor
            def _(pe):
                def turn(i, n, u):
                    pe.wait_ge(qk_loaded[u], i * 32 + 32 + CREDIT)
                    pe.wait_ge(s.qT_ready, n + CREDIT)
                    pe.wait_ge(s.kT_ready, n + CREDIT)
                    for k in range(2):
                        pe.transpose(pq[:, k * P:(k + 1) * P], qk[u][:, 0, k * P:(k + 1) * P], r.ident)
                    for k in range(2):
                        mm = pe.transpose(pk[:, k * P:(k + 1) * P], qk[u][:, 1, k * P:(k + 1) * P], r.ident)
                    mm.then_inc(early.turned, 1)

                def scores(n, u):
                    pe.wait_ge(s.qT_ready, n + 1 + CREDIT)
                    pe.wait_ge(s.kT_ready, n + 1 + CREDIT)
                    pe.wait_ge(early.masked, n * 2 + AHEAD)
                    for w in range(2):
                        at = slice(w * E, (w + 1) * E)
                        for k in range(2):
                            for j, keys in enumerate((kT[(u + 1) % 2], kT[u % 2])):
                                c = (2 * k + j) * P
                                mm = pe.matmul(sc[w][:, c:c + P], qT[at, k, :], keys[at, k, :], start=True, stop=True)
                        mm.then_inc(s.scores_ready, 1)

                pe.wait_ge(s.zeroed, 1 + CREDIT)
                turn(0, 0, 0)
                scores(0, 0)
                for i, n, u, more in tiles(pe):
                    if more:
                        turn(i + (u + 1) // UN, n + 1, (u + 1) % UN)
                    for w in range(2):
                        pe.wait_ge(s.probs_ready, n * HD + 2 * w + 2 + CREDIT)
                        pe.wait_ge(s.pT_ready, n * 2 + w + CREDIT)
                        for j in range(4):
                            mm = pe.transpose(pt[w][:, j * P:(j + 1) * P],
                                              p[:, 2 * w + j // 2, (j % 2) * P:(j % 2 + 1) * P], r.ident)
                        mm.then_inc(s.probs_turned, 1)
                    if more:
                        scores(n + 1, u + 1)
                    pe.wait_ge(s.pT_ready, n * 2 + 2 + CREDIT)
                    pe.wait_ge(s.u_ready, n + CREDIT)
                    pe.wait_ge(v_loaded[u], i * 32 + 32 + CREDIT)
                    for n4, h in enumerate(ORDER):
                        for j, vals in enumerate((v[(u - 1) % UN], v[u])):
                            mm = pe.matmul(po[:, h * E:(h + 1) * E], pT[:, n4, j, :], vals[:, h * E:(h + 1) * E],
                                           start=(j == 0), stop=(j == 1))
                    mm.then_inc(early.attended, 1)

            @block.scalar
            def _(act):
                def copy_q(n):
                    act.wait_ge(early.turned, n + 1 + AHEAD)
                    act.wait_ge(s.scores_ready, n * 2 + CREDIT)
                    act.copy(qT[:, :, :], pq[:, 0:2 * P].rearrange("p (k t) -> p k t", k=2)).then_inc(s.qT_ready, 1)

                copy_q(0)
                for i, n, u, more in tiles(act):
                    act.wait_ge(s.probs_turned, n * 2 + CREDIT)
                    for n4, h in enumerate(ORDER):
                        act.wait_ge(s.max_found, n * 2 + n4 // 2 + 1 + CREDIT)
                        act.activation(p[:, n4, :], sm[:, n4, :], ACT.Exp, bias=ou[u % 2][:, GE + h:GE + h + 1],
                                       accum_out=ou[u % 2][:, GE + HD + h:GE + HD + h + 1]).then_inc(s.probs_ready, 1)
                    if more:
                        copy_q(n + 1)

            @block.vector
            def _(dve):
                def copy_k(n, u):
                    dve.wait_ge(early.turned, n + 1 + AHEAD)
                    dve.wait_ge(s.scores_ready, n * 2 + CREDIT)
                    dve.tensor_copy(kT[u % 2][:, :, :], pk[:, 0:2 * P].rearrange("p (k t) -> p k t", k=2)
                                    ).then_inc(s.kT_ready, 1)

                def maxima(i, n, u):
                    dve.wait_ge(mask_loaded[u], i * 16 + 16 + CREDIT)
                    dve.wait_ge(s.probs_ready, n * HD + CREDIT)
                    for w in range(2):
                        dve.wait_ge(s.scores_ready, n * 2 + w + 1 + CREDIT)
                        dve.scalar_tensor_tensor(
                            out=sm[:, 2 * w:2 * w + 2, :], in0=sc[w][:, :].rearrange("p (h k) -> p h k", h=2),
                            scalar=DIL_SCALE, in1=mask[u][:, :].unsqueeze(1).broadcast_to([P, 2, 2 * P]),
                            op0=ALU.mult, op1=ALU.add).then_inc(early.masked, 1)
                        dve.wait_ge(early.masked, n * 2 + w + 1 + AHEAD)
                        dve.tensor_reduce(ou[u % 2][:, GE + w:GE + HD:2], sm[:, 2 * w:2 * w + 2, :], AX.X, ALU.max,
                                          negate=True).then_inc(s.max_found, 1)

                copy_k(0, 0)
                maxima(0, 0, 0)
                for i, n, u, more in tiles(dve):
                    if more:
                        copy_k(n + 1, u + 1)
                    for w in range(2):
                        dve.wait_ge(s.probs_turned, n * 2 + w + 1 + CREDIT)
                        dve.wait_ge(early.attended, n + AHEAD)
                        dve.tensor_copy(pT[:, 2 * w:2 * w + 2, :, :].rearrange("p h m t -> p (h m t)"), pt[w][:, :]
                                        ).then_inc(s.pT_ready, 1)
                    if more:
                        dve.wait_ge(s.ou_free, n + CREDIT)
                        maxima(i + (u + 1) // UN, n + 1, (u + 1) % UN)
                    dve.wait_ge(early.attended, n + 1 + AHEAD)
                    dve.tensor_copy(ou[u % 2][:, 0:GE], po[:, 0:GE]).then_inc(s.u_ready, 1)


def combine_groups(nc, a, r):
    ctx, sb, ps, sems = stage(nc, "comb")
    with ctx:
        x = sb("x", [P, NG, GE + 2 * HD])
        nmx, dm, w, wl, L = sb("nmx", [P, HD]), sb("dm", [P, NG, HD]), sb("w", [P, NG, HD]), sb("wl", [P, NG, HD]), sb("L", [P, HD])
        o = sb("o", [P, NG, GE])
        om = sb("om", [P, H_MLA * V_DIM])
        pd, pm = ps("pd", [P, 512]), ps("pm", [P, 512])
        s = sems("x_loaded om_loaded steps diff_ready weights_ready o_ready o_turned oT_ready om_turned omT_ready")
        N = 11
        with nc.Block() as block:
            @block.sync
            def _(sp):
                with sp.Fori(0, NTP) as i:
                    sp.wait_ge(s.o_ready, i + CREDIT)
                    for g in range(NG):
                        sp.dma_start(x[:, g, :], a.dilo[g, ds(i * P, P), :]).then_inc(s.x_loaded, 16)
                    sp.wait_ge(s.om_turned, i + CREDIT)
                    sp.dma_start(om[:, :], a.omla[ds(i * P, P), :]).then_inc(s.om_loaded, 16)

            @block.scalar
            def _(act):
                with act.Fori(0, NTP) as i:
                    act.wait_ge(s.diff_ready, i + 1 + CREDIT)
                    act.activation(w[:, :, :], dm[:, :, :], ACT.Exp).then_inc(s.weights_ready, 1)
                    act.wait_ge(s.om_turned, i + 1 + CREDIT)
                    act.copy(r.oT_mla[:, :, ds(i * P, P)], pm[:, :].rearrange("p (h t) -> p h t", h=4)).then_inc(s.omT_ready, 1)

            @block.vector
            def _(dve):
                with dve.Fori(0, NTP) as i:
                    step = Steps(dve, s.steps, i, N)
                    dve.wait_ge(s.x_loaded, i * 48 + 48 + CREDIT)
                    nm = x[:, :, GE:GE + HD]
                    step(dve.tensor_tensor(nmx[:, :], nm[:, 0, :], nm[:, 1, :], ALU.min))
                    step(dve.tensor_tensor(nmx[:, :], nmx[:, :], nm[:, 2, :], ALU.min))
                    dve.tensor_tensor(dm[:, :, :], nmx[:, :].unsqueeze(1).broadcast_to([P, NG, HD]), nm, ALU.subtract
                                      ).then_inc(s.diff_ready, 1)
                    dve.wait_ge(s.weights_ready, i + 1 + CREDIT)
                    step(dve.tensor_tensor(wl[:, :, :], w[:, :, :], x[:, :, GE + HD:GE + 2 * HD], ALU.mult))
                    step(dve.tensor_tensor(L[:, :], wl[:, 0, :], wl[:, 1, :], ALU.add))
                    step(dve.tensor_tensor(L[:, :], L[:, :], wl[:, 2, :], ALU.add))
                    step(dve.reciprocal(L[:, :], L[:, :]))
                    step(dve.tensor_tensor(wl[:, :, :], w[:, :, :], L[:, :].unsqueeze(1).broadcast_to([P, NG, HD]), ALU.mult))
                    dve.wait_ge(s.o_turned, i + CREDIT)
                    for g in range(NG):
                        step(dve.tensor_tensor(o[:, g, :].rearrange("p (h e) -> p h e", h=HD),
                                               x[:, g, 0:GE].rearrange("p (h e) -> p h e", h=HD),
                                               wl[:, g, :].unsqueeze(2).broadcast_to([P, HD, E]), ALU.mult))
                    step(dve.tensor_tensor(o[:, 1, :], o[:, 1, :], o[:, 2, :], ALU.add))
                    dve.tensor_tensor(o[:, 0, :], o[:, 0, :], o[:, 1, :], ALU.add).then_inc(s.o_ready, 1)
                    step.end()
                    dve.wait_ge(s.o_turned, i + 1 + CREDIT)
                    dve.tensor_copy(r.oT_dil[:, :, ds(i * P, P)], pd[:, 0:2 * P].rearrange("p (h t) -> p h t", h=2)
                                    ).then_inc(s.oT_ready, 1)

            @block.tensor
            def _(pe):
                with pe.Fori(0, NTP) as i:
                    pe.wait_ge(s.om_loaded, i * 16 + 16 + CREDIT)
                    pe.wait_ge(s.omT_ready, i + CREDIT)
                    for k in range(4):
                        mm = pe.transpose(pm[:, k * P:(k + 1) * P], om[:, k * P:(k + 1) * P], r.ident)
                    mm.then_inc(s.om_turned, 1)
                    pe.wait_ge(s.o_ready, i + 1 + CREDIT)
                    pe.wait_ge(s.oT_ready, i + CREDIT)
                    for k in range(2):
                        mm = pe.transpose(pd[:, k * P:(k + 1) * P], o[:, 0, k * P:(k + 1) * P], r.ident)
                    mm.then_inc(s.o_turned, 1)


def latent_attention(nc, a, r):
    ctx, sb, ps, sems = stage(nc, "mla")
    HALF = 512
    with ctx:
        qT, kT = sb("qT", [QK, SEQ]), sb("kT", [QK, SEQ])
        w, v = sb("w", [P, 2, NOPE + V_DIM]), sb("v", [P, NTP, V_DIM])
        mask = sb("mask", [P, P])
        nm, nb, l, rl = sb("nm", [P, 2]), sb("nb", [P, 2]), sb("l", [P, 2]), sb("rl", [P, 2])
        p = [sb(f"p{u}", [P, SEQ]) for u in range(2)]
        pT, o = sb("pT", [P, NTP, P]), sb("o", [P, NTP, V_DIM])
        sc = [ps(f"sc{u}", [P, SEQ]) for u in range(2)]
        pt = [ps(f"pt{u}", [P, 512]) for u in range(2)]
        pu, pkv = ps("pu", [P, 512]), ps("pkv", [P, 512])
        s = sems("mask_loaded pe_copied q_loaded w_loaded kv_product k_copied v_copied scores_ready max_found bias_ready "
                 "probs_ready turned_lo turned_hi copied_lo copied_hi attended sum_inverted o_ready stored")
        wkv = a.w_kv_up.rearrange("(k p) (h c) -> p k h c", p=P, h=H_MLA)
        with nc.Block() as block:
            @block.sync
            def _(sp):
                sp.dma_start(mask[:, :], a.mask_mla).then_inc(s.mask_loaded, 16)
                with sp.Fori(0, H_MLA) as i:
                    sp.wait_ge(s.scores_ready, i * NTP + CREDIT)
                    sp.dma_start(qT[:, :], a.qT[:, ds(i, 1), 0:SEQ].squeeze(1)).then_inc(s.q_loaded, 16)
                    sp.wait_ge(s.kv_product, i * 3 + CREDIT)
                    sp.dma_start(w[:, :, :], wkv[:, :, ds(i, 1), :].squeeze(2)).then_inc(s.w_loaded, 16)
                    sp.wait_ge(s.o_ready, i * NTP + NTP + CREDIT)
                    sp.dma_start(a.omla[0:SEQ, ds(i * V_DIM, V_DIM)].rearrange("(q p) e -> p q e", p=P), o[:, :, :]
                                 ).then_inc(s.stored, 16)
                sp.wait_ge(s.stored, 16 * H_MLA + CREDIT)

            @block.tensor
            def _(pe):
                pe.wait_ge(s.mask_loaded, 16 + CREDIT)
                pe.wait_ge(s.pe_copied, 1 + CREDIT)
                with pe.Fori(0, H_MLA) as i:
                    pe.wait_ge(s.w_loaded, i * 16 + 16 + CREDIT)
                    for c in range(2):
                        pe.wait_ge(s.k_copied, i * 2 + c + CREDIT)
                        if c == 0:
                            pe.wait_ge(s.v_copied, i + CREDIT)
                        for k in range(2):
                            mm = pe.matmul(pkv[0:NOPE, :], w[:, k, 0:NOPE], r.ckvT[:, k, c * HALF:(c + 1) * HALF],
                                           start=(k == 0), stop=(k == 1))
                        mm.then_inc(s.kv_product, 1)
                    pe.wait_ge(s.k_copied, i * 2 + 2 + CREDIT)
                    for t in range(NTP):
                        for k in range(2):
                            mm = pe.matmul(pkv[:, t * V_DIM:(t + 1) * V_DIM], r.ckvT[:, k, t * P:(t + 1) * P],
                                           w[:, k, NOPE:], start=(k == 0), stop=(k == 1))
                    mm.then_inc(s.kv_product, 1)
                    pe.wait_ge(s.q_loaded, i * 16 + 16 + CREDIT)

                    def scores(b):
                        n = (b + 1) * P
                        pe.wait_ge(s.probs_ready, i * NTP + max(b - 1, 0) + CREDIT)
                        for c in range(0, n, HALF):
                            e = min(n, c + HALF)
                            mm = pe.matmul(sc[b % 2][:, c:e], qT[:, b * P:(b + 1) * P], kT[:, c:e], start=True, stop=(e < n))
                        pe.matmul(sc[b % 2][:, b * P:n], r.ident, mask[:, :], start=False, stop=True
                                  ).then_inc(s.scores_ready, 1)

                    scores(0)
                    scores(1)
                    for b in range(NTP):
                        pe.wait_ge(s.probs_ready, i * NTP + b + 1 + CREDIT)
                        pe.wait_ge(s.copied_lo, i * NTP + b + CREDIT)
                        for k in range(min(b + 1, 4)):
                            mm = pe.transpose(pt[0][:, k * P:(k + 1) * P], p[b % 2][:, k * P:(k + 1) * P], r.ident)
                        mm.then_inc(s.turned_lo, 1)
                        if b >= 4:
                            pe.wait_ge(s.copied_hi, i * 4 + b - 4 + CREDIT)
                            for k in range(4, b + 1):
                                mm = pe.transpose(pt[1][:, (k - 4) * P:(k - 3) * P], p[b % 2][:, k * P:(k + 1) * P], r.ident)
                            mm.then_inc(s.turned_hi, 1)
                        if b + 2 < NTP:
                            scores(b + 2)
                        if b >= 4:
                            pe.wait_ge(s.copied_hi, i * 4 + b - 3 + CREDIT)
                        pe.wait_ge(s.copied_lo, i * NTP + b + 1 + CREDIT)
                        pe.wait_ge(s.o_ready, i * NTP + b + CREDIT)
                        if b == 0:
                            pe.wait_ge(s.v_copied, i + 1 + CREDIT)
                        for k in range(b + 1):
                            mm = pe.matmul(pu[:, 0:V_DIM], pT[:, k, :], v[:, k, :], start=(k == 0), stop=(k == b))
                        mm.then_inc(s.attended, 1)

            @block.scalar
            def _(act):
                act.copy(kT[NOPE:QK, :], r.kpeT[NOPE:QK, 0:SEQ]).then_inc(s.pe_copied, 1)
                with act.Fori(0, H_MLA) as i:
                    act.wait_ge(s.scores_ready, i * NTP + CREDIT)
                    for c in range(2):
                        act.wait_ge(s.kv_product, i * 3 + c + 1 + CREDIT)
                        act.copy(kT[0:NOPE, c * HALF:(c + 1) * HALF], pkv[0:NOPE, :]).then_inc(s.k_copied, 1)

                    def exp(b):
                        n = (b + 1) * P
                        act.wait_ge(s.bias_ready, i * NTP + b + 1 + CREDIT)
                        act.wait_ge(s.turned_lo, i * NTP + max(b - 1, 0) + CREDIT)
                        act.wait_ge(s.turned_hi, i * 4 + max(b - 5, 0) + CREDIT)
                        act.wait_ge(s.sum_inverted, i * NTP + max(b - 1, 0) + CREDIT)
                        act.activation(p[b % 2][:, 0:n], sc[b % 2][:, 0:n], ACT.Exp, bias=nb[:, b % 2:b % 2 + 1],
                                       scale=MLA_SCALE, accum_out=l[:, b % 2:b % 2 + 1]).then_inc(s.probs_ready, 1)

                    exp(0)
                    for b in range(NTP):
                        if b + 1 < NTP:
                            exp(b + 1)
                        if b >= 4:
                            act.wait_ge(s.turned_hi, i * 4 + b - 3 + CREDIT)
                            act.wait_ge(s.attended, i * NTP + b + CREDIT)
                            act.copy(pT[:, 4:b + 1, :], pt[1][:, 0:(b - 3) * P].rearrange("p (k t) -> p k t", t=P)
                                     ).then_inc(s.copied_hi, 1)

            @block.vector
            def _(dve):
                with dve.Fori(0, H_MLA) as i:
                    dve.wait_ge(s.attended, i * NTP + CREDIT)
                    dve.wait_ge(s.kv_product, i * 3 + 3 + CREDIT)
                    dve.tensor_copy(v[:, :, :], pkv[:, :].rearrange("p (t e) -> p t e", e=V_DIM)).then_inc(s.v_copied, 1)
                    dve.wait_ge(s.stored, i * 16 + CREDIT)

                    def maximum(b):
                        dve.wait_ge(s.scores_ready, i * NTP + b + 1 + CREDIT)
                        dve.tensor_reduce(nm[:, b % 2:b % 2 + 1], sc[b % 2][:, 0:(b + 1) * P], AX.X, ALU.max, negate=True
                                          ).then_inc(s.max_found, 1)
                        dve.wait_ge(s.max_found, i * NTP + b + 1 + CREDIT)
                        dve.wait_ge(s.probs_ready, i * NTP + max(b - 1, 0) + CREDIT)
                        dve.tensor_scalar(nb[:, b % 2:b % 2 + 1], nm[:, b % 2:b % 2 + 1], MLA_SCALE, None, ALU.mult
                                          ).then_inc(s.bias_ready, 1)

                    maximum(0)
                    maximum(1)
                    for b in range(NTP):
                        dve.wait_ge(s.turned_lo, i * NTP + b + 1 + CREDIT)
                        dve.wait_ge(s.attended, i * NTP + b + CREDIT)
                        m = min(b + 1, 4)
                        dve.tensor_copy(pT[:, 0:m, :], pt[0][:, 0:m * P].rearrange("p (k t) -> p k t", t=P)
                                        ).then_inc(s.copied_lo, 1)
                        if b + 2 < NTP:
                            maximum(b + 2)
                        dve.reciprocal(rl[:, b % 2:b % 2 + 1], l[:, b % 2:b % 2 + 1]).then_inc(s.sum_inverted, 1)
                        dve.wait_ge(s.sum_inverted, i * NTP + b + 1 + CREDIT)
                        dve.wait_ge(s.attended, i * NTP + b + 1 + CREDIT)
                        dve.tensor_scalar(o[:, b, :], pu[:, 0:V_DIM], rl[:, b % 2:b % 2 + 1], None, ALU.mult
                                          ).then_inc(s.o_ready, 1)


def sample_latent_attention(nc, a, r):
    ctx, sb, ps, sems = stage(nc, "smla")
    PG, RB = 4, 4
    NC = N_PAGES // PG
    ROUNDS = DB // RB
    QR = H_MLA * DT
    with ctx:
        w = sb("w", [P, 2, H_MLA, NOPE + V_DIM])
        wukT = sb("wukT", [NOPE, H_MLA, KV_LORA])
        qn, qp = sb("qn", [NOPE, H_MLA, NS]), sb("qp", [ROPE, H_MLA, NS])
        qlat, qpe = sb("qlat", [P, 2, DB, H_MLA, DT]), sb("qpe", [ROPE, DB, H_MLA, DT])
        kpn, rn = sb("kpn", [ROPE, NS]), sb("rn", [DT, DB, KV_LORA])
        mnew = sb("mnew", [P, DT])
        table = sb("table", [1, DB * N_PAGES], I32)
        kv = [sb(f"kv{u}", [P, RB, PG, ROW]) for u in range(2)]
        kT = [sb(f"kT{u}", [P, 2, PG * P]) for u in range(2)]
        kp = [sb(f"kp{u}", [ROPE, PG * P]) for u in range(2)]
        nm, nb, l = sb("nm", [P, 1]), sb("nb", [P, NC + 1]), sb("l", [P, NC + 1])
        p, pT = sb("p", [P, PG * P]), sb("pT", [P, PG, P])
        U = sb("U", [P, NC + 1, KV_LORA])
        sn, pn, pnT = sb("sn", [P, DT]), sb("pn", [P, DT]), sb("pnT", [DT, P])
        nmx, dm, wt, wl, L = sb("nmx", [P, 1]), sb("dm", [P, NC + 1]), sb("wt", [P, NC + 1]), sb("wl", [P, NC + 1]), sb("L", [P, 1])
        lat, latT = sb("lat", [P, KV_LORA]), sb("latT", [P, 2, H_MLA, RB * DT])
        o = sb("o", [RB * DT, H_MLA * V_DIM])
        b0 = [ps(f"b0{u}", [P, 512]) for u in range(2)]
        b1 = [ps(f"b1{u}", [P, 512]) for u in range(2)]
        bp = ps("bp", [P, 512])
        psc, ppt, pu = ps("psc", [P, 512]), ps("ppt", [P, 512]), ps("pu", [P, 512])
        s = sems("loaded zeroed w_turned wukT_ready q_product q_ready turned k0_copied k1_copied "
                 "kp_copied scores_ready max_found bias_ready probs_ready probs_turned pT_ready U_ready "
                 "new_scores new_masked new_max new_probs new_turned new_T new_attended new_copied steps diff_ready weights_ready "
                 "lat_ready lat_turned latT_ready o_product o_copied o_turned oT_ready")
        early = sems("attended", 2)
        names = lambda seqs: " ".join(f"pages_loaded{u}_{bb}" for u in range(2) for bb in seqs)
        by_sync, by_pool = sems(names(range(RB - 1))), sems(names([RB - 1]), 0)
        pages_loaded = [[*by_sync[u * (RB - 1):(u + 1) * (RB - 1)], by_pool[u]] for u in range(2)]
        N_MERGE = 6 + NC
        SEQUENCE = 16 * PG

        def load_pages(eng, rd, i, u, seqs):
            pages = [(bb, g, eng.value_load(table[0:1, ds(i * (2 * PG) + ((rd * RB + bb) * N_PAGES + u * PG + g), 1)],
                                            min_val=0, max_val=POOL_PAGES - 1)) for bb in seqs for g in range(PG)]
            eng.wait_ge(early.attended, i * 2 + (rd * NC + u - 1) + 2)
            for bb, g, page in pages:
                eng.dma_start(kv[u][:, bb, g, :], a.cache_mla[ds(page, 1), :, :].squeeze(0)).then_inc(pages_loaded[u][bb], 16)

        def chunks(eng, rd):
            loads = rd * (NC // 2)
            yield rd * NC, 0, 0, loads + 1, False
            with eng.Fori(0, NC // 2 - 1) as i:
                yield i * 2 + (rd * NC + 1), 1, i * 2 + 1, i + (loads + 1), True
                yield i * 2 + (rd * NC + 2), 0, i * 2 + 2, i + (loads + 2), True
            yield rd * NC + NC - 1, 1, NC - 1, loads + NC // 2, True

        def before(n, bb, prev):
            return n * RB + (bb - 1 if prev else max(bb - 1, 0))

        with nc.Block() as block:
            @block.sync
            def _(sp):
                for dst, src in (
                    (w[:, :, :, :], a.w_kv_up.rearrange("(k p) (h c) -> p k h c", p=P, h=H_MLA)),
                    (qn[:, :, :], a.qT[0:NOPE, :, SEQ:SEQ + NS]),
                    (qp[:, :, :], a.qT[NOPE:QK, :, SEQ:SEQ + NS]),
                    (rn[:, :, :], a.rows[SEQ:SEQ + NS, 0:KV_LORA].rearrange("(b t) c -> t b c", t=DT)),
                    (mnew[:, :], a.mask_new),
                    (table[:, :], a.page_table),
                ):
                    sp.dma_start(dst, src).then_inc(s.loaded, 16)
                with nc.allow_non_contiguous_dma("the new tokens' rotary keys, turned: 32 x 32 numbers"):
                    sp.dma_start(kpn[:, :], a.rows[SEQ:SEQ + NS, KV_LORA:ROW].rearrange("t c -> c t")).then_inc(s.loaded, 16)
                sp.wait_ge(s.loaded, 112 + CREDIT)
                for rd in range(ROUNDS):
                    with sp.Fori(0, NC // 2) as i:
                        for u in range(2):
                            load_pages(sp, rd, i, u, range(RB - 1))

            @block.gpsimd
            def _(pool):
                pool.memset(r.oT_mla[:, :, SEQ + NS:T], 0.0)
                pool.memset(r.oT_dil[:, :, SEQ + NS:T], 0.0)
                pool.memset(r.oT_mem[:, :, SEQ + NS:T], 0.0).then_inc(s.zeroed, 1)
                pool.wait_ge(s.zeroed, 1 + CREDIT)
                pool.wait_ge(s.loaded, 112 + CREDIT)
                for rd in range(ROUNDS):
                    with pool.Fori(0, NC // 2) as i:
                        for u in range(2):
                            load_pages(pool, rd, i, u, [RB - 1])

            @block.tensor
            def _(pe):
                pe.wait_ge(s.loaded, 112 + CREDIT)
                for h in range(H_MLA):
                    for k in range(2):
                        n = 2 * h + k
                        bank = (b0 + b1)[n // 4]
                        mm = pe.transpose(bank[:, n % 4 * P:(n % 4 + 1) * P], w[:, k, h, :], r.ident)
                mm.then_inc(s.w_turned, 1)
                pe.wait_ge(s.wukT_ready, 4 + CREDIT)
                for k in range(2):
                    for h in range(H_MLA):
                        n = k * H_MLA + h
                        mm = pe.matmul(psc[:, n * NS:(n + 1) * NS], wukT[:, h, k * P:(k + 1) * P], qn[:, h, :],
                                       start=True, stop=True)
                mm.then_inc(s.q_product, 1)
                pe.wait_ge(s.q_ready, 3 + CREDIT)
                for rd in range(ROUNDS):
                    def turn(n, u, bb, load, prev):
                        pe.wait_ge(pages_loaded[u][bb], load * SEQUENCE + (0 if bb == RB - 1 else CREDIT))
                        pe.wait_ge(s.k0_copied, before(n, bb, prev) + CREDIT)
                        pe.wait_ge(s.k1_copied, before(n, bb, prev) + CREDIT)
                        for g in range(PG):
                            pe.transpose(b0[bb % 2][:, g * P:(g + 1) * P], kv[u][:, bb, g, 0:P], r.ident)
                        for g in range(PG):
                            pe.transpose(b1[bb % 2][:, g * P:(g + 1) * P], kv[u][:, bb, g, P:2 * P], r.ident)
                        pe.wait_ge(s.kp_copied, n * RB + bb + CREDIT)
                        for g in range(PG):
                            mm = pe.transpose(bp[0:ROPE, g * P:(g + 1) * P], kv[u][:, bb, g, 2 * P:ROW], r.ident)
                        mm.then_inc(s.turned, 1)

                    def scores(m, bb):
                        pe.wait_ge(s.k0_copied, m + 1 + CREDIT)
                        pe.wait_ge(s.k1_copied, m + 1 + CREDIT)
                        pe.wait_ge(s.kp_copied, m + 1 + CREDIT)
                        b = rd * RB + bb
                        out = psc[bb * QR:(bb + 1) * QR, :]
                        for k in range(2):
                            pe.matmul(out, qlat[:, k, b, :, :].rearrange("p h t -> p (h t)"), kT[bb % 2][:, k, :],
                                      start=(k == 0), stop=False)
                        pe.matmul(out, qpe[:, b, :, :].rearrange("p h t -> p (h t)"), kp[bb % 2][:, :],
                                  start=False, stop=True).then_inc(s.scores_ready, 1)

                    def turn_probs(n):
                        pe.wait_ge(s.probs_ready, n + CREDIT)
                        pe.wait_ge(s.pT_ready, n - 1 + CREDIT)
                        for g in range(PG):
                            mm = pe.transpose(ppt[:, g * P:(g + 1) * P], p[:, g * P:(g + 1) * P], r.ident)
                        mm.then_inc(s.probs_turned, 1)

                    def weigh(n, u):
                        pe.wait_ge(s.pT_ready, n + CREDIT)
                        pe.wait_ge(s.U_ready, n - 1 + CREDIT)
                        for bb in range(RB):
                            for g in range(PG):
                                mm = pe.matmul(pu[bb * QR:(bb + 1) * QR, 0:KV_LORA], pT[:, g, bb * QR:(bb + 1) * QR],
                                               kv[u][:, bb, g, 0:KV_LORA], start=(g == 0), stop=(g == PG - 1))
                        mm.then_inc(early.attended, 1)

                    for n, u, slot, load, prev in chunks(pe, rd):
                        turn(n, u, 0, load, prev)
                        if prev:
                            scores(n * RB - 1, RB - 1)
                        turn(n, u, 1, load, prev)
                        if prev:
                            turn_probs(n)
                        scores(n * RB, 0)
                        turn(n, u, 2, load, prev)
                        if prev:
                            weigh(n, 1 - u)
                        scores(n * RB + 1, 1)
                        turn(n, u, 3, load, prev)
                        scores(n * RB + 2, 2)
                    done = (rd + 1) * NC
                    scores(done * RB - 1, RB - 1)
                    turn_probs(done)
                    weigh(done, 1)
                    pe.wait_ge(s.probs_ready, (rd + 1) * NC + CREDIT)
                    for bb in range(RB):
                        b = rd * RB + bb
                        out = psc[bb * QR:(bb + 1) * QR, 0:DT]
                        for k in range(2):
                            pe.matmul(out, qlat[:, k, b, :, :].rearrange("p h t -> p (h t)"),
                                      r.ckvT[:, k, SEQ + b * DT:SEQ + (b + 1) * DT], start=(k == 0), stop=False)
                        mm = pe.matmul(out, qpe[:, b, :, :].rearrange("p h t -> p (h t)"), kpn[:, b * DT:(b + 1) * DT],
                                       start=False, stop=True)
                    mm.then_inc(s.new_scores, 1)
                    pe.wait_ge(s.new_probs, rd + 1 + CREDIT)
                    pe.wait_ge(s.pT_ready, (rd + 1) * NC + CREDIT)
                    pe.transpose(ppt[0:DT, 0:P], pn[:, :], r.ident).then_inc(s.new_turned, 1)
                    pe.wait_ge(s.new_T, rd + 1 + CREDIT)
                    pe.wait_ge(s.U_ready, (rd + 1) * NC + CREDIT)
                    for bb in range(RB):
                        mm = pe.matmul(pu[bb * QR:(bb + 1) * QR, 0:KV_LORA], pnT[:, bb * QR:(bb + 1) * QR],
                                       rn[:, rd * RB + bb, :], start=True, stop=True)
                    mm.then_inc(s.new_attended, 1)
                    pe.wait_ge(s.lat_ready, rd + 1 + CREDIT)
                    for k in range(2):
                        mm = pe.transpose(b0[0][:, k * P:(k + 1) * P], lat[:, k * P:(k + 1) * P], r.ident)
                    mm.then_inc(s.lat_turned, 1)
                    pe.wait_ge(s.latT_ready, 2 * rd + 2 + CREDIT)
                    for h in range(H_MLA):
                        for k in range(2):
                            mm = pe.matmul(b1[0][0:RB * DT, h * V_DIM:(h + 1) * V_DIM], latT[:, k, h, :],
                                           w[:, k, h, NOPE:], start=(k == 0), stop=(k == 1))
                    mm.then_inc(s.o_product, 1)
                    pe.wait_ge(s.o_copied, rd + 1 + CREDIT)
                    for k in range(4):
                        mm = pe.transpose(b0[1][:, k * RB * DT:(k + 1) * RB * DT], o[:, k * P:(k + 1) * P],
                                          r.ident[0:RB * DT, 0:RB * DT])
                    mm.then_inc(s.o_turned, 1)
                    pe.wait_ge(s.oT_ready, rd + 1 + CREDIT)

            @block.scalar
            def _(act):
                for rd in range(ROUNDS):
                    def exp(n, slot):
                        act.wait_ge(s.probs_turned, n - 1 + CREDIT)
                        act.wait_ge(s.bias_ready, n + CREDIT)
                        act.activation(p[:, :], psc[:, :], ACT.Exp, bias=nb[:, ds(slot, 1)], scale=MLA_SCALE,
                                       accum_out=l[:, ds(slot, 1)]).then_inc(s.probs_ready, 1)

                    for n, u, slot, load, prev in chunks(act, rd):
                        for bb in range(RB):
                            act.wait_ge(s.turned, n * RB + bb + 1 + CREDIT)
                            act.wait_ge(s.scores_ready, before(n, bb, prev) + CREDIT)
                            act.copy(kT[bb % 2][:, 1, :], b1[bb % 2][:, :]).then_inc(s.k1_copied, 1)
                            if bb == 0 and prev:
                                exp(n, slot - 1)
                    exp((rd + 1) * NC, NC - 1)
                    act.wait_ge(s.new_max, rd + 1 + CREDIT)
                    act.activation(pn[:, :], sn[:, :], ACT.Exp, bias=nb[:, NC:NC + 1], accum_out=l[:, NC:NC + 1]
                                   ).then_inc(s.new_probs, 1)
                    act.wait_ge(s.diff_ready, rd + 1 + CREDIT)
                    act.activation(wt[:, :], dm[:, :], ACT.Exp).then_inc(s.weights_ready, 1)

            @block.vector
            def _(dve):
                dve.wait_ge(s.w_turned, 1 + CREDIT)
                for j, bank in enumerate(b0 + b1):
                    dve.tensor_copy(wukT[:, 2 * j:2 * j + 2, :].rearrange("n h c -> n (h c)"), bank[0:NOPE, :]
                                    ).then_inc(s.wukT_ready, 1)
                dve.wait_ge(s.q_product, 1 + CREDIT)
                for k in range(2):
                    src = psc[:, k * H_MLA * NS:(k + 1) * H_MLA * NS].rearrange("p (h b t) -> p h b t", h=H_MLA, b=DB)
                    dve.tensor_copy(qlat[:, k, :, :, :].rearrange("p b h t -> p h b t"), src).then_inc(s.q_ready, 1)
                dve.wait_ge(s.loaded, 112 + CREDIT)
                dve.tensor_copy(qpe[:, :, :, :].rearrange("p b h t -> p h b t"),
                                qp[:, :, :].rearrange("p h (b t) -> p h b t", b=DB)).then_inc(s.q_ready, 1)
                for rd in range(ROUNDS):
                    def maximum(n, slot):
                        dve.wait_ge(s.scores_ready, n * RB + CREDIT)
                        dve.tensor_reduce(nm[:, :], psc[:, :], AX.X, ALU.max, negate=True).then_inc(s.max_found, 1)
                        dve.wait_ge(s.max_found, n + CREDIT)
                        dve.tensor_scalar(nb[:, ds(slot, 1)], nm[:, :], MLA_SCALE, None, ALU.mult).then_inc(s.bias_ready, 1)

                    def copy_probs(n):
                        dve.wait_ge(s.probs_turned, n + CREDIT)
                        dve.wait_ge(early.attended, n - 1 + 2)
                        dve.tensor_copy(pT[:, :, :].rearrange("p g t -> p (g t)"), ppt[:, :]).then_inc(s.pT_ready, 1)

                    def copy_sums(n, slot):
                        dve.wait_ge(early.attended, n + 2)
                        dve.tensor_copy(U[:, ds(slot, 1), :].squeeze(1), pu[:, 0:KV_LORA]).then_inc(s.U_ready, 1)

                    for n, u, slot, load, prev in chunks(dve, rd):
                        for bb in range(RB):
                            dve.wait_ge(s.turned, n * RB + bb + 1 + CREDIT)
                            dve.wait_ge(s.scores_ready, before(n, bb, prev) + CREDIT)
                            dve.tensor_copy(kp[bb % 2][:, :], bp[0:ROPE, :]).then_inc(s.kp_copied, 1)
                            dve.tensor_copy(kT[bb % 2][:, 0, :], b0[bb % 2][:, :]).then_inc(s.k0_copied, 1)
                            if prev and bb == 0:
                                maximum(n, slot - 1)
                            if prev and bb == 1:
                                copy_probs(n)
                            if prev and bb == 2:
                                copy_sums(n, slot - 1)
                    maximum((rd + 1) * NC, NC - 1)
                    copy_probs((rd + 1) * NC)
                    copy_sums((rd + 1) * NC, NC - 1)
                    step = Steps(dve, s.steps)
                    step.n = rd * N_MERGE
                    dve.wait_ge(s.new_scores, rd + 1 + CREDIT)
                    step(dve.scalar_tensor_tensor(out=sn[:, :], in0=psc[:, 0:DT], scalar=MLA_SCALE, in1=mnew[:, :],
                                                  op0=ALU.mult, op1=ALU.add))
                    dve.tensor_reduce(nb[:, NC:NC + 1], sn[:, :], AX.X, ALU.max, negate=True).then_inc(s.new_max, 1)
                    dve.wait_ge(s.new_turned, rd + 1 + CREDIT)
                    dve.tensor_copy(pnT[:, :], ppt[0:DT, 0:P]).then_inc(s.new_T, 1)
                    dve.wait_ge(s.new_attended, rd + 1 + CREDIT)
                    dve.tensor_copy(U[:, NC, :], pu[:, 0:KV_LORA]).then_inc(s.new_copied, 1)
                    dve.wait_ge(s.new_max, rd + 1 + CREDIT)
                    step(dve.tensor_reduce(nmx[:, :], nb[:, :], AX.X, ALU.min))
                    dve.tensor_scalar(dm[:, :], nb[:, :], nmx[:, 0:1], -1.0, ALU.subtract, ALU.mult).then_inc(s.diff_ready, 1)
                    dve.wait_ge(s.weights_ready, rd + 1 + CREDIT)
                    step(dve.tensor_tensor(wl[:, :], wt[:, :], l[:, :], ALU.mult))
                    step(dve.tensor_reduce(L[:, :], wl[:, :], AX.X, ALU.add))
                    step(dve.reciprocal(L[:, :], L[:, :]))
                    step(dve.tensor_scalar(wt[:, :], wt[:, :], L[:, 0:1], None, ALU.mult))
                    dve.wait_ge(s.new_copied, rd + 1 + CREDIT)
                    step(dve.tensor_scalar(lat[:, :], U[:, 0, :], wt[:, 0:1], None, ALU.mult))
                    for c in range(1, NC + 1):
                        ins = dve.scalar_tensor_tensor(out=lat[:, :], in0=U[:, c, :], scalar=wt[:, c:c + 1], in1=lat[:, :],
                                                       op0=ALU.mult, op1=ALU.add)
                        if c < NC:
                            step(ins)
                        else:
                            ins.then_inc(s.lat_ready, 1)
                    assert step.n == (rd + 1) * N_MERGE, step.n
                    dve.wait_ge(s.lat_turned, rd + 1 + CREDIT)
                    for k in range(2):
                        dve.tensor_copy(latT[:, k, :, :].rearrange("p h (b t) -> p h b t", b=RB),
                                        b0[0][:, k * P:(k + 1) * P].rearrange("p (b h t) -> p h b t", b=RB, h=H_MLA)
                                        ).then_inc(s.latT_ready, 1)
                    dve.wait_ge(s.o_product, rd + 1 + CREDIT)
                    dve.tensor_copy(o[:, :], b1[0][0:RB * DT, :]).then_inc(s.o_copied, 1)
                    dve.wait_ge(s.o_turned, rd + 1 + CREDIT)
                    at = SEQ + rd * RB * DT
                    dve.tensor_copy(r.oT_mla[:, :, at:at + RB * DT],
                                    b0[1][:, 0:4 * RB * DT].rearrange("p (k t) -> p k t", k=4)).then_inc(s.oT_ready, 1)


def sample_dilated_attention(nc, a, r):
    ctx, sb, ps, sems = stage(nc, "sdil")
    W = P + 1
    with ctx:
        q = sb("q", [P, NG, E])
        k, v = sb("k", [P, W, E]), sb("v", [P, W, E])
        sc, p = sb("sc", [P, W]), sb("p", [P, W])
        nm, nb, l = sb("nm", [P, 1]), sb("nb", [P, NG]), sb("l", [P, NG])
        U = sb("U", [P, NG, E])
        nmx, dm, wt, wl, L = sb("nmx", [P, 1]), sb("dm", [P, NG]), sb("wt", [P, NG]), sb("wl", [P, NG]), sb("L", [P, 1])
        o = sb("o", [P, E])
        po = ps("po", [P, 512])
        s = sems("q_loaded k_loaded v_loaded steps scored bias_ready probs_ready weighed diff_ready weights_ready o_ready "
                 "o_turned oT_ready")

        def window(eng, dst, g, j, loaded):
            dil = GROUPS[g][1]
            new = a.dil[SEQ:SEQ + NS, (1 + j) * NG * GE + g * GE:(1 + j) * NG * GE + (g + 1) * GE
                        ].rearrange("(b t) c -> b t c", t=DT)
            for t in range(DT):
                n_old = P - t if g == 0 else P
                first = 0 if g == 0 else t
                for h in range(HD):
                    at = dst[(t * HD + h) * DB:(t * HD + h + 1) * DB, :, :]
                    part = slice(h * E, (h + 1) * E)
                    old = a.cache_dil[g][:, t:t + (n_old - 1) * dil + 1:dil, j, part]
                    eng.dma_start(at[:, 0:n_old, :], old).then_inc(loaded, 16)
                    eng.dma_start(at[:, n_old:W, :], new[:, first:t + 1, part]).then_inc(loaded, 16)

        FULL = 16 * 2 * DT * HD
        with nc.Block() as block:
            @block.sync
            def _(sp):
                qs = a.dil[SEQ:SEQ + NS, 0:NG * GE].rearrange("(b t) (g h e) -> t h b g e", t=DT, g=NG, h=HD)
                for t in range(DT):
                    for h in range(HD):
                        sp.dma_start(q[(t * HD + h) * DB:(t * HD + h + 1) * DB, :, :], qs[t, h]).then_inc(s.q_loaded, 16)
                for g in range(NG):
                    if g:
                        sp.wait_ge(s.scored, g + CREDIT)
                    window(sp, k, g, 0, s.k_loaded)

            @block.vector
            def _(dve):
                step = Steps(dve, s.steps)
                dve.wait_ge(s.q_loaded, 16 * DT * HD + CREDIT)
                for g in range(NG):
                    dve.wait_ge(s.k_loaded, FULL * (g + 1) + CREDIT)
                    step(dve.tensor_tensor(k[:, :, :], k[:, :, :], q[:, g, :].unsqueeze(1).broadcast_to([P, W, E]), ALU.mult))
                    dve.tensor_reduce(sc[:, :], k[:, :, :], AX.X, ALU.add).then_inc(s.scored, 1)
                    dve.wait_ge(s.scored, g + 1 + CREDIT)
                    step(dve.tensor_reduce(nm[:, :], sc[:, :], AX.X, ALU.max, negate=True))
                    dve.tensor_scalar(nb[:, g:g + 1], nm[:, :], DIL_SCALE, None, ALU.mult).then_inc(s.bias_ready, 1)
                    dve.wait_ge(s.probs_ready, g + 1 + CREDIT)
                    dve.wait_ge(s.v_loaded, FULL * (g + 1) + CREDIT)
                    step(dve.tensor_tensor(v[:, :, :], v[:, :, :], p[:, :].unsqueeze(2).broadcast_to([P, W, E]), ALU.mult))
                    dve.tensor_reduce(U[:, g, :], v[:, :, :].rearrange("p l e -> p e l"), AX.X, ALU.add).then_inc(s.weighed, 1)
                dve.wait_ge(s.bias_ready, NG + CREDIT)
                step(dve.tensor_reduce(nmx[:, :], nb[:, :], AX.X, ALU.min))
                dve.tensor_scalar(dm[:, :], nb[:, :], nmx[:, 0:1], -1.0, ALU.subtract, ALU.mult).then_inc(s.diff_ready, 1)
                dve.wait_ge(s.weights_ready, 1 + CREDIT)
                step(dve.tensor_tensor(wl[:, :], wt[:, :], l[:, :], ALU.mult))
                step(dve.tensor_reduce(L[:, :], wl[:, :], AX.X, ALU.add))
                step(dve.reciprocal(L[:, :], L[:, :]))
                step(dve.tensor_scalar(wt[:, :], wt[:, :], L[:, 0:1], None, ALU.mult))
                dve.wait_ge(s.weighed, NG + CREDIT)
                step(dve.tensor_scalar(o[:, :], U[:, 0, :], wt[:, 0:1], None, ALU.mult))
                step(dve.scalar_tensor_tensor(out=o[:, :], in0=U[:, 1, :], scalar=wt[:, 1:2], in1=o[:, :],
                                              op0=ALU.mult, op1=ALU.add))
                dve.scalar_tensor_tensor(out=o[:, :], in0=U[:, 2, :], scalar=wt[:, 2:3], in1=o[:, :],
                                         op0=ALU.mult, op1=ALU.add).then_inc(s.o_ready, 1)
                dve.wait_ge(s.o_turned, 1 + CREDIT)
                for h in range(HD):
                    at = slice(h % 2 * E, (h % 2 + 1) * E)
                    dve.tensor_copy(r.oT_dil[at, h // 2, SEQ:SEQ + NS].rearrange("e (b t) -> e t b", t=DT),
                                    po[0:E, 0:P].rearrange("e (t h b) -> e h t b", t=DT, h=HD)[:, h]).then_inc(s.oT_ready, 1)

            @block.scalar
            def _(act):
                for g in range(NG):
                    if g:
                        act.wait_ge(s.weighed, g + CREDIT)
                    window(act, v, g, 1, s.v_loaded)
                    act.wait_ge(s.bias_ready, g + 1 + CREDIT)
                    act.activation(p[:, :], sc[:, :], ACT.Exp, bias=nb[:, g:g + 1], scale=DIL_SCALE,
                                   accum_out=l[:, g:g + 1]).then_inc(s.probs_ready, 1)
                act.wait_ge(s.diff_ready, 1 + CREDIT)
                act.activation(wt[:, :], dm[:, :], ACT.Exp).then_inc(s.weights_ready, 1)

            @block.tensor
            def _(pe):
                pe.wait_ge(s.o_ready, 1 + CREDIT)
                pe.transpose(po[0:E, 0:P], o[:, :], r.ident).then_inc(s.o_turned, 1)


def sample_memory_attention(nc, a, r):
    ctx, sb, ps, sems = stage(nc, "smem")
    R = HM * DT
    with ctx:
        x, qT = sb("x", [NS, HM * EM]), sb("qT", [P, HM, NS])
        kv, kT = sb("kv", [P, 2, 2 * HM * EM]), sb("kT", [P, HM, 2, P])
        sT, p, pT = sb("sT", [P, 2, R]), sb("p", [P, MEM]), sb("pT", [P, 2, R])
        nm, nb, l = sb("nm", [R, 1]), sb("nb", [R, 1]), sb("l", [R, 1])
        pq = ps("pq", [P, 512])
        pk = [ps(f"pk{u}", [P, 512]) for u in range(2)]
        pst, psc, ppt, po = ps("pst", [P, 512]), ps("psc", [P, 512]), ps("ppt", [P, 512]), ps("po", [P, 512])
        s = sems("zeroed x_loaded q_turned qT_ready kv_loaded k_turned kT_ready product_ready sT_ready scores_ready max_found bias_ready "
                 "exp_ready inverted probs_ready probs_turned pT_ready attended oT_ready")
        with nc.Block() as block:
            @block.sync
            def _(sp):
                sp.dma_start(x[:, :], a.proj[SEQ:SEQ + NS, C_MEM:C_GATE]).then_inc(s.x_loaded, 16)
                with sp.Fori(0, DB) as i:
                    sp.wait_ge(s.attended, i + CREDIT)
                    sp.dma_start(kv[:, :, :], a.cache_mem[ds(i, 1), :, :].squeeze(0).rearrange("(m p) c -> p m c", p=P)
                                 ).then_inc(s.kv_loaded, 16)

            @block.gpsimd
            def _(pool):
                pool.memset(p[:, :], 0.0).then_inc(s.zeroed, 1)
                pool.wait_ge(s.zeroed, 1 + CREDIT)

            @block.tensor
            def _(pe):
                pe.wait_ge(s.x_loaded, 16 + CREDIT)
                for h in range(HM):
                    mm = pe.transpose(pq[:, h * NS:(h + 1) * NS], x[:, h * EM:(h + 1) * EM], r.ident[0:NS, 0:NS])
                mm.then_inc(s.q_turned, 1)
                pe.wait_ge(s.qT_ready, 1 + CREDIT)
                with pe.Fori(0, DB) as i:
                    pe.wait_ge(s.kv_loaded, i * 16 + 16 + CREDIT)
                    pe.wait_ge(s.kT_ready, i * 2 + CREDIT)
                    for h in range(HM):
                        for m in range(2):
                            mm = pe.transpose(pk[h // 2][:, (h % 2 * 2 + m) * P:(h % 2 * 2 + m + 1) * P],
                                              kv[:, m, h * EM:(h + 1) * EM], r.ident)
                    mm.then_inc(s.k_turned, 1)
                    pe.wait_ge(s.kT_ready, i * 2 + 2 + CREDIT)
                    pe.wait_ge(s.sT_ready, i + CREDIT)
                    for m in range(2):
                        for h in range(HM):
                            mm = pe.matmul(pst[:, m * R + h * DT:m * R + (h + 1) * DT], kT[:, h, m, :],
                                           qT[:, h, ds(i * DT, DT)], start=True, stop=True)
                    mm.then_inc(s.product_ready, 1)
                    pe.wait_ge(s.sT_ready, i + 1 + CREDIT)
                    pe.wait_ge(s.exp_ready, i + CREDIT)
                    for m in range(2):
                        mm = pe.transpose(psc[0:R, m * P:(m + 1) * P], sT[:, m, :], r.ident)
                    mm.then_inc(s.scores_ready, 1)
                    pe.wait_ge(s.probs_ready, i + 1 + CREDIT)
                    pe.wait_ge(s.pT_ready, i + CREDIT)
                    for m in range(2):
                        mm = pe.transpose(ppt[:, m * P:(m + 1) * P], p[:, m * P:(m + 1) * P], r.ident)
                    mm.then_inc(s.probs_turned, 1)
                    pe.wait_ge(s.pT_ready, i + 1 + CREDIT)
                    pe.wait_ge(s.oT_ready, i + CREDIT)
                    for h in range(HM):
                        for m in range(2):
                            mm = pe.matmul(po[:, h * DT:(h + 1) * DT], kv[:, m, (HM + h) * EM:(HM + h + 1) * EM],
                                           pT[:, m, h * DT:(h + 1) * DT], start=(m == 0), stop=(m == 1))
                    mm.then_inc(s.attended, 1)

            @block.scalar
            def _(act):
                act.wait_ge(s.zeroed, 1 + CREDIT)
                with act.Fori(0, DB) as i:
                    act.wait_ge(s.bias_ready, i + 1 + CREDIT)
                    act.wait_ge(s.probs_turned, i + CREDIT)
                    act.activation(p[0:R, :], psc[0:R, 0:MEM], ACT.Exp, bias=nb[:, :], scale=MEM_SCALE, accum_out=l[:, :]
                                   ).then_inc(s.exp_ready, 1)

            @block.vector
            def _(dve):
                dve.wait_ge(s.q_turned, 1 + CREDIT)
                dve.tensor_copy(qT[:, :, :].rearrange("p h t -> p (h t)"), pq[:, 0:HM * NS]).then_inc(s.qT_ready, 1)
                with dve.Fori(0, DB) as i:
                    dve.wait_ge(s.k_turned, i + 1 + CREDIT)
                    dve.wait_ge(s.product_ready, i + CREDIT)
                    for u in range(2):
                        dve.tensor_copy(kT[:, 2 * u:2 * u + 2, :, :].rearrange("p h m t -> p (h m t)"), pk[u][:, :]
                                        ).then_inc(s.kT_ready, 1)
                    dve.wait_ge(s.product_ready, i + 1 + CREDIT)
                    dve.wait_ge(s.scores_ready, i + CREDIT)
                    dve.tensor_copy(sT[:, :, :].rearrange("p m q -> p (m q)"), pst[:, 0:2 * R]).then_inc(s.sT_ready, 1)
                    dve.wait_ge(s.scores_ready, i + 1 + CREDIT)
                    dve.tensor_reduce(nm[:, :], psc[0:R, 0:MEM], AX.X, ALU.max, negate=True).then_inc(s.max_found, 1)
                    dve.wait_ge(s.max_found, i + 1 + CREDIT)
                    dve.tensor_scalar(nb[:, :], nm[:, :], MEM_SCALE, None, ALU.mult).then_inc(s.bias_ready, 1)
                    dve.wait_ge(s.exp_ready, i + 1 + CREDIT)
                    dve.reciprocal(nm[:, :], l[:, :]).then_inc(s.inverted, 1)
                    dve.wait_ge(s.inverted, i + 1 + CREDIT)
                    dve.tensor_scalar(p[0:R, :], p[0:R, :], nm[:, 0:1], None, ALU.mult).then_inc(s.probs_ready, 1)
                    dve.wait_ge(s.probs_turned, i + 1 + CREDIT)
                    dve.wait_ge(s.attended, i + CREDIT)
                    dve.tensor_copy(pT[:, :, :], ppt[:, 0:2 * P].rearrange("p (m q) -> p m q", m=2)[:, :, 0:R]).then_inc(s.pT_ready, 1)
                    dve.wait_ge(s.attended, i + 1 + CREDIT)
                    dve.tensor_copy(r.oT_mem[:, :, ds(i * DT + SEQ, DT)], po[:, 0:R].rearrange("p (h t) -> p h t", h=HM)
                                    ).then_inc(s.oT_ready, 1)


def mix_branches(nc, a, r, xT, mT):
    ctx, sb, ps, sems = stage(nc, "mix")
    TH = (SEQ + NS) // 3
    UN = 9
    with ctx:
        wg = [sb(f"wg{u}", [P, KD, 3, P]) for u in range(2)]
        wo = [sb(f"wo{u}", [P, 10, P]) for u in range(2)]
        sg = [sb(f"sg{u}", [P, TH]) for u in range(2)]
        pr = [sb(f"pr{u}", [P, TH]) for u in range(3)]
        pg, py = [ps(f"pg{u}", [P, 512]) for u in range(2)], [ps(f"py{u}", [P, 512]) for u in range(2)]
        s = sems("zeroed w_loaded0 w_loaded1 product_ready gate_ready weighed steps summed")
        w_loaded = (s.w_loaded0, s.w_loaded1)
        gates = a.w_in[:, C_GATE:].rearrange("(k p) (b n) -> p k b n", p=P, b=3)
        branches = ((a.w_o_mla, r.oT_mla, 0, 4), (a.w_o_dil, r.oT_dil, 4, 2), (a.w_o_mem, r.oT_mem, 6, 4))
        with nc.Block() as block:
            @block.sync
            def _(sp):
                def load(u, c):
                    col = ds(c * P, P)
                    for b in range(3):
                        sp.dma_start(wg[u][:, :, b, :], gates[:, :, b, col]).then_inc(w_loaded[u], 16)
                    for w, _, k0, kk in branches:
                        sp.dma_start(wo[u][:, k0:k0 + kk, :], w.rearrange("(k p) n -> p k n", p=P)[:, :, col]
                                     ).then_inc(w_loaded[u], 16)

                load_pairs(sp, KD // 2, s.product_ready, UN, load)

            @block.gpsimd
            def _(pool):
                pool.memset(mT[:, :, SEQ + NS:T], 0.0).then_inc(s.zeroed, 1)
                pool.wait_ge(s.zeroed, 1 + CREDIT)

            @block.tensor
            def _(pe):
                with pe.Fori(0, KD // 2) as i:
                    for u in range(2):
                        pe.wait_ge(w_loaded[u], i * 96 + 96 + CREDIT)
                        for n in range(UN):
                            m = u * UN + n
                            rows = slice(n // 3 * TH, (n // 3 + 1) * TH)
                            _, oT, k0, kk = branches[n % 3]
                            pe.wait_ge(s.weighed, i * (2 * UN) + max(m - 1, 0) + CREDIT)
                            for k in range(KD):
                                pe.matmul(pg[m % 2][:, 0:TH], wg[u][:, k, n % 3, :], xT[:, k, rows],
                                          start=(k == 0), stop=(k == KD - 1))
                            for k in range(kk):
                                mm = pe.matmul(py[m % 2][:, 0:TH], wo[u][:, k0 + k, :], oT[:, k, rows],
                                               start=(k == 0), stop=(k == kk - 1))
                            mm.then_inc(s.product_ready, 1)

            @block.scalar
            def _(act):
                with act.Fori(0, KD // 2) as i:
                    for m in range(2 * UN):
                        act.wait_ge(s.product_ready, i * (2 * UN) + m + 1 + CREDIT)
                        act.wait_ge(s.weighed, i * (2 * UN) + max(m - 1, 0) + CREDIT)
                        act.activation(sg[m % 2][:, :], pg[m % 2][:, 0:TH], ACT.Sigmoid).then_inc(s.gate_ready, 1)

            @block.vector
            def _(dve):
                with dve.Fori(0, KD // 2) as i:
                    step = Steps(dve, s.steps, i, 6)
                    for m in range(2 * UN):
                        dve.wait_ge(s.gate_ready, i * (2 * UN) + m + 1 + CREDIT)
                        dve.tensor_tensor(pr[m % 3][:, :], sg[m % 2][:, :], py[m % 2][:, 0:TH], ALU.mult).then_inc(s.weighed, 1)
                        if m % 3 == 2:
                            dve.wait_ge(s.weighed, i * (2 * UN) + m + 1 + CREDIT)
                            step(dve.tensor_tensor(pr[0][:, :], pr[0][:, :], pr[1][:, :], ALU.add))
                            third = m % UN // 3
                            dst = mT[:, ds(i * 2 + m // UN, 1), third * TH:(third + 1) * TH].squeeze(1)
                            dve.tensor_tensor(dst, pr[0][:, :], pr[2][:, :], ALU.add).then_inc(s.summed, 1)
                            dve.wait_ge(s.summed, i * 6 + m // 3 + 1 + CREDIT)
                    step.end()


def peer_scores(nc, a, r, xT):
    ctx, sb, ps, sems = stage(nc, "psc")
    TH = (SEQ + NS) // 3
    with ctx:
        keys, keysT = sb("keys", [P, 2, QH]), sb("keysT", [P, 2, NK])
        w = [sb(f"w{u}", [P, KD, QH]) for u in range(2)]
        qT = [sb(f"qT{u}", [P, T]) for u in range(2)]
        sc = [sb(f"sc{u}", [P, NT, NK]) for u in range(2)]
        pq = [ps(f"pq{u}", [P, 512]) for u in range(3)]
        psc = [ps(f"psc{u}", [P, 512]) for u in range(3)]
        s = sems("zeroed keys_loaded keys_turned keysT_ready w_loaded0 w_loaded1 q_product qT_ready scores_ready scores_copied "
                 "stored0 stored1")
        w_loaded, stored = (s.w_loaded0, s.w_loaded1), (s.stored0, s.stored1)
        wv = a.w_peer_q.rearrange("(k p) n -> p k n", p=P)
        dst = a.scores.rearrange("(t p) c n -> p t c n", p=P)
        with nc.Block() as block:
            @block.sync
            def _(sp):
                sp.dma_start(keys[:, :, :], a.peer_sub_keys.rearrange("c n e -> n c e")).then_inc(s.keys_loaded, 16)
                load_pairs(sp, HP, s.q_product, 3, lambda u, c: sp.dma_start(
                    w[u][:, :, :], wv[:, :, ds(c * QH, QH)]).then_inc(w_loaded[u], 16))

            @block.gpsimd
            def _(pool):
                for u in range(2):
                    pool.memset(qT[u][:, SEQ + NS:T], 0.0).then_inc(s.zeroed, 1)
                pool.wait_ge(s.zeroed, 2 + CREDIT)

            @block.tensor
            def _(pe):
                pe.wait_ge(s.keys_loaded, 16 + CREDIT)
                for u in range(2):
                    mm = pe.transpose(pq[0][:, u * P:(u + 1) * P], keys[:, u, :], r.ident)
                mm.then_inc(s.keys_turned, 1)
                pe.wait_ge(s.keysT_ready, 1 + CREDIT)
                pe.wait_ge(s.zeroed, 2 + CREDIT)
                with pe.Fori(0, HP) as i:
                    for u in range(2):
                        pe.wait_ge(w_loaded[u], i * 16 + 16 + CREDIT)
                        for c in range(3):
                            pe.wait_ge(s.qT_ready, i * 6 + (c + 1 if u else 0) + CREDIT)
                            for k in range(KD):
                                mm = pe.matmul(pq[c][:, 0:TH], w[u][:, k, :], xT[:, k, c * TH:(c + 1) * TH],
                                               start=(k == 0), stop=(k == KD - 1))
                            mm.then_inc(s.q_product, 1)
                        for c in range(3):
                            pe.wait_ge(s.qT_ready, i * 6 + 3 * u + min(c + 2, 3) + CREDIT)
                            pe.wait_ge(s.scores_copied, i * 6 + (c + 1 if u else 0) + CREDIT)
                            for t in range(3):
                                n = 3 * c + t
                                mm = pe.matmul(psc[c][:, t * NK:(t + 1) * NK], qT[u][:, n * P:(n + 1) * P], keysT[:, u, :],
                                               start=True, stop=True)
                            mm.then_inc(s.scores_ready, 1)

            @block.scalar
            def _(act):
                with act.Fori(0, HP) as i:
                    for u in range(2):
                        act.wait_ge(s.scores_ready, i * 6 + CREDIT)
                        for c in range(3):
                            act.wait_ge(s.q_product, i * 6 + 3 * u + c + 1 + CREDIT)
                            act.copy(qT[u][:, c * TH:(c + 1) * TH], pq[c][:, 0:TH]).then_inc(s.qT_ready, 1)
                        act.wait_ge(s.scores_copied, i * 6 + 3 * u + 3 + CREDIT)
                        act.dma_start(dst[:, :, ds(i * 2 + u, 1), :].squeeze(2), sc[u][:, :, :]).then_inc(stored[u], 16)
                for u in range(2):
                    act.wait_ge(stored[u], 16 * HP + CREDIT)

            @block.vector
            def _(dve):
                dve.wait_ge(s.keys_turned, 1 + CREDIT)
                dve.tensor_copy(keysT[:, :, :].rearrange("p c n -> p (c n)"), pq[0][:, 0:2 * P]).then_inc(s.keysT_ready, 1)
                with dve.Fori(0, HP) as i:
                    for u in range(2):
                        dve.wait_ge(stored[u], i * 16 + CREDIT)
                        for c in range(3):
                            dve.wait_ge(s.scores_ready, i * 6 + 3 * u + c + 1 + CREDIT)
                            dve.tensor_copy(sc[u][:, 3 * c:3 * c + 3, :].rearrange("p t n -> p (t n)"), psc[c][:, 0:3 * NK]
                                            ).then_inc(s.scores_copied, 1)


Turn = namedtuple("Turn", "t v u k")
Rows = namedtuple("Rows", "n slots")


def peer_experts(nc, a, r):
    ctx, sb, ps, sems = stage(nc, "peer")
    GROUP = 8
    NGR = SLOTS // GROUP
    RING = 2 * GROUP
    G2 = 2 * HP
    QUARTERS = P // NS
    PROMPT, SAMPLE = Rows(P, SLOTS), Rows(NS, SLOTS // QUARTERS)
    with ctx:
        S = sb("S", [P, G2, NK])
        m, ix, ixf = sb("m", [P, G2, TOPK]), sb("ix", [P, G2, TOPK], U32), sb("ixf", [P, G2, TOPK])
        cand = sb("cand", [P, HP, TOPK * TOPK])
        best, jx = sb("best", [P, HP, TOPK]), sb("jx", [P, HP, TOPK], U32)
        part, partf = sb("part", [P, 2, SLOTS], U32), sb("partf", [P, 2, SLOTS])
        hot = S[:, :, :].rearrange("p c n -> p (c n)").rearrange("p (s x) -> p s x", x=TOPK)
        num, ef, eid = sb("num", [P, 2, SLOTS]), sb("ef", [P, SLOTS]), sb("eid", [P, SLOTS], U32)
        d, ex, sm, gate = sb("d", [P, HP, TOPK]), sb("ex", [P, HP, TOPK]), sb("sm", [P, HP]), sb("gate", [P, HP, TOPK])
        iota, held = sb("iota", [P, TOPK]), sb("held", [P, 1])
        x, h = sb("x", [P, D]), sb("h", [P, D])
        eid_u, eid_v, gate_u = sb("eid_u", [P, SLOTS], U32), sb("eid_v", [P, SLOTS], U32), sb("gate_u", [P, SLOTS])
        ub = [sb(f"ub{u}", [P, D]) for u in range(RING)]
        vb = [sb(f"vb{u}", [P, D]) for u in range(RING)]
        zero, held_u, held_v = sb("zero", [P, 1]), sb("held_u", [P, 1]), sb("held_v", [P, 1])
        act_in, gl, coef = sb("act_in", [P, SLOTS]), sb("gl", [P, SLOTS]), sb("coef", [P, SLOTS])
        dg = [sb(f"dg{u}", [P, P]) for u in range(RING)]
        fold = sb("fold", [P, NS])
        g, y = sb("g", [P, D]), sb("y", [P, D])
        ss, ms, rt, rstd = sb("ss", [P, 1]), sb("ms", [P, 1]), sb("rt", [P, 1]), sb("rstd", [P, 1])
        acc = [ps(f"acc{u}", [P, 512]) for u in range(2)]
        own = sems("u_loaded0 u_loaded1 v_loaded0 v_loaded1", 0)
        s = sems("constants_loaded S_loaded steps steps2 chosen chosen_stored diff_ready exp_ready sum_ready sum_inverted "
                 "zeroed u_wait_taken v_wait_taken eid_u_loaded eid_v_loaded gate_loaded x_loaded h_loaded "
                 "dotted gelu_ready coef_ready diag_ready v_used squares_summed mean_ready root_ready rstd_ready y_ready "
                 "h_added stored")
        u_loaded, v_loaded = (own.u_loaded0, own.u_loaded1), (own.v_loaded0, own.v_loaded1)
        FULL = 16 * GROUP
        TILE = FULL * NGR // 2
        STEPS, STEPS2 = 11, 11

        def turns(eng):
            yield Turn(-2, None, None, True)
            yield Turn(-1, None, PROMPT, True)
            with eng.Fori(0, NTP - 1) as t:
                yield Turn(t, PROMPT, PROMPT, True)
            yield Turn(NTP - 1, PROMPT, SAMPLE, False)
            yield Turn(NTP, SAMPLE, None, False)

        with nc.Block() as block:
            @block.sync
            def _(sp):
                def load(dst, src, first, shape, sem, every=False):
                    if shape == PROMPT:
                        sp.dma_start(dst[:, :], src[ds(first, P), :]).then_inc(sem, 16)
                    else:
                        for q in range(QUARTERS):
                            rows, cols = slice(q * NS, (q + 1) * NS), slice(q * shape.slots, (q + 1) * shape.slots)
                            if every:
                                sp.dma_start(dst[rows, :], src[ds(first, NS), :]).then_inc(sem, 16)
                            else:
                                sp.dma_start(dst[rows, 0:shape.slots], src[ds(first, NS), cols]).then_inc(sem, 16)

                sp.dma_start(iota[:, :], a.iota16).then_inc(s.constants_loaded, 16)
                sp.dma_start(g[:, :], a.g_final.partition_broadcast(P)).then_inc(s.constants_loaded, 16)
                sp.dma_start(fold[:, :], a.fold).then_inc(s.constants_loaded, 16)
                for t, v, u, k in turns(sp):
                    if u:
                        sp.wait_ge(s.chosen_stored, t * 32 + 64 + CREDIT)
                        if v:
                            sp.wait_ge(u_loaded[1], t * TILE + TILE)
                        load(eid_u, a.experts, t * P + P, u, s.eid_u_loaded)
                    if k:
                        sp.wait_ge(s.chosen, t + 2 + CREDIT)
                        sp.dma_start(S[:, :, :], a.scores[ds(t * P + 2 * P, P), :, :]).then_inc(s.S_loaded, 16)
                    if u:
                        sp.wait_ge(s.dotted, t * NGR + NGR + CREDIT)
                        load(x, a.xn2, t * P + P, u, s.x_loaded, True)
                    if v:
                        sp.wait_ge(s.v_used, t * NGR + CREDIT)
                        load(eid_v, a.experts, t * P, v, s.eid_v_loaded)
                    if u:
                        sp.wait_ge(s.coef_ready, t + 1 + CREDIT)
                        load(gate_u, a.gates, t * P + P, u, s.gate_loaded)
                    if v:
                        sp.wait_ge(s.y_ready, t + CREDIT)
                        sp.dma_start(h[0:v.n, :], a.h[ds(t * P, v.n), :]).then_inc(s.h_loaded, 16)
                    if k:
                        sp.wait_ge(s.chosen, t + 3 + CREDIT)
                        rows = ds(t * P + 2 * P, P)
                        sp.dma_start(a.experts[rows, :], eid[:, :]).then_inc(s.chosen_stored, 16)
                        sp.dma_start(a.gates[rows, :], gate[:, :, :].rearrange("p h k -> p (h k)")).then_inc(s.chosen_stored, 16)

            @block.gpsimd
            def _(pool):
                pool.memset(zero[:, :], 0.0).then_inc(s.zeroed, 1)
                pool.wait_ge(s.zeroed, 1 + CREDIT)

                def gather(j, done, bufs, indices, loaded, used, table, held, taken):
                    pool.wait_ge(taken, done + j + CREDIT)
                    pool.wait_ge(used, done + max(j - 1, 0) + CREDIT)
                    pool.tensor_tensor(held[:, :], zero[:, :], zero[:, :], ALU.add).then_inc(taken, 1)
                    for k in range(j * GROUP, (j + 1) * GROUP):
                        pool.indirect_dma_start(bufs[k % RING][:, :], None, table,
                                                bass.IndirectOffsetOnAxis(ap=indices[:, k:k + 1], axis=0)
                                                ).then_inc(loaded[j % 2], 16)

                for t, v, u, k in turns(pool):
                    for j in range(NGR + 1):
                        if u and j * GROUP < u.slots:
                            if j == 0:
                                pool.wait_ge(s.eid_u_loaded, t * 16 + 16 + 16 * (P // u.n) + CREDIT)
                            gather(j, t * NGR + NGR, ub, eid_u, u_loaded, s.dotted, a.peer_u, held_u, s.u_wait_taken)
                        if v and 0 < j and (j - 1) * GROUP < v.slots:
                            if j == 1:
                                pool.wait_ge(s.eid_v_loaded, t * 16 + 16 * (P // v.n) + CREDIT)
                            gather(j - 1, t * NGR, vb, eid_v, v_loaded, s.v_used, a.peer_v, held_v, s.v_wait_taken)

            @block.vector
            def _(dve):
                square = [P, HP, TOPK, TOPK]
                mv = m[:, :, :].rearrange("p (h c) k -> p h c k", c=2)
                iv = ixf[:, :, :].rearrange("p (h c) k -> p h c k", c=2)

                def hold():
                    dve.memset(held[:, :], 0.0)

                def top16(what, values, n, out, index, step):
                    at = slice(8 * (what // 3), 8 * (what // 3) + 8)
                    hold()
                    for j in range(n):
                        if what % 3 == 0:
                            ins = dve.max(out[:, j, at], values[:, j, :])
                        elif what % 3 == 1:
                            ins = dve.max_index(index[:, j, at], out[:, j, at], values[:, j, :])
                        else:
                            ins = dve.match_replace(values[:, j, :], out[:, j, at], values[:, j, :], NEG)
                    step(ins)

                def choose(j, k, step, step2):
                    if j == 0:
                        dve.wait_ge(s.S_loaded, k * 16 + 16 + CREDIT)
                    if j < 5:
                        top16(j, S, G2, m, ix, step)
                    elif j == 5:
                        step(dve.tensor_copy(ixf[:, :, :], ix[:, :, :]))
                        step(dve.tensor_tensor(cand[:, :, :].rearrange("p h (x y) -> p h x y", x=TOPK),
                                               mv[:, :, 0, :].unsqueeze(3).broadcast_to(square),
                                               mv[:, :, 1, :].unsqueeze(2).broadcast_to(square), ALU.add))
                    elif j < 10:
                        top16(j - 6, cand, HP, best, jx, step)
                    elif j == 10:
                        top16(4, cand, HP, best, jx, step2)
                        dve.tensor_tensor(d[:, :, :], best[:, :, :], best[:, :, 0:1].broadcast_to([P, HP, TOPK]), ALU.subtract
                                          ).then_inc(s.diff_ready, 1)
                    elif j == 11:
                        jf = jx[:, :, :].rearrange("p h k -> p (h k)")
                        step2(dve.tensor_scalar(part[:, 0, :], jf, 4, None, ALU.logical_shift_right))
                        step2(dve.tensor_scalar(part[:, 1, :], jf, TOPK - 1, None, ALU.bitwise_and))
                        step2(dve.tensor_copy(partf[:, :, :], part[:, :, :]))
                    elif j < 14:
                        c = j - 12
                        hv = hot.rearrange("p (h k) x -> p h k x", h=HP)
                        step2(dve.tensor_tensor(hot, partf[:, c, :].unsqueeze(2).broadcast_to([P, SLOTS, TOPK]),
                                                iota[:, :].unsqueeze(1).broadcast_to([P, SLOTS, TOPK]), ALU.is_equal))
                        step2(dve.tensor_tensor(hv, hv, iv[:, :, c, :].unsqueeze(2).broadcast_to(square), ALU.mult))
                        step2(dve.tensor_reduce(num[:, c, :], hot, AX.X, ALU.add))
                    elif j == 14:
                        step2(dve.scalar_tensor_tensor(out=ef[:, :], in0=num[:, 0, :], scalar=float(NK), in1=num[:, 1, :],
                                                       op0=ALU.mult, op1=ALU.add))
                        dve.wait_ge(s.chosen_stored, k * 32 + CREDIT)
                        dve.tensor_copy(eid[:, :], ef[:, :])
                        dve.wait_ge(s.exp_ready, k + 1 + CREDIT)
                        dve.tensor_reduce(sm[:, :], ex[:, :, :], AX.X, ALU.add).then_inc(s.sum_ready, 1)
                        dve.wait_ge(s.sum_ready, k + 1 + CREDIT)
                        dve.reciprocal(sm[:, :], sm[:, :]).then_inc(s.sum_inverted, 1)
                        dve.wait_ge(s.sum_inverted, k + 1 + CREDIT)
                        dve.tensor_tensor(gate[:, :, :], ex[:, :, :], sm[:, :].unsqueeze(2).broadcast_to([P, HP, TOPK]),
                                          ALU.mult).then_inc(s.chosen, 1)

                dve.wait_ge(s.constants_loaded, 48 + CREDIT)
                for t, v, u, k in turns(dve):
                    step = Steps(dve, s.steps, t + 2, STEPS)
                    step2 = Steps(dve, s.steps2, t + 2, STEPS2)
                    if u:
                        dve.wait_ge(s.x_loaded, t * 16 + 16 + 16 * (P // u.n) + CREDIT)
                        dve.wait_ge(s.gelu_ready, t + 1 + CREDIT)
                    for j in range(NGR):
                        if u and j * GROUP < u.slots:
                            dve.wait_ge(u_loaded[j % 2], t * TILE + TILE + FULL * (j // 2 + 1))
                            for e in range(j * GROUP, (j + 1) * GROUP):
                                ins = dve.tensor_tensor_reduce(out=ub[e % RING][:, :], in0=ub[e % RING][:, :], in1=x[:, :],
                                                               scale=1.0, scalar=0.0, op0=ALU.mult, op1=ALU.add,
                                                               accum_out=act_in[:, e:e + 1])
                            ins.then_inc(s.dotted, 1)
                        if k:
                            choose(j, t + 2, step, step2)
                    if k:
                        step.end()
                        step2.end()
                    if u:
                        dve.wait_ge(s.gelu_ready, t + 2 + CREDIT)
                        dve.wait_ge(s.gate_loaded, t * 16 + 16 + 16 * (P // u.n) + CREDIT)
                        if v:
                            dve.wait_ge(s.diag_ready, t * NGR + NGR + CREDIT)
                        dve.tensor_tensor(coef[:, 0:u.slots], gl[:, 0:u.slots], gate_u[:, 0:u.slots], ALU.mult
                                          ).then_inc(s.coef_ready, 1)
                    if v:
                        dve.wait_ge(s.v_used, t * NGR + v.slots // GROUP + CREDIT)
                        dve.wait_ge(s.h_loaded, t * 16 + 16 + CREDIT)
                        for c in range(2):
                            half = slice(c * 512, (c + 1) * 512)
                            dve.tensor_tensor(h[0:v.n, half], acc[c][0:v.n, :], h[0:v.n, half], ALU.add).then_inc(s.h_added, 1)
                        dve.wait_ge(s.squares_summed, t + 1 + CREDIT)
                        dve.tensor_scalar(ms[0:v.n, :], ss[0:v.n, :], 1.0 / D, EPS, ALU.mult, ALU.add).then_inc(s.mean_ready, 1)
                        dve.wait_ge(s.root_ready, t + 1 + CREDIT)
                        dve.reciprocal(rstd[0:v.n, :], rt[0:v.n, :]).then_inc(s.rstd_ready, 1)
                        dve.wait_ge(s.rstd_ready, t + 1 + CREDIT)
                        dve.wait_ge(s.stored, t * 16 + CREDIT)
                        dve.scalar_tensor_tensor(out=y[0:v.n, :], in0=h[0:v.n, :], scalar=rstd[0:v.n, 0:1], in1=g[0:v.n, :],
                                                 op0=ALU.mult, op1=ALU.mult).then_inc(s.y_ready, 1)

            @block.scalar
            def _(act):
                def exp(k):
                    act.wait_ge(s.diff_ready, k + 1 + CREDIT)
                    act.activation(ex[:, :, :], d[:, :, :], ACT.Exp).then_inc(s.exp_ready, 1)

                act.wait_ge(s.constants_loaded, 48 + CREDIT)
                for t, v, u, k in turns(act):
                    for j in range(NGR):
                        if v and j * GROUP < v.slots:
                            act.wait_ge(s.v_used, t * NGR + max(j - 1, 0) + CREDIT)
                            for e in range(j * GROUP, (j + 1) * GROUP):
                                eye = r.ident if v == PROMPT else fold[:, :]
                                ins = act.activation(dg[e % RING][:, 0:v.n], eye, ACT.Copy, scale=coef[:, e:e + 1])
                            ins.then_inc(s.diag_ready, 1)
                        if k and j == NGR - 4:
                            exp(t + 2)
                    if u:
                        act.wait_ge(s.dotted, t * NGR + NGR + u.slots // GROUP + CREDIT)
                        act.wait_ge(s.coef_ready, t + 1 + CREDIT)
                        act.activation(gl[:, 0:u.slots], act_in[:, 0:u.slots], ACT.Gelu).then_inc(s.gelu_ready, 1)
                    if v:
                        act.wait_ge(s.h_added, t * 2 + 2 + CREDIT)
                        act.wait_ge(s.stored, t * 16 + CREDIT)
                        act.activation(y[0:v.n, :], h[0:v.n, :], ACT.Square, accum_out=ss[0:v.n, :]).then_inc(s.squares_summed, 1)
                        act.wait_ge(s.mean_ready, t + 1 + CREDIT)
                        act.activation(rt[0:v.n, :], ms[0:v.n, :], ACT.Sqrt).then_inc(s.root_ready, 1)
                        act.wait_ge(s.y_ready, t + 1 + CREDIT)
                        dst = a.y_prompt[ds(t * P, P), :] if v == PROMPT else a.y_sample
                        act.dma_start(dst, y[0:v.n, :]).then_inc(s.stored, 16)
                    if u:
                        act.wait_ge(s.coef_ready, t + 2 + CREDIT)
                act.wait_ge(s.stored, 16 * NT + CREDIT)

            @block.tensor
            def _(pe):
                for t, v, u, k in turns(pe):
                    if v:
                        pe.wait_ge(s.h_added, t * 2 + CREDIT)
                        for j in range(v.slots // GROUP):
                            pe.wait_ge(v_loaded[j % 2], t * TILE + FULL * (j // 2 + 1))
                            pe.wait_ge(s.diag_ready, t * NGR + j + 1 + CREDIT)
                            for e in range(j * GROUP, (j + 1) * GROUP):
                                for c in range(2):
                                    mm = pe.matmul(acc[c][0:v.n, :], dg[e % RING][:, 0:v.n], vb[e % RING][:, c * 512:(c + 1) * 512],
                                                   start=(e == 0), stop=(e == v.slots - 1))
                            mm.then_inc(s.v_used, 1)




OUTS = [(1, SEQ, D), (DB, DT, D), (1, 1, SEQ, ROW), (1, 1, 128, 2, HD, E), (1, 1, 512, 2, HD, E), (1, 1, SEQ, 2, HD, E),
        (1, 1, MEM, 2, HM, EM), (1, DB, DT, ROW), (1, DB, 128, 2, HD, E), (1, DB, 512, 2, HD, E), (1, DB, 2048, 2, HD, E)]


def keep_old_rows(nc, a, stored):
    for g in range(NG):
        L = GROUPS[g][0]
        for b in range(DB):
            nc.scalar.dma_start(a.new_dil_sample[g][b, 0:L - DT].rearrange("l j c -> l (j c)"),
                                a.cache_dil[g][b, DT:L].rearrange("l j c -> l (j c)")).then_inc(stored, 16)
    return 16 * NG * DB


def keep_new_rows(nc, a, stored):
    dil3 = a.dil.rearrange("t (j g c) -> t j g c", j=3, g=NG)
    nc.sync.dma_start(a.new_mla_prompt, a.rows[0:SEQ, :]).then_inc(stored, 16)
    nc.sync.dma_start(a.new_mla_sample, a.rows[SEQ:SEQ + NS, :]).then_inc(stored, 16)
    for g in range(NG):
        keep = min(GROUPS[g][0], SEQ)
        nc.sync.dma_start(a.new_dil_prompt[g], dil3[SEQ - keep:SEQ, 1:3, g, :]).then_inc(stored, 16)
        L = GROUPS[g][0]
        for b in range(DB):
            nc.sync.dma_start(a.new_dil_sample[g][b, L - DT:L], dil3[SEQ + b * DT:SEQ + (b + 1) * DT, 1:3, g, :]
                              ).then_inc(stored, 16)
    return 16 * (2 + NG * (1 + DB))


def build(nc, i, outs):
    def dram(name, shape, dt=F32):
        return nc.dram_tensor(name, shape, dt).ap()

    a = Dram()
    a.x = i["x"]
    a.mem = i["mem"]
    a.cache_mla = i["cache_mla"]
    a.page_table = i["page_table"]
    a.cache_mem = i["cache_mem"]
    a.w_in = i["w_in"]
    a.g_attn = i["g_attn"]
    a.g_q_lora = i["g_q_lora"]
    a.w_q_up = i["w_q_up"]
    a.g_kv_lora = i["g_kv_lora"]
    a.w_kv_up = i["w_kv_up"]
    a.w_o_mla = i["w_o_mla"]
    a.w_o_dil = i["w_o_dil"]
    a.w_mem_kv = i["w_mem_kv"]
    a.g_mem = i["g_mem"]
    a.w_o_mem = i["w_o_mem"]
    a.w_out = i["w_out"]
    a.g_ffn = i["g_ffn"]
    a.w_peer_q = i["w_peer_q"]
    a.peer_sub_keys = i["peer_sub_keys"]
    a.peer_u = i["peer_u"]
    a.peer_v = i["peer_v"]
    a.g_final = i["g_final"]
    a.identity = i["identity"]
    a.rope_mla = i["rope_mla"]
    a.rope_dil = i["rope_dil"]
    a.masks_dil = i["masks_dil"]
    a.mask_mla = i["mask_mla"]
    a.mask_new = i["mask_new"]
    a.iota16 = i["iota16"]
    a.fold = i["fold"]
    a.cache_dil = [v.rearrange("a b l j h e -> (a b) l j (h e)") for v in (i["cache_dil0"], i["cache_dil1"], i["cache_dil2"])]
    a.new_mla_prompt = outs[2].rearrange("a b s c -> (a b s) c")
    a.new_dil_prompt = [v.rearrange("a b s j h e -> (a b s) j (h e)") for v in outs[3:6]]
    a.mem_kv = outs[6].rearrange("a b m j h e -> (a b m) (j h e)")
    a.new_mla_sample = outs[7].rearrange("a b s c -> (a b s) c")
    a.new_dil_sample = [v.rearrange("a b l j h e -> (a b) l j (h e)") for v in outs[8:11]]
    a.proj = dram("proj_scratch", (T, PROJ))
    a.rows = dram("rows_scratch", (T, ROW))
    a.qT = dram("qT_scratch", (QK, H_MLA, T))
    a.dil = dram("dil_scratch", (T, DIL_COLS))
    a.dilo = dram("dilo_scratch", (NG, SEQ, GE + 2 * HD))
    a.omla = dram("omla_scratch", (T, H_MLA * V_DIM))
    a.h = dram("h_scratch", (T, D))
    a.xn2 = dram("xn2_scratch", (T, D))
    a.scores = dram("scores_scratch", (T, 2 * HP, NK))
    a.experts = dram("experts_scratch", (T, SLOTS), U32)
    a.gates = dram("gates_scratch", (T, SLOTS))
    a.y_prompt = outs[0].rearrange("a s d -> (a s) d")
    a.y_sample = outs[1].rearrange("b t d -> (b t) d")

    with ExitStack() as ctx, nc.semaphore("old_rows_stored") as old_rows_stored, nc.semaphore("new_rows_stored") as new_rows_stored:
        keep = lambda n, shape, dt=F32: ctx.enter_context(nc.sbuf_tensor(n, shape, dt))
        ident = keep("ident", [P, P])
        r = Resident()
        r.ident = ident[:, :]
        ident_loaded = ctx.enter_context(nc.semaphore("ident_loaded"))
        with nc.Block() as block:
            @block.sync
            def _(sp):
                sp.dma_start(ident[:, :], a.identity).then_inc(ident_loaded, 16)
                sp.wait_ge(ident_loaded, 16)
        with nc.sbuf_tensor("memT", [P, KD, MEM], F32) as memT:
            norm_rows(nc, "nmem", a.mem, a.g_mem, MEM // P, r.ident, memT)
            product_rows(nc, "pmem", memT, a.w_mem_kv, 2 * HM * EM, 512, MEM // P, a.mem_kv)
        xT = ctx.enter_context(nc.sbuf_tensor("xT", [P, KD, T], F32))
        norm_rows(nc, "nx", a.x, a.g_attn, NT, r.ident, xT)
        n_old = keep_old_rows(nc, a, old_rows_stored)
        product_rows(nc, "proj", xT, a.w_in[:, 0:PROJ], PROJ, PROJ // 8, NT, a.proj)
        with ExitStack() as turned:
            r.oT_mla = keep("oT_mla", [P, 4, T])
            r.oT_dil = keep("oT_dil", [P, 2, T])
            r.oT_mem = keep("oT_mem", [P, HM, T])
            r.ckvT = turned.enter_context(nc.sbuf_tensor("ckvT", [P, 2, T], F32))
            r.kpeT = turned.enter_context(nc.sbuf_tensor("kpeT", [P, T], F32))
            latents(nc, a, r)
            n_new = keep_new_rows(nc, a, new_rows_stored)
            memory_attention(nc, a, r)
            dilated_attention(nc, a, r)
            latent_attention(nc, a, r)
            combine_groups(nc, a, r)
            sample_latent_attention(nc, a, r)
        sample_dilated_attention(nc, a, r)
        sample_memory_attention(nc, a, r)
        mT = keep("mT", [P, KD, T])
        mix_branches(nc, a, r, xT, mT)
        product_rows(nc, "out", mT, a.w_out, D, 512, NT, a.h, add=a.x)
        nc.sync.wait_ge(old_rows_stored, n_old)
        nc.sync.wait_ge(new_rows_stored, n_new)
    with nc.sbuf_tensor("ident2", [P, P], F32) as ident:
        r = Resident()
        r.ident = ident[:, :]
        with nc.semaphore("ident2_loaded") as ident_loaded, nc.Block() as block:
            @block.sync
            def _(sp):
                sp.dma_start(ident[:, :], a.identity).then_inc(ident_loaded, 16)
                sp.wait_ge(ident_loaded, 16)
        with nc.sbuf_tensor("xT2", [P, KD, T], F32) as xT:
            norm_rows(nc, "nh", a.h, a.g_ffn, NT, r.ident, xT, a.xn2)
            peer_scores(nc, a, r, xT)
        peer_experts(nc, a, r)


def rope_table(dim):
    half = dim // 2
    inv = np.float32(THETA) ** (-np.arange(half, dtype=np.float32) * np.float32(2.0 / dim))
    pos = np.zeros(T, np.float32)
    pos[0:SEQ] = np.arange(SEQ)
    pos[SEQ:SEQ + NS] = PAST + np.arange(NS) % DT
    ang = pos[:, None] * inv[None, :]
    return np.concatenate([np.cos(ang), np.sin(ang)], axis=1).astype(np.float32)


def dilated_masks():
    q, k = np.arange(P)[:, None], np.arange(P)[None, :]
    m = np.full((NG * NTP, P, 2 * P), NEG, np.float32)
    own, before = k <= q, k >= q
    for t in range(NTP):
        m[t, :, P:] = np.where(own, 0, NEG)
        m[NTP + t, :, P:] = np.where(own, 0, NEG)
        m[2 * NTP + t, :, P:] = np.where(own & (q // 64 == k // 64), 0, NEG)
        if t > 0:
            m[t, :, :P] = np.where(before, 0, NEG)
        if t % 2:
            m[NTP + t, :, :P] = np.where(before, 0, NEG)
    return m


def constants():
    q, k = np.arange(P)[:, None], np.arange(P)[None, :]
    row = np.arange(P)[:, None]
    return {
        "identity": np.eye(P, dtype=np.float32),
        "rope_mla": rope_table(ROPE),
        "rope_dil": rope_table(ROT),
        "masks_dil": dilated_masks(),
        "mask_mla": np.where(k <= q, 0, NEG).astype(np.float32),
        "mask_new": np.where(np.arange(DT)[None, :] <= row % DT, 0, NEG).astype(np.float32),
        "fold": np.tile(np.eye(NS, dtype=np.float32), (P // NS, 1)),
        "iota16": np.broadcast_to(np.arange(TOPK, dtype=np.float32), (P, TOPK)).copy(),
    }


def kernel(**inputs):
    import concourse.bacc as bacc
    from concourse.bass_utils import run_bass_kernel_spmd

    given = {k: np.asarray(v) for k, v in inputs.items()}
    layer = {k: v[0] for k, v in given.items() if k.startswith(("w_", "g_", "peer_")) and k != "g_final"}
    layer["g_final"] = given["g_final"]
    arrays = {
        "x": np.concatenate([given["x_prompt"][0], given["x_sample"].reshape(NS, D),
                             np.zeros((T - SEQ - NS, D), np.float32)]),
        "mem": given["mem_prompt"][0],
        "cache_mla": given["cache_mla"][0],
        "page_table": given["page_table"].reshape(1, DB * N_PAGES),
        "cache_mem": given["cache_mem"][0].reshape(DB, MEM, 2 * HM * EM),
        **{f"cache_dil{g}": given[f"cache_dil{g}"] for g in range(NG)},
        **layer,
        **constants(),
    }
    nc = bacc.Bacc("TRN2", target_bir_lowering=False, num_devices=1)
    feed, ins = {}, {}
    for name, v in arrays.items():
        feed[f"in_{name}"] = np.ascontiguousarray(v)
        ins[name] = nc.dram_tensor(f"in_{name}", v.shape, mybir.dt.from_np(v.dtype), kind="ExternalInput").ap()
    outs = [nc.dram_tensor(f"out_{n}", shape, F32, kind="ExternalOutput").ap() for n, shape in enumerate(OUTS)]
    build(nc, ins, outs)
    got = run_bass_kernel_spmd(nc, [feed], core_ids=[0])
    return tuple(got.results[0][f"out_{n}"] for n in range(len(OUTS)))
```

```python
from collections import namedtuple
from contextlib import ExitStack

import numpy as np

import concourse.bass as bass
from concourse import mybir

F32 = mybir.dt.float32
I32 = mybir.dt.int32
U32 = mybir.dt.uint32
ALU = mybir.AluOpType
ACT = mybir.ActivationFunctionType
AX = mybir.AxisListType
ds = bass.ds

P = 128
D = 1024
SEQ = 1024
DB, DT = 8, 4
NS = DB * DT
PAST = 8192
PAGE = 128
N_PAGES = PAST // PAGE
POOL_PAGES = DB * N_PAGES + (DB * N_PAGES + 3) // 4
NTP = SEQ // P
NT = NTP + 1
T = NT * P
KD = D // P
H_MLA, Q_LORA, KV_LORA, NOPE, ROPE, V_DIM = 8, 384, 256, 64, 32, 64
QK = NOPE + ROPE
ROW = KV_LORA + ROPE
MLA_SCALE = float(QK) ** -0.5
GROUPS = ((128, 1), (512, 4), (2048, 16))
NG, HD, E = 3, 4, 64
GE = HD * E
ROT = E // 4
DIL_SCALE = float(E) ** -0.5
DIL_COLS = 3 * NG * GE
MEM, HM, EM = 256, 4, 128
MEM_SCALE = float(EM) ** -0.5
C_DIL = Q_LORA + ROW
C_MEM = C_DIL + DIL_COLS
C_GATE = C_MEM + HM * EM
PROJ = C_GATE
HP, NK, QH, TOPK = 8, 128, 128, 16
SLOTS = HP * TOPK
EPS = 1e-6
NEG = -1e30
THETA = 500000.0
CREDIT = 1


class Dram:
    pass


class Resident:
    pass


class Steps:

    def __init__(self, eng, sem, turn=0, per=0):
        self.eng, self.sem, self.base, self.per, self.n = eng, sem, turn * per if per else 0, per, 0

    def __call__(self, ins):
        self.n += 1
        ins.then_inc(self.sem, 1)
        self.eng.wait_ge(self.sem, self.base + self.n + CREDIT)

    def end(self):
        assert self.n == self.per, f"a turn has {self.n} steps, not {self.per}"


def stage(nc, tag):
    ctx, mine = ExitStack(), []

    @ctx.callback
    def _():
        nc.clear_and_free_semaphores(mine)
        nc.all_engine_barrier()

    sb = lambda n, shape, dt=F32: ctx.enter_context(nc.sbuf_tensor(f"{tag}_{n}", shape, dt))
    ps = lambda n, shape: ctx.enter_context(nc.psum_tensor(f"{tag}_{n}", shape, F32))

    def sem(name, credit):
        handle = nc.alloc_semaphore(f"{tag}_{name}")
        mine.append(handle)
        if credit:
            nc.gpsimd.sem_inc(handle, credit)
        return handle

    sems = lambda names, credit=CREDIT: namedtuple("Semaphores", names)(*[sem(n, credit) for n in names.split()])
    return ctx, sb, ps, sems


def pipelined(eng, turns, un):
    if turns > 1:
        with eng.Fori(0, turns - 1) as i:
            for u in range(un):
                yield i, i * un + u, u, True
    for u in range(un):
        yield turns - 1, (turns - 1) * un + u, u, u < un - 1


def following(i, n, u, un):
    return i + (u + 1) // un, n + 1, (u + 1) % un


def norm_rows(nc, tag, src, gain, n_tiles, ident, dst_T, dst_rows=None):
    ctx, sb, ps, sems = stage(nc, tag)
    UN = 3 if n_tiles % 3 == 0 else n_tiles
    TURNS = n_tiles // UN
    with ctx:
        x = [sb(f"x{u}", [P, D]) for u in range(UN)]
        xn = [sb(f"xn{u}", [P, D]) for u in range(UN)]
        sq, g = sb("sq", [P, D]), sb("g", [P, D])
        ss, ms, rt, rstd = sb("ss", [P, UN]), sb("ms", [P, UN]), sb("rt", [P, UN]), sb("rstd", [P, UN])
        lo, hi = [ps(f"lo{u}", [P, 4 * P]) for u in range(UN)], [ps(f"hi{u}", [P, 4 * P]) for u in range(UN)]
        s = sems("gain_loaded squares_summed mean_ready root_ready rstd_ready")
        early = sems("xn_ready lo_ready hi_ready lo_copied hi_copied", UN)
        x_loaded = sems(" ".join(f"x_loaded{u}" for u in range(UN)))
        rows_stored = sems(" ".join(f"rows_stored{u}" for u in range(UN)))
        with nc.Block() as block:
            @block.sync
            def _(sp):
                for u in range(UN):
                    sp.dma_start(x[u][:, :], src[u * P:(u + 1) * P, :]).then_inc(x_loaded[u], 16)
                    if u == 0:
                        sp.dma_start(g[:, :], gain.partition_broadcast(P)).then_inc(s.gain_loaded, 16)
                if TURNS > 1:
                    with sp.Fori(0, TURNS - 1) as i:
                        for u in range(UN):
                            sp.wait_ge(early.xn_ready, i * UN + u + 1 + UN)
                            sp.dma_start(x[u][:, :], src[ds(i * (UN * P) + (UN + u) * P, P), :]).then_inc(x_loaded[u], 16)

            @block.scalar
            def _(act):
                def squares(i, n, u):
                    act.wait_ge(x_loaded[u], i * 16 + 16 + CREDIT)
                    act.activation(sq[:, :], x[u][:, :], ACT.Square, accum_out=ss[:, u:u + 1]).then_inc(s.squares_summed, 1)
                    act.wait_ge(s.mean_ready, n + 1 + CREDIT)
                    act.activation(rt[:, u:u + 1], ms[:, u:u + 1], ACT.Sqrt).then_inc(s.root_ready, 1)

                squares(0, 0, 0)
                for i, n, u, more in pipelined(act, TURNS, UN):
                    if more:
                        squares(*following(i, n, u, UN))
                    act.wait_ge(early.hi_ready, n + 1 + UN)
                    act.copy(dst_T[:, 4:8, ds(n * P, P)], hi[u][:, :].rearrange("p (k t) -> p k t", k=4)
                             ).then_inc(early.hi_copied, 1)
                    if dst_rows is not None:
                        act.wait_ge(early.xn_ready, n + 1 + UN)
                        act.dma_start(dst_rows[ds(n * P, P), :], xn[u][:, :]).then_inc(rows_stored[u], 16)
                if dst_rows is not None:
                    for u in range(UN):
                        act.wait_ge(rows_stored[u], 16 * TURNS + CREDIT)

            @block.vector
            def _(dve):
                def norm(i, n, u):
                    dve.wait_ge(s.squares_summed, n + 1 + CREDIT)
                    dve.tensor_scalar(ms[:, u:u + 1], ss[:, u:u + 1], 1.0 / D, EPS, ALU.mult, ALU.add).then_inc(s.mean_ready, 1)
                    dve.wait_ge(s.root_ready, n + 1 + CREDIT)
                    dve.reciprocal(rstd[:, u:u + 1], rt[:, u:u + 1]).then_inc(s.rstd_ready, 1)
                    dve.wait_ge(s.rstd_ready, n + 1 + CREDIT)
                    dve.wait_ge(early.hi_ready, n - (UN - 1) + UN)
                    if dst_rows is not None:
                        dve.wait_ge(rows_stored[u], i * 16 + CREDIT)
                    dve.scalar_tensor_tensor(out=xn[u][:, :], in0=x[u][:, :], scalar=rstd[:, u:u + 1], in1=g[:, :],
                                             op0=ALU.mult, op1=ALU.mult).then_inc(early.xn_ready, 1)

                dve.wait_ge(s.gain_loaded, 16 + CREDIT)
                norm(0, 0, 0)
                for i, n, u, more in pipelined(dve, TURNS, UN):
                    if more:
                        norm(*following(i, n, u, UN))
                    dve.wait_ge(early.lo_ready, n + 1 + UN)
                    dve.tensor_copy(dst_T[:, 0:4, ds(n * P, P)], lo[u][:, :].rearrange("p (k t) -> p k t", k=4)
                                    ).then_inc(early.lo_copied, 1)

            @block.tensor
            def _(pe):
                for i, n, u, _ in pipelined(pe, TURNS, UN):
                    pe.wait_ge(early.xn_ready, n + 1 + UN)
                    for half, bank, copied, ready in ((0, lo[u], early.lo_copied, early.lo_ready),
                                                      (1, hi[u], early.hi_copied, early.hi_ready)):
                        pe.wait_ge(copied, n - (UN - 1) + UN)
                        for k in range(4):
                            c = (4 * half + k) * P
                            mm = pe.transpose(bank[:, k * P:(k + 1) * P], xn[u][:, c:c + P], ident)
                        mm.then_inc(ready, 1)


def load_pairs(sp, pairs, used, per, load):
    load(0, 0)
    if pairs > 1:
        with sp.Fori(0, pairs - 1) as i:
            sp.wait_ge(used, i * (2 * per) + CREDIT)
            load(1, i * 2 + 1)
            sp.wait_ge(used, i * (2 * per) + per + CREDIT)
            load(0, i * 2 + 2)
    sp.wait_ge(used, (pairs - 1) * 2 * per + CREDIT)
    load(1, 2 * pairs - 1)


def product_rows(nc, tag, xT, w, n_cols, chunk, n_tiles, dst, add=None):
    ctx, sb, ps, sems = stage(nc, tag)
    pairs = n_cols // chunk // 2
    assert pairs * 2 * chunk == n_cols
    with ctx:
        wt = [sb(f"w{u}", [P, KD, chunk]) for u in range(2)]
        o = [sb(f"o{u}", [P, n_tiles, chunk]) for u in range(2)]
        acc = [ps(f"acc{u}", [P, 512]) for u in range(2)]
        s = sems("w_loaded0 w_loaded1 add_loaded0 add_loaded1 product_ready w_used product_copied stored0 stored1")
        w_loaded, add_loaded, stored = (s.w_loaded0, s.w_loaded1), (s.add_loaded0, s.add_loaded1), (s.stored0, s.stored1)
        wv = w.rearrange("(k p) n -> p k n", p=P)
        dv = dst.rearrange("(t p) n -> p t n", p=P)
        av = add.rearrange("(t p) n -> p t n", p=P) if add is not None else None
        with nc.Block() as block:
            @block.sync
            def _(sp):
                load_pairs(sp, pairs, s.product_ready, n_tiles, lambda u, c: sp.dma_start(
                    wt[u][:, :, :], wv[:, :, ds(c * chunk, chunk)]).then_inc(w_loaded[u], 16))

            @block.scalar
            def _(act):
                with act.Fori(0, pairs) as i:
                    if add is not None:
                        for u in range(2):
                            act.wait_ge(stored[u], i * 16 + CREDIT)
                            act.dma_start(o[u][:, :, :], av[:, :, ds(i * (2 * chunk) + u * chunk, chunk)]
                                          ).then_inc(add_loaded[u], 16)
                    for u in range(2):
                        act.wait_ge(s.product_copied, i * (2 * n_tiles) + (u + 1) * n_tiles + CREDIT)
                        act.dma_start(dv[:, :, ds(i * (2 * chunk) + u * chunk, chunk)], o[u][:, :, :]
                                      ).then_inc(stored[u], 16)
                for u in range(2):
                    act.wait_ge(stored[u], 16 * pairs + CREDIT)

            @block.tensor
            def _(pe):
                with pe.Fori(0, pairs) as i:
                    for u in range(2):
                        pe.wait_ge(w_loaded[u], i * 16 + 16 + CREDIT)
                        for t in range(n_tiles):
                            n = u * n_tiles + t
                            pe.wait_ge(s.product_copied, i * (2 * n_tiles) + max(n - 1, 0) + CREDIT)
                            for k in range(KD):
                                mm = pe.matmul(acc[n % 2][:, 0:chunk], xT[:, k, t * P:(t + 1) * P], wt[u][:, k, :],
                                               start=(k == 0), stop=(k == KD - 1))
                            mm.then_inc(s.product_ready, 1)

            @block.vector
            def _(dve):
                with dve.Fori(0, pairs) as i:
                    for u in range(2):
                        if add is not None:
                            dve.wait_ge(add_loaded[u], i * 16 + 16 + CREDIT)
                        else:
                            dve.wait_ge(stored[u], i * 16 + CREDIT)
                        for t in range(n_tiles):
                            n = u * n_tiles + t
                            dve.wait_ge(s.product_ready, i * (2 * n_tiles) + n + 1 + CREDIT)
                            if add is not None:
                                dve.tensor_tensor(o[u][:, t, :], acc[n % 2][:, 0:chunk], o[u][:, t, :], ALU.add
                                                  ).then_inc(s.product_copied, 1)
                            else:
                                dve.tensor_copy(o[u][:, t, :], acc[n % 2][:, 0:chunk]).then_inc(s.product_copied, 1)


def latents(nc, a, r):
    ctx, sb, ps, sems = stage(nc, "lat")
    UN = 3
    with ctx:
        bufs = lambda name, shape: [sb(f"{name}{u}", shape) for u in range(UN)]
        x, tab = bufs("x", [P, C_DIL]), bufs("tab", [P, ROPE])
        cq, row, kpad = bufs("cq", [P, Q_LORA]), bufs("row", [P, ROW]), bufs("kpad", [P, QK])
        y, yv, ytab = bufs("y", [P, 2 * NG * HD, E]), bufs("yv", [P, NG * GE]), bufs("ytab", [P, ROT])
        sq = sb("sq", [P, Q_LORA])
        gq, gkv = sb("gq", [P, Q_LORA]), sb("gkv", [P, KV_LORA])
        wq = sb("wq", [P, 3, H_MLA * QK])
        ss, ms, rt, rstd = sb("ss", [P, 2]), sb("ms", [P, 2]), sb("rt", [P, 2]), sb("rstd", [P, 2])
        tmp = sb("tmp", [P, 4, H_MLA, 16])
        cqT, q, qT = sb("cqT", [P, 3, P]), sb("q", [P, H_MLA, QK]), sb("qT", [QK, H_MLA, P])
        ytmp = sb("ytmp", [P, 4, 2 * NG * HD, ROT // 2])
        pc, pk = ps("pc", [P, 512]), ps("pk", [P, 512])
        pq = [ps(f"pq{u}", [P, 512]) for u in range(2)]
        pt = [ps(f"pt{u}", [P, 512]) for u in range(2)]
        s = sems("const_loaded pad_zeroed squares_summed means_ready roots_ready steps rope_steps "
                 "cqT_ready kvT_ready q_product q_copied qT_lo qT_hi qT_stored y_steps y_roped")
        early = sems("latents_ready cq_turned kv_turned q_roped q_turned", 2 * UN)
        each = lambda name: sems(" ".join(f"{name}{u}" for u in range(UN)))
        x_loaded, y_loaded, row_stored, y_stored = each("x_loaded"), each("y_loaded"), each("row_stored"), each("y_stored")
        BACK = 2 * UN
        N, N2 = 9, 5
        with nc.Block() as block:
            @block.sync
            def _(sp):
                def load(i, n, u):
                    sp.wait_ge(early.latents_ready, n - (UN - 1) + BACK)
                    sp.wait_ge(early.q_roped, n - (UN - 1) + BACK)
                    sp.dma_start(x[u][:, :], a.proj[ds(n * P, P), 0:C_DIL]).then_inc(x_loaded[u], 16)
                    sp.dma_start(tab[u][:, :], a.rope_mla[ds(n * P, P), :]).then_inc(x_loaded[u], 16)
                    sp.wait_ge(y_stored[u], i * 32 + CREDIT)
                    sp.dma_start(y[u][:, :, :].rearrange("p h e -> p (h e)"), a.proj[ds(n * P, P), C_DIL:C_DIL + 2 * NG * GE]
                                 ).then_inc(y_loaded[u], 16)
                    sp.dma_start(yv[u][:, :], a.proj[ds(n * P, P), C_DIL + 2 * NG * GE:C_MEM]).then_inc(y_loaded[u], 16)
                    sp.dma_start(ytab[u][:, :], a.rope_dil[ds(n * P, P), :]).then_inc(y_loaded[u], 16)

                load(0, 0, 0)
                sp.dma_start(gq[:, :], a.g_q_lora.partition_broadcast(P)).then_inc(s.const_loaded, 16)
                sp.dma_start(gkv[:, :], a.g_kv_lora.partition_broadcast(P)).then_inc(s.const_loaded, 16)
                sp.dma_start(wq[:, :, :], a.w_q_up.rearrange("(k p) n -> p k n", p=P)).then_inc(s.const_loaded, 16)
                for i, n, u, more in pipelined(sp, NT // UN, UN):
                    if more:
                        load(*following(i, n, u, UN))
                    rows = ds(n * P, P)
                    sp.wait_ge(s.y_roped, n + 1 + CREDIT)
                    sp.dma_start(a.dil[rows, 0:2 * NG * GE], y[u][:, :, :].rearrange("p h e -> p (h e)")).then_inc(y_stored[u], 16)
                    sp.dma_start(a.dil[rows, 2 * NG * GE:DIL_COLS], yv[u][:, :]).then_inc(y_stored[u], 16)
                    sp.wait_ge(early.latents_ready, n + 1 + BACK)
                    sp.dma_start(a.rows[rows, :], row[u][:, :]).then_inc(row_stored[u], 16)
                for u in range(UN):
                    sp.wait_ge(row_stored[u], 16 * (NT // UN) + CREDIT)
                    sp.wait_ge(y_stored[u], 32 * (NT // UN) + CREDIT)

            @block.scalar
            def _(act):
                def squares(i, n, u):
                    act.wait_ge(x_loaded[u], i * 32 + 32 + CREDIT)
                    act.activation(sq[:, :], x[u][:, 0:Q_LORA], ACT.Square, accum_out=ss[:, 0:1]).then_inc(s.squares_summed, 1)
                    act.wait_ge(s.squares_summed, n * 2 + 1 + CREDIT)
                    act.activation(sq[:, 0:KV_LORA], x[u][:, Q_LORA:Q_LORA + KV_LORA], ACT.Square,
                                   accum_out=ss[:, 1:2]).then_inc(s.squares_summed, 1)
                    act.wait_ge(s.means_ready, n + 1 + CREDIT)
                    act.activation(rt[:, :], ms[:, :], ACT.Sqrt).then_inc(s.roots_ready, 1)

                def copy_latents(n):
                    act.wait_ge(early.cq_turned, n + 1 + BACK)
                    act.wait_ge(s.q_product, n * 2 + CREDIT)
                    act.copy(cqT[:, :, :], pc[:, 0:Q_LORA].rearrange("p (k t) -> p k t", k=3)).then_inc(s.cqT_ready, 1)

                squares(0, 0, 0)
                copy_latents(0)
                for i, n, u, more in pipelined(act, NT // UN, UN):
                    if more:
                        squares(*following(i, n, u, UN))
                    act.wait_ge(early.q_turned, n * 2 + BACK)
                    for w in range(2):
                        act.wait_ge(s.q_product, n * 2 + w + 1 + CREDIT)
                        act.copy(q[:, 4 * w:4 * w + 4, :], pq[w][:, 0:4 * QK].rearrange("p (h e) -> p h e", h=4)
                                 ).then_inc(s.q_copied, 1)
                    if more:
                        copy_latents(n + 1)
                    act.wait_ge(early.q_turned, n * 2 + 1 + BACK)
                    act.wait_ge(s.qT_stored, n * 16 + CREDIT)
                    act.copy(qT[:, 0:4, :], pt[0][0:QK, :].rearrange("p (h t) -> p h t", h=4)).then_inc(s.qT_lo, 1)
                    act.wait_ge(s.qT_lo, n + 1 + CREDIT)
                    act.wait_ge(s.qT_hi, n + 1 + CREDIT)
                    act.dma_start(a.qT[:, :, ds(n * P, P)], qT[:, :, :]).then_inc(s.qT_stored, 16)
                act.wait_ge(s.qT_stored, 16 * NT + CREDIT)

            @block.vector
            def _(dve):
                def norms(i, n, u):
                    step = Steps(dve, s.steps, n, N)
                    dve.wait_ge(s.squares_summed, n * 2 + 2 + CREDIT)
                    step(dve.tensor_scalar(ms[:, 0:1], ss[:, 0:1], 1.0 / Q_LORA, EPS, ALU.mult, ALU.add))
                    dve.tensor_scalar(ms[:, 1:2], ss[:, 1:2], 1.0 / KV_LORA, EPS, ALU.mult, ALU.add
                                      ).then_inc(s.means_ready, 1)
                    dve.wait_ge(s.roots_ready, n + 1 + CREDIT)
                    step(dve.reciprocal(rstd[:, :], rt[:, :]))
                    dve.wait_ge(row_stored[u], i * 16 + CREDIT)
                    dve.wait_ge(early.cq_turned, n - (UN - 1) + BACK)
                    dve.wait_ge(early.kv_turned, n - (UN - 1) + BACK)
                    dve.scalar_tensor_tensor(out=cq[u][:, :], in0=x[u][:, 0:Q_LORA], scalar=rstd[:, 0:1], in1=gq[:, :],
                                             op0=ALU.mult, op1=ALU.mult)
                    step(dve.scalar_tensor_tensor(out=row[u][:, 0:KV_LORA], in0=x[u][:, Q_LORA:Q_LORA + KV_LORA],
                                                  scalar=rstd[:, 1:2], in1=gkv[:, :], op0=ALU.mult, op1=ALU.mult))
                    x1, x2 = x[u][:, C_DIL - 32:C_DIL - 16], x[u][:, C_DIL - 16:C_DIL]
                    cos, sin = tab[u][:, 0:16], tab[u][:, 16:32]
                    for m, (v, w) in enumerate(((x1, cos), (x2, sin), (x2, cos), (x1, sin))):
                        step(dve.tensor_tensor(tmp[:, m, 0, :], v, w, ALU.mult))
                    step(dve.tensor_tensor(row[u][:, KV_LORA:KV_LORA + 16], tmp[:, 0, 0, :], tmp[:, 1, 0, :], ALU.subtract))
                    step(dve.tensor_tensor(row[u][:, KV_LORA + 16:ROW], tmp[:, 2, 0, :], tmp[:, 3, 0, :], ALU.add))
                    dve.tensor_copy(kpad[u][:, NOPE:QK], row[u][:, KV_LORA:ROW]).then_inc(early.latents_ready, 1)
                    step.end()

                def copy_keys(n):
                    dve.wait_ge(early.kv_turned, n + 1 + BACK)
                    dve.tensor_copy(r.ckvT[:, :, ds(n * P, P)], pk[:, 0:2 * P].rearrange("p (k t) -> p k t", k=2)
                                    ).then_inc(s.kvT_ready, 1)
                    dve.tensor_copy(r.kpeT[NOPE:QK, ds(n * P, P)], pk[NOPE:QK, 2 * P:3 * P]).then_inc(s.kvT_ready, 1)

                for u in range(UN):
                    dve.memset(kpad[u][:, :], 0.0).then_inc(s.pad_zeroed, 1)
                dve.wait_ge(s.pad_zeroed, UN + CREDIT)
                dve.wait_ge(s.const_loaded, 48 + CREDIT)
                norms(0, 0, 0)
                copy_keys(0)
                for i, n, u, more in pipelined(dve, NT // UN, UN):
                    if more:
                        norms(*following(i, n, u, UN))
                    dve.wait_ge(s.q_copied, n * 2 + 2 + CREDIT)
                    step = Steps(dve, s.rope_steps, n, N2)
                    q1, q2 = q[:, :, NOPE:NOPE + 16], q[:, :, NOPE + 16:QK]
                    cosb = tab[u][:, 0:16].unsqueeze(1).broadcast_to([P, H_MLA, 16])
                    sinb = tab[u][:, 16:32].unsqueeze(1).broadcast_to([P, H_MLA, 16])
                    for m, (v, w) in enumerate(((q1, cosb), (q2, sinb), (q2, cosb), (q1, sinb))):
                        step(dve.tensor_tensor(tmp[:, m, :, :], v, w, ALU.mult))
                    step(dve.tensor_tensor(q1, tmp[:, 0, :, :], tmp[:, 1, :, :], ALU.subtract))
                    dve.tensor_tensor(q2, tmp[:, 2, :, :], tmp[:, 3, :, :], ALU.add).then_inc(early.q_roped, 1)
                    step.end()
                    if more:
                        copy_keys(n + 1)
                    dve.wait_ge(early.q_turned, n * 2 + 2 + BACK)
                    dve.wait_ge(s.qT_stored, n * 16 + CREDIT)
                    dve.tensor_copy(qT[:, 4:8, :], pt[1][0:QK, :].rearrange("p (h t) -> p h t", h=4)).then_inc(s.qT_hi, 1)

            @block.tensor
            def _(pe):
                def turn_latents(i, n, u):
                    pe.wait_ge(early.latents_ready, n + 1 + BACK)
                    pe.wait_ge(s.cqT_ready, n + CREDIT)
                    pe.wait_ge(s.kvT_ready, n * 2 + CREDIT)
                    for k in range(3):
                        mm = pe.transpose(pc[:, k * P:(k + 1) * P], cq[u][:, k * P:(k + 1) * P], r.ident)
                    mm.then_inc(early.cq_turned, 1)
                    for k in range(2):
                        pe.transpose(pk[:, k * P:(k + 1) * P], row[u][:, k * P:(k + 1) * P], r.ident)
                    pe.transpose(pk[0:QK, 2 * P:3 * P], kpad[u][:, :], r.ident).then_inc(early.kv_turned, 1)

                pe.wait_ge(s.const_loaded, 48 + CREDIT)
                turn_latents(0, 0, 0)
                for i, n, u, more in pipelined(pe, NT // UN, UN):
                    pe.wait_ge(s.cqT_ready, n + 1 + CREDIT)
                    pe.wait_ge(s.q_copied, n * 2 + CREDIT)
                    for w in range(2):
                        for k in range(3):
                            mm = pe.matmul(pq[w][:, 0:4 * QK], cqT[:, k, :], wq[:, k, 4 * QK * w:4 * QK * (w + 1)],
                                           start=(k == 0), stop=(k == 2))
                        mm.then_inc(s.q_product, 1)
                    if more:
                        turn_latents(*following(i, n, u, UN))
                    pe.wait_ge(early.q_roped, n + 1 + BACK)
                    pe.wait_ge(s.qT_lo, n + CREDIT)
                    pe.wait_ge(s.qT_hi, n + CREDIT)
                    for w in range(2):
                        for h in range(4):
                            mm = pe.transpose(pt[w][0:QK, h * P:(h + 1) * P], q[:, 4 * w + h, :], r.ident)
                        mm.then_inc(early.q_turned, 1)

            @block.gpsimd
            def _(pool):
                NY = 5
                for i, n, u, _ in pipelined(pool, NT // UN, UN):
                    step = Steps(pool, s.y_steps, n, NY)
                    pool.wait_ge(y_loaded[u], i * 48 + 48 + CREDIT)
                    h2 = ROT // 2
                    y1, y2 = y[u][:, :, 0:h2], y[u][:, :, h2:ROT]
                    cosb = ytab[u][:, 0:h2].unsqueeze(1).broadcast_to([P, 2 * NG * HD, h2])
                    sinb = ytab[u][:, h2:ROT].unsqueeze(1).broadcast_to([P, 2 * NG * HD, h2])
                    for m, (v, w) in enumerate(((y1, cosb), (y2, sinb), (y2, cosb), (y1, sinb))):
                        step(pool.tensor_tensor(ytmp[:, m, :, :], v, w, ALU.mult))
                    step(pool.tensor_tensor(y1, ytmp[:, 0, :, :], ytmp[:, 1, :, :], ALU.subtract))
                    pool.tensor_tensor(y2, ytmp[:, 2, :, :], ytmp[:, 3, :, :], ALU.add).then_inc(s.y_roped, 1)
                    step.end()


def memory_attention(nc, a, r):
    ctx, sb, ps, sems = stage(nc, "mem")
    with ctx:
        kv, kT = sb("kv", [P, 2, 2 * HM * EM]), sb("kT", [P, HM, MEM])
        x, qT = sb("x", [P, HM * EM]), sb("qT", [P, HM, P])
        nm, nb, l, rl = sb("nm", [P, HM]), sb("nb", [P, HM]), sb("l", [P, HM]), sb("rl", [P, HM])
        p, pT, o = sb("p", [P, HM, MEM]), sb("pT", [P, HM, 2, P]), sb("o", [P, HM, EM])
        pq = ps("pq", [P, 512])
        sc = [ps(f"sc{u}", [P, 512]) for u in range(2)]
        pt = [ps(f"pt{u}", [P, 512]) for u in range(2)]
        po, pot = ps("po", [P, 512]), ps("pot", [P, 512])
        s = sems("kv_loaded k_turned kT_ready x_loaded q_turned qT_ready scores_ready max_found bias_ready probs_ready "
                 "probs_turned pT_ready attended sum_inverted o_ready o_turned oT_stored")
        with nc.Block() as block:
            @block.sync
            def _(sp):
                sp.dma_start(kv[:, :, :], a.mem_kv.rearrange("(m p) c -> p m c", p=P)).then_inc(s.kv_loaded, 16)
                with sp.Fori(0, NTP) as i:
                    sp.wait_ge(s.q_turned, i + CREDIT)
                    sp.dma_start(x[:, :], a.proj[ds(i * P, P), C_MEM:C_GATE]).then_inc(s.x_loaded, 16)

            @block.tensor
            def _(pe):
                pe.wait_ge(s.kv_loaded, 16 + CREDIT)
                for h in range(HM):
                    for m in range(2):
                        mm = pe.transpose(sc[h // 2][:, (h % 2 * 2 + m) * P:(h % 2 * 2 + m + 1) * P],
                                          kv[:, m, h * EM:(h + 1) * EM], r.ident)
                mm.then_inc(s.k_turned, 1)
                pe.wait_ge(s.kT_ready, 2 + CREDIT)

                def turn(n):
                    pe.wait_ge(s.x_loaded, n * 16 + 16 + CREDIT)
                    pe.wait_ge(s.qT_ready, n + CREDIT)
                    for h in range(HM):
                        mm = pe.transpose(pq[:, h * P:(h + 1) * P], x[:, h * EM:(h + 1) * EM], r.ident)
                    mm.then_inc(s.q_turned, 1)

                def scores(n):
                    pe.wait_ge(s.qT_ready, n + 1 + CREDIT)
                    pe.wait_ge(s.probs_ready, n * HM + CREDIT)
                    for h in range(HM):
                        mm = pe.matmul(sc[h // 2][:, h % 2 * MEM:(h % 2 + 1) * MEM], qT[:, h, :], kT[:, h, :],
                                       start=True, stop=True)
                        if h % 2:
                            mm.then_inc(s.scores_ready, 1)

                turn(0)
                scores(0)
                for i, n, _, more in pipelined(pe, NTP, 1):
                    if more:
                        turn(n + 1)
                    for u in range(2):
                        pe.wait_ge(s.probs_ready, n * HM + 2 * u + 2 + CREDIT)
                        pe.wait_ge(s.pT_ready, n * 2 + u + CREDIT)
                        for j in range(4):
                            mm = pe.transpose(pt[u][:, j * P:(j + 1) * P],
                                              p[:, 2 * u + j // 2, (j % 2) * P:(j % 2 + 1) * P], r.ident)
                        mm.then_inc(s.probs_turned, 1)
                    if more:
                        scores(n + 1)
                    pe.wait_ge(s.pT_ready, n * 2 + 2 + CREDIT)
                    pe.wait_ge(s.o_ready, n + CREDIT)
                    for h in range(HM):
                        for m in range(2):
                            mm = pe.matmul(po[:, h * EM:(h + 1) * EM], pT[:, h, m, :],
                                           kv[:, m, (HM + h) * EM:(HM + h + 1) * EM], start=(m == 0), stop=(m == 1))
                    mm.then_inc(s.attended, 1)
                    pe.wait_ge(s.o_ready, n + 1 + CREDIT)
                    pe.wait_ge(s.oT_stored, n + CREDIT)
                    for h in range(HM):
                        mm = pe.transpose(pot[:, h * P:(h + 1) * P], o[:, h, :], r.ident)
                    mm.then_inc(s.o_turned, 1)

            @block.scalar
            def _(act):
                def copy_q(n):
                    act.wait_ge(s.q_turned, n + 1 + CREDIT)
                    act.wait_ge(s.scores_ready, n * 2 + CREDIT)
                    act.copy(qT[:, :, :], pq[:, :].rearrange("p (h t) -> p h t", h=HM)).then_inc(s.qT_ready, 1)

                copy_q(0)
                for i, n, _, more in pipelined(act, NTP, 1):
                    act.wait_ge(s.probs_turned, n * 2 + CREDIT)
                    act.wait_ge(s.sum_inverted, n + CREDIT)
                    for h in range(HM):
                        act.wait_ge(s.bias_ready, n * 2 + h // 2 + 1 + CREDIT)
                        act.activation(p[:, h, :], sc[h // 2][:, h % 2 * MEM:(h % 2 + 1) * MEM], ACT.Exp,
                                       bias=nb[:, h:h + 1], scale=MEM_SCALE, accum_out=l[:, h:h + 1]
                                       ).then_inc(s.probs_ready, 1)
                    if more:
                        copy_q(n + 1)
                    act.wait_ge(s.o_turned, n + 1 + CREDIT)
                    act.copy(r.oT_mem[:, :, ds(n * P, P)], pot[:, :].rearrange("p (h t) -> p h t", h=HM)
                             ).then_inc(s.oT_stored, 1)

            @block.vector
            def _(dve):
                dve.wait_ge(s.k_turned, 1 + CREDIT)
                for u in range(2):
                    dve.tensor_copy(kT[:, 2 * u:2 * u + 2, :], sc[u][:, :].rearrange("p (h m) -> p h m", h=2)
                                    ).then_inc(s.kT_ready, 1)

                def maxima(n):
                    dve.wait_ge(s.probs_ready, n * HM + CREDIT)
                    for u in range(2):
                        dve.wait_ge(s.scores_ready, n * 2 + u + 1 + CREDIT)
                        dve.tensor_reduce(nm[:, 2 * u:2 * u + 2], sc[u][:, :].rearrange("p (h m) -> p h m", h=2),
                                          AX.X, ALU.max, negate=True).then_inc(s.max_found, 1)
                        dve.wait_ge(s.max_found, n * 2 + u + 1 + CREDIT)
                        dve.tensor_scalar(nb[:, 2 * u:2 * u + 2], nm[:, 2 * u:2 * u + 2], MEM_SCALE, None, ALU.mult
                                          ).then_inc(s.bias_ready, 1)

                maxima(0)
                for i, n, _, more in pipelined(dve, NTP, 1):
                    dve.wait_ge(s.attended, n + CREDIT)
                    for u in range(2):
                        dve.wait_ge(s.probs_turned, n * 2 + u + 1 + CREDIT)
                        dve.tensor_copy(pT[:, 2 * u:2 * u + 2, :, :].rearrange("p h m t -> p (h m t)"), pt[u][:, :]
                                        ).then_inc(s.pT_ready, 1)
                    dve.reciprocal(rl[:, :], l[:, :]).then_inc(s.sum_inverted, 1)
                    if more:
                        maxima(n + 1)
                    dve.wait_ge(s.sum_inverted, n + 1 + CREDIT)
                    dve.wait_ge(s.attended, n + 1 + CREDIT)
                    dve.wait_ge(s.o_turned, n + CREDIT)
                    dve.tensor_tensor(o[:, :, :], po[:, :].rearrange("p (h e) -> p h e", h=HM),
                                      rl[:, :].unsqueeze(2).broadcast_to([P, HM, EM]), ALU.mult).then_inc(s.o_ready, 1)


def dilated_attention(nc, a, r):
    ctx, sb, ps, sems = stage(nc, "dil")
    UN = 4
    TILES = NG * NTP
    AHEAD = 8
    ORDER = (0, 2, 1, 3)
    with ctx:
        qk = [sb(f"qk{u}", [P, 2, GE]) for u in range(UN)]
        v = [sb(f"v{u}", [P, GE]) for u in range(UN)]
        mask = [sb(f"mask{u}", [P, 2 * P]) for u in range(UN)]
        qT, kT = sb("qT", [P, HD // 2, P]), [sb(f"kT{u}", [P, HD // 2, P]) for u in range(2)]
        sm, p, pT = sb("sm", [P, HD, 2 * P]), sb("p", [P, HD, 2 * P]), sb("pT", [P, HD, 2, P])
        ou = [sb(f"ou{u}", [P, GE + 2 * HD]) for u in range(UN)]
        pq, pk = ps("pq", [P, 512]), ps("pk", [P, 512])
        sc = [ps(f"sc{u}", [P, 512]) for u in range(2)]
        pt = [ps(f"pt{u}", [P, 512]) for u in range(2)]
        po = ps("po", [P, 512])
        s = sems("zeroed qT_ready kT_ready scores_ready max_found probs_ready "
                 "probs_turned pT_ready u_ready")
        qk_loaded = sems(" ".join(f"qk_loaded{u}" for u in range(UN)))
        v_loaded = sems(" ".join(f"v_loaded{u}" for u in range(UN)))
        mask_loaded = sems(" ".join(f"mask_loaded{u}" for u in range(UN)))
        early = sems("turned masked attended ou_free", AHEAD)
        own = sems("stored", 0)
        dil3 = a.dil.rearrange("t (j g c) -> t j g c", j=3, g=NG)

        def group_tiles(eng):
            for g in range(NG):
                with eng.Fori(0, NTP // UN) as i:
                    for u in range(UN):
                        halves = []
                        for half in range(2):
                            at = (i * (UN * P) + u * P + half * 64, i * 2 + (u // 2 + 4 * (P * (u % 2) + 64 * half)),
                                  i * (2 * UN) + 2 * u + half)[g]
                            halves.append(ds(at, 64, step=GROUPS[g][1]))
                        yield g, i * UN + (g * NTP + u), u, halves

        with nc.Block() as block:
            @block.sync
            def _(sp):
                sp.wait_ge(s.zeroed, 1 + CREDIT)
                for g, n, u, halves in group_tiles(sp):
                    sp.wait_ge(early.turned, n - (UN - 1) + AHEAD)
                    for half, rows in enumerate(halves):
                        sp.dma_start(qk[u][half * 64:half * 64 + 64, :, :], dil3[rows, 0:2, g, :]).then_inc(qk_loaded[u], 16)
                    sp.wait_ge(early.masked, n * 2 - 2 * (UN - 1) + AHEAD)
                    sp.dma_start(mask[u][:, :], a.masks_dil[ds(n, 1), :, :].squeeze(0)).then_inc(mask_loaded[u], 16)
                    sp.wait_ge(early.attended, n - (UN - 2) + AHEAD)
                    for half, rows in enumerate(halves):
                        sp.dma_start(v[u][half * 64:half * 64 + 64, :], dil3[rows, 2, g, :]).then_inc(v_loaded[u], 16)

            @block.gpsimd
            def _(pool):
                pool.memset(kT[1][:, :, :], 0.0)
                pool.memset(v[UN - 1][:, :], 0.0).then_inc(s.zeroed, 1)
                for g, n, u, halves in group_tiles(pool):
                    pool.wait_ge(s.u_ready, n + 1 + CREDIT)
                    for half, rows in enumerate(halves):
                        pool.dma_start(a.dilo[g, rows, :], ou[u][half * 64:half * 64 + 64, :]).then_inc(own.stored, 16)
                    pool.wait_ge(own.stored, n * 32 + 32)
                    pool.sem_inc(early.ou_free, 1)

            @block.tensor
            def _(pe):
                def turn(i, n, u):
                    pe.wait_ge(qk_loaded[u], i * 32 + 32 + CREDIT)
                    pe.wait_ge(s.qT_ready, n + CREDIT)
                    pe.wait_ge(s.kT_ready, n + CREDIT)
                    for k in range(2):
                        pe.transpose(pq[:, k * P:(k + 1) * P], qk[u][:, 0, k * P:(k + 1) * P], r.ident)
                    for k in range(2):
                        mm = pe.transpose(pk[:, k * P:(k + 1) * P], qk[u][:, 1, k * P:(k + 1) * P], r.ident)
                    mm.then_inc(early.turned, 1)

                def scores(n, u):
                    pe.wait_ge(s.qT_ready, n + 1 + CREDIT)
                    pe.wait_ge(s.kT_ready, n + 1 + CREDIT)
                    pe.wait_ge(early.masked, n * 2 + AHEAD)
                    for w in range(2):
                        at = slice(w * E, (w + 1) * E)
                        for k in range(2):
                            for j, keys in enumerate((kT[(u + 1) % 2], kT[u % 2])):
                                c = (2 * k + j) * P
                                mm = pe.matmul(sc[w][:, c:c + P], qT[at, k, :], keys[at, k, :], start=True, stop=True)
                        mm.then_inc(s.scores_ready, 1)

                pe.wait_ge(s.zeroed, 1 + CREDIT)
                turn(0, 0, 0)
                scores(0, 0)
                for i, n, u, more in pipelined(pe, TILES // UN, UN):
                    if more:
                        turn(*following(i, n, u, UN))
                    for w in range(2):
                        pe.wait_ge(s.probs_ready, n * HD + 2 * w + 2 + CREDIT)
                        pe.wait_ge(s.pT_ready, n * 2 + w + CREDIT)
                        for j in range(4):
                            mm = pe.transpose(pt[w][:, j * P:(j + 1) * P],
                                              p[:, 2 * w + j // 2, (j % 2) * P:(j % 2 + 1) * P], r.ident)
                        mm.then_inc(s.probs_turned, 1)
                    if more:
                        scores(n + 1, u + 1)
                    pe.wait_ge(s.pT_ready, n * 2 + 2 + CREDIT)
                    pe.wait_ge(s.u_ready, n + CREDIT)
                    pe.wait_ge(v_loaded[u], i * 32 + 32 + CREDIT)
                    for n4, h in enumerate(ORDER):
                        for j, vals in enumerate((v[(u - 1) % UN], v[u])):
                            mm = pe.matmul(po[:, h * E:(h + 1) * E], pT[:, n4, j, :], vals[:, h * E:(h + 1) * E],
                                           start=(j == 0), stop=(j == 1))
                    mm.then_inc(early.attended, 1)

            @block.scalar
            def _(act):
                def copy_q(n):
                    act.wait_ge(early.turned, n + 1 + AHEAD)
                    act.wait_ge(s.scores_ready, n * 2 + CREDIT)
                    act.copy(qT[:, :, :], pq[:, 0:2 * P].rearrange("p (k t) -> p k t", k=2)).then_inc(s.qT_ready, 1)

                copy_q(0)
                for i, n, u, more in pipelined(act, TILES // UN, UN):
                    act.wait_ge(s.probs_turned, n * 2 + CREDIT)
                    for n4, h in enumerate(ORDER):
                        act.wait_ge(s.max_found, n * 2 + n4 // 2 + 1 + CREDIT)
                        act.activation(p[:, n4, :], sm[:, n4, :], ACT.Exp, bias=ou[u][:, GE + h:GE + h + 1],
                                       accum_out=ou[u][:, GE + HD + h:GE + HD + h + 1]).then_inc(s.probs_ready, 1)
                    if more:
                        copy_q(n + 1)

            @block.vector
            def _(dve):
                def copy_k(n, u):
                    dve.wait_ge(early.turned, n + 1 + AHEAD)
                    dve.wait_ge(s.scores_ready, n * 2 + CREDIT)
                    dve.tensor_copy(kT[u % 2][:, :, :], pk[:, 0:2 * P].rearrange("p (k t) -> p k t", k=2)
                                    ).then_inc(s.kT_ready, 1)

                def maxima(i, n, u):
                    dve.wait_ge(mask_loaded[u], i * 16 + 16 + CREDIT)
                    dve.wait_ge(s.probs_ready, n * HD + CREDIT)
                    for w in range(2):
                        dve.wait_ge(s.scores_ready, n * 2 + w + 1 + CREDIT)
                        dve.scalar_tensor_tensor(
                            out=sm[:, 2 * w:2 * w + 2, :], in0=sc[w][:, :].rearrange("p (h k) -> p h k", h=2),
                            scalar=DIL_SCALE, in1=mask[u][:, :].unsqueeze(1).broadcast_to([P, 2, 2 * P]),
                            op0=ALU.mult, op1=ALU.add).then_inc(early.masked, 1)
                        dve.wait_ge(early.masked, n * 2 + w + 1 + AHEAD)
                        dve.tensor_reduce(ou[u][:, GE + w:GE + HD:2], sm[:, 2 * w:2 * w + 2, :], AX.X, ALU.max,
                                          negate=True).then_inc(s.max_found, 1)

                copy_k(0, 0)
                maxima(0, 0, 0)
                for i, n, u, more in pipelined(dve, TILES // UN, UN):
                    if more:
                        copy_k(n + 1, u + 1)
                    for w in range(2):
                        dve.wait_ge(s.probs_turned, n * 2 + w + 1 + CREDIT)
                        dve.wait_ge(early.attended, n + AHEAD)
                        dve.tensor_copy(pT[:, 2 * w:2 * w + 2, :, :].rearrange("p h m t -> p (h m t)"), pt[w][:, :]
                                        ).then_inc(s.pT_ready, 1)
                    if more:
                        dve.wait_ge(early.ou_free, n + 1 - (UN - 1) + AHEAD)
                        maxima(*following(i, n, u, UN))
                    dve.wait_ge(early.attended, n + 1 + AHEAD)
                    dve.tensor_copy(ou[u][:, 0:GE], po[:, 0:GE]).then_inc(s.u_ready, 1)


def combine_groups(nc, a, r):
    ctx, sb, ps, sems = stage(nc, "comb")
    with ctx:
        x = [sb(f"x{u}", [P, NG, GE + 2 * HD]) for u in range(2)]
        nmx, dm, w, wl, L = sb("nmx", [P, HD]), sb("dm", [P, NG, HD]), sb("w", [P, NG, HD]), sb("wl", [P, NG, HD]), sb("L", [P, HD])
        o = sb("o", [P, NG, GE])
        om = [sb(f"om{u}", [P, H_MLA * V_DIM]) for u in range(2)]
        pd, pm = ps("pd", [P, 512]), ps("pm", [P, 512])
        s = sems("steps diff_ready weights_ready o_turned oT_ready omT_ready")
        early = sems("o_ready om_turned", 2)
        x_loaded, om_loaded = sems("x_loaded0 x_loaded1"), sems("om_loaded0 om_loaded1")

        def tiles(eng):
            with eng.Fori(0, NTP // 2) as t:
                for u in range(2):
                    yield t, t * 2 + u, u

        N = 11
        with nc.Block() as block:
            @block.sync
            def _(sp):
                for t, i, u in tiles(sp):
                    sp.wait_ge(early.o_ready, i - 1 + 2)
                    for g in range(NG):
                        sp.dma_start(x[u][:, g, :], a.dilo[g, ds(i * P, P), :]).then_inc(x_loaded[u], 16)
                    sp.wait_ge(early.om_turned, i - 1 + 2)
                    sp.dma_start(om[u][:, :], a.omla[ds(i * P, P), :]).then_inc(om_loaded[u], 16)

            @block.scalar
            def _(act):
                for t, i, u in tiles(act):
                    act.wait_ge(s.diff_ready, i + 1 + CREDIT)
                    act.activation(w[:, :, :], dm[:, :, :], ACT.Exp).then_inc(s.weights_ready, 1)
                    act.wait_ge(early.om_turned, i + 1 + 2)
                    act.copy(r.oT_mla[:, :, ds(i * P, P)], pm[:, :].rearrange("p (h t) -> p h t", h=4)).then_inc(s.omT_ready, 1)

            @block.vector
            def _(dve):
                for t, i, u in tiles(dve):
                    step = Steps(dve, s.steps, i, N)
                    dve.wait_ge(x_loaded[u], t * 48 + 48 + CREDIT)
                    nm = x[u][:, :, GE:GE + HD]
                    step(dve.tensor_tensor(nmx[:, :], nm[:, 0, :], nm[:, 1, :], ALU.min))
                    step(dve.tensor_tensor(nmx[:, :], nmx[:, :], nm[:, 2, :], ALU.min))
                    dve.tensor_tensor(dm[:, :, :], nmx[:, :].unsqueeze(1).broadcast_to([P, NG, HD]), nm, ALU.subtract
                                      ).then_inc(s.diff_ready, 1)
                    dve.wait_ge(s.weights_ready, i + 1 + CREDIT)
                    step(dve.tensor_tensor(wl[:, :, :], w[:, :, :], x[u][:, :, GE + HD:GE + 2 * HD], ALU.mult))
                    step(dve.tensor_tensor(L[:, :], wl[:, 0, :], wl[:, 1, :], ALU.add))
                    step(dve.tensor_tensor(L[:, :], L[:, :], wl[:, 2, :], ALU.add))
                    step(dve.reciprocal(L[:, :], L[:, :]))
                    step(dve.tensor_tensor(wl[:, :, :], w[:, :, :], L[:, :].unsqueeze(1).broadcast_to([P, NG, HD]), ALU.mult))
                    dve.wait_ge(s.o_turned, i + CREDIT)
                    for g in range(NG):
                        step(dve.tensor_tensor(o[:, g, :].rearrange("p (h e) -> p h e", h=HD),
                                               x[u][:, g, 0:GE].rearrange("p (h e) -> p h e", h=HD),
                                               wl[:, g, :].unsqueeze(2).broadcast_to([P, HD, E]), ALU.mult))
                    step(dve.tensor_tensor(o[:, 1, :], o[:, 1, :], o[:, 2, :], ALU.add))
                    dve.tensor_tensor(o[:, 0, :], o[:, 0, :], o[:, 1, :], ALU.add).then_inc(early.o_ready, 1)
                    step.end()
                    dve.wait_ge(s.o_turned, i + 1 + CREDIT)
                    dve.tensor_copy(r.oT_dil[:, :, ds(i * P, P)], pd[:, 0:2 * P].rearrange("p (h t) -> p h t", h=2)
                                    ).then_inc(s.oT_ready, 1)

            @block.tensor
            def _(pe):
                for t, i, u in tiles(pe):
                    pe.wait_ge(om_loaded[u], t * 16 + 16 + CREDIT)
                    pe.wait_ge(s.omT_ready, i + CREDIT)
                    for k in range(4):
                        mm = pe.transpose(pm[:, k * P:(k + 1) * P], om[u][:, k * P:(k + 1) * P], r.ident)
                    mm.then_inc(early.om_turned, 1)
                    pe.wait_ge(early.o_ready, i + 1 + 2)
                    pe.wait_ge(s.oT_ready, i + CREDIT)
                    for k in range(2):
                        mm = pe.transpose(pd[:, k * P:(k + 1) * P], o[:, 0, k * P:(k + 1) * P], r.ident)
                    mm.then_inc(s.o_turned, 1)


def latent_attention(nc, a, r):
    ctx, sb, ps, sems = stage(nc, "mla")
    HALF = 512
    LO = 4
    with ctx:
        qT, kT = [sb(f"qT{u}", [QK, SEQ]) for u in range(2)], [sb(f"kT{u}", [QK, SEQ]) for u in range(2)]
        w, v = [sb(f"w{u}", [P, 2, NOPE + V_DIM]) for u in range(2)], [sb(f"v{u}", [P, NTP, V_DIM]) for u in range(2)]
        o = [sb(f"o{u}", [P, NTP, V_DIM]) for u in range(2)]
        mask = sb("mask", [P, P])
        nm, nb, l, rl = sb("nm", [P, 2]), sb("nb", [P, 2]), sb("l", [P, 2]), sb("rl", [P, 2])
        p = [sb(f"p{u}", [P, SEQ]) for u in range(2)]
        pT = sb("pT", [P, NTP, P])
        sc = [ps(f"sc{u}", [P, SEQ]) for u in range(2)]
        pt = [ps(f"pt{u}", [P, 512]) for u in range(2)]
        pu, pkv = ps("pu", [P, 512]), ps("pkv", [P, 512])
        s = sems("mask_loaded pe_copied kv_product k_copied v_copied scores_ready max_found bias_ready "
                 "turned_hi copied_lo copied_hi attended o_ready")
        early = sems("probs_ready turned_lo sum_inverted", 2)
        q_loaded, w_loaded, stored = sems("q_loaded0 q_loaded1"), sems("w_loaded0 w_loaded1"), sems("stored0 stored1")
        wkv = a.w_kv_up.rearrange("(k p) (h c) -> p k h c", p=P, h=H_MLA)
        HEADS = (H_MLA // 2, 2)

        def ahead(i, hd, u, b, more, do):
            if b < NTP:
                do(hd, u, b)
            elif more:
                do(hd + 1, 1 - u, b - NTP)

        with nc.Block() as block:
            @block.sync
            def _(sp):
                def load(i, hd, u):
                    sp.dma_start(w[u][:, :, :], wkv[:, :, ds(hd, 1), :].squeeze(2)).then_inc(w_loaded[u], 16)
                    sp.dma_start(qT[u][:, :], a.qT[:, ds(hd, 1), 0:SEQ].squeeze(1)).then_inc(q_loaded[u], 16)

                load(0, 0, 0)
                sp.dma_start(mask[:, :], a.mask_mla).then_inc(s.mask_loaded, 16)
                for i, hd, u, more in pipelined(sp, *HEADS):
                    if more:
                        sp.wait_ge(s.kv_product, hd * 3 + CREDIT)
                        sp.wait_ge(s.scores_ready, hd * NTP + CREDIT)
                        load(*following(i, hd, u, 2))
                    sp.wait_ge(s.o_ready, hd * NTP + NTP + CREDIT)
                    sp.dma_start(a.omla[0:SEQ, ds(hd * V_DIM, V_DIM)].rearrange("(q p) e -> p q e", p=P), o[u][:, :, :]
                                 ).then_inc(stored[u], 16)
                for u in range(2):
                    sp.wait_ge(stored[u], 16 * HEADS[0] + CREDIT)

            @block.tensor
            def _(pe):
                def keys(i, hd, u, c):
                    if c == 0:
                        pe.wait_ge(w_loaded[u], i * 16 + 16 + CREDIT)
                        pe.wait_ge(s.v_copied, hd + CREDIT)
                    pe.wait_ge(s.k_copied, hd * 2 + c + CREDIT)
                    for k in range(2):
                        mm = pe.matmul(pkv[0:NOPE, :], w[u][:, k, 0:NOPE], r.ckvT[:, k, c * HALF:(c + 1) * HALF],
                                       start=(k == 0), stop=(k == 1))
                    mm.then_inc(s.kv_product, 1)

                def values(i, hd, u):
                    pe.wait_ge(s.k_copied, hd * 2 + 2 + CREDIT)
                    for t in range(NTP):
                        for k in range(2):
                            mm = pe.matmul(pkv[:, t * V_DIM:(t + 1) * V_DIM], r.ckvT[:, k, t * P:(t + 1) * P],
                                           w[u][:, k, NOPE:], start=(k == 0), stop=(k == 1))
                    mm.then_inc(s.kv_product, 1)

                def scores(hd, u, b):
                    n = (b + 1) * P
                    pe.wait_ge(early.probs_ready, hd * NTP + b - 1 + 2)
                    for c in range(0, n, HALF):
                        e = min(n, c + HALF)
                        pe.matmul(sc[b % 2][:, c:e], qT[u][:, b * P:(b + 1) * P], kT[u][:, c:e], start=True, stop=(e < n))
                    pe.matmul(sc[b % 2][:, b * P:n], r.ident, mask[:, :], start=False, stop=True).then_inc(s.scores_ready, 1)

                pe.wait_ge(s.mask_loaded, 16 + CREDIT)
                pe.wait_ge(s.pe_copied, 2 + CREDIT)
                keys(0, 0, 0, 0)
                keys(0, 0, 0, 1)
                values(0, 0, 0)
                pe.wait_ge(q_loaded[0], 16 + CREDIT)
                scores(0, 0, 0)
                scores(0, 0, 1)
                for i, hd, u, more in pipelined(pe, *HEADS):
                    nxt = following(i, hd, u, 2)
                    for b in range(NTP):
                        pe.wait_ge(early.probs_ready, hd * NTP + b + 1 + 2)
                        pe.wait_ge(s.copied_lo, hd * NTP + b + CREDIT)
                        for k in range(min(b + 1, LO)):
                            mm = pe.transpose(pt[0][:, k * P:(k + 1) * P], p[b % 2][:, k * P:(k + 1) * P], r.ident)
                        mm.then_inc(early.turned_lo, 1)
                        if b >= LO:
                            pe.wait_ge(s.copied_hi, hd * LO + b - LO + CREDIT)
                            for k in range(LO, b + 1):
                                mm = pe.transpose(pt[1][:, (k - LO) * P:(k - LO + 1) * P], p[b % 2][:, k * P:(k + 1) * P], r.ident)
                            mm.then_inc(s.turned_hi, 1)
                        if more and b in (2, 3):
                            keys(*nxt, b - 2)
                        if more and b == 4:
                            values(*nxt)
                        if more and b + 2 == NTP:
                            pe.wait_ge(s.k_copied, hd * 2 + 4 + CREDIT)
                            pe.wait_ge(q_loaded[nxt[2]], nxt[0] * 16 + 16 + CREDIT)
                        ahead(i, hd, u, b + 2, more, scores)
                        if b >= LO:
                            pe.wait_ge(s.copied_hi, hd * LO + b - LO + 1 + CREDIT)
                        pe.wait_ge(s.copied_lo, hd * NTP + b + 1 + CREDIT)
                        pe.wait_ge(s.o_ready, hd * NTP + b + CREDIT)
                        if b == 0:
                            pe.wait_ge(s.v_copied, hd + 1 + CREDIT)
                        for k in range(b + 1):
                            mm = pe.matmul(pu[:, 0:V_DIM], pT[:, k, :], v[u][:, k, :], start=(k == 0), stop=(k == b))
                        mm.then_inc(s.attended, 1)

            @block.scalar
            def _(act):
                def copy_keys(hd, u, c):
                    act.wait_ge(s.kv_product, hd * 3 + c + 1 + CREDIT)
                    act.copy(kT[u][0:NOPE, c * HALF:(c + 1) * HALF], pkv[0:NOPE, :]).then_inc(s.k_copied, 1)

                def exp(hd, u, b):
                    n = (b + 1) * P
                    act.wait_ge(s.bias_ready, hd * NTP + b + 1 + CREDIT)
                    act.wait_ge(early.turned_lo, hd * NTP + b - 1 + 2)
                    if b >= LO:
                        act.wait_ge(s.turned_hi, hd * LO + max(b - LO - 1, 0) + CREDIT)
                    act.wait_ge(early.sum_inverted, hd * NTP + b - 1 + 2)
                    act.activation(p[b % 2][:, 0:n], sc[b % 2][:, 0:n], ACT.Exp, bias=nb[:, b % 2:b % 2 + 1],
                                   scale=MLA_SCALE, accum_out=l[:, b % 2:b % 2 + 1]).then_inc(early.probs_ready, 1)

                for u in range(2):
                    act.copy(kT[u][NOPE:QK, :], r.kpeT[NOPE:QK, 0:SEQ]).then_inc(s.pe_copied, 1)
                copy_keys(0, 0, 0)
                copy_keys(0, 0, 1)
                exp(0, 0, 0)
                for i, hd, u, more in pipelined(act, *HEADS):
                    for b in range(NTP):
                        ahead(i, hd, u, b + 1, more, exp)
                        if more and b in (2, 3):
                            act.wait_ge(s.scores_ready, hd * NTP + CREDIT)
                            copy_keys(hd + 1, 1 - u, b - 2)
                        if b >= LO:
                            act.wait_ge(s.turned_hi, hd * LO + b - LO + 1 + CREDIT)
                            act.wait_ge(s.attended, hd * NTP + b + CREDIT)
                            act.copy(pT[:, LO:b + 1, :], pt[1][:, 0:(b - LO + 1) * P].rearrange("p (k t) -> p k t", t=P)
                                     ).then_inc(s.copied_hi, 1)

            @block.vector
            def _(dve):
                def copy_values(hd, u):
                    dve.wait_ge(s.kv_product, hd * 3 + 3 + CREDIT)
                    dve.tensor_copy(v[u][:, :, :], pkv[:, :].rearrange("p (t e) -> p t e", e=V_DIM)).then_inc(s.v_copied, 1)

                def maximum(hd, u, b):
                    dve.wait_ge(s.scores_ready, hd * NTP + b + 1 + CREDIT)
                    dve.tensor_reduce(nm[:, b % 2:b % 2 + 1], sc[b % 2][:, 0:(b + 1) * P], AX.X, ALU.max, negate=True
                                      ).then_inc(s.max_found, 1)
                    dve.wait_ge(s.max_found, hd * NTP + b + 1 + CREDIT)
                    dve.wait_ge(early.probs_ready, hd * NTP + b - 1 + 2)
                    dve.tensor_scalar(nb[:, b % 2:b % 2 + 1], nm[:, b % 2:b % 2 + 1], MLA_SCALE, None, ALU.mult
                                      ).then_inc(s.bias_ready, 1)

                copy_values(0, 0)
                maximum(0, 0, 0)
                maximum(0, 0, 1)
                for i, hd, u, more in pipelined(dve, *HEADS):
                    for b in range(NTP):
                        dve.wait_ge(early.turned_lo, hd * NTP + b + 1 + 2)
                        dve.wait_ge(s.attended, hd * NTP + b + CREDIT)
                        m = min(b + 1, LO)
                        dve.tensor_copy(pT[:, 0:m, :], pt[0][:, 0:m * P].rearrange("p (k t) -> p k t", t=P)
                                        ).then_inc(s.copied_lo, 1)
                        if more and b == 4:
                            copy_values(hd + 1, 1 - u)
                        ahead(i, hd, u, b + 2, more, maximum)
                        dve.reciprocal(rl[:, b % 2:b % 2 + 1], l[:, b % 2:b % 2 + 1]).then_inc(early.sum_inverted, 1)
                        dve.wait_ge(early.sum_inverted, hd * NTP + b + 1 + 2)
                        dve.wait_ge(s.attended, hd * NTP + b + 1 + CREDIT)
                        if b == 0:
                            dve.wait_ge(stored[u], i * 16 + CREDIT)
                        dve.tensor_scalar(o[u][:, b, :], pu[:, 0:V_DIM], rl[:, b % 2:b % 2 + 1], None, ALU.mult
                                          ).then_inc(s.o_ready, 1)




def sample_latent_attention(nc, a, r):
    ctx, sb, ps, sems = stage(nc, "smla")
    PG, RB = 4, 4
    NC = N_PAGES // PG
    ROUNDS = DB // RB
    QR = H_MLA * DT
    with ctx:
        w = sb("w", [P, 2, H_MLA, NOPE + V_DIM])
        wukT = sb("wukT", [NOPE, H_MLA, KV_LORA])
        qn, qp = sb("qn", [NOPE, H_MLA, NS]), sb("qp", [ROPE, H_MLA, NS])
        qlat, qpe = sb("qlat", [P, 2, DB, H_MLA, DT]), sb("qpe", [ROPE, DB, H_MLA, DT])
        kpn, rn = sb("kpn", [ROPE, NS]), sb("rn", [DT, DB, KV_LORA])
        mnew = sb("mnew", [P, DT])
        table = sb("table", [1, DB * N_PAGES], I32)
        kv = [sb(f"kv{u}", [P, RB, PG, ROW]) for u in range(2)]
        kT = [sb(f"kT{u}", [P, 2, PG * P]) for u in range(2)]
        kp = [sb(f"kp{u}", [ROPE, PG * P]) for u in range(2)]
        nm, nb, l = sb("nm", [P, 1]), sb("nb", [P, NC + 1]), sb("l", [P, NC + 1])
        p, pT = sb("p", [P, PG * P]), sb("pT", [P, PG, P])
        U = sb("U", [P, NC + 1, KV_LORA])
        sn, pn, pnT = sb("sn", [P, DT]), sb("pn", [P, DT]), sb("pnT", [DT, P])
        nmx, dm, wt, wl, L = sb("nmx", [P, 1]), sb("dm", [P, NC + 1]), sb("wt", [P, NC + 1]), sb("wl", [P, NC + 1]), sb("L", [P, 1])
        lat, latT = sb("lat", [P, KV_LORA]), sb("latT", [P, 2, H_MLA, RB * DT])
        o = sb("o", [RB * DT, H_MLA * V_DIM])
        b0 = [ps(f"b0{u}", [P, 512]) for u in range(2)]
        b1 = [ps(f"b1{u}", [P, 512]) for u in range(2)]
        bp = ps("bp", [P, 512])
        psc, ppt, pu = ps("psc", [P, 512]), ps("ppt", [P, 512]), ps("pu", [P, 512])
        s = sems("loaded zeroed w_turned wukT_ready q_product q_ready k0_turned k1_turned kp_turned k0_copied k1_copied "
                 "kp_copied scores_ready max_found bias_ready probs_ready probs_turned pT_ready U_ready "
                 "new_scores new_masked new_max new_probs new_turned new_T new_attended new_copied steps diff_ready weights_ready "
                 "lat_ready lat_turned latT_ready o_product o_copied o_turned oT_ready")
        early = sems("attended", 2)
        BY_SYNC = 3
        BY_POOL = RB - BY_SYNC
        names = lambda seqs: " ".join(f"pages_loaded{u}_{bb}" for u in range(2) for bb in seqs)
        by_sync, by_pool = sems(names(range(BY_SYNC))), sems(names(range(BY_SYNC, RB)), 0)
        pages_loaded = [[*by_sync[u * BY_SYNC:(u + 1) * BY_SYNC], *by_pool[u * BY_POOL:(u + 1) * BY_POOL]] for u in range(2)]
        N_MERGE = 6 + NC
        SEQUENCE = 16 * PG

        def load_pages(eng, rd, i, u, seqs):
            pages = [(bb, g, eng.value_load(table[0:1, ds(i * (2 * PG) + ((rd * RB + bb) * N_PAGES + u * PG + g), 1)],
                                            min_val=0, max_val=POOL_PAGES - 1)) for bb in seqs for g in range(PG)]
            eng.wait_ge(early.attended, i * 2 + (rd * NC + u - 1) + 2)
            for bb, g, page in pages:
                eng.dma_start(kv[u][:, bb, g, :], a.cache_mla[ds(page, 1), :, :].squeeze(0)).then_inc(pages_loaded[u][bb], 16)

        def chunks(eng, rd):
            loads = rd * (NC // 2)
            yield rd * NC, 0, 0, loads + 1, False
            with eng.Fori(0, NC // 2 - 1) as i:
                yield i * 2 + (rd * NC + 1), 1, i * 2 + 1, i + (loads + 1), True
                yield i * 2 + (rd * NC + 2), 0, i * 2 + 2, i + (loads + 2), True
            yield rd * NC + NC - 1, 1, NC - 1, loads + NC // 2, True

        def before(n, bb, prev):
            return n * RB + (bb - 1 if prev else max(bb - 1, 0))

        with nc.Block() as block:
            @block.sync
            def _(sp):
                for dst, src in (
                    (w[:, :, :, :], a.w_kv_up.rearrange("(k p) (h c) -> p k h c", p=P, h=H_MLA)),
                    (qn[:, :, :], a.qT[0:NOPE, :, SEQ:SEQ + NS]),
                    (qp[:, :, :], a.qT[NOPE:QK, :, SEQ:SEQ + NS]),
                    (rn[:, :, :], a.rows[SEQ:SEQ + NS, 0:KV_LORA].rearrange("(b t) c -> t b c", t=DT)),
                    (mnew[:, :], a.mask_new),
                    (table[:, :], a.page_table),
                ):
                    sp.dma_start(dst, src).then_inc(s.loaded, 16)
                with nc.allow_non_contiguous_dma("the new tokens' rotary keys, turned: 32 x 32 numbers"):
                    sp.dma_start(kpn[:, :], a.rows[SEQ:SEQ + NS, KV_LORA:ROW].rearrange("t c -> c t")).then_inc(s.loaded, 16)
                sp.wait_ge(s.loaded, 112 + CREDIT)
                for rd in range(ROUNDS):
                    with sp.Fori(0, NC // 2) as i:
                        for u in range(2):
                            load_pages(sp, rd, i, u, range(BY_SYNC))

            @block.gpsimd
            def _(pool):
                pool.memset(r.oT_mla[:, :, SEQ + NS:T], 0.0)
                pool.memset(r.oT_dil[:, :, SEQ + NS:T], 0.0)
                pool.memset(r.oT_mem[:, :, SEQ + NS:T], 0.0).then_inc(s.zeroed, 1)
                pool.wait_ge(s.zeroed, 1 + CREDIT)
                pool.wait_ge(s.loaded, 112 + CREDIT)
                for rd in range(ROUNDS):
                    with pool.Fori(0, NC // 2) as i:
                        for u in range(2):
                            load_pages(pool, rd, i, u, range(BY_SYNC, RB))

            @block.tensor
            def _(pe):
                pe.wait_ge(s.loaded, 112 + CREDIT)
                for h in range(H_MLA):
                    for k in range(2):
                        n = 2 * h + k
                        bank = (b0 + b1)[n // 4]
                        mm = pe.transpose(bank[:, n % 4 * P:(n % 4 + 1) * P], w[:, k, h, :], r.ident)
                mm.then_inc(s.w_turned, 1)
                pe.wait_ge(s.wukT_ready, 4 + CREDIT)
                for k in range(2):
                    for h in range(H_MLA):
                        n = k * H_MLA + h
                        mm = pe.matmul(psc[:, n * NS:(n + 1) * NS], wukT[:, h, k * P:(k + 1) * P], qn[:, h, :],
                                       start=True, stop=True)
                mm.then_inc(s.q_product, 1)
                pe.wait_ge(s.q_ready, 3 + CREDIT)
                for rd in range(ROUNDS):
                    def turn(n, u, bb, load, prev):
                        pe.wait_ge(pages_loaded[u][bb], load * SEQUENCE + (CREDIT if bb < BY_SYNC else 0))
                        pe.wait_ge(s.k0_copied, before(n, bb, prev) + CREDIT)
                        pe.wait_ge(s.k1_copied, before(n, bb, prev) + CREDIT)
                        for g in range(PG):
                            mm = pe.transpose(b0[bb % 2][:, g * P:(g + 1) * P], kv[u][:, bb, g, 0:P], r.ident)
                        mm.then_inc(s.k0_turned, 1)
                        for g in range(PG):
                            mm = pe.transpose(b1[bb % 2][:, g * P:(g + 1) * P], kv[u][:, bb, g, P:2 * P], r.ident)
                        mm.then_inc(s.k1_turned, 1)
                        pe.wait_ge(s.kp_copied, n * RB + bb + CREDIT)
                        for g in range(PG):
                            mm = pe.transpose(bp[0:ROPE, g * P:(g + 1) * P], kv[u][:, bb, g, 2 * P:ROW], r.ident)
                        mm.then_inc(s.kp_turned, 1)

                    def scores(m, bb):
                        pe.wait_ge(s.k0_copied, m + 1 + CREDIT)
                        pe.wait_ge(s.k1_copied, m + 1 + CREDIT)
                        pe.wait_ge(s.kp_copied, m + 1 + CREDIT)
                        b = rd * RB + bb
                        out = psc[bb * QR:(bb + 1) * QR, :]
                        for k in range(2):
                            pe.matmul(out, qlat[:, k, b, :, :].rearrange("p h t -> p (h t)"), kT[bb % 2][:, k, :],
                                      start=(k == 0), stop=False)
                        pe.matmul(out, qpe[:, b, :, :].rearrange("p h t -> p (h t)"), kp[bb % 2][:, :],
                                  start=False, stop=True).then_inc(s.scores_ready, 1)

                    def turn_probs(n):
                        pe.wait_ge(s.probs_ready, n + CREDIT)
                        pe.wait_ge(s.pT_ready, n - 1 + CREDIT)
                        for g in range(PG):
                            mm = pe.transpose(ppt[:, g * P:(g + 1) * P], p[:, g * P:(g + 1) * P], r.ident)
                        mm.then_inc(s.probs_turned, 1)

                    def weigh(n, u):
                        pe.wait_ge(s.pT_ready, n + CREDIT)
                        pe.wait_ge(s.U_ready, n - 1 + CREDIT)
                        for bb in range(RB):
                            for g in range(PG):
                                mm = pe.matmul(pu[bb * QR:(bb + 1) * QR, 0:KV_LORA], pT[:, g, bb * QR:(bb + 1) * QR],
                                               kv[u][:, bb, g, 0:KV_LORA], start=(g == 0), stop=(g == PG - 1))
                        mm.then_inc(early.attended, 1)

                    for n, u, slot, load, prev in chunks(pe, rd):
                        turn(n, u, 0, load, prev)
                        if prev:
                            scores(n * RB - 1, RB - 1)
                        turn(n, u, 1, load, prev)
                        if prev:
                            turn_probs(n)
                        scores(n * RB, 0)
                        if prev:
                            weigh(n, 1 - u)
                        turn(n, u, 2, load, prev)
                        scores(n * RB + 1, 1)
                        turn(n, u, 3, load, prev)
                        scores(n * RB + 2, 2)
                    done = (rd + 1) * NC
                    scores(done * RB - 1, RB - 1)
                    turn_probs(done)
                    weigh(done, 1)
                    pe.wait_ge(s.probs_ready, (rd + 1) * NC + CREDIT)
                    for bb in range(RB):
                        b = rd * RB + bb
                        out = psc[bb * QR:(bb + 1) * QR, 0:DT]
                        for k in range(2):
                            pe.matmul(out, qlat[:, k, b, :, :].rearrange("p h t -> p (h t)"),
                                      r.ckvT[:, k, SEQ + b * DT:SEQ + (b + 1) * DT], start=(k == 0), stop=False)
                        mm = pe.matmul(out, qpe[:, b, :, :].rearrange("p h t -> p (h t)"), kpn[:, b * DT:(b + 1) * DT],
                                       start=False, stop=True)
                    mm.then_inc(s.new_scores, 1)
                    pe.wait_ge(s.new_probs, rd + 1 + CREDIT)
                    pe.wait_ge(s.pT_ready, (rd + 1) * NC + CREDIT)
                    pe.transpose(ppt[0:DT, 0:P], pn[:, :], r.ident).then_inc(s.new_turned, 1)
                    pe.wait_ge(s.new_T, rd + 1 + CREDIT)
                    pe.wait_ge(s.U_ready, (rd + 1) * NC + CREDIT)
                    for bb in range(RB):
                        mm = pe.matmul(pu[bb * QR:(bb + 1) * QR, 0:KV_LORA], pnT[:, bb * QR:(bb + 1) * QR],
                                       rn[:, rd * RB + bb, :], start=True, stop=True)
                    mm.then_inc(s.new_attended, 1)
                    pe.wait_ge(s.lat_ready, rd + 1 + CREDIT)
                    for k in range(2):
                        mm = pe.transpose(b0[0][:, k * P:(k + 1) * P], lat[:, k * P:(k + 1) * P], r.ident)
                    mm.then_inc(s.lat_turned, 1)
                    pe.wait_ge(s.latT_ready, 2 * rd + 2 + CREDIT)
                    for h in range(H_MLA):
                        for k in range(2):
                            mm = pe.matmul(b1[0][0:RB * DT, h * V_DIM:(h + 1) * V_DIM], latT[:, k, h, :],
                                           w[:, k, h, NOPE:], start=(k == 0), stop=(k == 1))
                    mm.then_inc(s.o_product, 1)
                    pe.wait_ge(s.o_copied, rd + 1 + CREDIT)
                    for k in range(4):
                        mm = pe.transpose(b0[1][:, k * RB * DT:(k + 1) * RB * DT], o[:, k * P:(k + 1) * P],
                                          r.ident[0:RB * DT, 0:RB * DT])
                    mm.then_inc(s.o_turned, 1)
                    pe.wait_ge(s.oT_ready, rd + 1 + CREDIT)

            @block.scalar
            def _(act):
                for rd in range(ROUNDS):
                    def exp(n, slot):
                        act.wait_ge(s.probs_turned, n - 1 + CREDIT)
                        act.wait_ge(s.bias_ready, n + CREDIT)
                        act.activation(p[:, :], psc[:, :], ACT.Exp, bias=nb[:, ds(slot, 1)], scale=MLA_SCALE,
                                       accum_out=l[:, ds(slot, 1)]).then_inc(s.probs_ready, 1)

                    for n, u, slot, load, prev in chunks(act, rd):
                        for bb in range(RB):
                            act.wait_ge(s.k1_turned, n * RB + bb + 1 + CREDIT)
                            act.wait_ge(s.scores_ready, before(n, bb, prev) + CREDIT)
                            act.copy(kT[bb % 2][:, 1, :], b1[bb % 2][:, :]).then_inc(s.k1_copied, 1)
                            if bb == 0 and prev:
                                exp(n, slot - 1)
                    exp((rd + 1) * NC, NC - 1)
                    act.wait_ge(s.new_max, rd + 1 + CREDIT)
                    act.activation(pn[:, :], sn[:, :], ACT.Exp, bias=nb[:, NC:NC + 1], accum_out=l[:, NC:NC + 1]
                                   ).then_inc(s.new_probs, 1)
                    act.wait_ge(s.diff_ready, rd + 1 + CREDIT)
                    act.activation(wt[:, :], dm[:, :], ACT.Exp).then_inc(s.weights_ready, 1)

            @block.vector
            def _(dve):
                dve.wait_ge(s.w_turned, 1 + CREDIT)
                for j, bank in enumerate(b0 + b1):
                    dve.tensor_copy(wukT[:, 2 * j:2 * j + 2, :].rearrange("n h c -> n (h c)"), bank[0:NOPE, :]
                                    ).then_inc(s.wukT_ready, 1)
                dve.wait_ge(s.q_product, 1 + CREDIT)
                for k in range(2):
                    src = psc[:, k * H_MLA * NS:(k + 1) * H_MLA * NS].rearrange("p (h b t) -> p h b t", h=H_MLA, b=DB)
                    dve.tensor_copy(qlat[:, k, :, :, :].rearrange("p b h t -> p h b t"), src).then_inc(s.q_ready, 1)
                dve.wait_ge(s.loaded, 112 + CREDIT)
                dve.tensor_copy(qpe[:, :, :, :].rearrange("p b h t -> p h b t"),
                                qp[:, :, :].rearrange("p h (b t) -> p h b t", b=DB)).then_inc(s.q_ready, 1)
                for rd in range(ROUNDS):
                    def maximum(n, slot):
                        dve.wait_ge(s.scores_ready, n * RB + CREDIT)
                        dve.tensor_reduce(nm[:, :], psc[:, :], AX.X, ALU.max, negate=True).then_inc(s.max_found, 1)
                        dve.wait_ge(s.max_found, n + CREDIT)
                        dve.tensor_scalar(nb[:, ds(slot, 1)], nm[:, :], MLA_SCALE, None, ALU.mult).then_inc(s.bias_ready, 1)

                    def copy_probs(n):
                        dve.wait_ge(s.probs_turned, n + CREDIT)
                        dve.wait_ge(early.attended, n - 1 + 2)
                        dve.tensor_copy(pT[:, :, :].rearrange("p g t -> p (g t)"), ppt[:, :]).then_inc(s.pT_ready, 1)

                    def copy_sums(n, slot):
                        dve.wait_ge(early.attended, n + 2)
                        dve.tensor_copy(U[:, ds(slot, 1), :].squeeze(1), pu[:, 0:KV_LORA]).then_inc(s.U_ready, 1)

                    for n, u, slot, load, prev in chunks(dve, rd):
                        for bb in range(RB):
                            dve.wait_ge(s.k0_turned, n * RB + bb + 1 + CREDIT)
                            dve.wait_ge(s.scores_ready, before(n, bb, prev) + CREDIT)
                            dve.tensor_copy(kT[bb % 2][:, 0, :], b0[bb % 2][:, :]).then_inc(s.k0_copied, 1)
                            dve.wait_ge(s.kp_turned, n * RB + bb + 1 + CREDIT)
                            dve.tensor_copy(kp[bb % 2][:, :], bp[0:ROPE, :]).then_inc(s.kp_copied, 1)
                            if prev and bb == 0:
                                maximum(n, slot - 1)
                            if prev and bb == 1:
                                copy_probs(n)
                                copy_sums(n, slot - 1)
                    maximum((rd + 1) * NC, NC - 1)
                    copy_probs((rd + 1) * NC)
                    copy_sums((rd + 1) * NC, NC - 1)
                    step = Steps(dve, s.steps)
                    step.n = rd * N_MERGE
                    dve.wait_ge(s.new_scores, rd + 1 + CREDIT)
                    step(dve.scalar_tensor_tensor(out=sn[:, :], in0=psc[:, 0:DT], scalar=MLA_SCALE, in1=mnew[:, :],
                                                  op0=ALU.mult, op1=ALU.add))
                    dve.tensor_reduce(nb[:, NC:NC + 1], sn[:, :], AX.X, ALU.max, negate=True).then_inc(s.new_max, 1)
                    dve.wait_ge(s.new_turned, rd + 1 + CREDIT)
                    dve.tensor_copy(pnT[:, :], ppt[0:DT, 0:P]).then_inc(s.new_T, 1)
                    dve.wait_ge(s.new_attended, rd + 1 + CREDIT)
                    dve.tensor_copy(U[:, NC, :], pu[:, 0:KV_LORA]).then_inc(s.new_copied, 1)
                    dve.wait_ge(s.new_max, rd + 1 + CREDIT)
                    step(dve.tensor_reduce(nmx[:, :], nb[:, :], AX.X, ALU.min))
                    dve.tensor_scalar(dm[:, :], nb[:, :], nmx[:, 0:1], -1.0, ALU.subtract, ALU.mult).then_inc(s.diff_ready, 1)
                    dve.wait_ge(s.weights_ready, rd + 1 + CREDIT)
                    step(dve.tensor_tensor(wl[:, :], wt[:, :], l[:, :], ALU.mult))
                    step(dve.tensor_reduce(L[:, :], wl[:, :], AX.X, ALU.add))
                    step(dve.reciprocal(L[:, :], L[:, :]))
                    step(dve.tensor_scalar(wt[:, :], wt[:, :], L[:, 0:1], None, ALU.mult))
                    dve.wait_ge(s.new_copied, rd + 1 + CREDIT)
                    step(dve.tensor_scalar(lat[:, :], U[:, 0, :], wt[:, 0:1], None, ALU.mult))
                    for c in range(1, NC + 1):
                        ins = dve.scalar_tensor_tensor(out=lat[:, :], in0=U[:, c, :], scalar=wt[:, c:c + 1], in1=lat[:, :],
                                                       op0=ALU.mult, op1=ALU.add)
                        if c < NC:
                            step(ins)
                        else:
                            ins.then_inc(s.lat_ready, 1)
                    assert step.n == (rd + 1) * N_MERGE, step.n
                    dve.wait_ge(s.lat_turned, rd + 1 + CREDIT)
                    for k in range(2):
                        dve.tensor_copy(latT[:, k, :, :].rearrange("p h (b t) -> p h b t", b=RB),
                                        b0[0][:, k * P:(k + 1) * P].rearrange("p (b h t) -> p h b t", b=RB, h=H_MLA)
                                        ).then_inc(s.latT_ready, 1)
                    dve.wait_ge(s.o_product, rd + 1 + CREDIT)
                    dve.tensor_copy(o[:, :], b1[0][0:RB * DT, :]).then_inc(s.o_copied, 1)
                    dve.wait_ge(s.o_turned, rd + 1 + CREDIT)
                    at = SEQ + rd * RB * DT
                    dve.tensor_copy(r.oT_mla[:, :, at:at + RB * DT],
                                    b0[1][:, 0:4 * RB * DT].rearrange("p (k t) -> p k t", k=4)).then_inc(s.oT_ready, 1)


def sample_dilated_and_memory_attention(nc, a, r):
    ctx, sb, ps, sems = stage(nc, "sdil")
    W = P + 1
    R = HM * DT
    HALF = HM * EM
    with ctx:
        q = sb("q", [P, NG, E])
        k, v = sb("k", [P, W, E]), sb("v", [P, W, E])
        sc, p = sb("sc", [P, W]), sb("p", [P, W])
        nm, nb, l = sb("nm", [P, 1]), sb("nb", [P, NG]), sb("l", [P, NG])
        U = sb("U", [P, NG, E])
        nmx, dm, wt, wl, L = sb("nmx", [P, 1]), sb("dm", [P, NG]), sb("wt", [P, NG]), sb("wl", [P, NG]), sb("L", [P, 1])
        o = sb("o", [P, E])
        x, qT = sb("x", [NS, HALF]), sb("qT", [P, HM, NS])
        mk = [sb(f"mk{u}", [P, 2, HALF]) for u in range(2)]
        kT = [sb(f"kT{u}", [P, HM, 2, P]) for u in range(2)]
        mv = k[:, 0:P, :].rearrange("p l e -> p (l e)").rearrange("p (b m c) -> p b m c", b=DB, m=2)
        sT, m_p, pT = sb("sT", [P, 2, P]), sb("m_p", [P, MEM]), sb("pT", [P, 2, P])
        m_nm, m_nb, m_l, m_rl = sb("m_nm", [P, 1]), sb("m_nb", [P, 1]), sb("m_l", [P, 1]), sb("m_rl", [P, 1])
        pk = [[ps(f"pk{u}{w}", [P, 512]) for w in range(2)] for u in range(2)]
        pq, pst, psc, po = ps("pq", [P, 512]), ps("pst", [P, 512]), ps("psc", [P, 512]), ps("po", [P, 512])
        d = sems("q_loaded k_loaded v_loaded steps scored bias_ready probs_ready weighed diff_ready weights_ready o_ready "
                 "o_turned oT_ready")
        s = sems("x_loaded q_turned qT_ready mk_loaded0 mk_loaded1 m_v_loaded k_turned k0_copied k1_copied product_ready "
                 "sT_ready scores_ready max_found m_bias_ready exp_ready inverted m_probs_ready probs_turned pT_ready "
                 "attended m_oT_ready")
        mk_loaded = (s.mk_loaded0, s.mk_loaded1)
        cache = a.cache_mem.rearrange("b (m p) c -> b p m c", p=P)

        def window(eng, dst, g, j, loaded):
            dil = GROUPS[g][1]
            new = a.dil[SEQ:SEQ + NS, (1 + j) * NG * GE + g * GE:(1 + j) * NG * GE + (g + 1) * GE
                        ].rearrange("(b t) c -> b t c", t=DT)
            for t in range(DT):
                n_old = P - t if g == 0 else P
                first = 0 if g == 0 else t
                for h in range(HD):
                    at = dst[(t * HD + h) * DB:(t * HD + h + 1) * DB, :, :]
                    part = slice(h * E, (h + 1) * E)
                    old = a.cache_dil[g][:, t:t + (n_old - 1) * dil + 1:dil, j, part]
                    eng.dma_start(at[:, 0:n_old, :], old).then_inc(loaded, 16)
                    eng.dma_start(at[:, n_old:W, :], new[:, first:t + 1, part]).then_inc(loaded, 16)

        FULL = 16 * 2 * DT * HD
        with nc.Block() as block:
            @block.sync
            def _(sp):
                sp.dma_start(x[:, :], a.proj[SEQ:SEQ + NS, C_MEM:C_GATE]).then_inc(s.x_loaded, 16)
                qs = a.dil[SEQ:SEQ + NS, 0:NG * GE].rearrange("(b t) (g h e) -> t h b g e", t=DT, g=NG, h=HD)
                for t in range(DT):
                    for h in range(HD):
                        sp.dma_start(q[(t * HD + h) * DB:(t * HD + h + 1) * DB, :, :], qs[t, h]).then_inc(d.q_loaded, 16)
                window(sp, k, 0, 0, d.k_loaded)
                with sp.Fori(0, DB // 2) as i:
                    for u in range(2):
                        sp.wait_ge(s.k_turned, i * 2 + CREDIT)
                        sp.dma_start(mk[u][:, :, :], cache[ds(i * 2 + u, 1), :, :, 0:HALF].squeeze(0)).then_inc(mk_loaded[u], 16)
                for g in range(1, NG):
                    sp.wait_ge(d.scored, g + CREDIT)
                    window(sp, k, g, 0, d.k_loaded)
                sp.wait_ge(d.scored, NG + CREDIT)
                with sp.Fori(0, DB) as b:
                    sp.dma_start(mv[:, ds(b, 1), :, :].squeeze(1), cache[ds(b, 1), :, :, HALF:2 * HALF].squeeze(0)
                                 ).then_inc(s.m_v_loaded, 16)

            @block.vector
            def _(dve):
                def memory_softmax():
                    dve.wait_ge(s.product_ready, DB + CREDIT)
                    dve.tensor_copy(sT[:, :, :].rearrange("p m q -> p (m q)"), pst[:, 0:2 * P]).then_inc(s.sT_ready, 1)
                    dve.wait_ge(s.scores_ready, 1 + CREDIT)
                    dve.tensor_reduce(m_nm[:, :], psc[:, 0:MEM], AX.X, ALU.max, negate=True).then_inc(s.max_found, 1)
                    dve.wait_ge(s.max_found, 1 + CREDIT)
                    dve.tensor_scalar(m_nb[:, :], m_nm[:, :], MEM_SCALE, None, ALU.mult).then_inc(s.m_bias_ready, 1)
                    dve.wait_ge(s.exp_ready, 1 + CREDIT)
                    dve.reciprocal(m_rl[:, :], m_l[:, :]).then_inc(s.inverted, 1)
                    dve.wait_ge(s.inverted, 1 + CREDIT)
                    dve.tensor_scalar(m_p[:, :], m_p[:, :], m_rl[:, 0:1], None, ALU.mult).then_inc(s.m_probs_ready, 1)
                    dve.wait_ge(s.probs_turned, 1 + CREDIT)
                    dve.tensor_copy(pT[:, :, :].rearrange("p m q -> p (m q)"), pst[:, 0:2 * P]).then_inc(s.pT_ready, 1)

                dve.wait_ge(s.q_turned, 1 + CREDIT)
                dve.tensor_copy(qT[:, :, :].rearrange("p h t -> p (h t)"), pq[:, 0:HM * NS]).then_inc(s.qT_ready, 1)
                with dve.Fori(0, DB // 2) as i:
                    for u in range(2):
                        dve.wait_ge(s.k_turned, i * 2 + u + 1 + CREDIT)
                        dve.wait_ge(s.product_ready, i * 2 + CREDIT)
                        dve.tensor_copy(kT[u][:, 0:2, :, :].rearrange("p h m t -> p (h m t)"), pk[u][0][:, :]
                                        ).then_inc(s.k0_copied, 1)
                step = Steps(dve, d.steps)
                dve.wait_ge(d.q_loaded, 16 * DT * HD + CREDIT)
                for g in range(NG):
                    dve.wait_ge(d.k_loaded, FULL * (g + 1) + CREDIT)
                    step(dve.tensor_tensor(k[:, :, :], k[:, :, :], q[:, g, :].unsqueeze(1).broadcast_to([P, W, E]), ALU.mult))
                    dve.tensor_reduce(sc[:, :], k[:, :, :], AX.X, ALU.add).then_inc(d.scored, 1)
                    dve.wait_ge(d.scored, g + 1 + CREDIT)
                    step(dve.tensor_reduce(nm[:, :], sc[:, :], AX.X, ALU.max, negate=True))
                    dve.tensor_scalar(nb[:, g:g + 1], nm[:, :], DIL_SCALE, None, ALU.mult).then_inc(d.bias_ready, 1)
                    if g == 0:
                        memory_softmax()
                    dve.wait_ge(d.probs_ready, g + 1 + CREDIT)
                    dve.wait_ge(d.v_loaded, FULL * (g + 1) + CREDIT)
                    step(dve.tensor_tensor(v[:, :, :], v[:, :, :], p[:, :].unsqueeze(2).broadcast_to([P, W, E]), ALU.mult))
                    dve.tensor_reduce(U[:, g, :], v[:, :, :].rearrange("p l e -> p e l"), AX.X, ALU.add).then_inc(d.weighed, 1)
                dve.wait_ge(d.bias_ready, NG + CREDIT)
                step(dve.tensor_reduce(nmx[:, :], nb[:, :], AX.X, ALU.min))
                dve.tensor_scalar(dm[:, :], nb[:, :], nmx[:, 0:1], -1.0, ALU.subtract, ALU.mult).then_inc(d.diff_ready, 1)
                dve.wait_ge(d.weights_ready, 1 + CREDIT)
                step(dve.tensor_tensor(wl[:, :], wt[:, :], l[:, :], ALU.mult))
                step(dve.tensor_reduce(L[:, :], wl[:, :], AX.X, ALU.add))
                step(dve.reciprocal(L[:, :], L[:, :]))
                step(dve.tensor_scalar(wt[:, :], wt[:, :], L[:, 0:1], None, ALU.mult))
                dve.wait_ge(d.weighed, NG + CREDIT)
                step(dve.tensor_scalar(o[:, :], U[:, 0, :], wt[:, 0:1], None, ALU.mult))
                step(dve.scalar_tensor_tensor(out=o[:, :], in0=U[:, 1, :], scalar=wt[:, 1:2], in1=o[:, :],
                                              op0=ALU.mult, op1=ALU.add))
                dve.scalar_tensor_tensor(out=o[:, :], in0=U[:, 2, :], scalar=wt[:, 2:3], in1=o[:, :],
                                         op0=ALU.mult, op1=ALU.add).then_inc(d.o_ready, 1)
                dve.wait_ge(s.attended, 1 + CREDIT)
                dve.tensor_copy(r.oT_mem[:, :, SEQ:SEQ + NS], po[:, 0:HM * NS].rearrange("p (h t) -> p h t", h=HM)
                                ).then_inc(s.m_oT_ready, 1)
                dve.wait_ge(d.o_turned, 1 + CREDIT)
                for h in range(HD):
                    at = slice(h % 2 * E, (h % 2 + 1) * E)
                    dve.tensor_copy(r.oT_dil[at, h // 2, SEQ:SEQ + NS].rearrange("e (b t) -> e t b", t=DT),
                                    pq[0:E, 0:P].rearrange("e (t h b) -> e h t b", t=DT, h=HD)[:, h]).then_inc(d.oT_ready, 1)

            @block.scalar
            def _(act):
                window(act, v, 0, 1, d.v_loaded)
                with act.Fori(0, DB // 2) as i:
                    for u in range(2):
                        act.wait_ge(s.k_turned, i * 2 + u + 1 + CREDIT)
                        act.wait_ge(s.product_ready, i * 2 + CREDIT)
                        act.copy(kT[u][:, 2:4, :, :].rearrange("p h m t -> p (h m t)"), pk[u][1][:, :]).then_inc(s.k1_copied, 1)
                for g in range(NG):
                    if g:
                        act.wait_ge(d.weighed, g + CREDIT)
                        window(act, v, g, 1, d.v_loaded)
                    act.wait_ge(d.bias_ready, g + 1 + CREDIT)
                    act.activation(p[:, :], sc[:, :], ACT.Exp, bias=nb[:, g:g + 1], scale=DIL_SCALE,
                                   accum_out=l[:, g:g + 1]).then_inc(d.probs_ready, 1)
                    if g == 0:
                        act.wait_ge(s.m_bias_ready, 1 + CREDIT)
                        act.activation(m_p[:, :], psc[:, 0:MEM], ACT.Exp, bias=m_nb[:, :], scale=MEM_SCALE,
                                       accum_out=m_l[:, :]).then_inc(s.exp_ready, 1)
                act.wait_ge(d.diff_ready, 1 + CREDIT)
                act.activation(wt[:, :], dm[:, :], ACT.Exp).then_inc(d.weights_ready, 1)

            @block.tensor
            def _(pe):
                pe.wait_ge(s.x_loaded, 16 + CREDIT)
                for h in range(HM):
                    mm = pe.transpose(pq[:, h * NS:(h + 1) * NS], x[:, h * EM:(h + 1) * EM], r.ident[0:NS, 0:NS])
                mm.then_inc(s.q_turned, 1)
                pe.wait_ge(s.qT_ready, 1 + CREDIT)
                with pe.Fori(0, DB // 2) as i:
                    for u in range(2):
                        pe.wait_ge(mk_loaded[u], i * 16 + 16 + CREDIT)
                        pe.wait_ge(s.k0_copied, i * 2 + CREDIT)
                        pe.wait_ge(s.k1_copied, i * 2 + CREDIT)
                        for h in range(HM):
                            for m in range(2):
                                at = (h % 2 * 2 + m) * P
                                mm = pe.transpose(pk[u][h // 2][:, at:at + P], mk[u][:, m, h * EM:(h + 1) * EM], r.ident)
                        mm.then_inc(s.k_turned, 1)
                    for u in range(2):
                        pe.wait_ge(s.k0_copied, i * 2 + u + 1 + CREDIT)
                        pe.wait_ge(s.k1_copied, i * 2 + u + 1 + CREDIT)
                        for m in range(2):
                            for h in range(HM):
                                mm = pe.matmul(pst[:, ds(i * (2 * R) + (m * P + u * R + h * DT), DT)], kT[u][:, h, m, :],
                                               qT[:, h, ds(i * (2 * DT) + u * DT, DT)], start=True, stop=True)
                        mm.then_inc(s.product_ready, 1)
                pe.wait_ge(s.sT_ready, 1 + CREDIT)
                for m in range(2):
                    mm = pe.transpose(psc[:, m * P:(m + 1) * P], sT[:, m, :], r.ident)
                mm.then_inc(s.scores_ready, 1)
                pe.wait_ge(s.m_probs_ready, 1 + CREDIT)
                for m in range(2):
                    mm = pe.transpose(pst[:, m * P:(m + 1) * P], m_p[:, m * P:(m + 1) * P], r.ident)
                mm.then_inc(s.probs_turned, 1)
                pe.wait_ge(s.pT_ready, 1 + CREDIT)
                pe.wait_ge(s.m_v_loaded, 16 * DB + CREDIT)
                for b in range(DB):
                    for h in range(HM):
                        for m in range(2):
                            mm = pe.matmul(po[:, h * NS + b * DT:h * NS + (b + 1) * DT], mv[:, b, m, h * EM:(h + 1) * EM],
                                           pT[:, m, b * R + h * DT:b * R + (h + 1) * DT], start=(m == 0), stop=(m == 1))
                mm.then_inc(s.attended, 1)
                pe.wait_ge(d.o_ready, 1 + CREDIT)
                pe.transpose(pq[0:E, 0:P], o[:, :], r.ident).then_inc(d.o_turned, 1)


def mix_branches(nc, a, r, xT, mT):
    ctx, sb, ps, sems = stage(nc, "mix")
    TH = (SEQ + NS) // 3
    UN = 9
    with ctx:
        wg = [sb(f"wg{u}", [P, KD, 3, P]) for u in range(2)]
        wo = [sb(f"wo{u}", [P, 10, P]) for u in range(2)]
        sg = [sb(f"sg{u}", [P, TH]) for u in range(2)]
        pr = [sb(f"pr{u}", [P, TH]) for u in range(3)]
        pg, py = [ps(f"pg{u}", [P, 512]) for u in range(2)], [ps(f"py{u}", [P, 512]) for u in range(2)]
        s = sems("zeroed w_loaded0 w_loaded1 product_ready gate_ready weighed steps summed")
        w_loaded = (s.w_loaded0, s.w_loaded1)
        gates = a.w_in[:, C_GATE:].rearrange("(k p) (b n) -> p k b n", p=P, b=3)
        branches = ((a.w_o_mla, r.oT_mla, 0, 4), (a.w_o_dil, r.oT_dil, 4, 2), (a.w_o_mem, r.oT_mem, 6, 4))
        with nc.Block() as block:
            @block.sync
            def _(sp):
                def load(u, c):
                    col = ds(c * P, P)
                    for b in range(3):
                        sp.dma_start(wg[u][:, :, b, :], gates[:, :, b, col]).then_inc(w_loaded[u], 16)
                    for w, _, k0, kk in branches:
                        sp.dma_start(wo[u][:, k0:k0 + kk, :], w.rearrange("(k p) n -> p k n", p=P)[:, :, col]
                                     ).then_inc(w_loaded[u], 16)

                load_pairs(sp, KD // 2, s.product_ready, UN, load)

            @block.gpsimd
            def _(pool):
                pool.memset(mT[:, :, SEQ + NS:T], 0.0).then_inc(s.zeroed, 1)
                pool.wait_ge(s.zeroed, 1 + CREDIT)

            @block.tensor
            def _(pe):
                with pe.Fori(0, KD // 2) as i:
                    for u in range(2):
                        pe.wait_ge(w_loaded[u], i * 96 + 96 + CREDIT)
                        for n in range(UN):
                            m = u * UN + n
                            rows = slice(n // 3 * TH, (n // 3 + 1) * TH)
                            _, oT, k0, kk = branches[n % 3]
                            pe.wait_ge(s.weighed, i * (2 * UN) + max(m - 1, 0) + CREDIT)
                            for k in range(KD):
                                pe.matmul(pg[m % 2][:, 0:TH], wg[u][:, k, n % 3, :], xT[:, k, rows],
                                          start=(k == 0), stop=(k == KD - 1))
                            for k in range(kk):
                                mm = pe.matmul(py[m % 2][:, 0:TH], wo[u][:, k0 + k, :], oT[:, k, rows],
                                               start=(k == 0), stop=(k == kk - 1))
                            mm.then_inc(s.product_ready, 1)

            @block.scalar
            def _(act):
                with act.Fori(0, KD // 2) as i:
                    for m in range(2 * UN):
                        act.wait_ge(s.product_ready, i * (2 * UN) + m + 1 + CREDIT)
                        act.wait_ge(s.weighed, i * (2 * UN) + max(m - 1, 0) + CREDIT)
                        act.activation(sg[m % 2][:, :], pg[m % 2][:, 0:TH], ACT.Sigmoid).then_inc(s.gate_ready, 1)

            @block.vector
            def _(dve):
                with dve.Fori(0, KD // 2) as i:
                    step = Steps(dve, s.steps, i, 6)
                    for m in range(2 * UN):
                        dve.wait_ge(s.gate_ready, i * (2 * UN) + m + 1 + CREDIT)
                        dve.tensor_tensor(pr[m % 3][:, :], sg[m % 2][:, :], py[m % 2][:, 0:TH], ALU.mult).then_inc(s.weighed, 1)
                        if m % 3 == 2:
                            dve.wait_ge(s.weighed, i * (2 * UN) + m + 1 + CREDIT)
                            step(dve.tensor_tensor(pr[0][:, :], pr[0][:, :], pr[1][:, :], ALU.add))
                            third = m % UN // 3
                            dst = mT[:, ds(i * 2 + m // UN, 1), third * TH:(third + 1) * TH].squeeze(1)
                            dve.tensor_tensor(dst, pr[0][:, :], pr[2][:, :], ALU.add).then_inc(s.summed, 1)
                            dve.wait_ge(s.summed, i * 6 + m // 3 + 1 + CREDIT)
                    step.end()


def peer_scores(nc, a, r, xT):
    ctx, sb, ps, sems = stage(nc, "psc")
    TH = (SEQ + NS) // 3
    with ctx:
        keys, keysT = sb("keys", [P, 2, QH]), sb("keysT", [P, 2, NK])
        w = [sb(f"w{u}", [P, KD, QH]) for u in range(2)]
        qT = [sb(f"qT{u}", [P, T]) for u in range(2)]
        sc = [sb(f"sc{u}", [P, NT, NK]) for u in range(2)]
        pq = [ps(f"pq{u}", [P, 512]) for u in range(3)]
        psc = [ps(f"psc{u}", [P, 512]) for u in range(3)]
        s = sems("zeroed keys_loaded keys_turned keysT_ready w_loaded0 w_loaded1 q_product qT_ready scores_ready scores_copied "
                 "stored0 stored1")
        w_loaded, stored = (s.w_loaded0, s.w_loaded1), (s.stored0, s.stored1)
        wv = a.w_peer_q.rearrange("(k p) n -> p k n", p=P)
        dst = a.scores.rearrange("(t p) c n -> p t c n", p=P)
        with nc.Block() as block:
            @block.sync
            def _(sp):
                sp.dma_start(keys[:, :, :], a.peer_sub_keys.rearrange("c n e -> n c e")).then_inc(s.keys_loaded, 16)
                load_pairs(sp, HP, s.q_product, 3, lambda u, c: sp.dma_start(
                    w[u][:, :, :], wv[:, :, ds(c * QH, QH)]).then_inc(w_loaded[u], 16))

            @block.gpsimd
            def _(pool):
                for u in range(2):
                    pool.memset(qT[u][:, SEQ + NS:T], 0.0).then_inc(s.zeroed, 1)
                pool.wait_ge(s.zeroed, 2 + CREDIT)

            @block.tensor
            def _(pe):
                pe.wait_ge(s.keys_loaded, 16 + CREDIT)
                for u in range(2):
                    mm = pe.transpose(pq[0][:, u * P:(u + 1) * P], keys[:, u, :], r.ident)
                mm.then_inc(s.keys_turned, 1)
                pe.wait_ge(s.keysT_ready, 1 + CREDIT)
                pe.wait_ge(s.zeroed, 2 + CREDIT)
                with pe.Fori(0, HP) as i:
                    for u in range(2):
                        pe.wait_ge(w_loaded[u], i * 16 + 16 + CREDIT)
                        for c in range(3):
                            pe.wait_ge(s.qT_ready, i * 6 + (c + 1 if u else 0) + CREDIT)
                            for k in range(KD):
                                mm = pe.matmul(pq[c][:, 0:TH], w[u][:, k, :], xT[:, k, c * TH:(c + 1) * TH],
                                               start=(k == 0), stop=(k == KD - 1))
                            mm.then_inc(s.q_product, 1)
                        for c in range(3):
                            pe.wait_ge(s.qT_ready, i * 6 + 3 * u + min(c + 2, 3) + CREDIT)
                            pe.wait_ge(s.scores_copied, i * 6 + (c + 1 if u else 0) + CREDIT)
                            for t in range(3):
                                n = 3 * c + t
                                mm = pe.matmul(psc[c][:, t * NK:(t + 1) * NK], qT[u][:, n * P:(n + 1) * P], keysT[:, u, :],
                                               start=True, stop=True)
                            mm.then_inc(s.scores_ready, 1)

            @block.scalar
            def _(act):
                with act.Fori(0, HP) as i:
                    for u in range(2):
                        act.wait_ge(s.scores_ready, i * 6 + CREDIT)
                        for c in range(3):
                            act.wait_ge(s.q_product, i * 6 + 3 * u + c + 1 + CREDIT)
                            act.copy(qT[u][:, c * TH:(c + 1) * TH], pq[c][:, 0:TH]).then_inc(s.qT_ready, 1)
                        act.wait_ge(s.scores_copied, i * 6 + 3 * u + 3 + CREDIT)
                        act.dma_start(dst[:, :, ds(i * 2 + u, 1), :].squeeze(2), sc[u][:, :, :]).then_inc(stored[u], 16)
                for u in range(2):
                    act.wait_ge(stored[u], 16 * HP + CREDIT)

            @block.vector
            def _(dve):
                dve.wait_ge(s.keys_turned, 1 + CREDIT)
                dve.tensor_copy(keysT[:, :, :].rearrange("p c n -> p (c n)"), pq[0][:, 0:2 * P]).then_inc(s.keysT_ready, 1)
                with dve.Fori(0, HP) as i:
                    for u in range(2):
                        dve.wait_ge(stored[u], i * 16 + CREDIT)
                        for c in range(3):
                            dve.wait_ge(s.scores_ready, i * 6 + 3 * u + c + 1 + CREDIT)
                            dve.tensor_copy(sc[u][:, 3 * c:3 * c + 3, :].rearrange("p t n -> p (t n)"), psc[c][:, 0:3 * NK]
                                            ).then_inc(s.scores_copied, 1)


Turn = namedtuple("Turn", "t v u k")
Rows = namedtuple("Rows", "n slots")


def peer_experts(nc, a, r):
    ctx, sb, ps, sems = stage(nc, "peer")
    GROUP = 8
    NGR = SLOTS // GROUP
    RING = 2 * GROUP
    G2 = 2 * HP
    QUARTERS = P // NS
    PROMPT, SAMPLE = Rows(P, SLOTS), Rows(NS, SLOTS // QUARTERS)
    with ctx:
        S = sb("S", [P, G2, NK])
        m, ix, ixf = sb("m", [P, G2, TOPK]), sb("ix", [P, G2, TOPK], U32), sb("ixf", [P, G2, TOPK])
        cand = sb("cand", [P, HP, TOPK * TOPK])
        best, jx = sb("best", [P, HP, TOPK]), sb("jx", [P, HP, TOPK], U32)
        part, partf = sb("part", [P, 2, SLOTS], U32), sb("partf", [P, 2, SLOTS])
        hot = S[:, :, :].rearrange("p c n -> p (c n)").rearrange("p (s x) -> p s x", x=TOPK)
        num, ef, eid = sb("num", [P, 2, SLOTS]), sb("ef", [P, SLOTS]), sb("eid", [P, SLOTS], U32)
        d, ex, sm, gate = sb("d", [P, HP, TOPK]), sb("ex", [P, HP, TOPK]), sb("sm", [P, HP]), sb("gate", [P, HP, TOPK])
        iota, held = sb("iota", [P, TOPK]), sb("held", [P, 1])
        x, h = sb("x", [P, D]), sb("h", [P, D])
        eid_u, eid_v, gate_u = sb("eid_u", [P, SLOTS], U32), sb("eid_v", [P, SLOTS], U32), sb("gate_u", [P, SLOTS])
        ub = [sb(f"ub{u}", [P, D]) for u in range(RING)]
        vb = [sb(f"vb{u}", [P, D]) for u in range(RING)]
        zero, held_u, held_v = sb("zero", [P, 1]), sb("held_u", [P, 1]), sb("held_v", [P, 1])
        act_in, gl, coef = sb("act_in", [P, SLOTS]), sb("gl", [P, SLOTS]), sb("coef", [P, SLOTS])
        dg = [sb(f"dg{u}", [P, P]) for u in range(RING)]
        fold = sb("fold", [P, NS])
        g, y = sb("g", [P, D]), sb("y", [P, D])
        ss, ms, rt, rstd = sb("ss", [P, 1]), sb("ms", [P, 1]), sb("rt", [P, 1]), sb("rstd", [P, 1])
        acc = [ps(f"acc{u}", [P, 512]) for u in range(2)]
        own = sems("u_loaded0 u_loaded1 v_loaded0 v_loaded1", 0)
        s = sems("constants_loaded S_loaded steps steps2 chosen chosen_stored diff_ready exp_ready sum_ready sum_inverted "
                 "zeroed u_wait_taken v_wait_taken eid_u_loaded eid_v_loaded gate_loaded x_loaded h_loaded "
                 "dotted gelu_ready coef_ready diag_ready v_used squares_summed mean_ready root_ready rstd_ready y_ready "
                 "h_added stored")
        u_loaded, v_loaded = (own.u_loaded0, own.u_loaded1), (own.v_loaded0, own.v_loaded1)
        FULL = 16 * GROUP
        TILE = FULL * NGR // 2
        STEPS, STEPS2 = 11, 11

        def turns(eng):
            yield Turn(-2, None, None, True)
            yield Turn(-1, None, PROMPT, True)
            with eng.Fori(0, NTP - 1) as t:
                yield Turn(t, PROMPT, PROMPT, True)
            yield Turn(NTP - 1, PROMPT, SAMPLE, False)
            yield Turn(NTP, SAMPLE, None, False)

        with nc.Block() as block:
            @block.sync
            def _(sp):
                def load(dst, src, first, shape, sem, every=False):
                    if shape == PROMPT:
                        sp.dma_start(dst[:, :], src[ds(first, P), :]).then_inc(sem, 16)
                    else:
                        for q in range(QUARTERS):
                            rows, cols = slice(q * NS, (q + 1) * NS), slice(q * shape.slots, (q + 1) * shape.slots)
                            if every:
                                sp.dma_start(dst[rows, :], src[ds(first, NS), :]).then_inc(sem, 16)
                            else:
                                sp.dma_start(dst[rows, 0:shape.slots], src[ds(first, NS), cols]).then_inc(sem, 16)

                sp.dma_start(iota[:, :], a.iota16).then_inc(s.constants_loaded, 16)
                sp.dma_start(g[:, :], a.g_final.partition_broadcast(P)).then_inc(s.constants_loaded, 16)
                sp.dma_start(fold[:, :], a.fold).then_inc(s.constants_loaded, 16)
                for t, v, u, k in turns(sp):
                    if u:
                        sp.wait_ge(s.chosen_stored, t * 32 + 64 + CREDIT)
                        if v:
                            sp.wait_ge(u_loaded[1], t * TILE + TILE)
                        load(eid_u, a.experts, t * P + P, u, s.eid_u_loaded)
                    if k:
                        sp.wait_ge(s.chosen, t + 2 + CREDIT)
                        sp.dma_start(S[:, :, :], a.scores[ds(t * P + 2 * P, P), :, :]).then_inc(s.S_loaded, 16)
                    if u:
                        sp.wait_ge(s.dotted, t * NGR + NGR + CREDIT)
                        load(x, a.xn2, t * P + P, u, s.x_loaded, True)
                    if v:
                        sp.wait_ge(s.v_used, t * NGR + CREDIT)
                        load(eid_v, a.experts, t * P, v, s.eid_v_loaded)
                    if u:
                        sp.wait_ge(s.coef_ready, t + 1 + CREDIT)
                        load(gate_u, a.gates, t * P + P, u, s.gate_loaded)
                    if v:
                        sp.wait_ge(s.y_ready, t + CREDIT)
                        sp.dma_start(h[0:v.n, :], a.h[ds(t * P, v.n), :]).then_inc(s.h_loaded, 16)
                    if k:
                        sp.wait_ge(s.chosen, t + 3 + CREDIT)
                        rows = ds(t * P + 2 * P, P)
                        sp.dma_start(a.experts[rows, :], eid[:, :]).then_inc(s.chosen_stored, 16)
                        sp.dma_start(a.gates[rows, :], gate[:, :, :].rearrange("p h k -> p (h k)")).then_inc(s.chosen_stored, 16)

            @block.gpsimd
            def _(pool):
                pool.memset(zero[:, :], 0.0).then_inc(s.zeroed, 1)
                pool.wait_ge(s.zeroed, 1 + CREDIT)

                def gather(j, done, bufs, indices, loaded, used, table, held, taken):
                    pool.wait_ge(taken, done + j + CREDIT)
                    pool.wait_ge(used, done + max(j - 1, 0) + CREDIT)
                    pool.tensor_tensor(held[:, :], zero[:, :], zero[:, :], ALU.add).then_inc(taken, 1)
                    for k in range(j * GROUP, (j + 1) * GROUP):
                        pool.indirect_dma_start(bufs[k % RING][:, :], None, table,
                                                bass.IndirectOffsetOnAxis(ap=indices[:, k:k + 1], axis=0)
                                                ).then_inc(loaded[j % 2], 16)

                for t, v, u, k in turns(pool):
                    for j in range(NGR + 1):
                        if u and j * GROUP < u.slots:
                            if j == 0:
                                pool.wait_ge(s.eid_u_loaded, t * 16 + 16 + 16 * (P // u.n) + CREDIT)
                            gather(j, t * NGR + NGR, ub, eid_u, u_loaded, s.dotted, a.peer_u, held_u, s.u_wait_taken)
                        if v and 0 < j and (j - 1) * GROUP < v.slots:
                            if j == 1:
                                pool.wait_ge(s.eid_v_loaded, t * 16 + 16 * (P // v.n) + CREDIT)
                            gather(j - 1, t * NGR, vb, eid_v, v_loaded, s.v_used, a.peer_v, held_v, s.v_wait_taken)

            @block.vector
            def _(dve):
                square = [P, HP, TOPK, TOPK]
                mv = m[:, :, :].rearrange("p (h c) k -> p h c k", c=2)
                iv = ixf[:, :, :].rearrange("p (h c) k -> p h c k", c=2)

                def hold():
                    dve.memset(held[:, :], 0.0)

                def top16(what, values, n, out, index, step):
                    at = slice(8 * (what // 3), 8 * (what // 3) + 8)
                    hold()
                    for j in range(n):
                        if what % 3 == 0:
                            ins = dve.max(out[:, j, at], values[:, j, :])
                        elif what % 3 == 1:
                            ins = dve.max_index(index[:, j, at], out[:, j, at], values[:, j, :])
                        else:
                            ins = dve.match_replace(values[:, j, :], out[:, j, at], values[:, j, :], NEG)
                    step(ins)

                def choose(j, k, step, step2):
                    if j == 0:
                        dve.wait_ge(s.S_loaded, k * 16 + 16 + CREDIT)
                    if j < 5:
                        top16(j, S, G2, m, ix, step)
                    elif j == 5:
                        step(dve.tensor_copy(ixf[:, :, :], ix[:, :, :]))
                        step(dve.tensor_tensor(cand[:, :, :].rearrange("p h (x y) -> p h x y", x=TOPK),
                                               mv[:, :, 0, :].unsqueeze(3).broadcast_to(square),
                                               mv[:, :, 1, :].unsqueeze(2).broadcast_to(square), ALU.add))
                    elif j < 10:
                        top16(j - 6, cand, HP, best, jx, step)
                    elif j == 10:
                        top16(4, cand, HP, best, jx, step2)
                        dve.tensor_tensor(d[:, :, :], best[:, :, :], best[:, :, 0:1].broadcast_to([P, HP, TOPK]), ALU.subtract
                                          ).then_inc(s.diff_ready, 1)
                    elif j == 11:
                        jf = jx[:, :, :].rearrange("p h k -> p (h k)")
                        step2(dve.tensor_scalar(part[:, 0, :], jf, 4, None, ALU.logical_shift_right))
                        step2(dve.tensor_scalar(part[:, 1, :], jf, TOPK - 1, None, ALU.bitwise_and))
                        step2(dve.tensor_copy(partf[:, :, :], part[:, :, :]))
                    elif j < 14:
                        c = j - 12
                        hv = hot.rearrange("p (h k) x -> p h k x", h=HP)
                        step2(dve.tensor_tensor(hot, partf[:, c, :].unsqueeze(2).broadcast_to([P, SLOTS, TOPK]),
                                                iota[:, :].unsqueeze(1).broadcast_to([P, SLOTS, TOPK]), ALU.is_equal))
                        step2(dve.tensor_tensor(hv, hv, iv[:, :, c, :].unsqueeze(2).broadcast_to(square), ALU.mult))
                        step2(dve.tensor_reduce(num[:, c, :], hot, AX.X, ALU.add))
                    elif j == 14:
                        step2(dve.scalar_tensor_tensor(out=ef[:, :], in0=num[:, 0, :], scalar=float(NK), in1=num[:, 1, :],
                                                       op0=ALU.mult, op1=ALU.add))
                        dve.wait_ge(s.chosen_stored, k * 32 + CREDIT)
                        dve.tensor_copy(eid[:, :], ef[:, :])
                        dve.wait_ge(s.exp_ready, k + 1 + CREDIT)
                        dve.tensor_reduce(sm[:, :], ex[:, :, :], AX.X, ALU.add).then_inc(s.sum_ready, 1)
                        dve.wait_ge(s.sum_ready, k + 1 + CREDIT)
                        dve.reciprocal(sm[:, :], sm[:, :]).then_inc(s.sum_inverted, 1)
                        dve.wait_ge(s.sum_inverted, k + 1 + CREDIT)
                        dve.tensor_tensor(gate[:, :, :], ex[:, :, :], sm[:, :].unsqueeze(2).broadcast_to([P, HP, TOPK]),
                                          ALU.mult).then_inc(s.chosen, 1)

                dve.wait_ge(s.constants_loaded, 48 + CREDIT)
                for t, v, u, k in turns(dve):
                    step = Steps(dve, s.steps, t + 2, STEPS)
                    step2 = Steps(dve, s.steps2, t + 2, STEPS2)
                    if u:
                        dve.wait_ge(s.x_loaded, t * 16 + 16 + 16 * (P // u.n) + CREDIT)
                        dve.wait_ge(s.gelu_ready, t + 1 + CREDIT)
                    for j in range(NGR):
                        if u and j * GROUP < u.slots:
                            dve.wait_ge(u_loaded[j % 2], t * TILE + TILE + FULL * (j // 2 + 1))
                            for e in range(j * GROUP, (j + 1) * GROUP):
                                ins = dve.tensor_tensor_reduce(out=ub[e % RING][:, :], in0=ub[e % RING][:, :], in1=x[:, :],
                                                               scale=1.0, scalar=0.0, op0=ALU.mult, op1=ALU.add,
                                                               accum_out=act_in[:, e:e + 1])
                            ins.then_inc(s.dotted, 1)
                        if k:
                            choose(j, t + 2, step, step2)
                    if k:
                        step.end()
                        step2.end()
                    if u:
                        dve.wait_ge(s.gelu_ready, t + 2 + CREDIT)
                        dve.wait_ge(s.gate_loaded, t * 16 + 16 + 16 * (P // u.n) + CREDIT)
                        if v:
                            dve.wait_ge(s.diag_ready, t * NGR + NGR + CREDIT)
                        dve.tensor_tensor(coef[:, 0:u.slots], gl[:, 0:u.slots], gate_u[:, 0:u.slots], ALU.mult
                                          ).then_inc(s.coef_ready, 1)
                    if v:
                        dve.wait_ge(s.v_used, t * NGR + v.slots // GROUP + CREDIT)
                        dve.wait_ge(s.h_loaded, t * 16 + 16 + CREDIT)
                        for c in range(2):
                            half = slice(c * 512, (c + 1) * 512)
                            dve.tensor_tensor(h[0:v.n, half], acc[c][0:v.n, :], h[0:v.n, half], ALU.add).then_inc(s.h_added, 1)
                        dve.wait_ge(s.squares_summed, t + 1 + CREDIT)
                        dve.tensor_scalar(ms[0:v.n, :], ss[0:v.n, :], 1.0 / D, EPS, ALU.mult, ALU.add).then_inc(s.mean_ready, 1)
                        dve.wait_ge(s.root_ready, t + 1 + CREDIT)
                        dve.reciprocal(rstd[0:v.n, :], rt[0:v.n, :]).then_inc(s.rstd_ready, 1)
                        dve.wait_ge(s.rstd_ready, t + 1 + CREDIT)
                        dve.wait_ge(s.stored, t * 16 + CREDIT)
                        dve.scalar_tensor_tensor(out=y[0:v.n, :], in0=h[0:v.n, :], scalar=rstd[0:v.n, 0:1], in1=g[0:v.n, :],
                                                 op0=ALU.mult, op1=ALU.mult).then_inc(s.y_ready, 1)

            @block.scalar
            def _(act):
                def exp(k):
                    act.wait_ge(s.diff_ready, k + 1 + CREDIT)
                    act.activation(ex[:, :, :], d[:, :, :], ACT.Exp).then_inc(s.exp_ready, 1)

                act.wait_ge(s.constants_loaded, 48 + CREDIT)
                for t, v, u, k in turns(act):
                    for j in range(NGR):
                        if v and j * GROUP < v.slots:
                            act.wait_ge(s.v_used, t * NGR + max(j - 1, 0) + CREDIT)
                            for e in range(j * GROUP, (j + 1) * GROUP):
                                eye = r.ident if v == PROMPT else fold[:, :]
                                ins = act.activation(dg[e % RING][:, 0:v.n], eye, ACT.Copy, scale=coef[:, e:e + 1])
                            ins.then_inc(s.diag_ready, 1)
                        if k and j == NGR - 4:
                            exp(t + 2)
                    if u:
                        act.wait_ge(s.dotted, t * NGR + NGR + u.slots // GROUP + CREDIT)
                        act.wait_ge(s.coef_ready, t + 1 + CREDIT)
                        act.activation(gl[:, 0:u.slots], act_in[:, 0:u.slots], ACT.Gelu).then_inc(s.gelu_ready, 1)
                    if v:
                        act.wait_ge(s.h_added, t * 2 + 2 + CREDIT)
                        act.wait_ge(s.stored, t * 16 + CREDIT)
                        act.activation(y[0:v.n, :], h[0:v.n, :], ACT.Square, accum_out=ss[0:v.n, :]).then_inc(s.squares_summed, 1)
                        act.wait_ge(s.mean_ready, t + 1 + CREDIT)
                        act.activation(rt[0:v.n, :], ms[0:v.n, :], ACT.Sqrt).then_inc(s.root_ready, 1)
                        act.wait_ge(s.y_ready, t + 1 + CREDIT)
                        dst = a.y_prompt[ds(t * P, P), :] if v == PROMPT else a.y_sample
                        act.dma_start(dst, y[0:v.n, :]).then_inc(s.stored, 16)
                    if u:
                        act.wait_ge(s.coef_ready, t + 2 + CREDIT)
                act.wait_ge(s.stored, 16 * NT + CREDIT)

            @block.tensor
            def _(pe):
                for t, v, u, k in turns(pe):
                    if v:
                        pe.wait_ge(s.h_added, t * 2 + CREDIT)
                        for j in range(v.slots // GROUP):
                            pe.wait_ge(v_loaded[j % 2], t * TILE + FULL * (j // 2 + 1))
                            pe.wait_ge(s.diag_ready, t * NGR + j + 1 + CREDIT)
                            for e in range(j * GROUP, (j + 1) * GROUP):
                                for c in range(2):
                                    mm = pe.matmul(acc[c][0:v.n, :], dg[e % RING][:, 0:v.n], vb[e % RING][:, c * 512:(c + 1) * 512],
                                                   start=(e == 0), stop=(e == v.slots - 1))
                            mm.then_inc(s.v_used, 1)




OUTS = [(1, SEQ, D), (DB, DT, D), (1, 1, SEQ, ROW), (1, 1, 128, 2, HD, E), (1, 1, 512, 2, HD, E), (1, 1, SEQ, 2, HD, E),
        (1, 1, MEM, 2, HM, EM), (1, DB, DT, ROW), (1, DB, 128, 2, HD, E), (1, DB, 512, 2, HD, E), (1, DB, 2048, 2, HD, E)]


def keep_old_rows(nc, a, stored):
    for g in range(NG):
        L = GROUPS[g][0]
        for b in range(DB):
            nc.scalar.dma_start(a.new_dil_sample[g][b, 0:L - DT].rearrange("l j c -> l (j c)"),
                                a.cache_dil[g][b, DT:L].rearrange("l j c -> l (j c)")).then_inc(stored, 16)
    return 16 * NG * DB


def keep_new_rows(nc, a, stored):
    dil3 = a.dil.rearrange("t (j g c) -> t j g c", j=3, g=NG)
    nc.sync.dma_start(a.new_mla_prompt, a.rows[0:SEQ, :]).then_inc(stored, 16)
    nc.sync.dma_start(a.new_mla_sample, a.rows[SEQ:SEQ + NS, :]).then_inc(stored, 16)
    for g in range(NG):
        keep = min(GROUPS[g][0], SEQ)
        nc.sync.dma_start(a.new_dil_prompt[g], dil3[SEQ - keep:SEQ, 1:3, g, :]).then_inc(stored, 16)
        L = GROUPS[g][0]
        for b in range(DB):
            nc.sync.dma_start(a.new_dil_sample[g][b, L - DT:L], dil3[SEQ + b * DT:SEQ + (b + 1) * DT, 1:3, g, :]
                              ).then_inc(stored, 16)
    return 16 * (2 + NG * (1 + DB))


def build(nc, i, outs):
    def dram(name, shape, dt=F32):
        return nc.dram_tensor(name, shape, dt).ap()

    a = Dram()
    a.x = i["x"]
    a.mem = i["mem"]
    a.cache_mla = i["cache_mla"]
    a.page_table = i["page_table"]
    a.cache_mem = i["cache_mem"]
    a.w_in = i["w_in"]
    a.g_attn = i["g_attn"]
    a.g_q_lora = i["g_q_lora"]
    a.w_q_up = i["w_q_up"]
    a.g_kv_lora = i["g_kv_lora"]
    a.w_kv_up = i["w_kv_up"]
    a.w_o_mla = i["w_o_mla"]
    a.w_o_dil = i["w_o_dil"]
    a.w_mem_kv = i["w_mem_kv"]
    a.g_mem = i["g_mem"]
    a.w_o_mem = i["w_o_mem"]
    a.w_out = i["w_out"]
    a.g_ffn = i["g_ffn"]
    a.w_peer_q = i["w_peer_q"]
    a.peer_sub_keys = i["peer_sub_keys"]
    a.peer_u = i["peer_u"]
    a.peer_v = i["peer_v"]
    a.g_final = i["g_final"]
    a.identity = i["identity"]
    a.rope_mla = i["rope_mla"]
    a.rope_dil = i["rope_dil"]
    a.masks_dil = i["masks_dil"]
    a.mask_mla = i["mask_mla"]
    a.mask_new = i["mask_new"]
    a.iota16 = i["iota16"]
    a.fold = i["fold"]
    a.cache_dil = [v.rearrange("a b l j h e -> (a b) l j (h e)") for v in (i["cache_dil0"], i["cache_dil1"], i["cache_dil2"])]
    a.new_mla_prompt = outs[2].rearrange("a b s c -> (a b s) c")
    a.new_dil_prompt = [v.rearrange("a b s j h e -> (a b s) j (h e)") for v in outs[3:6]]
    a.mem_kv = outs[6].rearrange("a b m j h e -> (a b m) (j h e)")
    a.new_mla_sample = outs[7].rearrange("a b s c -> (a b s) c")
    a.new_dil_sample = [v.rearrange("a b l j h e -> (a b) l j (h e)") for v in outs[8:11]]
    a.proj = dram("proj_scratch", (T, PROJ))
    a.rows = dram("rows_scratch", (T, ROW))
    a.qT = dram("qT_scratch", (QK, H_MLA, T))
    a.dil = dram("dil_scratch", (T, DIL_COLS))
    a.dilo = dram("dilo_scratch", (NG, SEQ, GE + 2 * HD))
    a.omla = dram("omla_scratch", (T, H_MLA * V_DIM))
    a.h = dram("h_scratch", (T, D))
    a.xn2 = dram("xn2_scratch", (T, D))
    a.scores = dram("scores_scratch", (T, 2 * HP, NK))
    a.experts = dram("experts_scratch", (T, SLOTS), U32)
    a.gates = dram("gates_scratch", (T, SLOTS))
    a.y_prompt = outs[0].rearrange("a s d -> (a s) d")
    a.y_sample = outs[1].rearrange("b t d -> (b t) d")

    with ExitStack() as ctx, nc.semaphore("old_rows_stored") as old_rows_stored, nc.semaphore("new_rows_stored") as new_rows_stored:
        keep = lambda n, shape, dt=F32: ctx.enter_context(nc.sbuf_tensor(n, shape, dt))
        ident = keep("ident", [P, P])
        r = Resident()
        r.ident = ident[:, :]
        ident_loaded = ctx.enter_context(nc.semaphore("ident_loaded"))
        with nc.Block() as block:
            @block.sync
            def _(sp):
                sp.dma_start(ident[:, :], a.identity).then_inc(ident_loaded, 16)
                sp.wait_ge(ident_loaded, 16)
        with nc.sbuf_tensor("memT", [P, KD, MEM], F32) as memT:
            norm_rows(nc, "nmem", a.mem, a.g_mem, MEM // P, r.ident, memT)
            product_rows(nc, "pmem", memT, a.w_mem_kv, 2 * HM * EM, 512, MEM // P, a.mem_kv)
        xT = ctx.enter_context(nc.sbuf_tensor("xT", [P, KD, T], F32))
        norm_rows(nc, "nx", a.x, a.g_attn, NT, r.ident, xT)
        n_old = keep_old_rows(nc, a, old_rows_stored)
        product_rows(nc, "proj", xT, a.w_in[:, 0:PROJ], PROJ, PROJ // 8, NT, a.proj)
        with ExitStack() as turned:
            r.oT_mla = keep("oT_mla", [P, 4, T])
            r.oT_dil = keep("oT_dil", [P, 2, T])
            r.oT_mem = keep("oT_mem", [P, HM, T])
            r.ckvT = turned.enter_context(nc.sbuf_tensor("ckvT", [P, 2, T], F32))
            r.kpeT = turned.enter_context(nc.sbuf_tensor("kpeT", [P, T], F32))
            latents(nc, a, r)
            n_new = keep_new_rows(nc, a, new_rows_stored)
            memory_attention(nc, a, r)
            dilated_attention(nc, a, r)
            latent_attention(nc, a, r)
            combine_groups(nc, a, r)
            sample_latent_attention(nc, a, r)
        sample_dilated_and_memory_attention(nc, a, r)
        mT = keep("mT", [P, KD, T])
        mix_branches(nc, a, r, xT, mT)
        product_rows(nc, "out", mT, a.w_out, D, 512, NT, a.h, add=a.x)
        nc.sync.wait_ge(old_rows_stored, n_old)
        nc.sync.wait_ge(new_rows_stored, n_new)
    with nc.sbuf_tensor("ident2", [P, P], F32) as ident:
        r = Resident()
        r.ident = ident[:, :]
        with nc.semaphore("ident2_loaded") as ident_loaded, nc.Block() as block:
            @block.sync
            def _(sp):
                sp.dma_start(ident[:, :], a.identity).then_inc(ident_loaded, 16)
                sp.wait_ge(ident_loaded, 16)
        with nc.sbuf_tensor("xT2", [P, KD, T], F32) as xT:
            norm_rows(nc, "nh", a.h, a.g_ffn, NT, r.ident, xT, a.xn2)
            peer_scores(nc, a, r, xT)
        peer_experts(nc, a, r)


def rope_table(dim):
    half = dim // 2
    inv = np.float32(THETA) ** (-np.arange(half, dtype=np.float32) * np.float32(2.0 / dim))
    pos = np.zeros(T, np.float32)
    pos[0:SEQ] = np.arange(SEQ)
    pos[SEQ:SEQ + NS] = PAST + np.arange(NS) % DT
    ang = pos[:, None] * inv[None, :]
    return np.concatenate([np.cos(ang), np.sin(ang)], axis=1).astype(np.float32)


def dilated_masks():
    q, k = np.arange(P)[:, None], np.arange(P)[None, :]
    m = np.full((NG * NTP, P, 2 * P), NEG, np.float32)
    own, before = k <= q, k >= q
    for t in range(NTP):
        m[t, :, P:] = np.where(own, 0, NEG)
        m[NTP + t, :, P:] = np.where(own, 0, NEG)
        m[2 * NTP + t, :, P:] = np.where(own & (q // 64 == k // 64), 0, NEG)
        if t > 0:
            m[t, :, :P] = np.where(before, 0, NEG)
        if t % 2:
            m[NTP + t, :, :P] = np.where(before, 0, NEG)
    return m


def constants():
    q, k = np.arange(P)[:, None], np.arange(P)[None, :]
    row = np.arange(P)[:, None]
    return {
        "identity": np.eye(P, dtype=np.float32),
        "rope_mla": rope_table(ROPE),
        "rope_dil": rope_table(ROT),
        "masks_dil": dilated_masks(),
        "mask_mla": np.where(k <= q, 0, NEG).astype(np.float32),
        "mask_new": np.where(np.arange(DT)[None, :] <= row % DT, 0, NEG).astype(np.float32),
        "fold": np.tile(np.eye(NS, dtype=np.float32), (P // NS, 1)),
        "iota16": np.broadcast_to(np.arange(TOPK, dtype=np.float32), (P, TOPK)).copy(),
    }


def kernel(**inputs):
    import concourse.bacc as bacc
    from concourse.bass_utils import run_bass_kernel_spmd

    given = {k: np.asarray(v) for k, v in inputs.items()}
    layer = {k: v[0] for k, v in given.items() if k.startswith(("w_", "g_", "peer_")) and k != "g_final"}
    layer["g_final"] = given["g_final"]
    arrays = {
        "x": np.concatenate([given["x_prompt"][0], given["x_sample"].reshape(NS, D),
                             np.zeros((T - SEQ - NS, D), np.float32)]),
        "mem": given["mem_prompt"][0],
        "cache_mla": given["cache_mla"][0],
        "page_table": given["page_table"].reshape(1, DB * N_PAGES),
        "cache_mem": given["cache_mem"][0].reshape(DB, MEM, 2 * HM * EM),
        **{f"cache_dil{g}": given[f"cache_dil{g}"] for g in range(NG)},
        **layer,
        **constants(),
    }
    nc = bacc.Bacc("TRN2", target_bir_lowering=False, num_devices=1)
    feed, ins = {}, {}
    for name, v in arrays.items():
        feed[f"in_{name}"] = np.ascontiguousarray(v)
        ins[name] = nc.dram_tensor(f"in_{name}", v.shape, mybir.dt.from_np(v.dtype), kind="ExternalInput").ap()
    outs = [nc.dram_tensor(f"out_{n}", shape, F32, kind="ExternalOutput").ap() for n, shape in enumerate(OUTS)]
    build(nc, ins, outs)
    got = run_bass_kernel_spmd(nc, [feed], core_ids=[0])
    return tuple(got.results[0][f"out_{n}"] for n in range(len(OUTS)))
```
